# Optimizing a Trainium2 kernel written in Bass

```python
import math
import jax, jax.numpy as jnp
from jax import lax
import numpy as np

D_MODEL = 1024
BATCH = 1
SEQ = 1024
DEPTH = 1
DEC_BATCH = 8
DEC_SEQ = 8
PAST_LEN = 8192
PAGE_SIZE = 128

D_MIX = 2 * D_MODEL
CONV_K = 4
CHUNK = 64
DN_HEADS = 8
DN_DK = 128
DN_DV = 128
DN_WIDTH = DN_HEADS * DN_DV
DN_QKV = 2 * DN_HEADS * DN_DK + DN_WIDTH
SSM_HEADDIM = 64
SSM_HEADS = (D_MIX - DN_WIDTH) // SSM_HEADDIM
SSM_GROUPS = 2
SSM_HPG = SSM_HEADS // SSM_GROUPS
SSM_STATE = 128
SSM_WIDTH = SSM_HEADS * SSM_HEADDIM
SSM_XBC = SSM_WIDTH + 2 * SSM_GROUPS * SSM_STATE
IN_SIZES = (DN_QKV, SSM_XBC, DN_WIDTH, SSM_WIDTH, DN_HEADS, DN_HEADS, SSM_HEADS)
D_IN_PROJ = DN_QKV + SSM_XBC + DN_WIDTH + SSM_WIDTH + 2 * DN_HEADS + SSM_HEADS
MEM_LEN = 256
MEM_HEADS = 4
MEM_HD = D_MODEL // MEM_HEADS
PEER_HEADS = 8
PEER_NKEYS = 128
PEER_EXPERTS = PEER_NKEYS * PEER_NKEYS
PEER_TOPK = 16
PEER_DKEY = 256
PEER_HALF = PEER_DKEY // 2
PEER_BLOCK = 256
EPS = 1e-6

kernel_name = 'hybrid_deltanet_ssd_peer_decoder'

def rmsnorm(x, w):
    xf = x.astype(jnp.float32)
    y = xf * lax.rsqrt(jnp.mean(xf * xf, axis=-1, keepdims=True) + EPS)
    return (y * w.astype(jnp.float32)).astype(x.dtype)

def l2norm(x):
    xf = x.astype(jnp.float32)
    return (xf * lax.rsqrt(jnp.sum(xf * xf, axis=-1, keepdims=True) + EPS)).astype(x.dtype)

def split_cols(t, sizes):
    out, o = [], 0
    for s in sizes:
        out.append(t[..., o:o + s])
        o += s
    return out

def causal_dwconv(x, buf, w, b=None):
    xp = jnp.concatenate([buf.astype(x.dtype), x], axis=1)
    c = x.shape[-1]
    y = lax.conv_general_dilated(xp, w[:, None, :], window_strides=(1,), padding='VALID',
                                 dimension_numbers=('NWC', 'WIO', 'NWC'), feature_group_count=c)
    if b is not None:
        y = y + b
    return y, xp[:, -(CONV_K - 1):]

def _pad_time(t, pad):
    return jnp.pad(t, [(0, 0), (0, pad)] + [(0, 0)] * (t.ndim - 2))

def _to_chunks(t, nc):
    b = t.shape[0]
    t = t.reshape((b, nc, CHUNK) + t.shape[2:])
    return t.transpose((1, 0, 3, 2) + tuple(range(4, t.ndim)))

def gated_delta_rule(q, k, v, beta, g, s0):
    f32 = jnp.float32
    b, l, h, _ = q.shape
    dv = v.shape[-1]
    nc = -(-l // CHUNK)
    pad = nc * CHUNK - l
    q, k, v, beta, g = [_to_chunks(_pad_time(t.astype(f32), pad), nc) for t in (q, k, v, beta, g)]
    gc = jnp.cumsum(g, axis=-1)
    incl = jnp.tril(jnp.ones((CHUNK, CHUNK), bool))
    strict = jnp.tril(jnp.ones((CHUNK, CHUNK), bool), -1)
    diff = gc[..., :, None] - gc[..., None, :]
    decay = jnp.where(incl, jnp.exp(jnp.where(incl, diff, 0.0)), 0.0)
    kb = k * beta[..., None]
    lower = jnp.where(strict, jnp.einsum('nbhid,nbhjd->nbhij', kb, k) * decay, 0.0)
    rhs = jnp.concatenate([v * beta[..., None], kb * jnp.exp(gc)[..., None]], axis=-1)
    uw = lax.linalg.triangular_solve(jnp.eye(CHUNK, dtype=f32) + lower, rhs,
                                     left_side=True, lower=True, unit_diagonal=True)
    u, w = uw[..., :dv], uw[..., dv:]
    attn = jnp.einsum('nbhid,nbhjd->nbhij', q, k) * decay
    q_dec = q * jnp.exp(gc)[..., None]
    k_dec = k * jnp.exp(gc[..., -1:] - gc)[..., None]
    g_tot = jnp.exp(gc[..., -1])

    def step(s, inp):
        u_c, w_c, qd_c, kd_c, a_c, gt_c = inp
        v_new = u_c - jnp.einsum('bhcd,bhde->bhce', w_c, s)
        o_c = jnp.einsum('bhcd,bhde->bhce', qd_c, s) + jnp.einsum('bhij,bhje->bhie', a_c, v_new)
        s = s * gt_c[..., None, None] + jnp.einsum('bhcd,bhce->bhde', kd_c, v_new)
        return s, o_c

    s, o = lax.scan(step, s0.astype(f32), (u, w, q_dec, k_dec, attn, g_tot))
    o = o.transpose(1, 0, 3, 2, 4).reshape(b, nc * CHUNK, h, dv)[:, :l]
    return o, s

def ssd_scan(x, dt, a_head, bm, cm, s0):
    f32 = jnp.float32
    b, l, ng, ne, p = x.shape
    n = bm.shape[-1]
    nc = -(-l // CHUNK)
    pad = nc * CHUNK - l
    dt = dt.astype(f32)
    xd = _pad_time(x.astype(f32) * dt[..., None], pad).reshape(b, nc, CHUNK, ng, ne, p)
    ac = _pad_time(dt * a_head, pad).reshape(b, nc, CHUNK, ng, ne).transpose(0, 1, 3, 4, 2)
    bc = _pad_time(bm.astype(f32), pad).reshape(b, nc, CHUNK, ng, n)
    cc = _pad_time(cm.astype(f32), pad).reshape(b, nc, CHUNK, ng, n)
    acs = jnp.cumsum(ac, axis=-1)
    incl = jnp.tril(jnp.ones((CHUNK, CHUNK), bool))
    diff = acs[..., :, None] - acs[..., None, :]
    lmat = jnp.where(incl, jnp.exp(jnp.where(incl, diff, 0.0)), 0.0)
    cb = jnp.einsum('bclgn,bcsgn->bcgls', cc, bc)
    y_diag = jnp.einsum('bcgls,bcgels,bcsgep->bclgep', cb, lmat, xd)
    ends = jnp.exp(acs[..., -1:] - acs)
    states = jnp.einsum('bclgn,bcgel,bclgep->bcgepn', bc, ends, xd)
    chunk_decay = jnp.exp(acs[..., -1])

    def step(hs, inp):
        st, dc = inp
        return hs * dc[..., None, None] + st, hs

    s, prev = lax.scan(step, s0.astype(f32), (jnp.moveaxis(states, 1, 0), jnp.moveaxis(chunk_decay, 1, 0)))
    prev = jnp.moveaxis(prev, 0, 1)
    y_off = jnp.einsum('bclgn,bcgepn,bcgel->bclgep', cc, prev, jnp.exp(acs))
    y = (y_diag + y_off).reshape(b, nc * CHUNK, ng, ne, p)[:, :l]
    return y, s

def memory_kv(mem, g_mem, w_mkv):
    b, m, _ = mem.shape
    mk, mv = split_cols(rmsnorm(mem, g_mem) @ w_mkv, (D_MODEL, D_MODEL))
    return mk.reshape(b, m, MEM_HEADS, MEM_HD), mv.reshape(b, m, MEM_HEADS, MEM_HD)

def memory_cross_attention(c, mem_k, mem_v, w_xq, w_xo):
    b, l, _ = c.shape
    q = (c @ w_xq).reshape(b, l, MEM_HEADS, MEM_HD)
    s = jnp.einsum('blhd,bmhd->bhlm', q, mem_k.astype(c.dtype)).astype(jnp.float32) * (MEM_HD ** -0.5)
    pr = jax.nn.softmax(s, axis=-1).astype(c.dtype)
    o = jnp.einsum('bhlm,bmhd->blhd', pr, mem_v.astype(c.dtype)).reshape(b, l, D_MODEL)
    return o @ w_xo

def peer_ffn(h, w_pq, sub_keys, peer_u, peer_v):
    bsz, l, d = h.shape
    n = bsz * l
    nb = -(-n // PEER_BLOCK)
    t = jnp.pad(h.reshape(n, d), ((0, nb * PEER_BLOCK - n), (0, 0))).reshape(nb, PEER_BLOCK, d)

    def block(tb):
        q = (tb @ w_pq).reshape(PEER_BLOCK, PEER_HEADS, 2, PEER_HALF)
        s = jnp.einsum('thcd,ckd->thck', q, sub_keys).astype(jnp.float32)
        s_top, i_top = lax.top_k(s, PEER_TOPK)
        cand_s = (s_top[:, :, 0, :, None] + s_top[:, :, 1, None, :]).reshape(PEER_BLOCK, PEER_HEADS, PEER_TOPK * PEER_TOPK)
        cand_i = (i_top[:, :, 0, :, None] * PEER_NKEYS + i_top[:, :, 1, None, :]).reshape(PEER_BLOCK, PEER_HEADS, PEER_TOPK * PEER_TOPK)
        best_s, pos = lax.top_k(cand_s, PEER_TOPK)
        idx = jnp.take_along_axis(cand_i, pos, axis=-1)
        gate = jax.nn.softmax(best_s, axis=-1).astype(tb.dtype)
        act = jax.nn.gelu(jnp.einsum('thkd,td->thk', peer_u[idx], tb), approximate=False)
        return jnp.einsum('thk,thkd->td', gate * act, peer_v[idx])

    out = lax.map(block, t)
    return out.reshape(nb * PEER_BLOCK, d)[:n].reshape(bsz, l, d)

def trunk_layer(x, mem_k, mem_v, dn_buf, dn_s, ssm_buf, ssm_s,
                g_mix, w_in, dn_conv_w, dn_A_log, dn_dt_bias, dn_norm_w,
                ssm_conv_w, ssm_conv_b, ssm_A_log, ssm_dt_bias, ssm_D, ssm_norm_w, w_out,
                g_xattn, w_xq, w_xo, g_ffn, w_pq, peer_sub_keys, peer_u, peer_v):
    f32 = jnp.float32
    bsz, l, _ = x.shape
    dtype = x.dtype
    proj = rmsnorm(x, g_mix) @ w_in
    qkv, xbc, z_dn, z_ssm, beta_raw, alpha_raw, dt_raw = split_cols(proj, IN_SIZES)
    qkv, dn_buf_new = causal_dwconv(qkv, dn_buf, dn_conv_w)
    q, k, v = split_cols(jax.nn.silu(qkv), (DN_HEADS * DN_DK, DN_HEADS * DN_DK, DN_WIDTH))
    q = l2norm(q.reshape(bsz, l, DN_HEADS, DN_DK)) * (DN_DK ** -0.5)
    k = l2norm(k.reshape(bsz, l, DN_HEADS, DN_DK))
    v = v.reshape(bsz, l, DN_HEADS, DN_DV)
    beta = jax.nn.sigmoid(beta_raw.astype(f32))
    g = -jnp.exp(dn_A_log.astype(f32)) * jax.nn.softplus(alpha_raw.astype(f32) + dn_dt_bias.astype(f32))
    o, dn_s_new = gated_delta_rule(q, k, v, beta, g, dn_s)
    o = rmsnorm(o.astype(dtype), dn_norm_w) * jax.nn.silu(z_dn.reshape(bsz, l, DN_HEADS, DN_DV))
    o_dn = o.reshape(bsz, l, DN_WIDTH)
    xbc, ssm_buf_new = causal_dwconv(xbc, ssm_buf, ssm_conv_w, ssm_conv_b)
    xs, bm, cm = split_cols(jax.nn.silu(xbc), (SSM_WIDTH, SSM_GROUPS * SSM_STATE, SSM_GROUPS * SSM_STATE))
    xs = xs.reshape(bsz, l, SSM_GROUPS, SSM_HPG, SSM_HEADDIM)
    bm = bm.reshape(bsz, l, SSM_GROUPS, SSM_STATE)
    cm = cm.reshape(bsz, l, SSM_GROUPS, SSM_STATE)
    dt = jax.nn.softplus(dt_raw.astype(f32) + ssm_dt_bias.astype(f32)).reshape(bsz, l, SSM_GROUPS, SSM_HPG)
    a_head = -jnp.exp(ssm_A_log.astype(f32)).reshape(SSM_GROUPS, SSM_HPG)
    y, ssm_s_new = ssd_scan(xs, dt, a_head, bm, cm,
                            ssm_s.reshape(bsz, SSM_GROUPS, SSM_HPG, SSM_HEADDIM, SSM_STATE))
    y = y + ssm_D.astype(f32).reshape(SSM_GROUPS, SSM_HPG)[..., None] * xs.astype(f32)
    y = y.astype(dtype) * jax.nn.silu(z_ssm.reshape(bsz, l, SSM_GROUPS, SSM_HPG, SSM_HEADDIM))
    y = rmsnorm(y.reshape(bsz, l, SSM_GROUPS, SSM_WIDTH // SSM_GROUPS), ssm_norm_w.reshape(SSM_GROUPS, -1))
    o_ssm = y.reshape(bsz, l, SSM_WIDTH)
    x = x + jnp.concatenate([o_dn, o_ssm], axis=-1) @ w_out
    x = x + memory_cross_attention(rmsnorm(x, g_xattn), mem_k, mem_v, w_xq, w_xo)
    x = x + peer_ffn(rmsnorm(x, g_ffn), w_pq, peer_sub_keys, peer_u, peer_v)
    ssm_s_out = ssm_s_new.reshape(bsz, SSM_HEADS, SSM_HEADDIM, SSM_STATE).astype(dtype)
    return x, dn_buf_new, dn_s_new.astype(dtype), ssm_buf_new, ssm_s_out

def setup_inputs(seed: int = 0) -> dict:
    key = jax.random.key(seed)
    ks = jax.random.split(key, 40)
    f32 = jnp.float32

    def nrm(i, shape, scale):
        return jax.random.normal(ks[i], shape, f32) * scale

    def gain(i, shape):
        return 1.0 + 0.05 * jax.random.normal(ks[i], shape, f32)

    def a_log(i, n):
        return jnp.log(jax.random.uniform(ks[i], (DEPTH, n), f32, 1.0, 16.0))

    def dt_bias(i, n):
        dt = jnp.exp(jax.random.uniform(ks[i], (DEPTH, n), f32, math.log(1e-3), math.log(1e-1)))
        return dt + jnp.log(-jnp.expm1(-dt))

    return {
        'x_prompt': nrm(0, (BATCH, SEQ, D_MODEL), 1.0),
        'x_sample': nrm(1, (DEC_BATCH, DEC_SEQ, D_MODEL), 1.0),
        'state_dn_conv': nrm(2, (DEPTH, DEC_BATCH, CONV_K - 1, DN_QKV), 1.0),
        'state_dn': nrm(3, (DEPTH, DEC_BATCH, DN_HEADS, DN_DK, DN_DV), 0.1),
        'state_ssm_conv': nrm(4, (DEPTH, DEC_BATCH, CONV_K - 1, SSM_XBC), 1.0),
        'state_ssm': nrm(5, (DEPTH, DEC_BATCH, SSM_HEADS, SSM_HEADDIM, SSM_STATE), 0.1),
        'cache_mem_k': nrm(6, (DEPTH, DEC_BATCH, MEM_LEN, MEM_HEADS, MEM_HD), 1.0),
        'cache_mem_v': nrm(7, (DEPTH, DEC_BATCH, MEM_LEN, MEM_HEADS, MEM_HD), 1.0),
        'mem_prompt': nrm(8, (BATCH, MEM_LEN, D_MODEL), 1.0),
        'g_mix': gain(9, (DEPTH, D_MODEL)),
        'w_in': nrm(10, (DEPTH, D_MODEL, D_IN_PROJ), D_MODEL ** -0.5),
        'dn_conv_w': nrm(11, (DEPTH, CONV_K, DN_QKV), CONV_K ** -0.5),
        'dn_A_log': a_log(12, DN_HEADS),
        'dn_dt_bias': dt_bias(13, DN_HEADS),
        'dn_norm_w': gain(14, (DEPTH, DN_DV)),
        'ssm_conv_w': nrm(15, (DEPTH, CONV_K, SSM_XBC), CONV_K ** -0.5),
        'ssm_conv_b': nrm(16, (DEPTH, SSM_XBC), 0.02),
        'ssm_A_log': a_log(17, SSM_HEADS),
        'ssm_dt_bias': dt_bias(18, SSM_HEADS),
        'ssm_D': gain(19, (DEPTH, SSM_HEADS)),
        'ssm_norm_w': gain(20, (DEPTH, SSM_WIDTH)),
        'w_out': nrm(21, (DEPTH, D_MIX, D_MODEL), D_MIX ** -0.5),
        'g_xattn': gain(22, (DEPTH, D_MODEL)),
        'g_mem': gain(23, (DEPTH, D_MODEL)),
        'w_xq': nrm(24, (DEPTH, D_MODEL, D_MODEL), D_MODEL ** -0.5),
        'w_mkv': nrm(25, (DEPTH, D_MODEL, 2 * D_MODEL), D_MODEL ** -0.5),
        'w_xo': nrm(26, (DEPTH, D_MODEL, D_MODEL), D_MODEL ** -0.5),
        'g_ffn': gain(27, (DEPTH, D_MODEL)),
        'w_pq': nrm(28, (DEPTH, D_MODEL, PEER_HEADS * PEER_DKEY), D_MODEL ** -0.5),
        'peer_sub_keys': nrm(29, (DEPTH, 2, PEER_NKEYS, PEER_HALF), PEER_HALF ** -0.5),
        'peer_u': nrm(30, (DEPTH, PEER_EXPERTS, D_MODEL), D_MODEL ** -0.5),
        'peer_v': nrm(31, (DEPTH, PEER_EXPERTS, D_MODEL), 0.25),
        'g_final': gain(32, (D_MODEL,)),
    }

def reference(x_prompt, x_sample, state_dn_conv, state_dn, state_ssm_conv, state_ssm,
              cache_mem_k, cache_mem_v, mem_prompt,
              g_mix, w_in, dn_conv_w, dn_A_log, dn_dt_bias, dn_norm_w,
              ssm_conv_w, ssm_conv_b, ssm_A_log, ssm_dt_bias, ssm_D, ssm_norm_w, w_out,
              g_xattn, g_mem, w_xq, w_mkv, w_xo, g_ffn, w_pq, peer_sub_keys, peer_u, peer_v, g_final):
    bp = x_prompt.shape[0]
    dtype = x_prompt.dtype
    hp, hs = x_prompt, x_sample
    p_dnc, p_dn, p_sc, p_ss, p_mk, p_mv = [], [], [], [], [], []
    s_dnc, s_dn, s_sc, s_ss = [], [], [], []
    for i in range(DEPTH):
        lp = (g_mix[i], w_in[i], dn_conv_w[i], dn_A_log[i], dn_dt_bias[i], dn_norm_w[i],
              ssm_conv_w[i], ssm_conv_b[i], ssm_A_log[i], ssm_dt_bias[i], ssm_D[i], ssm_norm_w[i], w_out[i],
              g_xattn[i], w_xq[i], w_xo[i], g_ffn[i], w_pq[i], peer_sub_keys[i], peer_u[i], peer_v[i])
        mk_p, mv_p = memory_kv(mem_prompt, g_mem[i], w_mkv[i])
        hp, dnc, dns, sc, ss = trunk_layer(
            hp, mk_p, mv_p,
            jnp.zeros((bp, CONV_K - 1, DN_QKV), dtype),
            jnp.zeros((bp, DN_HEADS, DN_DK, DN_DV), dtype),
            jnp.zeros((bp, CONV_K - 1, SSM_XBC), dtype),
            jnp.zeros((bp, SSM_HEADS, SSM_HEADDIM, SSM_STATE), dtype),
            *lp)
        p_dnc.append(dnc); p_dn.append(dns); p_sc.append(sc); p_ss.append(ss)
        p_mk.append(mk_p); p_mv.append(mv_p)
        hs, dnc, dns, sc, ss = trunk_layer(
            hs, cache_mem_k[i], cache_mem_v[i],
            state_dn_conv[i], state_dn[i], state_ssm_conv[i], state_ssm[i], *lp)
        s_dnc.append(dnc); s_dn.append(dns); s_sc.append(sc); s_ss.append(ss)
    y_prompt = rmsnorm(hp, g_final)
    y_sample = rmsnorm(hs, g_final)
    return (y_prompt, y_sample,
            jnp.stack(p_dnc), jnp.stack(p_dn), jnp.stack(p_sc), jnp.stack(p_ss),
            jnp.stack(p_mk), jnp.stack(p_mv),
            jnp.stack(s_dnc), jnp.stack(s_dn), jnp.stack(s_sc), jnp.stack(s_ss))


_drawn_inputs = setup_inputs


def setup_inputs(seed=0):
    import zlib

    import numpy as np

    out = dict(_drawn_inputs(seed))
    spreads = {}
    factors = {'dn_norm_w': 2.732, 'ssm_D': 2.785, 'g_xattn': 7.168, 'g_ffn': 3.591}
    for name, (base, spread) in spreads.items():
        noise = np.random.default_rng([zlib.crc32(name.encode()), seed]).standard_normal(out[name].shape)
        drawn = base * np.exp(spread * noise) if base else spread * noise
        out[name] = __import__('jax').numpy.asarray(drawn.astype(out[name].dtype))
    for name, factor in factors.items():
        out[name] = (out[name] * factor).astype(out[name].dtype)
    return out
```

```python
from contextlib import ExitStack

import concourse.bass as bass
import numpy as np
from concourse import mybir
from concourse.alu_op_type import AluOpType as ALU

F32 = mybir.dt.float32
U32 = mybir.dt.uint32
ACT = mybir.ActivationFunctionType
AX = mybir.AxisListType

D_MODEL, SEQ, SEQS, STEPS = 1024, 1024, 8, 8
SAMPLE = SEQS * STEPS
T = SEQ + SAMPLE
P = 128
CK = 128
NC = SEQ // CK + 1
TP = NC * CK
KT = D_MODEL // P
DN_HEADS, SSM_HEADS, SSM_GROUPS = 8, 16, 2
PAIRS = SSM_HEADS // 2
GP = PAIRS // SSM_GROUPS
HALF = 64
GATED = DN_HEADS + SSM_HEADS
MEM, MEM_HEADS = 256, 4
CONV = 4
CW = SEQ + CONV - 1 + SEQS * (STEPS + CONV - 1)
SOFF = SEQ + CONV - 1
SW = STEPS + CONV - 1
CHUNKS = [(0, 384), (384, 384), (768, 320)]
EPS = 1e-6
PHEADS, NKEYS, TOPK = 8, 128, 16


class Phase(ExitStack):

    def __init__(self, nc):
        super().__init__()
        self.nc, self.sems = nc, []

    def semaphore(self, name):
        self.sems.append(self.nc.alloc_semaphore(name))
        return self.sems[-1]

    def __exit__(self, *failure):
        if self.sems and failure[0] is None:
            self.nc.clear_and_free_semaphores(self.sems)
            self.nc.all_engine_barrier()
        return super().__exit__(*failure)


class Signal:

    def __init__(self, nc, ctx, name, per=1, unit=1, primed=False):
        self.sem = ctx.semaphore(name)
        self.per, self.unit, self.primed = per, unit, primed

    def at(self, n, turn=0):
        if isinstance(turn, int) and turn == 0 and not self.primed:
            return n * self.unit
        return turn * (self.per * self.unit) + (n + (self.per if self.primed else 0)) * self.unit


class Steps:

    def __init__(self, nc, ctx, name, per=0):
        self.sem = ctx.semaphore(name)
        self.per, self.n = per, 0

    def now(self, turn=0):
        return turn * self.per + self.n if self.per else self.n

    def step(self):
        self.n += 1
        return self.sem


def psum_banks(nc, ctx, name):
    return [ctx.enter_context(nc.psum_tensor(f"{name}_bank{i}", [P, 512], F32)) for i in range(8)]


def rmsnorm(nc, bank, name, src, dst, gain, ones, tokens, width):
    with Phase(nc) as ctx:
        sq = ctx.enter_context(nc.sbuf_tensor(f"{name}_squares", [P, 2, tokens], F32))
        rstd = ctx.enter_context(nc.sbuf_tensor(f"{name}_rstd", [P, tokens], F32))
        squared = Signal(nc, ctx, f"{name}_squared", KT)
        summed = Signal(nc, ctx, f"{name}_summed", KT)
        mean_ready = Signal(nc, ctx, f"{name}_mean_ready")
        root_ready = Signal(nc, ctx, f"{name}_root_ready")
        vec = Steps(nc, ctx, f"{name}_vector_steps")
        cols = CHUNKS if tokens == T else [(0, tokens)]
        with nc.Block() as block:
            @block.scalar
            def _(act):
                for k in range(KT):
                    if k >= 2:
                        act.wait_ge(summed.sem, summed.at(k - 1))
                    nc.scalar.activation(sq[:, k % 2, :], src[:, k, 0:tokens], ACT.Square).then_inc(squared.sem, 1)
                act.wait_ge(mean_ready.sem, 1)
                nc.scalar.activation(rstd[:, :], rstd[:, :], ACT.Sqrt).then_inc(root_ready.sem, 1)

            @block.tensor
            def _(pe):
                for k in range(KT):
                    pe.wait_ge(squared.sem, squared.at(k + 1))
                    for c, (a, n) in enumerate(cols):
                        mm = nc.tensor.matmul(bank[c][:, 0:n], ones, sq[:, k % 2, a:a + n],
                                              start=(k == 0), stop=(k == KT - 1))
                    mm.then_inc(summed.sem, 1)

            @block.vector
            def _(v):
                v.wait_ge(summed.sem, summed.at(KT))
                for c, (a, n) in enumerate(cols):
                    op = nc.vector.tensor_scalar(rstd[:, a:a + n], bank[c][:, 0:n], 1.0 / width, EPS,
                                                 ALU.mult, ALU.add)
                op.then_inc(mean_ready.sem, 1)
                v.wait_ge(root_ready.sem, 1)
                nc.vector.reciprocal(rstd[:, :], rstd[:, :]).then_inc(vec.step(), 1)
                v.wait_ge(vec.sem, vec.now())
                for k in range(KT):
                    nc.vector.scalar_tensor_tensor(dst[:, k, 0:tokens], src[:, k, 0:tokens], gain[:, k:k + 1],
                                                   rstd[:, :], ALU.mult, ALU.mult)


def gates(nc, bank, xn, w_small, tri, total, d, tab):
    G = GATED
    with Phase(nc) as ctx:
        def sb(name, shape):
            return ctx.enter_context(nc.sbuf_tensor(f"gates_{name}", shape, F32))
        raw, neg, e, u, z, sp = (sb(x, [P, NC, G]) for x in ("raw", "neg", "e", "u", "z", "sp"))
        bias, rate = sb("bias", [P, G]), sb("rate", [P, G])
        loaded = Signal(nc, ctx, "gates_loaded", 2, 16)
        projected = Signal(nc, ctx, "gates_projected")
        cumulated = Signal(nc, ctx, "gates_cumulated")
        vec = Steps(nc, ctx, "gates_vector_steps")
        sca = Steps(nc, ctx, "gates_scalar_steps")
        vector_at, scalar_at = {"neg": 4, "u": 5, "decays": 14, "sums": 15, "left": 16}, {"sigmoid": 1, "exp": 3, "ln": 4, "decayed": 6}
        with nc.Block() as block:
            @block.sync
            def _(sp_):
                sp_.dma_start(bias[:, :], d["gate_bias"].partition_broadcast(P)).then_inc(loaded.sem, 16)
                sp_.dma_start(rate[:, :], d["gate_rate"].partition_broadcast(P)).then_inc(loaded.sem, 16)

            @block.tensor
            def _(pe):
                for c in range(NC):
                    for k in range(KT):
                        mm = nc.tensor.matmul(bank[0][:, 32 * c:32 * c + 32], xn[:, k, CK * c:CK * c + CK],
                                              w_small[:, k, :], start=(k == 0), stop=(k == KT - 1))
                mm.then_inc(projected.sem, 1)
                pe.wait_ge(vec.sem, vector_at["decays"])
                for c in range(NC):
                    m = int(c == NC - 1)
                    nc.tensor.matmul(bank[1][:, G * c:G * c + G], tri[:, m, :], tab[:, 0, c, :], start=True, stop=True)
                    mm = nc.tensor.matmul(bank[2][:, G * c:G * c + G], total[:, m, :], tab[:, 0, c, :],
                                          start=True, stop=True)
                mm.then_inc(cumulated.sem, 1)

            @block.scalar
            def _(act):
                projection = bank[0][:, 0:32 * NC].rearrange("p (c h) -> p c h", h=32)
                act.wait_ge(projected.sem, 1)
                nc.scalar.activation(tab[:, 4, :, 0:DN_HEADS], projection[:, :, 0:DN_HEADS],
                                     ACT.Sigmoid).then_inc(sca.step(), 1)
                act.wait_ge(loaded.sem, loaded.at(2))
                nc.scalar.activation(rate[:, :], rate[:, :], ACT.Exp).then_inc(sca.step(), 1)
                act.wait_ge(vec.sem, vector_at["neg"])
                nc.scalar.activation(e[:, :, :], neg[:, :, :], ACT.Exp).then_inc(sca.step(), 1)
                assert sca.n == scalar_at["exp"]
                act.wait_ge(vec.sem, vector_at["u"])
                nc.scalar.activation(z[:, :, :], u[:, :, :], ACT.Ln).then_inc(sca.step(), 1)
                act.wait_ge(vec.sem, vector_at["sums"])
                nc.scalar.activation(tab[:, 2, :, :], tab[:, 1, :, :], ACT.Exp).then_inc(sca.step(), 1)
                act.wait_ge(vec.sem, vector_at["left"])
                nc.scalar.activation(tab[:, 3, :, :], tab[:, 3, :, :], ACT.Exp).then_inc(sca.step(), 1)
                assert sca.n == scalar_at["decayed"]

            @block.vector
            def _(v):
                projection = bank[0][:, 0:32 * NC].rearrange("p (c h) -> p c h", h=32)
                wide = lambda x: x[:, None, :].to_broadcast([P, NC, G])
                v.wait_ge(sca.sem, scalar_at["sigmoid"])
                v.wait_ge(loaded.sem, loaded.at(2))

                def then(op):
                    op.then_inc(vec.step(), 1)
                    v.wait_ge(vec.sem, vec.now())
                then(nc.vector.tensor_tensor(raw[:, :, :], projection[:, :, DN_HEADS:32], wide(bias), ALU.add))
                then(nc.vector.tensor_scalar(sp[:, :, :], raw[:, :, :], 0.0, None, ALU.max))
                then(nc.vector.tensor_scalar(neg[:, :, :], raw[:, :, :], -1.0, None, ALU.mult))
                then(nc.vector.tensor_tensor(neg[:, :, :], neg[:, :, :], raw[:, :, :], ALU.min))
                assert vec.n == vector_at["neg"]
                v.wait_ge(sca.sem, scalar_at["exp"])
                then(nc.vector.tensor_scalar(u[:, :, :], e[:, :, :], 1.0, None, ALU.add))
                then(nc.vector.tensor_scalar(raw[:, :, :], u[:, :, :], 1.0, None, ALU.is_equal))
                then(nc.vector.scalar_tensor_tensor(neg[:, :, :], u[:, :, :], -1.0, raw[:, :, :], ALU.add, ALU.add))
                then(nc.vector.reciprocal(neg[:, :, :], neg[:, :, :]))
                then(nc.vector.tensor_tensor(neg[:, :, :], neg[:, :, :], e[:, :, :], ALU.mult))
                then(nc.vector.tensor_tensor(raw[:, :, :], raw[:, :, :], e[:, :, :], ALU.mult))
                v.wait_ge(sca.sem, scalar_at["ln"])
                then(nc.vector.tensor_tensor(neg[:, :, :], neg[:, :, :], z[:, :, :], ALU.mult))
                then(nc.vector.tensor_tensor(neg[:, :, :], neg[:, :, :], raw[:, :, :], ALU.add))
                then(nc.vector.tensor_tensor(sp[:, :, :], sp[:, :, :], neg[:, :, :], ALU.add))
                then(nc.vector.scalar_tensor_tensor(tab[:, 0, :, :], sp[:, :, :], -1.0, wide(rate), ALU.mult, ALU.mult))
                assert vec.n == vector_at["decays"]
                v.wait_ge(cumulated.sem, 1)
                then(nc.vector.tensor_copy(tab[:, 1, :, :], bank[1][:, 0:NC * G].rearrange("p (c h) -> p c h", h=G)))
                then(nc.vector.tensor_tensor(tab[:, 3, :, :], bank[2][:, 0:NC * G].rearrange("p (c h) -> p c h", h=G),
                                             tab[:, 1, :, :], ALU.subtract))
                assert vec.n == vector_at["left"]
                then(nc.vector.tensor_copy(tab[:, 4, :, DN_HEADS:G], sp[:, :, DN_HEADS:G]))


def delta_net(nc, bank, xn, tab, d, const, mix, out):
    LEVELS = [1, 2, 4, 8, 16, 32, 64]
    A, B, KS_BANK, VN_BANK = bank[0:3], bank[4:7], bank[3], bank[7]
    with Phase(nc) as ctx:
        def sb(name, shape):
            return ctx.enter_context(nc.sbuf_tensor(f"dn_{name}", shape, F32))

        def signal(name, per=1, unit=1, primed=False):
            return Signal(nc, ctx, f"dn_{name}", per, unit, primed)
        w = sb("weights", [P, KT, 4, P])
        hist, cw, nw = sb("history", [P, 3, SEQS, 3]), sb("conv_w", [P, 3, CONV]), sb("norm_w", [P, 1])
        cbuf, acc, qkv = sb("padded", [P, 3, CW]), sb("conv", [P, 3, CW]), sb("qkv", [P, 3, TP])
        zs, cur, negbeg = sb("gate", [P, T]), sb("columns", [P, 5, NC]), sb("neg_beta_decay", [P, NC])
        tail = sb("conv_state", [P, 3, SEQS + 1, 3])
        root, erow = sb("root", [P, 2, T]), sb("row_decay", [P, TP])
        D, Ds, LT, attn, qdec = (sb(x, [P, TP]) for x in ("decay", "beta_decay", "lower", "attn", "q_decayed"))
        X, Y, BX, Vb, Kd = (sb(x, [P, TP]) for x in ("inv", "inv_t", "bx", "v_beta", "k_decayed"))
        BT = sb("block", [P, 2, TP])
        R, vn, S = sb("residual", [P, P]), sb("v_new", [P, 2, P]), sb("state", [P, 2, P])
        km, S0, vm, S1 = sb("k_masked", [P, SEQS * (P + STEPS)]), sb("sample_in", [P, SEQS, P]), sb("v_masked", [P, SEQS, P]), sb("sample_out", [P, SEQS, P])
        o = sb("o", [P, T])
        ident, ones = const["ident"], const["ones"]
        const = const | {"level": sb("level_masks", [P, 7, P]), "strict": sb("strict_mask", [P, TP])}

        loaded = signal("loaded", 4, 16)
        started = signal("inputs_once", 1, 16)
        cur_ready = signal("columns_ready")
        projected = signal("projected", 12)
        evacuated = signal("evacuated", 12)
        hist_in = signal("history_in")
        conv_done = signal("conv_done", 3)
        silu_done = signal("silu_done", 3)
        tail_ready = signal("tail_ready", 2)
        tail_stored = signal("conv_state_stored", 1, 16, primed=True)
        state_stored = signal("state_stored", 1, 16, primed=True)
        sample_stored = signal("sample_state_stored", 1, 16, primed=True)
        o_stored = signal("o_stored", 1, 16, primed=True)
        squared = signal("squared", 2)
        ssq_ready = signal("ssq_ready", 2)
        root_ready = signal("root_ready", 2)
        qk_ready = signal("qk_ready", 2)
        rows_ready = signal("rows_ready", 2)
        diff_ready = signal("diff_ready")
        erow_ready = signal("row_decay_ready")
        dexp_ready = signal("decay_exp_ready")
        rowb_used = signal("beta_rows_used")
        prod_ready = signal("products_ready", 2)
        lt_ready, attn_ready = signal("lower_ready"), signal("attn_ready")
        qdec_ready = signal("q_decayed_ready")
        turned = signal("tokens_turned", 2)
        v_turned_used = signal("v_turned_used")
        k_turned_used = signal("k_turned_used")
        y1_ready = signal("first_level_ready")
        x_turned = signal("x_turned", 3)
        x1_ready = signal("x_first_ready", 3)
        bt_ready = signal("block_ready", 7)
        bx_mm = signal("bx_product", 18)
        bx_ready = signal("bx_ready", 18)
        yx_mm = signal("yx_product", 18)
        y_ready = signal("inverse_ready", 18)
        ks_ready, r_ready = signal("ks_ready", 9), signal("residual_ready", 9)
        vn_mm, vn_ready = signal("v_new_product", 9), signal("v_new_ready", 9)
        ds_ready, s_ready = signal("state_product", 9), signal("state_ready", 10)
        o_ready, o_out = signal("o_product", 3), signal("o_out", 3)
        km_ready, vm_ready = signal("k_masked_ready"), signal("v_masked_ready")
        osq, o_ssq, o_root = signal("o_squared"), signal("o_summed"), signal("o_root", 1, 1, True)
        o_done = signal("o_done")
        zeroed = signal("zeroed", 2)
        VSTEPS = 17
        vec = Steps(nc, ctx, "dn_vector_steps", VSTEPS)

        def c3(t, n):
            return t[:, 384 * n:384 * n + 384]

        with nc.Block() as block:
            @block.sync
            def _(sp):
                sp.dma_start(nw[:, :], d["dn_norm_w"]).then_inc(started.sem, 16)
                sp.dma_start(const["level"][:, :, :], d["level"]).then_inc(started.sem, 16)
                sp.dma_start(const["strict"][:, :], d["strict"]).then_inc(started.sem, 16)
                with sp.Fori(0, DN_HEADS) as h:
                    sp.wait_ge(o_root.sem, o_root.at(1, h - 1))
                    sp.wait_ge(sample_stored.sem, sample_stored.at(1, h - 1))
                    sp.dma_start(w[:, :, :, :], d["w_dn"][bass.ds(h, 1)].rearrange("a p k j n -> (a p) k j n")).then_inc(loaded.sem, 16)
                    sp.dma_start(hist[:, :, :, :], d["dn_hist"][bass.ds(h, 1)].rearrange("a p j b n -> (a p) j b n")).then_inc(loaded.sem, 16)
                    sp.dma_start(cw[:, :, :], d["dn_conv_w"][bass.ds(h, 1)].rearrange("a p j n -> (a p) j n")).then_inc(loaded.sem, 16)
                    sp.dma_start(S0[:, :, :], d["dn_s0"][bass.ds(h, 1)].rearrange("a p b n -> (a p) b n")).then_inc(loaded.sem, 16)
                    sp.wait_ge(tail_ready.sem, tail_ready.at(2, h))
                    sp.dma_start(out["dn_conv"][bass.ds(h, 1)].rearrange("a p j b n -> (a p) j b n"), tail[:, :, :, :]).then_inc(tail_stored.sem, 16)
                    sp.wait_ge(s_ready.sem, s_ready.at(9, h))
                    sp.dma_start(out["dn_p"][bass.ds(h, 1)].rearrange("a p n -> (a p) n"), S[:, 0, :]).then_inc(state_stored.sem, 16)
                    sp.wait_ge(s_ready.sem, s_ready.at(10, h))
                    sp.dma_start(out["dn_s"][bass.ds(h, 1)].rearrange("a p b n -> (a p) b n"), S1[:, :, :]).then_inc(sample_stored.sem, 16)
                    sp.wait_ge(o_done.sem, o_done.at(1, h))
                    sp.dma_start(mix[bass.ds(h, 1)].rearrange("a p n -> (a p) n"), o[:, :]).then_inc(o_stored.sem, 16)
                for sig in (tail_stored, state_stored, sample_stored, o_stored):
                    sp.wait_ge(sig.sem, sig.at(1, DN_HEADS - 1))

            @block.tensor
            def _(pe):
                with pe.Fori(0, DN_HEADS) as h:
                    pe.wait_ge(loaded.sem, loaded.at(4, h))
                    pe.wait_ge(o_root.sem, o_root.at(1, h - 1))
                    for j in range(4):
                        for c, (a, n) in enumerate(CHUNKS):
                            if j >= 2:
                                pe.wait_ge(evacuated.sem, evacuated.at(3 * (j - 2) + c + 1, h))
                            for k in range(KT):
                                mm = nc.tensor.matmul((A, B)[j % 2][c][:, 0:n], w[:, k, j, :], xn[:, k, a:a + n],
                                                      start=(k == 0), stop=(k == KT - 1))
                            mm.then_inc(projected.sem, 1)
                    pe.wait_ge(cur_ready.sem, cur_ready.at(1, h))
                    for q, banks, mask in ((0, A, const["tri"]), (4, B, None)):
                        pe.wait_ge(evacuated.sem, evacuated.at(9 if q == 0 else 12, h))
                        for c in range(NC):
                            rhs = ident[:, :] if mask is None else mask[:, int(c == NC - 1), :]
                            mm = nc.tensor.matmul(banks[c // 3][:, CK * (c % 3):CK * (c % 3) + CK],
                                                  cur[:, q, c:c + 1].to_broadcast([P, P]), rhs, start=True, stop=True)
                        mm.then_inc(rows_ready.sem, 1)
                    for j, banks in ((0, A), (1, B)):
                        if j == 0:
                            pe.wait_ge(diff_ready.sem, diff_ready.at(1, h))
                            pe.wait_ge(erow_ready.sem, erow_ready.at(1, h))
                        else:
                            pe.wait_ge(rowb_used.sem, rowb_used.at(1, h))
                        pe.wait_ge(squared.sem, squared.at(j + 1, h))
                        for c, (a, n) in enumerate(CHUNKS):
                            mm = nc.tensor.matmul(banks[c][:, 0:n], ones[:, :], acc[:, j, a:a + n], start=True, stop=True)
                        mm.then_inc(ssq_ready.sem, 1)
                    pe.wait_ge(qk_ready.sem, qk_ready.at(2, h))
                    for j, banks in ((1, A), (0, B)):
                        pe.wait_ge(root_ready.sem, root_ready.at(1 if j else 2, h))
                        for c in range(NC):
                            s = slice(CK * c, CK * c + CK)
                            mm = nc.tensor.matmul(banks[c // 3][:, CK * (c % 3):CK * (c % 3) + CK], qkv[:, 1, s],
                                                  qkv[:, j, s], start=True, stop=True)
                        mm.then_inc(prod_ready.sem, 1)
                    for j, banks, free in ((2, A, lt_ready), (1, B, attn_ready)):
                        pe.wait_ge(silu_done.sem, silu_done.at(3, h))
                        pe.wait_ge(free.sem, free.at(1, h))
                        for c in range(NC):
                            mm = nc.tensor.transpose(banks[c // 3][:, CK * (c % 3):CK * (c % 3) + CK],
                                                     qkv[:, j, CK * c:CK * c + CK], ident[:, :])
                        mm.then_inc(turned.sem, 1)
                    pe.wait_ge(v_turned_used.sem, v_turned_used.at(1, h))
                    pe.wait_ge(k_turned_used.sem, k_turned_used.at(1, h))
                    pe.wait_ge(y1_ready.sem, y1_ready.at(1, h))
                    for t in range(3):
                        for c in range(3 * t, 3 * t + 3):
                            mm = nc.tensor.transpose(A[t][:, CK * (c % 3):CK * (c % 3) + CK],
                                                     Y[:, CK * c:CK * c + CK], ident[:, :])
                        mm.then_inc(x_turned.sem, 1)
                    for l in range(1, len(LEVELS)):
                        def block_times_x(t):
                            n = 3 * (l - 1) + t
                            if l == 1:
                                pe.wait_ge(x1_ready.sem, x1_ready.at(t + 1, h))
                            else:
                                pe.wait_ge(y_ready.sem, y_ready.at(n - 2, h))
                            pe.wait_ge(bt_ready.sem, bt_ready.at(l + 1, h))
                            for c in range(3 * t, 3 * t + 3):
                                s = slice(CK * c, CK * c + CK)
                                mm = nc.tensor.matmul(A[t][:, CK * (c % 3):CK * (c % 3) + CK], BT[:, l % 2, s], X[:, s],
                                                      start=True, stop=True)
                            mm.then_inc(bx_mm.sem, 1)

                        def corrections(t):
                            n = 3 * (l - 1) + t
                            pe.wait_ge(bx_ready.sem, bx_ready.at(n + 1, h))
                            for c in range(3 * t, 3 * t + 3):
                                s = slice(CK * c, CK * c + CK)
                                mm = nc.tensor.matmul(B[t][:, CK * (c % 3):CK * (c % 3) + CK], BX[:, s], Y[:, s],
                                                      start=True, stop=True)
                                if l < len(LEVELS) - 1:
                                    mm = nc.tensor.matmul(A[t][:, CK * (c % 3):CK * (c % 3) + CK], Y[:, s], BX[:, s],
                                                          start=True, stop=True)
                            mm.then_inc(yx_mm.sem, 1)
                        for t in range(3):
                            block_times_x(t)
                        for t in range(3):
                            corrections(t)
                    pe.wait_ge(y_ready.sem, y_ready.at(18, h))
                    pe.wait_ge(qdec_ready.sem, qdec_ready.at(1, h))
                    for c in range(NC):
                        s = slice(CK * c, CK * c + CK)
                        old = S[:, c % 2, :]
                        pe.wait_ge(s_ready.sem, s_ready.at(c + 1, h))
                        if c < NC - 1:
                            nc.tensor.matmul(KS_BANK[:, 0:P], qkv[:, 1, s], old, start=True, stop=True).then_inc(ks_ready.sem, 1)
                        else:
                            pe.wait_ge(km_ready.sem, km_ready.at(1, h))
                            for b in range(SEQS):
                                mm = nc.tensor.matmul(KS_BANK[:, 0:P], km[:, P * b:P * b + P], S0[:, b, :], start=(b == 0), stop=(b == SEQS - 1))
                            mm.then_inc(ks_ready.sem, 1)
                        pe.wait_ge(r_ready.sem, r_ready.at(c + 1, h))
                        nc.tensor.matmul(VN_BANK[:, 0:P], Y[:, s], R[:, :], start=True, stop=True).then_inc(vn_mm.sem, 1)
                        pe.wait_ge(vn_ready.sem, vn_ready.at(c + 1, h))
                        if c < NC - 1:
                            nc.tensor.matmul(A[0][:, 0:P], Kd[:, s], vn[:, c % 2, :], start=True, stop=True).then_inc(ds_ready.sem, 1)
                            to = B[c // 3][:, CK * (c % 3):CK * (c % 3) + CK]
                            nc.tensor.matmul(to, old, qdec[:, s], start=True, stop=False)
                            mm = nc.tensor.matmul(to, vn[:, c % 2, :], attn[:, s], start=False, stop=True)
                        else:
                            pe.wait_ge(vm_ready.sem, vm_ready.at(1, h))
                            for half in range(2):
                                mm = nc.tensor.matmul(A[1 + half][:, 0:512], Kd[:, s],
                                                      vm[:, 4 * half:4 * half + 4, :].rearrange("p b n -> p (b n)"),
                                                      start=True, stop=True)
                            mm.then_inc(ds_ready.sem, 1)
                            a = CK * (c % 3)
                            nc.tensor.matmul(B[2][:, a:a + SAMPLE], vn[:, c % 2, :], attn[:, SEQ:T], start=True, stop=False)
                            for b in range(SEQS):
                                mm = nc.tensor.matmul(B[2][:, a + STEPS * b:a + STEPS * b + STEPS], S0[:, b, :],
                                                      qdec[:, SEQ + STEPS * b:SEQ + STEPS * b + STEPS],
                                                      start=False, stop=(b == SEQS - 1))
                        if c % 3 == 2:
                            mm.then_inc(o_ready.sem, 1)
                    pe.wait_ge(osq.sem, osq.at(1, h))
                    pe.wait_ge(s_ready.sem, s_ready.at(10, h))
                    for c, (a, n) in enumerate(CHUNKS):
                        mm = nc.tensor.matmul(A[c][:, 0:n], ones[:, :], acc[:, 0, a:a + n], start=True, stop=True)
                    mm.then_inc(o_ssq.sem, 1)

            @block.scalar
            def _(act):
                act.sem_inc(o_root.sem, 1)
                for sig in (tail_stored, state_stored, sample_stored, o_stored):
                    act.sem_inc(sig.sem, 16)
                with act.Fori(0, DN_HEADS) as h:
                    for j in range(4):
                        for c, (a, n) in enumerate(CHUNKS):
                            act.wait_ge(projected.sem, projected.at(3 * j + c + 1, h))
                            psum = (A, B)[j % 2][c]
                            if j == 3:
                                if c == 0:
                                    act.wait_ge(o_stored.sem, o_stored.at(1, h - 1))
                                nc.scalar.activation(zs[:, a:a + n], psum[:, 0:n], ACT.Silu).then_inc(evacuated.sem, 1)
                            elif c < 2:
                                nc.scalar.activation(cbuf[:, j, a + 3:a + 3 + n], psum[:, 0:n], ACT.Copy).then_inc(evacuated.sem, 1)
                            else:
                                nc.scalar.activation(cbuf[:, j, a + 3:SOFF], psum[:, 0:SEQ - a], ACT.Copy)
                                nc.scalar.activation(
                                    cbuf[:, j, SOFF:CW].rearrange("p (b n) -> p b n", n=SW)[:, :, 3:SW],
                                    psum[:, SEQ - a:n].rearrange("p (b n) -> p b n", n=STEPS), ACT.Copy).then_inc(evacuated.sem, 1)
                    for j in range(3):
                        act.wait_ge(conv_done.sem, conv_done.at(j + 1, h))
                        nc.scalar.activation(qkv[:, j, 0:SEQ], acc[:, j, 0:SEQ], ACT.Silu)
                        nc.scalar.activation(
                            qkv[:, j, SEQ:T].rearrange("p (b n) -> p b n", n=STEPS),
                            acc[:, j, SOFF:CW].rearrange("p (b n) -> p b n", n=SW)[:, :, 0:STEPS], ACT.Silu).then_inc(silu_done.sem, 1)
                    for j in range(2):
                        act.wait_ge(silu_done.sem, silu_done.at(3, h))
                        nc.scalar.activation(acc[:, j, 0:T], qkv[:, j, 0:T], ACT.Square).then_inc(squared.sem, 1)
                    act.wait_ge(rows_ready.sem, rows_ready.at(1, h))
                    for t in range(3):
                        op = nc.scalar.activation(c3(erow, t), A[t][:, 0:384], ACT.Exp)
                    op.then_inc(erow_ready.sem, 1)
                    act.wait_ge(diff_ready.sem, diff_ready.at(1, h))
                    nc.scalar.activation(D[:, :], D[:, :], ACT.Exp).then_inc(dexp_ready.sem, 1)
                    for j, banks in ((0, A), (1, B)):
                        act.wait_ge(ssq_ready.sem, ssq_ready.at(j + 1, h))
                        for c, (a, n) in enumerate(CHUNKS):
                            op = nc.scalar.activation(root[:, j, a:a + n], banks[c][:, 0:n], ACT.Sqrt, bias=const["eps"][:, 0:1])
                        op.then_inc(root_ready.sem, 1)
                    for l in range(1, len(LEVELS)):
                        for t in range(3):
                            act.wait_ge(bx_mm.sem, bx_mm.at(3 * (l - 1) + t + 1, h))
                            nc.scalar.activation(c3(BX, t), A[t][:, 0:384], ACT.Copy).then_inc(bx_ready.sem, 1)
                    for c in range(NC):
                        act.wait_ge(vn_mm.sem, vn_mm.at(c + 1, h))
                        nc.scalar.activation(vn[:, c % 2, :], VN_BANK[:, 0:P], ACT.Copy).then_inc(vn_ready.sem, 1)
                        if c % 3 == 2:
                            t = c // 3
                            act.wait_ge(o_ready.sem, o_ready.at(t + 1, h))
                            if t == 0:
                                act.wait_ge(o_stored.sem, o_stored.at(1, h - 1))
                            n = CHUNKS[t][1]
                            nc.scalar.activation(o[:, 384 * t:384 * t + n], B[t][:, 0:n], ACT.Copy).then_inc(o_out.sem, 1)
                    act.wait_ge(o_out.sem, o_out.at(3, h))
                    nc.scalar.activation(acc[:, 0, 0:T], o[:, :], ACT.Square).then_inc(osq.sem, 1)
                    act.wait_ge(o_ssq.sem, o_ssq.at(1, h))
                    for c, (a, n) in enumerate(CHUNKS):
                        op = nc.scalar.activation(root[:, 0, a:a + n], A[c][:, 0:n], ACT.Sqrt, scale=1.0 / P, bias=const["eps"][:, 0:1])
                    op.then_inc(o_root.sem, 1)

            @block.gpsimd
            def _(pool):
                nc.gpsimd.memset(qkv[:, :, T:TP], 0.0)
                nc.gpsimd.memset(km[:, :], 0.0)
                nc.gpsimd.memset(cbuf[:, :, 0:3], 0.0).then_inc(zeroed.sem, 1)
                pool.wait_ge(started.sem, started.at(3))
                with pool.Fori(0, DN_HEADS) as h:
                    pool.wait_ge(lt_ready.sem, lt_ready.at(1, h))
                    for l in range(len(LEVELS)):
                        if l >= 2:
                            if l == 2:
                                pool.wait_ge(y1_ready.sem, y1_ready.at(1, h))
                            else:
                                pool.wait_ge(bx_mm.sem, bx_mm.at(3 * (l - 2), h))
                        nc.gpsimd.tensor_tensor(BT[:, l % 2, :].rearrange("p (c n) -> p c n", n=CK),
                                                LT[:, :].rearrange("p (c n) -> p c n", n=CK),
                                                const["level"][:, l:l + 1, :].to_broadcast([P, NC, CK]),
                                                ALU.mult).then_inc(bt_ready.sem, 1)

            @block.vector
            def _(v):
                v.wait_ge(started.sem, started.at(3))
                with v.Fori(0, DN_HEADS) as h:
                    vec.n = 0

                    def then(op):
                        op.then_inc(vec.step(), 1)
                        v.wait_ge(vec.sem, vec.now(h))
                    nc.vector.tensor_copy(cur[:, :, :], tab[:, :, :, bass.ds(h, 1)].rearrange("p q c o -> p q (c o)")).then_inc(cur_ready.sem, 1)
                    v.wait_ge(loaded.sem, loaded.at(4, h))
                    v.wait_ge(zeroed.sem, 1)
                    nc.vector.tensor_copy(cbuf[:, :, SOFF:CW].rearrange("p j (b n) -> p j b n", n=SW)[:, :, :, 0:3],
                                          hist[:, :, :, :]).then_inc(hist_in.sem, 1)
                    v.wait_ge(hist_in.sem, hist_in.at(1, h))
                    v.wait_ge(cur_ready.sem, cur_ready.at(1, h))
                    then(nc.vector.scalar_tensor_tensor(negbeg[:, :], cur[:, 4, :], -1.0, cur[:, 2, :], ALU.mult, ALU.mult))
                    W = CW - 3
                    for j in range(3):
                        v.wait_ge(evacuated.sem, evacuated.at(3 * j + 3, h))
                        if j == 0:
                            v.wait_ge(o_root.sem, o_root.at(1, h - 1))
                        then(nc.vector.tensor_scalar(acc[:, j, 0:W], cbuf[:, j, 0:W], cw[:, j, 0:1], None, ALU.mult))
                        for k in range(1, CONV):
                            op = nc.vector.scalar_tensor_tensor(acc[:, j, 0:W], cbuf[:, j, k:k + W], cw[:, j, k:k + 1],
                                                                acc[:, j, 0:W], ALU.mult, ALU.add)
                            if k < CONV - 1:
                                then(op)
                            else:
                                op.then_inc(conv_done.sem, 1)
                    v.wait_ge(tail_stored.sem, tail_stored.at(1, h - 1))
                    nc.vector.tensor_copy(tail[:, :, 0, :], cbuf[:, :, SEQ:SOFF]).then_inc(tail_ready.sem, 1)
                    nc.vector.tensor_copy(tail[:, :, 1:SEQS + 1, :],
                                          cbuf[:, :, SOFF:CW].rearrange("p j (b n) -> p j b n", n=SW)[:, :, :, STEPS:SW]).then_inc(tail_ready.sem, 1)
                    v.wait_ge(erow_ready.sem, erow_ready.at(1, h))
                    for c in range(NC):
                        op = nc.vector.tensor_scalar(D[:, CK * c:CK * c + CK], A[c // 3][:, CK * (c % 3):CK * (c % 3) + CK],
                                                     cur[:, 1, c:c + 1], 0.0, ALU.subtract, ALU.min)
                    op.then_inc(diff_ready.sem, 1)
                    v.wait_ge(dexp_ready.sem, dexp_ready.at(1, h))
                    then(nc.vector.tensor_tensor(D[:, :], D[:, :], const["incl"][:, :], ALU.mult))
                    then(nc.vector.tensor_tensor(Ds[:, :], D[:, :], const["strict"][:, :], ALU.mult))
                    v.wait_ge(rows_ready.sem, rows_ready.at(2, h))
                    for t in range(3):
                        op = nc.vector.tensor_tensor(c3(Ds, t), c3(Ds, t), B[t][:, 0:384], ALU.mult)
                    op.then_inc(rowb_used.sem, 1)
                    for j in range(2):
                        v.wait_ge(root_ready.sem, root_ready.at(j + 1, h))
                        then(nc.vector.reciprocal(root[:, j, :], root[:, j, :]))
                        nc.vector.scalar_tensor_tensor(qkv[:, j, 0:T], qkv[:, j, 0:T], (float(P) ** -0.5, 1.0)[j],
                                                       root[:, j, :], ALU.mult, ALU.mult).then_inc(qk_ready.sem, 1)
                    v.wait_ge(qk_ready.sem, qk_ready.at(2, h))
                    nc.vector.tensor_copy(km[:, :].rearrange("p (b n) -> p b n", n=P + STEPS)[:, :, 0:STEPS],
                                          qkv[:, 1, SEQ:T].rearrange("p (b n) -> p b n", n=STEPS)).then_inc(km_ready.sem, 1)
                    v.wait_ge(erow_ready.sem, erow_ready.at(1, h))
                    nc.vector.tensor_tensor(qdec[:, :], qkv[:, 0, :], erow[:, :], ALU.mult).then_inc(qdec_ready.sem, 1)
                    v.wait_ge(prod_ready.sem, prod_ready.at(1, h))
                    v.wait_ge(rowb_used.sem, rowb_used.at(1, h))
                    for t in range(3):
                        op = nc.vector.tensor_tensor(c3(LT, t), A[t][:, 0:384], c3(Ds, t), ALU.mult)
                    op.then_inc(lt_ready.sem, 1)
                    v.wait_ge(prod_ready.sem, prod_ready.at(2, h))
                    for t in range(3):
                        op = nc.vector.tensor_tensor(c3(attn, t), B[t][:, 0:384], c3(D, t), ALU.mult)
                    op.then_inc(attn_ready.sem, 1)
                    v.wait_ge(bt_ready.sem, bt_ready.at(1, h))
                    nc.vector.tensor_tensor(Y[:, :].rearrange("p (c n) -> p c n", n=CK),
                                            ident[:, None, :].to_broadcast([P, NC, CK]),
                                            BT[:, 0, :].rearrange("p (c n) -> p c n", n=CK), ALU.subtract).then_inc(y1_ready.sem, 1)
                    v.wait_ge(turned.sem, turned.at(1, h))
                    for c in range(NC):
                        op = nc.vector.tensor_scalar(Vb[:, CK * c:CK * c + CK], A[c // 3][:, CK * (c % 3):CK * (c % 3) + CK],
                                                     cur[:, 4, c:c + 1], None, ALU.mult)
                    op.then_inc(v_turned_used.sem, 1)
                    v.wait_ge(turned.sem, turned.at(2, h))
                    for c in range(NC):
                        op = nc.vector.tensor_scalar(Kd[:, CK * c:CK * c + CK], B[c // 3][:, CK * (c % 3):CK * (c % 3) + CK],
                                                     cur[:, 3, c:c + 1], None, ALU.mult)
                    op.then_inc(k_turned_used.sem, 1)
                    for t in range(3):
                        v.wait_ge(x_turned.sem, x_turned.at(t + 1, h))
                        nc.vector.tensor_copy(c3(X, t), A[t][:, 0:384]).then_inc(x1_ready.sem, 1)
                    v.wait_ge(y1_ready.sem, y1_ready.at(1, h))
                    for l in range(1, len(LEVELS)):
                        for t in range(3):
                            n = 3 * (l - 1) + t
                            v.wait_ge(yx_mm.sem, yx_mm.at(n + 1, h))
                            if n < 3:
                                v.wait_ge(x1_ready.sem, x1_ready.at(3, h))
                            else:
                                v.wait_ge(y_ready.sem, y_ready.at(n - 2, h))
                            if l < len(LEVELS) - 1:
                                nc.vector.tensor_tensor(c3(X, t), c3(X, t), A[t][:, 0:384], ALU.subtract)
                            nc.vector.tensor_tensor(c3(Y, t), c3(Y, t), B[t][:, 0:384], ALU.subtract).then_inc(y_ready.sem, 1)
                    v.wait_ge(state_stored.sem, state_stored.at(1, h - 1))
                    nc.vector.memset(S[:, 0, :], 0.0).then_inc(s_ready.sem, 1)
                    for c in range(NC):
                        s = slice(CK * c, CK * c + CK)
                        v.wait_ge(ks_ready.sem, ks_ready.at(c + 1, h))
                        nc.vector.scalar_tensor_tensor(R[:, :], KS_BANK[:, 0:P], negbeg[:, c:c + 1], Vb[:, s],
                                                       ALU.mult, ALU.add).then_inc(r_ready.sem, 1)
                        if c < NC - 1:
                            v.wait_ge(ds_ready.sem, ds_ready.at(c + 1, h))
                            v.wait_ge(s_ready.sem, s_ready.at(c + 1, h))
                            nc.vector.scalar_tensor_tensor(S[:, (c + 1) % 2, :], S[:, c % 2, :],
                                                           erow[:, CK * c + CK - 1:CK * c + CK], A[0][:, 0:P],
                                                           ALU.mult, ALU.add).then_inc(s_ready.sem, 1)
                        else:
                            v.wait_ge(vn_ready.sem, vn_ready.at(9, h))
                            nc.vector.tensor_tensor(vm[:, :, :], vn[:, c % 2:c % 2 + 1, :].to_broadcast([P, SEQS, P]),
                                                    const["seq_of"][:, :, None].to_broadcast([P, SEQS, P]), ALU.mult).then_inc(vm_ready.sem, 1)
                            v.wait_ge(sample_stored.sem, sample_stored.at(1, h - 1))
                            last = erow[:, SEQ:T].rearrange("p (b n) -> p b n", n=STEPS)[:, :, STEPS - 1:STEPS]
                            then(nc.vector.tensor_tensor(S1[:, :, :], S0[:, :, :], last.to_broadcast([P, SEQS, P]), ALU.mult))
                            v.wait_ge(ds_ready.sem, ds_ready.at(9, h))
                            nc.vector.tensor_tensor(S1[:, 0:4, :], S1[:, 0:4, :], A[1][:, 0:512].rearrange("p (b n) -> p b n", n=P), ALU.add)
                            nc.vector.tensor_tensor(S1[:, 4:8, :], S1[:, 4:8, :], A[2][:, 0:512].rearrange("p (b n) -> p b n", n=P), ALU.add).then_inc(s_ready.sem, 1)
                    v.wait_ge(o_root.sem, o_root.at(1, h))
                    then(nc.vector.reciprocal(root[:, 0, :], root[:, 0, :]))
                    then(nc.vector.scalar_tensor_tensor(o[:, :], o[:, :], nw[:, 0:1], root[:, 0, :], ALU.mult, ALU.mult))
                    nc.vector.tensor_tensor(o[:, :], o[:, :], zs[:, :], ALU.mult).then_inc(o_done.sem, 1)
                    assert vec.n == VSTEPS, vec.n


def ssd(nc, bank, xn, tab, d, const, mix, out):
    A, B = bank[0:3], bank[4:7]
    SMALL = 3 * SEQS + CONV + 2
    W = CW - 3
    with Phase(nc) as ctx:
        def sb(name, shape):
            return ctx.enter_context(nc.sbuf_tensor(f"ssd_{name}", shape, F32))

        def signal(name, per=1, unit=1, primed=False):
            return Signal(nc, ctx, f"ssd_{name}", per, unit, primed)
        wg, wp = sb("w_bc", [P, KT, 2, P]), sb("w_xz", [P, KT, 2, P])
        sg, sm = sb("small_bc", [P, 2, SMALL]), sb("small_x", [P, SMALL])
        nw = sb("norm_w", [P, PAIRS])
        cb, acc = sb("padded", [P, 2, CW]), sb("conv", [P, 2, CW])
        Bt, Ct, CB, Btok = (sb(x, [P, TP]) for x in ("b", "c", "cb", "b_tokens"))
        xT, zs = sb("x", [P, TP]), sb("gate", [P, T])
        cur = sb("columns", [P, 5, NC, 2])
        erow, D, Cdec = (sb(x, [P, 2, TP]) for x in ("row_decay", "decay", "c_decayed"))
        xd, xde = sb("x_dt", [P, TP]), sb("x_dt_decayed", [P, TP])
        H, S0, S1, xm = sb("states", [P, NC, P]), sb("sample_in", [P, SEQS, P]), sb("sample_out", [P, SEQS, P]), sb("x_masked", [P, SEQS, P])
        tg, tx = sb("tail_bc", [P, 2, SEQS + 1, 3]), sb("tail_x", [P, SEQS + 1, 3])
        y, rstd = sb("y", [P, GP, T]), sb("rstd", [P, T])
        ident, ones = const["ident"], const["ones"]

        once = signal("norm_w_loaded", 1, 16)
        zeroed = signal("zeroed")
        g_loaded = signal("group_loaded", 2, 16)
        g_projected, g_evacuated = signal("bc_projected", 2), signal("bc_evacuated", 2)
        g_conv, g_silu = signal("bc_conv_done", 2), signal("bc_silu_done", 2)
        g_tail = signal("bc_tail_ready")
        g_tail_stored = signal("bc_tail_stored", 1, 16, True)
        g_products = signal("bc_products", 2)
        cb_ready, btok_ready = signal("cb_ready"), signal("b_tokens_ready")
        g_squared, g_summed = signal("group_squared", GP), signal("group_summed", GP)
        g_mean, g_root = signal("group_mean"), signal("group_root")
        g_normed, g_stored = signal("group_normed", 1, 1, True), signal("group_stored", GP, 16, True)
        loaded = signal("pair_loaded", 3, 16)
        cur_ready = signal("columns_ready")
        projected, evacuated = signal("projected", 2), signal("evacuated", 2)
        conv_done, silu_done = signal("conv_done"), signal("silu_done")
        tail_ready, tail_stored = signal("tail_ready"), signal("tail_stored", 1, 16, True)
        rows, erow_ready, diff_ready = signal("rows", 2), signal("row_decay_ready", 2), signal("diff_ready", 2)
        dexp = signal("decay_exp_ready", 2)
        turned, xde_ready = signal("x_turned"), signal("x_ready")
        m_ready, cdec_ready = signal("weights_ready"), signal("c_decayed_ready")
        xm_ready = signal("x_masked_ready")
        u_ready, h_ready = signal("state_products"), signal("states_ready")
        state_stored = signal("states_stored", 2, 16, True)
        s1_ready = signal("sample_states_ready")
        y_mm, y_ready = signal("y_product"), signal("y_ready", 1, 1, True)
        VSTEPS, GSTEPS = 15, 8
        vec = Steps(nc, ctx, "ssd_vector_steps", VSTEPS)
        gvec = Steps(nc, ctx, "ssd_group_steps", GSTEPS)

        def sample(t):
            return t[:, SOFF:CW].rearrange("p (b n) -> p b n", n=SW)

        def row(a, n):
            names = "pqrs"[:len(a.shape) - 1]
            return a[bass.ds(n, 1)].rearrange(f"a {' '.join(names)} -> (a p) {' '.join(names[1:])}")

        with nc.Block() as block:
            @block.sync
            def _(sp):
                sp.dma_start(nw[:, :], d["ssm_norm_w"]).then_inc(once.sem, 16)
                with sp.Fori(0, SSM_GROUPS) as g:
                    sp.wait_ge(g_normed.sem, g_normed.at(1, g - 1))
                    sp.dma_start(wg[:, :, :, :], row(d["w_bc"], g)).then_inc(g_loaded.sem, 16)
                    sp.dma_start(sg[:, :, :], row(d["ssm_small_bc"], g)).then_inc(g_loaded.sem, 16)
                    with sp.Fori(0, GP) as p:
                        u = g * GP + p
                        sp.wait_ge(y_ready.sem, y_ready.at(1, u - 1))
                        sp.dma_start(wp[:, :, :, :], row(d["w_xz"], u)).then_inc(loaded.sem, 16)
                        sp.dma_start(sm[:, :], row(d["ssm_small_x"], u)).then_inc(loaded.sem, 16)
                        sp.dma_start(S0[:, :, :], row(d["ssm_s0"], u)).then_inc(loaded.sem, 16)
                        sp.wait_ge(tail_ready.sem, tail_ready.at(1, u))
                        sp.dma_start(row(out["ssm_conv_x"], u), tx[:, :, :]).then_inc(tail_stored.sem, 16)
                        sp.wait_ge(h_ready.sem, h_ready.at(1, u))
                        sp.dma_start(row(out["ssm_p"], u), H[:, NC - 1, :]).then_inc(state_stored.sem, 16)
                        sp.wait_ge(s1_ready.sem, s1_ready.at(1, u))
                        sp.dma_start(row(out["ssm_s"], u), S1[:, :, :]).then_inc(state_stored.sem, 16)
                    sp.wait_ge(g_tail.sem, g_tail.at(1, g))
                    sp.dma_start(row(out["ssm_conv_bc"], g), tg[:, :, :, :]).then_inc(g_tail_stored.sem, 16)
                    sp.wait_ge(g_normed.sem, g_normed.at(1, g))
                    for k in range(GP):
                        sp.dma_start(row(mix, g * GP + (DN_HEADS + k)), y[:, k, :]).then_inc(g_stored.sem, 16)
                for sig, n, turn in ((tail_stored, 1, PAIRS - 1), (state_stored, 2, PAIRS - 1),
                                     (g_tail_stored, 1, SSM_GROUPS - 1), (g_stored, GP, SSM_GROUPS - 1)):
                    sp.wait_ge(sig.sem, sig.at(n, turn))

            @block.tensor
            def _(pe):
                def project(w, j, banks, done):
                    for c, (a, n) in enumerate(CHUNKS):
                        for k in range(KT):
                            mm = nc.tensor.matmul(banks[c][:, 0:n], w[:, k, j, :], xn[:, k, a:a + n],
                                                  start=(k == 0), stop=(k == KT - 1))
                    mm.then_inc(done.sem, 1)

                with pe.Fori(0, SSM_GROUPS) as g:
                    pe.wait_ge(g_loaded.sem, g_loaded.at(2, g))
                    pe.wait_ge(g_normed.sem, g_normed.at(1, g - 1))
                    project(wg, 0, A, g_projected)
                    project(wg, 1, B, g_projected)
                    pe.wait_ge(g_silu.sem, g_silu.at(2, g))
                    for c in range(NC):
                        s = slice(CK * c, CK * c + CK)
                        mm = nc.tensor.matmul(A[c // 3][:, CK * (c % 3):CK * (c % 3) + CK], Bt[:, s], Ct[:, s], start=True, stop=True)
                    mm.then_inc(g_products.sem, 1)
                    for c in range(NC):
                        s = slice(CK * c, CK * c + CK)
                        mm = nc.tensor.transpose(B[c // 3][:, CK * (c % 3):CK * (c % 3) + CK], Bt[:, s], ident[:, :])
                    mm.then_inc(g_products.sem, 1)
                    with pe.Fori(0, GP) as p:
                        u = g * GP + p
                        pe.wait_ge(loaded.sem, loaded.at(3, u))
                        pe.wait_ge(cb_ready.sem, cb_ready.at(1, g))
                        pe.wait_ge(btok_ready.sem, btok_ready.at(1, g))
                        pe.wait_ge(y_ready.sem, y_ready.at(1, u - 1))
                        project(wp, 0, A, projected)
                        project(wp, 1, B, projected)
                        pe.wait_ge(cur_ready.sem, cur_ready.at(1, u))
                        for e, banks in ((0, A), (1, B)):
                            pe.wait_ge(evacuated.sem, evacuated.at(e + 1, u))
                            for c in range(NC):
                                mm = nc.tensor.matmul(banks[c // 3][:, CK * (c % 3):CK * (c % 3) + CK],
                                                      cur[:, 0, c, e:e + 1].to_broadcast([P, P]),
                                                      const["tri"][:, int(c == NC - 1), :], start=True, stop=True)
                            mm.then_inc(rows.sem, 1)
                        pe.wait_ge(silu_done.sem, silu_done.at(1, u))
                        pe.wait_ge(diff_ready.sem, diff_ready.at(1, u))
                        for c in range(NC):
                            mm = nc.tensor.transpose(A[c // 3][:, CK * (c % 3):CK * (c % 3) + CK], xT[:, CK * c:CK * c + CK], ident[:, :])
                        mm.then_inc(turned.sem, 1)
                        pe.wait_ge(diff_ready.sem, diff_ready.at(2, u))
                        pe.wait_ge(xde_ready.sem, xde_ready.at(1, u))
                        pe.wait_ge(xm_ready.sem, xm_ready.at(1, u))
                        for c in range(NC - 1):
                            s = slice(CK * c, CK * c + CK)
                            nc.tensor.matmul(B[c // 4][:, P * (c % 4):P * (c % 4) + P], Btok[:, s], xde[:, s], start=True, stop=True)
                        for half, to in enumerate((bank[3], bank[7])):
                            mm = nc.tensor.matmul(to[:, 0:512], Btok[:, SEQ:TP],
                                                  xm[:, 4 * half:4 * half + 4, :].rearrange("p b n -> p (b n)"), start=True, stop=True)
                        mm.then_inc(u_ready.sem, 1)
                        pe.wait_ge(m_ready.sem, m_ready.at(1, u))
                        pe.wait_ge(cdec_ready.sem, cdec_ready.at(1, u))
                        pe.wait_ge(h_ready.sem, h_ready.at(1, u))
                        for c in range(NC):
                            s = slice(CK * c, CK * c + CK)
                            n = CK if c < NC - 1 else SAMPLE
                            for e in range(2):
                                a, ch = CK * (c % 3), slice(HALF * e, HALF * e + HALF)
                                nc.tensor.matmul(A[c // 3][ch, a:a + n], xd[:, CK * c + HALF * e:CK * c + HALF * e + HALF],
                                                 D[:, e, CK * c:CK * c + n], start=True, stop=False)
                                if c < NC - 1:
                                    mm = nc.tensor.matmul(A[c // 3][ch, a:a + n], H[:, c, ch], Cdec[:, e, s], start=False, stop=True)
                                    continue
                                for b in range(SEQS):
                                    t = slice(SEQ + STEPS * b, SEQ + STEPS * b + STEPS)
                                    mm = nc.tensor.matmul(A[c // 3][ch, a + STEPS * b:a + STEPS * b + STEPS], S0[:, b, ch],
                                                          Cdec[:, e, t], start=False, stop=(b == SEQS - 1))
                        mm.then_inc(y_mm.sem, 1)
                    for k in range(GP):
                        pe.wait_ge(g_squared.sem, g_squared.at(k + 1, g))
                        for c, (a, n) in enumerate(CHUNKS):
                            mm = nc.tensor.matmul(A[c][:, 0:n], ones[:, :], acc[:, k % 2, a:a + n], start=(k == 0), stop=(k == GP - 1))
                        mm.then_inc(g_summed.sem, 1)

            @block.scalar
            def _(act):
                for sig in (g_tail_stored, tail_stored):
                    act.sem_inc(sig.sem, 16)
                act.sem_inc(g_normed.sem, 1)
                act.sem_inc(g_stored.sem, 16 * GP)
                act.sem_inc(state_stored.sem, 32)
                act.sem_inc(y_ready.sem, 1)

                def evacuate(banks, to, done):
                    for c, (a, n) in enumerate(CHUNKS):
                        if c < 2:
                            nc.scalar.activation(to[:, a + 3:a + 3 + n], banks[c][:, 0:n], ACT.Copy)
                    nc.scalar.activation(to[:, a + 3:SOFF], banks[2][:, 0:SEQ - a], ACT.Copy)
                    nc.scalar.activation(sample(to)[:, :, 3:SW], banks[2][:, SEQ - a:n].rearrange("p (b n) -> p b n", n=STEPS),
                                         ACT.Copy).then_inc(done.sem, 1)

                def silu(to, src, bias, done):
                    nc.scalar.activation(to[:, 0:SEQ], src[:, 0:SEQ], ACT.Silu, bias=bias)
                    nc.scalar.activation(to[:, SEQ:T].rearrange("p (b n) -> p b n", n=STEPS), sample(src)[:, :, 0:STEPS],
                                         ACT.Silu, bias=bias).then_inc(done.sem, 1)

                with act.Fori(0, SSM_GROUPS) as g:
                    for j, banks in ((0, A), (1, B)):
                        act.wait_ge(g_projected.sem, g_projected.at(j + 1, g))
                        evacuate(banks, cb[:, j, :], g_evacuated)
                    for j, to in ((0, Bt), (1, Ct)):
                        act.wait_ge(g_conv.sem, g_conv.at(j + 1, g))
                        silu(to, acc[:, j, :], sg[:, j, SMALL - 2:SMALL - 1], g_silu)
                    act.wait_ge(g_products.sem, g_products.at(2, g))
                    for t in range(3):
                        op = nc.scalar.activation(Btok[:, 384 * t:384 * t + 384], B[t][:, 0:384], ACT.Copy)
                    op.then_inc(btok_ready.sem, 1)
                    act.wait_ge(g_tail.sem, g_tail.at(1, g))
                    with act.Fori(0, GP) as p:
                        u = g * GP + p
                        act.wait_ge(projected.sem, projected.at(1, u))
                        evacuate(A, cb[:, 0, :], evacuated)
                        act.wait_ge(projected.sem, projected.at(2, u))
                        for c, (a, n) in enumerate(CHUNKS):
                            op = nc.scalar.activation(zs[:, a:a + n], B[c][:, 0:n], ACT.Silu)
                        op.then_inc(evacuated.sem, 1)
                        act.wait_ge(conv_done.sem, conv_done.at(1, u))
                        silu(xT, acc[:, 0, :], sm[:, SMALL - 2:SMALL - 1], silu_done)
                        for e, banks in ((0, A), (1, B)):
                            act.wait_ge(rows.sem, rows.at(e + 1, u))
                            for t in range(3):
                                op = nc.scalar.activation(erow[:, e, 384 * t:384 * t + 384], banks[t][:, 0:384], ACT.Exp)
                            op.then_inc(erow_ready.sem, 1)
                        for e in range(2):
                            act.wait_ge(diff_ready.sem, diff_ready.at(e + 1, u))
                            nc.scalar.activation(D[:, e, :], D[:, e, :], ACT.Exp).then_inc(dexp.sem, 1)
                    act.wait_ge(y_ready.sem, y_ready.at(1, g * GP + (GP - 1)))
                    for k in range(GP):
                        if k >= 2:
                            act.wait_ge(g_summed.sem, g_summed.at(k - 1, g))
                        nc.scalar.activation(acc[:, k % 2, 0:T], y[:, k, :], ACT.Square).then_inc(g_squared.sem, 1)
                    act.wait_ge(g_mean.sem, g_mean.at(1, g))
                    nc.scalar.activation(rstd[:, :], rstd[:, :], ACT.Sqrt).then_inc(g_root.sem, 1)

            @block.gpsimd
            def _(pool):
                nc.gpsimd.memset(xT[:, T:TP], 0.0)
                nc.gpsimd.memset(Bt[:, T:TP], 0.0)
                nc.gpsimd.memset(Ct[:, T:TP], 0.0)
                nc.gpsimd.memset(cb[:, :, 0:3], 0.0).then_inc(zeroed.sem, 1)
                with pool.Fori(0, SSM_GROUPS) as g:
                    with pool.Fori(0, GP) as p:
                        u = g * GP + p
                        pool.wait_ge(g_silu.sem, g_silu.at(2, g))
                        for e in range(2):
                            pool.wait_ge(erow_ready.sem, erow_ready.at(e + 1, u))
                            op = nc.gpsimd.tensor_tensor(Cdec[:, e, :], Ct[:, :], erow[:, e, :], ALU.mult)
                        op.then_inc(cdec_ready.sem, 1)

            @block.vector
            def _(v):
                def conv(j, small, then, done):
                    then(nc.vector.tensor_scalar(acc[:, j, 0:W], cb[:, j, 0:W], small[:, 24:25], None, ALU.mult))
                    for k in range(1, CONV):
                        op = nc.vector.scalar_tensor_tensor(acc[:, j, 0:W], cb[:, j, k:k + W], small[:, 24 + k:25 + k],
                                                            acc[:, j, 0:W], ALU.mult, ALU.add)
                        if k < CONV - 1:
                            then(op)
                        else:
                            op.then_inc(done.sem, 1)

                v.wait_ge(once.sem, once.at(1))
                v.wait_ge(zeroed.sem, 1)
                with v.Fori(0, SSM_GROUPS) as g:
                    gvec.n = 0

                    def gthen(op):
                        op.then_inc(gvec.step(), 1)
                        v.wait_ge(gvec.sem, gvec.now(g))
                    v.wait_ge(g_loaded.sem, g_loaded.at(2, g))
                    for j in range(2):
                        hist = nc.vector.tensor_copy(sample(cb[:, j, :])[:, :, 0:3], sg[:, j, 0:24].rearrange("p (b n) -> p b n", n=3))
                    gthen(hist)
                    for j in range(2):
                        v.wait_ge(g_evacuated.sem, g_evacuated.at(j + 1, g))
                        conv(j, sg[:, j, :], gthen, g_conv)
                    v.wait_ge(g_tail_stored.sem, g_tail_stored.at(1, g - 1))
                    nc.vector.tensor_copy(tg[:, :, 0, :], cb[:, :, SEQ:SOFF])
                    nc.vector.tensor_copy(tg[:, :, 1:SEQS + 1, :],
                                          cb[:, :, SOFF:CW].rearrange("p j (b n) -> p j b n", n=SW)[:, :, :, STEPS:SW]).then_inc(g_tail.sem, 1)
                    v.wait_ge(g_products.sem, g_products.at(1, g))
                    for t in range(3):
                        s = slice(384 * t, 384 * t + 384)
                        op = nc.vector.tensor_tensor(CB[:, s], A[t][:, 0:384], const["incl"][:, s], ALU.mult)
                    op.then_inc(cb_ready.sem, 1)
                    with v.Fori(0, GP) as p:
                        u = g * GP + p
                        vec.n = 0

                        def then(op):
                            op.then_inc(vec.step(), 1)
                            v.wait_ge(vec.sem, vec.now(u))
                        nc.vector.tensor_copy(cur[:, :, :, :].rearrange("p q c e -> p (q c) e"),
                                              tab[:, :, :, bass.ds(u * 2 + DN_HEADS, 2)].rearrange("p q c e -> p (q c) e")).then_inc(cur_ready.sem, 1)
                        v.wait_ge(loaded.sem, loaded.at(3, u))
                        then(nc.vector.tensor_copy(sample(cb[:, 0, :])[:, :, 0:3], sm[:, 0:24].rearrange("p (b n) -> p b n", n=3)))
                        v.wait_ge(evacuated.sem, evacuated.at(1, u))
                        conv(0, sm, then, conv_done)
                        v.wait_ge(tail_stored.sem, tail_stored.at(1, u - 1))
                        nc.vector.tensor_copy(tx[:, 0, :], cb[:, 0, SEQ:SOFF])
                        nc.vector.tensor_copy(tx[:, 1:SEQS + 1, :], sample(cb[:, 0, :])[:, :, STEPS:SW]).then_inc(tail_ready.sem, 1)
                        for e, banks in ((0, A), (1, B)):
                            v.wait_ge(erow_ready.sem, erow_ready.at(e + 1, u))
                            v.wait_ge(cur_ready.sem, cur_ready.at(1, u))
                            for c in range(NC):
                                op = nc.vector.tensor_scalar(D[:, e, CK * c:CK * c + CK], banks[c // 3][:, CK * (c % 3):CK * (c % 3) + CK],
                                                             cur[:, 1, c, e:e + 1], 0.0, ALU.subtract, ALU.min)
                            op.then_inc(diff_ready.sem, 1)
                        v.wait_ge(turned.sem, turned.at(1, u))
                        heads = lambda t: t.rearrange("p (c n) -> p c n", n=HALF)
                        col = lambda q: cur[:, q, :, :].rearrange("p c e -> p (c e)")
                        for t in range(3):
                            op = nc.vector.tensor_tensor(heads(xd[:, 384 * t:384 * t + 384]), heads(A[t][:, 0:384]),
                                                         col(4)[:, 6 * t:6 * t + 6, None].to_broadcast([P, 6, HALF]), ALU.mult)
                        then(op)
                        nc.vector.tensor_tensor(heads(xde[:, :]), heads(xd[:, :]),
                                                col(3)[:, :, None].to_broadcast([P, 2 * NC, HALF]), ALU.mult).then_inc(xde_ready.sem, 1)
                        v.wait_ge(xde_ready.sem, xde_ready.at(1, u))
                        nc.vector.tensor_tensor(xm[:, :, :], xde[:, None, SEQ:TP].to_broadcast([P, SEQS, P]),
                                                const["seq_of"][:, :, None].to_broadcast([P, SEQS, P]), ALU.mult).then_inc(xm_ready.sem, 1)
                        v.wait_ge(cb_ready.sem, cb_ready.at(1, g))
                        v.wait_ge(dexp.sem, dexp.at(2, u))
                        nc.vector.tensor_tensor(D[:, :, :], D[:, :, :], CB[:, None, :].to_broadcast([P, 2, TP]), ALU.mult).then_inc(m_ready.sem, 1)
                        v.wait_ge(state_stored.sem, state_stored.at(2, u - 1))
                        then(nc.vector.memset(H[:, 0, :], 0.0))
                        v.wait_ge(u_ready.sem, u_ready.at(1, u))
                        for c in range(NC - 1):
                            last = CK * c + CK - 1
                            for e in range(2):
                                ch = slice(HALF * e, HALF * e + HALF)
                                op = nc.vector.scalar_tensor_tensor(H[:, c + 1, ch], H[:, c, ch], erow[:, e, last:last + 1],
                                                                    B[c // 4][:, P * (c % 4) + HALF * e:P * (c % 4) + HALF * e + HALF],
                                                                    ALU.mult, ALU.add)
                            if c < NC - 2:
                                then(op)
                            else:
                                op.then_inc(h_ready.sem, 1)
                        for e in range(2):
                            ch = slice(HALF * e, HALF * e + HALF)
                            lasts = erow[:, e, SEQ:T].rearrange("p (b n) -> p b n", n=STEPS)[:, :, STEPS - 1:STEPS]
                            op = nc.vector.tensor_tensor(S1[:, :, ch], S0[:, :, ch], lasts.to_broadcast([P, SEQS, HALF]), ALU.mult)
                        then(op)
                        nc.vector.tensor_tensor(S1[:, 0:4, :], S1[:, 0:4, :], bank[3][:, 0:512].rearrange("p (b n) -> p b n", n=P), ALU.add)
                        nc.vector.tensor_tensor(S1[:, 4:8, :], S1[:, 4:8, :], bank[7][:, 0:512].rearrange("p (b n) -> p b n", n=P), ALU.add).then_inc(s1_ready.sem, 1)
                        v.wait_ge(y_mm.sem, y_mm.at(1, u))
                        v.wait_ge(g_stored.sem, g_stored.at(GP, g - 1))
                        yp = y[:, bass.ds(p, 1), :].rearrange("p o n -> p (o n)")
                        for c, (a, n) in enumerate(CHUNKS):
                            op = nc.vector.scalar_tensor_tensor(xT[:, a:a + n], xT[:, a:a + n], sm[:, SMALL - 1:SMALL], A[c][:, 0:n],
                                                                ALU.mult, ALU.add)
                        then(op)
                        nc.vector.tensor_tensor(yp, xT[:, 0:T], zs[:, :], ALU.mult).then_inc(y_ready.sem, 1)
                        assert vec.n == VSTEPS, vec.n
                    v.wait_ge(g_summed.sem, g_summed.at(GP, g))
                    for c, (a, n) in enumerate(CHUNKS):
                        op = nc.vector.tensor_scalar(rstd[:, a:a + n], A[c][:, 0:n], 1.0 / (GP * P), EPS, ALU.mult, ALU.add)
                    op.then_inc(g_mean.sem, 1)
                    v.wait_ge(g_root.sem, g_root.at(1, g))
                    gthen(nc.vector.reciprocal(rstd[:, :], rstd[:, :]))
                    v.wait_ge(y_ready.sem, y_ready.at(1, g * GP + (GP - 1)))
                    for k in range(GP):
                        op = nc.vector.scalar_tensor_tensor(y[:, k, :], y[:, k, :], nw[:, bass.ds(g * GP + k, 1)], rstd[:, :],
                                                            ALU.mult, ALU.mult)
                    op.then_inc(g_normed.sem, 1)
                    assert gvec.n == GSTEPS, gvec.n


def row_of(a, n):
    names = " ".join("pqrs"[:len(a.shape) - 1])
    return a[bass.ds(n, 1)].rearrange(f"a {names} -> (a {names[0]}) {names[1:]}")


def linear(nc, bank, name, rhs, w, K, outs, tokens, how, to):
    cols = CHUNKS if tokens == T else [(0, tokens)]
    wide = to.shape[-1]
    with Phase(nc) as ctx:
        wb = [ctx.enter_context(nc.sbuf_tensor(f"{name}_w{r}", [P, K, P], F32)) for r in range(2)]
        loaded = [Signal(nc, ctx, f"{name}_loaded{r}", 1, 16) for r in range(2)]
        product = [Signal(nc, ctx, f"{name}_product{r}", 1, 1, True) for r in range(2)]
        taken = [Signal(nc, ctx, f"{name}_taken{r}", 1, 1, True) for r in range(2)]
        if how == "store":
            stage = [ctx.enter_context(nc.sbuf_tensor(f"{name}_stage{r}", [P, wide], F32)) for r in range(2)]
            zeroed = Signal(nc, ctx, f"{name}_zeroed", 2)
            stored = [Signal(nc, ctx, f"{name}_stored{r}", 1, 16, True) for r in range(2)]
        with nc.Block() as block:
            @block.sync
            def _(sp):
                with sp.Fori(0, outs // 2) as i:
                    for r in range(2):
                        sp.wait_ge(product[r].sem, product[r].at(1, i - 1))
                        sp.dma_start(wb[r][:, :, :], row_of(w, i * 2 + r)).then_inc(loaded[r].sem, 16)

            @block.tensor
            def _(pe):
                with pe.Fori(0, outs // 2) as i:
                    for r in range(2):
                        pe.wait_ge(loaded[r].sem, loaded[r].at(1, i))
                        pe.wait_ge(taken[r].sem, taken[r].at(1, i - 1))
                        for c, (a, n) in enumerate(cols):
                            for k in range(K):
                                mm = nc.tensor.matmul(bank[3 * r + c][:, 0:n], wb[r][:, k, :], rhs[:, k, a:a + n],
                                                      start=(k == 0), stop=(k == K - 1))
                        mm.then_inc(product[r].sem, 1)

            @block.vector
            def _(v):
                if how == "store":
                    return
                for r in range(2):
                    v.sem_inc(product[r].sem, 1)
                    v.sem_inc(taken[r].sem, 1)
                with v.Fori(0, outs // 2) as i:
                    for r in range(2):
                        v.wait_ge(product[r].sem, product[r].at(1, i))
                        for c, (a, n) in enumerate(cols):
                            dst = to[:, bass.ds(i * 2 + r, 1), a:a + n].rearrange("p o n -> p (o n)")
                            if how == "add":
                                op = nc.vector.tensor_tensor(dst, dst, bank[3 * r + c][:, 0:n], ALU.add)
                            else:
                                op = nc.vector.tensor_copy(dst, bank[3 * r + c][:, 0:n])
                        op.then_inc(taken[r].sem, 1)

            @block.gpsimd
            def _(pool):
                if how == "store" and wide > tokens:
                    for r in range(2):
                        nc.gpsimd.memset(stage[r][:, tokens:wide], 0.0).then_inc(zeroed.sem, 1)

            @block.scalar
            def _(act):
                if how != "store":
                    return
                for r in range(2):
                    act.sem_inc(product[r].sem, 1)
                    act.sem_inc(taken[r].sem, 1)
                    act.sem_inc(stored[r].sem, 16)
                if wide > tokens:
                    act.wait_ge(zeroed.sem, zeroed.at(2))
                with act.Fori(0, outs // 2) as i:
                    for r in range(2):
                        act.wait_ge(product[r].sem, product[r].at(1, i))
                        act.wait_ge(stored[r].sem, stored[r].at(1, i - 1))
                        for c, (a, n) in enumerate(cols):
                            op = nc.scalar.activation(stage[r][:, a:a + n], bank[3 * r + c][:, 0:n], ACT.Copy)
                        op.then_inc(taken[r].sem, 1)
                        act.wait_ge(taken[r].sem, taken[r].at(1, i))
                        act.dma_start(row_of(to, i * 2 + r), stage[r][:, :]).then_inc(stored[r].sem, 16)
                for r in range(2):
                    act.wait_ge(stored[r].sem, stored[r].at(1, outs // 2 - 1))


def load(nc, ctx, name, pairs):
    sig = Signal(nc, ctx, f"{name}_loaded", 1, 16)
    with nc.Block() as block:
        @block.sync
        def _(sp):
            for to, src in pairs:
                sp.dma_start(to, src).then_inc(sig.sem, 16)
            sp.wait_ge(sig.sem, sig.at(len(pairs)))


def memory_kv(nc, bank, const, d, out, mkT, mv):
    with Phase(nc) as ctx:
        mn = ctx.enter_context(nc.sbuf_tensor("mem_normed", [P, KT, MEM], F32))
        wv = ctx.enter_context(nc.sbuf_tensor("w_mem_v", [P, KT, D_MODEL], F32))
        load(nc, ctx, "mem", [(mn[:, :, :], d["memT"]), (wv[:, :, :], d["w_mv"])])
        rmsnorm(nc, bank, "mem_norm", mn, mn, const["gains"][:, 2, :], const["ones"][:, :], MEM, D_MODEL)
        linear(nc, bank, "mem_k", mn, d["w_mk"], KT, KT, MEM, "copy", mkT)
        product, ready = Signal(nc, ctx, "mem_v_product", 4), Signal(nc, ctx, "mem_v_ready", 4)
        stored = Signal(nc, ctx, "mem_stored", 2, 16)
        with nc.Block() as block:
            @block.tensor
            def _(pe):
                for m in range(2):
                    for half in range(2):
                        for k in range(KT):
                            mm = nc.tensor.matmul(bank[2 * m + half][:, :], mn[:, k, P * m:P * m + P],
                                                  wv[:, k, 512 * half:512 * half + 512], start=(k == 0), stop=(k == KT - 1))
                        mm.then_inc(product.sem, 1)

            @block.vector
            def _(v):
                for m in range(2):
                    for half in range(2):
                        v.wait_ge(product.sem, product.at(2 * m + half + 1))
                        nc.vector.tensor_copy(mv[:, m, 512 * half:512 * half + 512], bank[2 * m + half][:, :]).then_inc(ready.sem, 1)

            @block.sync
            def _(sp):
                sp.dma_start(out["mem_k"], mkT[:, :, :]).then_inc(stored.sem, 16)
                sp.wait_ge(ready.sem, ready.at(4))
                sp.dma_start(out["mem_v"], mv[:, :, :]).then_inc(stored.sem, 16)
                sp.wait_ge(stored.sem, stored.at(2))


def attend_prompt(nc, bank, const, d, qx, mkT, mv, ao):
    H, SC = MEM_HEADS, (D_MODEL // MEM_HEADS) ** -0.5
    with Phase(nc) as ctx:
        def sb(name, shape):
            return ctx.enter_context(nc.sbuf_tensor(f"att_{name}", shape, F32))

        def signal(name, per=1, unit=1, primed=False):
            return Signal(nc, ctx, f"att_{name}", per, unit, primed)
        q, pr, pT = sb("q", [P, KT, P]), sb("probs", [P, H, MEM]), sb("probs_t", [P, 2, H, P])
        top, neg, total, inv = (sb(x, [P, H]) for x in ("top", "neg_top", "total", "inv"))
        loaded, scores = signal("loaded", 1, 16), signal("scores", 1, 1, True)
        top_ready, exped, probs, turned, pT_ready = (signal(x) for x in ("top_ready", "exp_ready", "probs_ready", "turned", "probs_t_ready"))
        product, taken = signal("product"), signal("taken", 1, 1, True)
        vec = Steps(nc, ctx, "att_vector_steps", 2)
        with nc.Block() as block:
            @block.sync
            def _(sp):
                with sp.Fori(0, SEQ // P) as i:
                    sp.wait_ge(scores.sem, scores.at(1, i - 1))
                    sp.dma_start(q[:, :, :], qx[:, :, bass.ds(i * P, P)].rearrange("k p n -> p k n")).then_inc(loaded.sem, 16)

            @block.tensor
            def _(pe):
                with pe.Fori(0, SEQ // P) as i:
                    pe.wait_ge(loaded.sem, loaded.at(1, i))
                    pe.wait_ge(taken.sem, taken.at(1, i - 1))
                    for h in range(H):
                        for k in range(2):
                            mm = nc.tensor.matmul(bank[h // 2][:, MEM * (h % 2):MEM * (h % 2) + MEM], q[:, 2 * h + k, :],
                                                  mkT[:, 2 * h + k, :], start=(k == 0), stop=(k == 1))
                    mm.then_inc(scores.sem, 1)
                    pe.wait_ge(probs.sem, probs.at(1, i))
                    for m in range(2):
                        for h in range(H):
                            mm = nc.tensor.transpose(bank[2 + m][:, P * h:P * h + P], pr[:, h, P * m:P * m + P], const["ident"][:, :])
                    mm.then_inc(turned.sem, 1)
                    pe.wait_ge(pT_ready.sem, pT_ready.at(1, i))
                    for k in range(KT):
                        for m in range(2):
                            mm = nc.tensor.matmul(bank[4 + k // 4][:, P * (k % 4):P * (k % 4) + P], mv[:, m, P * k:P * k + P],
                                                  pT[:, m, k // 2, :], start=(m == 0), stop=(m == 1))
                    mm.then_inc(product.sem, 1)

            @block.scalar
            def _(act):
                act.sem_inc(scores.sem, 1)
                act.sem_inc(taken.sem, 1)
                with act.Fori(0, SEQ // P) as i:
                    act.wait_ge(top_ready.sem, top_ready.at(1, i))
                    for h in range(H):
                        op = nc.scalar.activation(pr[:, h, :], bank[h // 2][:, MEM * (h % 2):MEM * (h % 2) + MEM], ACT.Exp,
                                                  bias=neg[:, h:h + 1], scale=SC, accum_out=total[:, h:h + 1])
                    op.then_inc(exped.sem, 1)
                    act.wait_ge(turned.sem, turned.at(1, i))
                    for m in range(2):
                        op = nc.scalar.activation(pT[:, m, :, :], bank[2 + m][:, :].rearrange("p (h n) -> p h n", n=P), ACT.Copy)
                    op.then_inc(pT_ready.sem, 1)

            @block.vector
            def _(v):
                with v.Fori(0, SEQ // P) as i:
                    vec.n = 0
                    v.wait_ge(scores.sem, scores.at(1, i))
                    for b in range(2):
                        op = nc.vector.tensor_reduce(top[:, 2 * b:2 * b + 2], bank[b][:, :].rearrange("p (h n) -> p h n", n=MEM), AX.X, ALU.max)
                    op.then_inc(vec.step(), 1)
                    v.wait_ge(vec.sem, vec.now(i))
                    nc.vector.tensor_scalar(neg[:, :], top[:, :], -SC, None, ALU.mult).then_inc(top_ready.sem, 1)
                    v.wait_ge(exped.sem, exped.at(1, i))
                    nc.vector.reciprocal(inv[:, :], total[:, :]).then_inc(vec.step(), 1)
                    v.wait_ge(vec.sem, vec.now(i))
                    nc.vector.tensor_tensor(pr[:, :, :], pr[:, :, :], inv[:, :, None].to_broadcast([P, H, MEM]), ALU.mult).then_inc(probs.sem, 1)
                    v.wait_ge(product.sem, product.at(1, i))
                    for b in range(2):
                        op = nc.vector.tensor_copy(ao[:, 4 * b:4 * b + 4, bass.ds(i * P, P)], bank[4 + b][:, :].rearrange("p (k n) -> p k n", n=P))
                    op.then_inc(taken.sem, 1)


def attend_sample(nc, bank, const, d, qx, ao):
    H, SC, R = MEM_HEADS, (D_MODEL // MEM_HEADS) ** -0.5, MEM_HEADS * STEPS
    with Phase(nc) as ctx:
        def sb(name, shape):
            return ctx.enter_context(nc.sbuf_tensor(f"satt_{name}", shape, F32))

        def signal(name, per=1, unit=1, primed=False):
            return Signal(nc, ctx, f"satt_{name}", per, unit, primed)
        q, qm = sb("q", [P, KT, SAMPLE]), sb("q_masked", [P, KT, 4, H, STEPS])
        K, V = sb("k", [P, 4, KT, MEM]), sb("v", [P, 4, 2, D_MODEL])
        pr, pT = sb("probs", [P, MEM]), sb("probs_t", [P, 2, P])
        top, neg, total, inv = (sb(x, [P, 1]) for x in ("top", "neg_top", "total", "inv"))
        q_loaded, zeroed = signal("q_loaded", 1, 16), signal("zeroed")
        k_loaded = [signal(f"k_loaded{b}", 1, 16) for b in range(4)]
        v_loaded = [signal(f"v_loaded{b}", 1, 16) for b in range(4)]
        masked, scores = signal("masked"), signal("scores", 1, 1, True)
        top_ready, exped, probs, turned, pT_ready = (signal(x) for x in ("top_ready", "exp_ready", "probs_ready", "turned", "probs_t_ready"))
        product, taken = signal("product"), signal("taken", 1, 1, True)
        vec = Steps(nc, ctx, "satt_vector_steps", 2)
        with nc.Block() as block:
            @block.sync
            def _(sp):
                sp.dma_start(q[:, :, :], qx[:, :, SEQ:T].rearrange("k p n -> p k n")).then_inc(q_loaded.sem, 16)
                with sp.Fori(0, SEQS // 4) as i:
                    sp.wait_ge(scores.sem, scores.at(1, i - 1))
                    for b in range(4):
                        sp.dma_start(K[:, b, :, :], row_of(d["cache_k"], i * 4 + b)).then_inc(k_loaded[b].sem, 16)
                    sp.wait_ge(taken.sem, taken.at(1, i - 1))
                    for b in range(4):
                        sp.dma_start(V[:, b, :, :], row_of(d["cache_v"], i * 4 + b)).then_inc(v_loaded[b].sem, 16)

            @block.gpsimd
            def _(pool):
                nc.gpsimd.memset(qm[:, :, :, :, :].rearrange("p k b h n -> p (k b h n)"), 0.0).then_inc(zeroed.sem, 1)

            @block.tensor
            def _(pe):
                with pe.Fori(0, SEQS // 4) as i:
                    pe.wait_ge(masked.sem, masked.at(1, i))
                    pe.wait_ge(taken.sem, taken.at(1, i - 1))
                    for b in range(4):
                        pe.wait_ge(k_loaded[b].sem, k_loaded[b].at(1, i))
                        for k in range(KT):
                            mm = nc.tensor.matmul(bank[0][R * b:R * b + R, 0:MEM], qm[:, k, b, :, :].rearrange("p h n -> p (h n)"),
                                                  K[:, b, k, :], start=(k == 0), stop=(k == KT - 1))
                    mm.then_inc(scores.sem, 1)
                    pe.wait_ge(probs.sem, probs.at(1, i))
                    for m in range(2):
                        mm = nc.tensor.transpose(bank[2][:, P * m:P * m + P], pr[:, P * m:P * m + P], const["ident"][:, :])
                    mm.then_inc(turned.sem, 1)
                    pe.wait_ge(pT_ready.sem, pT_ready.at(1, i))
                    for b in range(4):
                        pe.wait_ge(v_loaded[b].sem, v_loaded[b].at(1, i))
                        for k in range(KT):
                            a = STEPS * (4 * k + b)
                            for m in range(2):
                                p0 = R * b + STEPS * (k // 2)
                                mm = nc.tensor.matmul(bank[4][:, a:a + STEPS], V[:, b, m, P * k:P * k + P],
                                                      pT[:, m, p0:p0 + STEPS], start=(m == 0), stop=(m == 1))
                    mm.then_inc(product.sem, 1)

            @block.scalar
            def _(act):
                act.sem_inc(scores.sem, 1)
                act.sem_inc(taken.sem, 1)
                with act.Fori(0, SEQS // 4) as i:
                    act.wait_ge(top_ready.sem, top_ready.at(1, i))
                    nc.scalar.activation(pr[:, :], bank[0][:, 0:MEM], ACT.Exp, bias=neg[:, 0:1], scale=SC,
                                         accum_out=total[:, 0:1]).then_inc(exped.sem, 1)
                    act.wait_ge(turned.sem, turned.at(1, i))
                    nc.scalar.activation(pT[:, :, :], bank[2][:, 0:2 * P].rearrange("p (m n) -> p m n", n=P), ACT.Copy).then_inc(pT_ready.sem, 1)

            @block.vector
            def _(v):
                v.wait_ge(q_loaded.sem, q_loaded.at(1))
                v.wait_ge(zeroed.sem, zeroed.at(1))
                with v.Fori(0, SEQS // 4) as i:
                    vec.n = 0
                    for h in range(H):
                        op = nc.vector.tensor_copy(qm[:, 2 * h:2 * h + 2, :, h, :],
                                                   q[:, 2 * h:2 * h + 2, bass.ds(i * (4 * STEPS), 4 * STEPS)].rearrange("p k (b n) -> p k b n", n=STEPS))
                    op.then_inc(masked.sem, 1)
                    v.wait_ge(scores.sem, scores.at(1, i))
                    nc.vector.tensor_reduce(top[:, :], bank[0][:, 0:MEM], AX.X, ALU.max).then_inc(vec.step(), 1)
                    v.wait_ge(vec.sem, vec.now(i))
                    nc.vector.tensor_scalar(neg[:, :], top[:, :], -SC, None, ALU.mult).then_inc(top_ready.sem, 1)
                    v.wait_ge(exped.sem, exped.at(1, i))
                    nc.vector.reciprocal(inv[:, :], total[:, :]).then_inc(vec.step(), 1)
                    v.wait_ge(vec.sem, vec.now(i))
                    nc.vector.tensor_scalar(pr[:, :], pr[:, :], inv[:, 0:1], None, ALU.mult).then_inc(probs.sem, 1)
                    v.wait_ge(product.sem, product.at(1, i))
                    nc.vector.tensor_copy(ao[:, :, bass.ds(i * (4 * STEPS) + SEQ, 4 * STEPS)],
                                          bank[4][:, 0:KT * 4 * STEPS].rearrange("p (k n) -> p k n", n=4 * STEPS)).then_inc(taken.sem, 1)


def route(nc, bank, const, d, qp, gd):
    PH, TK, NK = PHEADS, TOPK, NKEYS
    LOW = -3.0e38
    PICK = 4
    with Phase(nc) as ctx:
        def sb(name, shape, dt=F32):
            return ctx.enter_context(nc.sbuf_tensor(f"route_{name}", shape, dt))

        def signal(name, per=1, unit=1, primed=False):
            return Signal(nc, ctx, f"route_{name}", per, unit, primed)
        keys, iota = sb("keys", [P, 2, NK]), sb("iota", [P, NK])
        q, s, s2 = sb("q", [P, 2 * PH, P]), sb("scores", [P, 2 * PH, NK]), sb("scores_left", [P, 2 * PH, NK])
        top, ix = sb("top", [P, 2 * PH, TK]), sb("top_index", [P, 2 * PH, TK], U32)
        ixf = sb("top_index_f", [P, 2 * PH, TK])
        cand, cand2 = sb("sums", [P, PH, TK, TK]), sb("sums_left", [P, PH, TK * TK])
        best, pos = sb("best", [P, PH, TK]), sb("position", [P, PH, TK], U32)
        half, halff = sb("rank", [P, 2, PH * TK], U32), sb("rank_f", [P, 2, PH * TK])
        total, blank = sb("total", [P, PH]), sb("blank", [P, 1])
        pick = sb("picks", [P, 3, P])
        pickT = sb("picks_t", [P, 3, P])
        E = [[sb(f"onehot{x}{r}", [P, PICK, NK]) for r in range(2)] for x in "ij"]
        G = sb("gates", [P, NK, P])
        once, loaded = signal("keys_loaded", 2, 16), signal("loaded", 1, 16)
        scored, s_ready = signal("scored", 1, 1, True), signal("scores_ready", 1)
        shifted, exped = signal("shifted"), signal("exp_ready")
        picked, turned, pickT_ready = signal("picked"), signal("turned"), signal("picks_t_ready")
        onehots = [signal(f"onehots_ready{r}") for r in range(2)]
        gmm = [signal(f"gates_product{r}", 1, 1, True) for r in range(2)]
        gout = [signal(f"gates_taken{r}", 1, 1, True) for r in range(2)]
        stored = signal("stored", 1, 16, True)
        VSTEPS = 17
        vec = Steps(nc, ctx, "route_vector_steps", VSTEPS)
        TURNS = P // (2 * PICK)

        with nc.Block() as block:
            @block.sync
            def _(sp):
                sp.dma_start(keys[:, :, :], d["keysT"]).then_inc(once.sem, 16)
                sp.dma_start(iota[:, :], d["iota"].partition_broadcast(P)).then_inc(once.sem, 16)
                with sp.Fori(0, NC) as i:
                    sp.wait_ge(scored.sem, scored.at(1, i - 1))
                    sp.dma_start(q[:, :, :], qp[:, :, bass.ds(i * P, P)].rearrange("k p n -> p k n")).then_inc(loaded.sem, 16)
                    for r in range(2):
                        sp.wait_ge(gout[r].sem, gout[r].at(1, i * TURNS + (TURNS - 1)))
                    sp.dma_start(gd[:, :, bass.ds(i * P, P)].rearrange("j i n -> i j n"), G[:, :, :]).then_inc(stored.sem, 16)
                sp.wait_ge(stored.sem, stored.at(1, NC - 1))

            @block.tensor
            def _(pe):
                pe.wait_ge(once.sem, once.at(2))
                with pe.Fori(0, NC) as i:
                    pe.wait_ge(loaded.sem, loaded.at(1, i))
                    for n in range(2 * PH):
                        mm = nc.tensor.matmul(bank[n // 4][:, P * (n % 4):P * (n % 4) + P], q[:, n, :], keys[:, n % 2, :], start=True, stop=True)
                    mm.then_inc(scored.sem, 1)
                    pe.wait_ge(picked.sem, picked.at(1, i))
                    for x in range(3):
                        mm = nc.tensor.transpose(bank[4][:, P * x:P * x + P], pick[:, x, :], const["ident"][:, :])
                    mm.then_inc(turned.sem, 1)
                    with pe.Fori(0, TURNS) as j:
                        w = i * TURNS + j
                        for r in range(2):
                            pe.wait_ge(onehots[r].sem, onehots[r].at(1, w))
                            pe.wait_ge(gout[r].sem, gout[r].at(1, w - 1))
                            for t in range(PICK):
                                mm = nc.tensor.matmul(bank[5 + r][:, P * t:P * t + P], E[0][r][:, t, :], E[1][r][:, t, :], start=True, stop=True)
                            mm.then_inc(gmm[r].sem, 1)

            @block.scalar
            def _(act):
                act.sem_inc(scored.sem, 1)
                act.sem_inc(stored.sem, 16)
                for r in range(2):
                    act.sem_inc(gmm[r].sem, 1)
                    act.sem_inc(gout[r].sem, 1)
                with act.Fori(0, NC) as i:
                    act.wait_ge(scored.sem, scored.at(1, i))
                    for b in range(4):
                        op = nc.scalar.activation(s[:, 4 * b:4 * b + 4, :], bank[b][:, :].rearrange("p (n k) -> p n k", k=NK), ACT.Copy)
                    op.then_inc(s_ready.sem, 1)
                    act.wait_ge(shifted.sem, shifted.at(1, i))
                    nc.scalar.activation(best[:, :, :], best[:, :, :], ACT.Exp).then_inc(exped.sem, 1)
                    act.wait_ge(turned.sem, turned.at(1, i))
                    nc.scalar.activation(pickT[:, :, :], bank[4][:, 0:3 * P].rearrange("p (x n) -> p x n", n=P), ACT.Copy).then_inc(pickT_ready.sem, 1)
                    with act.Fori(0, TURNS) as j:
                        w = i * TURNS + j
                        for r in range(2):
                            act.wait_ge(stored.sem, stored.at(1, i - 1))
                            act.wait_ge(gmm[r].sem, gmm[r].at(1, w))
                            nc.scalar.activation(G[:, :, bass.ds(j * (2 * PICK) + PICK * r, PICK)].rearrange("p j n -> p n j"),
                                                 bank[5 + r][:, :].rearrange("p (n j) -> p n j", j=NK), ACT.Copy).then_inc(gout[r].sem, 1)

            @block.vector
            def _(v):
                v.wait_ge(once.sem, once.at(2))
                with v.Fori(0, NC) as i:
                    vec.n = 0

                    def then(op):
                        op.then_inc(vec.step(), 1)
                        v.wait_ge(vec.sem, vec.now(i))

                    def settled(op):
                        then(op)
                        nc.vector.memset(blank[:, :], 0.0)

                    def top16(rows, values, left, at, index):
                        settled([nc.vector.max(at(n)[:, 0:8], values(n)) for n in range(rows)][-1])
                        for n in range(rows):
                            nc.vector.max_index(index(n)[:, 0:8], at(n)[:, 0:8], values(n))
                            op = nc.vector.match_replace(left(n), at(n)[:, 0:8], values(n), LOW)
                        settled(op)
                        settled([nc.vector.max(at(n)[:, 8:16], left(n)) for n in range(rows)][-1])
                        then([nc.vector.max_index(index(n)[:, 8:16], at(n)[:, 8:16], left(n)) for n in range(rows)][-1])
                    v.wait_ge(s_ready.sem, s_ready.at(1, i))
                    nc.vector.memset(blank[:, :], 0.0)
                    top16(2 * PH, lambda n: s[:, n, :], lambda n: s2[:, n, :], lambda n: top[:, n, :], lambda n: ix[:, n, :])
                    halves = top[:, :, :].rearrange("p (h c) k -> p h c k", c=2)
                    for h in range(PH):
                        op = nc.vector.tensor_tensor(cand[:, h, :, :], halves[:, h, 0, :, None].to_broadcast([P, TK, TK]),
                                                     halves[:, h, 1, None, :].to_broadcast([P, TK, TK]), ALU.add)
                    settled(op)
                    flat = cand[:, :, :, :].rearrange("p h a b -> p h (a b)")
                    top16(PH, lambda n: flat[:, n, :], lambda n: cand2[:, n, :], lambda n: best[:, n, :], lambda n: pos[:, n, :])
                    flatpos = pos[:, :, :].rearrange("p h k -> p (h k)")
                    nc.vector.tensor_scalar(half[:, 0, :], flatpos, 4, None, ALU.logical_shift_right)
                    nc.vector.tensor_scalar(half[:, 1, :], flatpos, 15, None, ALU.bitwise_and)
                    nc.vector.tensor_copy(ixf[:, :, :], ix[:, :, :])
                    then(nc.vector.tensor_copy(total[:, :], best[:, :, 0]))
                    nc.vector.tensor_copy(halff[:, :, :], half[:, :, :])
                    nc.vector.tensor_tensor(best[:, :, :], best[:, :, :], total[:, :, None].to_broadcast([P, PH, TK]),
                                            ALU.subtract).then_inc(shifted.sem, 1)
                    v.wait_ge(shifted.sem, shifted.at(1, i))
                    index = ixf[:, :, :].rearrange("p (h c) k -> p h c k", c=2)
                    for c in range(2):
                        eq = cand[:, :, :, :].rearrange("p h a b -> p (h a) b")
                        then(nc.vector.tensor_tensor(eq, halff[:, c, :, None].to_broadcast([P, PH * TK, TK]),
                                                     iota[:, None, 0:TK].to_broadcast([P, PH * TK, TK]), ALU.is_equal))
                        for h in range(PH):
                            op = nc.vector.tensor_tensor(cand[:, h, :, :], cand[:, h, :, :], index[:, h, c, None, :].to_broadcast([P, TK, TK]), ALU.mult)
                        then(op)
                        if c == 0:
                            then(nc.vector.tensor_reduce(pick[:, 1, :], eq, AX.X, ALU.add))
                        else:
                            nc.vector.tensor_reduce(pick[:, 2, :], eq, AX.X, ALU.add)
                    v.wait_ge(exped.sem, exped.at(1, i))
                    then(nc.vector.tensor_reduce(total[:, :], best[:, :, :], AX.X, ALU.add))
                    then(nc.vector.reciprocal(total[:, :], total[:, :]))
                    nc.vector.tensor_tensor(pick[:, 0, :].rearrange("p (h k) -> p h k", k=TK), best[:, :, :],
                                            total[:, :, None].to_broadcast([P, PH, TK]), ALU.mult).then_inc(picked.sem, 1)
                    assert vec.n == VSTEPS, vec.n
                    with v.Fori(0, TURNS) as j:
                        w = i * TURNS + j
                        for r in range(2):
                            v.wait_ge(pickT_ready.sem, pickT_ready.at(1, i))
                            v.wait_ge(gmm[r].sem, gmm[r].at(1, w - 1))
                            for t in range(PICK):
                                at = bass.ds(j * (2 * PICK) + (PICK * r + t), 1)
                                nc.vector.tensor_scalar(E[0][r][:, t, :], iota[:, :], pickT[:, 1, at], None, ALU.is_equal)
                                op = nc.vector.tensor_scalar(E[1][r][:, t, :], iota[:, :], pickT[:, 2, at], pickT[:, 0, at],
                                                             ALU.is_equal, ALU.mult)
                            op.then_inc(onehots[r].sem, 1)


def experts(nc, bank, const, d, gd, fn, h):
    GROUP = 8
    with Phase(nc) as ctx:
        def sb(name, shape):
            return ctx.enter_context(nc.sbuf_tensor(f"exp_{name}", shape, F32))

        def signal(name, per=1, unit=1, primed=False):
            return Signal(nc, ctx, f"exp_{name}", per, unit, primed)
        U = [sb(f"u{r}", [P, KT, P]) for r in range(2)]
        G = [sb(f"g{r}", [P, T]) for r in range(2)]
        V, Aj = sb("v", [P, GROUP, D_MODEL]), sb("hidden", [P, GROUP, T])
        u_loaded = [signal(f"u_loaded{r}", GROUP // 2, 16) for r in range(2)]
        g_loaded = [signal(f"g_loaded{r}", GROUP // 2, 16) for r in range(2)]
        v_loaded = [signal(f"v_loaded{j}", 1, 16) for j in range(GROUP)]
        hidden = signal("hidden_product", 3 * GROUP, 1, True)
        gelu = signal("gelu_ready", 3 * GROUP, 1, True)
        gated = signal("gated", GROUP, 1, True)
        product, added = signal("product", 3 * KT, 1, True), signal("added", 3 * KT, 1, True)
        TURNS = NKEYS // GROUP
        with nc.Block() as block:
            @block.sync
            def _(sp):
                with sp.Fori(0, TURNS) as i:
                    for j in range(GROUP):
                        r = j % 2
                        if j >= 2:
                            sp.wait_ge(hidden.sem, hidden.at(3 * (j - 1), i))
                            sp.dma_start(U[r][:, :, :], row_of(d["peer_u"], i * GROUP + j)).then_inc(u_loaded[r].sem, 16)
                            sp.wait_ge(gated.sem, gated.at(j - 1, i))
                        else:
                            sp.wait_ge(hidden.sem, hidden.at(3 * (GROUP - 2 + j) + 3, i - 1))
                            sp.dma_start(U[r][:, :, :], row_of(d["peer_u"], i * GROUP + j)).then_inc(u_loaded[r].sem, 16)
                            sp.wait_ge(gated.sem, gated.at(GROUP - 1 + j, i - 1))
                        sp.dma_start(G[r][:, :], row_of(gd, i * GROUP + j)[:, 0:T]).then_inc(g_loaded[r].sem, 16)
                        if j == 1:
                            sp.wait_ge(product.sem, product.at(3 * KT, i - 1))
                            for n in range(GROUP):
                                sp.dma_start(V[:, n, :], row_of(d["peer_v"], i * GROUP + n)).then_inc(v_loaded[n].sem, 16)

            @block.tensor
            def _(pe):
                with pe.Fori(0, TURNS) as i:
                    for j in range(GROUP):
                        pe.wait_ge(u_loaded[j % 2].sem, u_loaded[j % 2].at(j // 2 + 1, i))
                        for c, (a, n) in enumerate(CHUNKS):
                            m = 3 * j + c
                            if m >= 4:
                                pe.wait_ge(gelu.sem, gelu.at(m - 3, i))
                            else:
                                pe.wait_ge(gelu.sem, gelu.at(3 * GROUP - 3 + m, i - 1))
                            for k in range(KT):
                                mm = nc.tensor.matmul(bank[m % 4][:, 0:n], U[j % 2][:, k, :], fn[:, k, a:a + n], start=(k == 0), stop=(k == KT - 1))
                            mm.then_inc(hidden.sem, 1)
                    for j in range(GROUP):
                        pe.wait_ge(v_loaded[j].sem, v_loaded[j].at(1, i))
                    pe.wait_ge(gated.sem, gated.at(GROUP, i))
                    for k in range(KT):
                        for c, (a, n) in enumerate(CHUNKS):
                            m = 3 * k + c
                            if m >= 4:
                                pe.wait_ge(added.sem, added.at(m - 3, i))
                            else:
                                pe.wait_ge(added.sem, added.at(3 * KT - 3 + m, i - 1))
                            for j in range(GROUP):
                                mm = nc.tensor.matmul(bank[4 + m % 4][:, 0:n], V[:, j, P * k:P * k + P], Aj[:, j, a:a + n], start=(j == 0), stop=(j == GROUP - 1))
                            mm.then_inc(product.sem, 1)

            @block.scalar
            def _(act):
                act.sem_inc(hidden.sem, 3 * GROUP)
                act.sem_inc(gelu.sem, 3 * GROUP)
                act.sem_inc(gated.sem, GROUP)
                act.sem_inc(product.sem, 3 * KT)
                act.sem_inc(added.sem, 3 * KT)
                with act.Fori(0, TURNS) as i:
                    for j in range(GROUP):
                        for c, (a, n) in enumerate(CHUNKS):
                            act.wait_ge(hidden.sem, hidden.at(3 * j + c + 1, i))
                            nc.scalar.activation(Aj[:, j, a:a + n], bank[(3 * j + c) % 4][:, 0:n], ACT.Gelu).then_inc(gelu.sem, 1)

            @block.vector
            def _(v):
                with v.Fori(0, TURNS) as i:
                    for j in range(GROUP):
                        v.wait_ge(gelu.sem, gelu.at(3 * j + 3, i))
                        v.wait_ge(g_loaded[j % 2].sem, g_loaded[j % 2].at(j // 2 + 1, i))
                        nc.vector.tensor_tensor(Aj[:, j, :], Aj[:, j, :], G[j % 2][:, :], ALU.mult).then_inc(gated.sem, 1)
                    for k in range(KT):
                        for c, (a, n) in enumerate(CHUNKS):
                            m = 3 * k + c
                            v.wait_ge(product.sem, product.at(m + 1, i))
                            if m == 0:
                                v.wait_ge(added.sem, added.at(3 * KT, i - 1))
                            nc.vector.tensor_tensor(h[:, k, a:a + n], h[:, k, a:a + n], bank[4 + m % 4][:, 0:n], ALU.add).then_inc(added.sem, 1)


def trunk(nc, d, out):
    with Phase(nc) as ctx:
        bank = psum_banks(nc, ctx, "psum")
        mix = nc.dram_tensor("mixed_heads", (2 * KT, P, T), F32, kind="Internal").ap()
        const = {n: ctx.enter_context(nc.sbuf_tensor(f"const_{n}", s, F32)) for n, s in (
            ("ident", [P, P]), ("ones", [P, P]), ("tri", [P, 2, P]), ("total", [P, 2, P]), ("seq_of", [P, SEQS]),
            ("gains", [P, 5, KT]))}
        eps = const["eps"] = ctx.enter_context(nc.sbuf_tensor("const_eps", [P, 1], F32))
        names = [n for n in const if n != "eps"]
        loaded = Signal(nc, ctx, "setup_loaded", 1, 16)
        with Phase(nc) as mixer:
            def sb(name, shape):
                return mixer.enter_context(nc.sbuf_tensor(name, shape, F32))
            xn = sb("x_normed", [P, KT, TP])
            tab = sb("gate_table", [P, 5, NC, GATED])
            const["incl"] = sb("const_incl", [P, TP])
            names += ["incl"]
            with Phase(nc) as first:
                x = first.enter_context(nc.sbuf_tensor("x_in", [P, KT, T], F32))
                ws = first.enter_context(nc.sbuf_tensor("w_small", [P, KT, 32], F32))
                with nc.Block() as block:
                    @block.sync
                    def _(sp):
                        for n in names:
                            sp.dma_start(const[n].ap() if hasattr(const[n], "ap") else const[n], d[n]).then_inc(loaded.sem, 16)
                        for k in range(KT):
                            sp.dma_start(x[:, k, :], d["xT"][k]).then_inc(loaded.sem, 16)
                        sp.dma_start(ws[:, :, :], d["w_small"]).then_inc(loaded.sem, 16)
                        sp.wait_ge(loaded.sem, loaded.at(len(names) + KT + 1))

                    @block.vector
                    def _(v):
                        nc.vector.memset(eps[:, :], EPS)
                        nc.vector.memset(xn[:, :, T:TP], 0.0)
                rmsnorm(nc, bank, "mix_norm", x, xn, const["gains"][:, 0, :], const["ones"][:, :], T, D_MODEL)
                gates(nc, bank, xn, ws, const["tri"], const["total"], d, tab)
            delta_net(nc, bank, xn, tab, d, const, mix, out)
            ssd(nc, bank, xn, tab, d, const, mix, out)
        h = ctx.enter_context(nc.sbuf_tensor("residual", [P, KT, T], F32))
        with Phase(nc) as part:
            heads = part.enter_context(nc.sbuf_tensor("heads", [P, 2 * KT, T], F32))
            load(nc, part, "heads", [(h[:, k, :], d["xT"][k]) for k in range(KT)]
                 + [(heads[:, k, :], mix[k]) for k in range(2 * KT)])
            linear(nc, bank, "w_out", heads, d["w_out"], 2 * KT, KT, T, "add", h)
        with Phase(nc) as part:
            mkT = part.enter_context(nc.sbuf_tensor("mem_keys", [P, KT, MEM], F32))
            mv = part.enter_context(nc.sbuf_tensor("mem_values", [P, 2, D_MODEL], F32))
            qx = nc.dram_tensor("attention_q", (KT, P, T), F32, kind="Internal").ap()
            memory_kv(nc, bank, const, d, out, mkT, mv)
            with Phase(nc) as inner:
                cn = inner.enter_context(nc.sbuf_tensor("c_normed", [P, KT, T], F32))
                rmsnorm(nc, bank, "att_norm", h, cn, const["gains"][:, 1, :], const["ones"][:, :], T, D_MODEL)
                linear(nc, bank, "w_xq", cn, d["w_xq"], KT, KT, T, "store", qx)
            ao = part.enter_context(nc.sbuf_tensor("attended", [P, KT, T], F32))
            attend_prompt(nc, bank, const, d, qx, mkT, mv, ao)
            attend_sample(nc, bank, const, d, qx, ao)
            linear(nc, bank, "w_xo", ao, d["w_xo"], KT, KT, T, "add", h)
        with Phase(nc) as part:
            fn = part.enter_context(nc.sbuf_tensor("f_normed", [P, KT, T], F32))
            qp = nc.dram_tensor("retrieval_q", (2 * PHEADS, P, TP), F32, kind="Internal").ap()
            gd = nc.dram_tensor("expert_gates", (NKEYS, P, TP), F32, kind="Internal").ap()
            rmsnorm(nc, bank, "ffn_norm", h, fn, const["gains"][:, 3, :], const["ones"][:, :], T, D_MODEL)
            linear(nc, bank, "w_pq", fn, d["w_pq"], KT, 2 * PHEADS, T, "store", qp)
            route(nc, bank, const, d, qp, gd)
            experts(nc, bank, const, d, gd, fn, h)
        with Phase(nc) as part:
            y = part.enter_context(nc.sbuf_tensor("y_out", [P, KT, T], F32))
            rmsnorm(nc, bank, "final_norm", h, y, const["gains"][:, 4, :], const["ones"][:, :], T, D_MODEL)
            stored = Signal(nc, part, "y_stored", 1, 16)
            with nc.Block() as block:
                @block.sync
                def _(sp):
                    for k in range(KT):
                        sp.dma_start(out["y"][k], y[:, k, :]).then_inc(stored.sem, 16)
                    sp.wait_ge(stored.sem, stored.at(KT))


def layouts(i):
    f = lambda a: np.ascontiguousarray(a)
    tiles = lambda a, k: a.reshape(k, P, -1).transpose(1, 0, 2)
    w_in = i["w_in"][0]
    qkv, xbc, z_dn, z_ssm, small = np.split(w_in, np.cumsum([3072, 1536, 1024, 1024]), axis=1)
    d = {}
    x = np.concatenate([i["x_prompt"][0], i["x_sample"].reshape(SAMPLE, D_MODEL)])
    d["xT"] = f(x.T.reshape(KT, P, T))
    d["w_small"] = f(tiles(small, KT))
    d["gate_bias"] = f(np.concatenate([i["dn_dt_bias"][0], i["ssm_dt_bias"][0]]))
    d["gate_rate"] = f(np.concatenate([i["dn_A_log"][0], i["ssm_A_log"][0]]))
    col = lambda a: a.reshape(KT, P).T
    d["gains"] = f(np.stack([col(a) for a in (i["g_mix"][0], i["g_xattn"][0], i["g_mem"][0], i["g_ffn"][0], i["g_final"])], 1))
    w = np.concatenate([qkv, z_dn], 1).reshape(KT, P, 4, DN_HEADS, P)
    d["w_dn"] = f(w.transpose(3, 1, 0, 2, 4))
    d["dn_conv_w"] = f(i["dn_conv_w"][0].reshape(CONV, 3, DN_HEADS, P).transpose(2, 3, 1, 0))
    d["dn_hist"] = f(i["state_dn_conv"][0].reshape(SEQS, 3, 3, DN_HEADS, P).transpose(3, 4, 2, 0, 1))
    d["dn_s0"] = f(i["state_dn"][0].transpose(1, 2, 0, 3))
    d["dn_norm_w"] = f(i["dn_norm_w"][0].reshape(P, 1))
    wx, wb, wc = np.split(xbc, [1024, 1280], axis=1)
    d["w_bc"] = f(np.stack([wb, wc], 1).reshape(KT, P, 2, SSM_GROUPS, P).transpose(3, 1, 0, 2, 4))
    d["w_xz"] = f(np.stack([wx, z_ssm], 1).reshape(KT, P, 2, PAIRS, P).transpose(3, 1, 0, 2, 4))
    channels = np.concatenate([i["state_ssm_conv"][0].transpose(2, 0, 1).reshape(-1, 3 * SEQS), i["ssm_conv_w"][0].T,
                               i["ssm_conv_b"][0][:, None]], 1)
    skip = np.repeat(i["ssm_D"][0], HALF)[:, None]
    d["ssm_small_x"] = f(np.concatenate([channels[:1024], skip], 1).reshape(PAIRS, P, -1))
    d["ssm_small_bc"] = f(np.concatenate([channels[1024:], skip[:512]], 1).reshape(2, SSM_GROUPS, P, -1).transpose(1, 2, 0, 3))
    d["ssm_s0"] = f(i["state_ssm"][0].reshape(SEQS, PAIRS, P, P).transpose(1, 3, 0, 2))
    d["ssm_norm_w"] = f(i["ssm_norm_w"][0].reshape(PAIRS, P).T)
    by_out = lambda a, k: f(a.reshape(k, P, -1, P).transpose(2, 1, 0, 3))
    d["w_out"] = by_out(i["w_out"][0], 2 * KT)
    d["w_xq"], d["w_xo"], d["w_pq"] = (by_out(i[n][0], KT) for n in ("w_xq", "w_xo", "w_pq"))
    d["w_mk"] = by_out(i["w_mkv"][0][:, :D_MODEL], KT)
    d["w_mv"] = f(tiles(i["w_mkv"][0][:, D_MODEL:], KT))
    d["memT"] = f(tiles(i["mem_prompt"][0].T, KT))
    d["cache_k"] = f(i["cache_mem_k"][0].reshape(SEQS, MEM, KT, P).transpose(0, 3, 2, 1))
    d["cache_v"] = f(i["cache_mem_v"][0].reshape(SEQS, 2, P, D_MODEL).transpose(0, 2, 1, 3))
    d["keysT"] = f(i["peer_sub_keys"][0].transpose(2, 0, 1))
    d["peer_u"] = f(i["peer_u"][0].reshape(NKEYS, NKEYS, KT, P).transpose(1, 3, 2, 0))
    d["peer_v"] = f(i["peer_v"][0].reshape(NKEYS, NKEYS, D_MODEL).transpose(1, 0, 2))
    return d


def shape_constants():
    j, i = np.arange(P)[:, None], np.arange(P)[None, :]
    seq = np.where(np.arange(P) < SAMPLE, np.arange(P) // STEPS, -1 - np.arange(P))
    same = seq[:, None] == seq[None, :]
    d = {"ident": np.eye(P), "ones": np.ones((P, P)), "tri": np.stack([j <= i, (j <= i) & same], 1),
         "total": np.stack([same | True, same], 1)}
    d["seq_of"] = seq[:, None] == np.arange(SEQS)[None, :]
    for name, m in (("incl", j <= i), ("strict", j < i)):
        d[name] = np.concatenate([np.tile(m, (1, NC - 1)), m & same], 1)
    d["iota"] = np.arange(P)
    s = 2 ** np.arange(7)[:, None, None]
    d["level"] = ((i // (2 * s) == j // (2 * s)) & (i // s % 2 == 1) & (j // s % 2 == 0)).transpose(1, 0, 2)
    return {k: np.ascontiguousarray(v, dtype=np.float32) for k, v in d.items()}


OUTS = {"dn_conv": (DN_HEADS, P, 3, SEQS + 1, 3), "dn_p": (DN_HEADS, P, P), "dn_s": (DN_HEADS, P, SEQS, P),
        "ssm_conv_x": (PAIRS, P, SEQS + 1, 3), "ssm_conv_bc": (SSM_GROUPS, P, 2, SEQS + 1, 3),
        "mem_k": (P, KT, MEM), "mem_v": (P, 2, D_MODEL), "y": (KT, P, T),
        "ssm_p": (PAIRS, P, P), "ssm_s": (PAIRS, P, SEQS, P)}


def kernel(**inputs):
    import concourse.bacc as bacc
    from concourse.bass_utils import run_bass_kernel_spmd

    arrays = layouts({k: np.asarray(v) for k, v in inputs.items()}) | shape_constants()
    nc = bacc.Bacc("TRN2", target_bir_lowering=False, num_devices=1)
    d = {k: nc.dram_tensor(f"in_{k}", a.shape, F32, kind="ExternalInput").ap() for k, a in arrays.items()}
    out = {k: nc.dram_tensor(f"out_{k}", s, F32, kind="ExternalOutput").ap() for k, s in OUTS.items()}
    trunk(nc, d, out)
    got = run_bass_kernel_spmd(nc, [{f"in_{k}": a for k, a in arrays.items()}], core_ids=[0]).results[0]
    g = {k: np.asarray(got[f"out_{k}"]) for k in OUTS}
    conv = lambda a: a.transpose(3, 4, 2, 0, 1).reshape(SEQS + 1, 3, -1)
    dn_conv = conv(g["dn_conv"])
    rows = np.concatenate([g["ssm_conv_x"].reshape(1024, SEQS + 1, 3),
                           g["ssm_conv_bc"].transpose(2, 0, 1, 3, 4).reshape(512, SEQS + 1, 3)])
    ssm_conv = rows.transpose(1, 2, 0)
    ssm_p = g["ssm_p"].transpose(0, 2, 1).reshape(1, 1, SSM_HEADS, HALF, P)
    ssm_s = g["ssm_s"].transpose(2, 0, 3, 1).reshape(1, SEQS, SSM_HEADS, HALF, P)
    y = g["y"].reshape(D_MODEL, T).T
    mem_k = g["mem_k"].transpose(2, 1, 0).reshape(1, 1, MEM, MEM_HEADS, -1)
    mem_v = g["mem_v"].transpose(1, 0, 2).reshape(1, 1, MEM, MEM_HEADS, -1)
    return (y[:SEQ].reshape(1, SEQ, D_MODEL), y[SEQ:].reshape(SEQS, STEPS, D_MODEL),
            dn_conv[None, 0:1], g["dn_p"][None, None], ssm_conv[None, 0:1], ssm_p, mem_k, mem_v,
            dn_conv[None, 1:], g["dn_s"].transpose(2, 0, 1, 3)[None], ssm_conv[None, 1:], ssm_s)
```

```python
from contextlib import ExitStack

import concourse.bass as bass
import numpy as np
from concourse import mybir
from concourse.alu_op_type import AluOpType as ALU

F32 = mybir.dt.float32
F32R = mybir.dt.float32r
U32 = mybir.dt.uint32
ACT = mybir.ActivationFunctionType
AX = mybir.AxisListType

D_MODEL, SEQ, SEQS, STEPS = 1024, 1024, 8, 8
SAMPLE = SEQS * STEPS
T = SEQ + SAMPLE
P = 128
CK = 128
NC = SEQ // CK + 1
TP = NC * CK
KT = D_MODEL // P
DN_HEADS, SSM_HEADS, SSM_GROUPS = 8, 16, 2
PAIRS = SSM_HEADS // 2
GP = PAIRS // SSM_GROUPS
HALF = 64
GATED = DN_HEADS + SSM_HEADS
MEM, MEM_HEADS = 256, 4
CONV = 4
CW = SEQ + CONV - 1 + SEQS * (STEPS + CONV - 1)
SOFF = SEQ + CONV - 1
SW = STEPS + CONV - 1
CHUNKS = [(0, 384), (384, 384), (768, 320)]
EPS = 1e-6
PHEADS, NKEYS, TOPK = 8, 128, 16


class Phase(ExitStack):

    def __init__(self, nc):
        super().__init__()
        self.nc, self.sems = nc, []

    def semaphore(self, name):
        self.sems.append(self.nc.alloc_semaphore(name))
        return self.sems[-1]

    def __exit__(self, *failure):
        if self.sems and failure[0] is None:
            self.nc.clear_and_free_semaphores(self.sems)
            self.nc.all_engine_barrier()
        return super().__exit__(*failure)


class Signal:

    def __init__(self, nc, ctx, name, per=1, unit=1, primed=False):
        self.sem = ctx.semaphore(name)
        self.per, self.unit, self.primed = per, unit, primed

    def at(self, n, turn=0):
        if isinstance(turn, int) and turn == 0 and not self.primed:
            return n * self.unit
        return turn * (self.per * self.unit) + (n + (self.per if self.primed else 0)) * self.unit


class Steps:

    def __init__(self, nc, ctx, name, per=0):
        self.sem = ctx.semaphore(name)
        self.per, self.n = per, 0

    def now(self, turn=0):
        return turn * self.per + self.n if self.per else self.n

    def step(self):
        self.n += 1
        return self.sem


def psum_banks(nc, ctx, name):
    return [ctx.enter_context(nc.psum_tensor(f"{name}_bank{i}", [P, 512], F32)) for i in range(8)]


def split_product(nc, out, w, x, start, stop):
    nc.tensor.matmul(out, w[0], x[0], start=start, stop=False)
    nc.tensor.matmul(out, w[0], x[1], start=False, stop=False)
    return nc.tensor.matmul(out, w[1], x[0], start=False, stop=stop)


def rmsnorm(nc, bank, name, src, dst, gain, ident, ones, tokens, width):
    tiles = -(-tokens // P)
    cols = CHUNKS if tokens == T else [(0, tokens)]
    split = isinstance(dst, tuple)
    with Phase(nc) as ctx:
        sq = ctx.enter_context(nc.sbuf_tensor(f"{name}_squares", [P, KT, P * tiles], F32))
        rstd = ctx.enter_context(nc.sbuf_tensor(f"{name}_rstd", [P, tiles], F32))
        val = ctx.enter_context(nc.sbuf_tensor(f"{name}_value", [P, 2, tokens], F32))
        zeroed = Signal(nc, ctx, f"{name}_zeroed")
        squared = Signal(nc, ctx, f"{name}_squared", KT)
        added = Signal(nc, ctx, f"{name}_added", KT - 1)
        summed = Signal(nc, ctx, f"{name}_summed")
        mean_ready = Signal(nc, ctx, f"{name}_mean_ready")
        root_ready = Signal(nc, ctx, f"{name}_root_ready")
        rstd_ready = Signal(nc, ctx, f"{name}_rstd_ready")
        spread = Signal(nc, ctx, f"{name}_spread")
        val_ready, hi_ready = Signal(nc, ctx, f"{name}_value_ready", KT), Signal(nc, ctx, f"{name}_hi_ready", KT)
        lo_ready = [Signal(nc, ctx, f"{name}_lo_ready{r}", KT // 2) for r in range(2)]
        with nc.Block() as block:
            @block.scalar
            def _(act):
                for k in range(KT):
                    nc.scalar.activation(sq[:, k, 0:tokens], src[:, k, 0:tokens], ACT.Square).then_inc(squared.sem, 1)
                act.wait_ge(mean_ready.sem, 1)
                nc.scalar.activation(rstd[:, :], rstd[:, :], ACT.Sqrt).then_inc(root_ready.sem, 1)
                if split:
                    for k in range(KT):
                        act.wait_ge(val_ready.sem, val_ready.at(k + 1))
                        nc.scalar.activation(dst[0][:, k, 0:tokens], val[:, k % 2, :], ACT.Copy).then_inc(hi_ready.sem, 1)

            @block.tensor
            def _(pe):
                pe.wait_ge(added.sem, added.at(KT - 1))
                pe.wait_ge(zeroed.sem, 1)
                for t in range(tiles):
                    mm = nc.tensor.matmul(bank[0][:, t:t + 1], sq[:, 0, P * t:P * t + P], ones[:, 0:1], start=True, stop=True)
                mm.then_inc(summed.sem, 1)
                pe.wait_ge(rstd_ready.sem, 1)
                for t in range(tiles):
                    mm = nc.tensor.matmul(bank[1 + t // 3][:, P * (t % 3):P * (t % 3) + P],
                                          rstd[:, t:t + 1].to_broadcast([P, P]), ident, start=True, stop=True)
                mm.then_inc(spread.sem, 1)

            def low(engine, r):
                for k in range(r, KT, 2):
                    engine.wait_ge(hi_ready.sem, hi_ready.at(k + 1))
                    (nc.vector, nc.gpsimd)[r].tensor_tensor(dst[1][:, k, 0:tokens], val[:, k % 2, :],
                                                            dst[0][:, k, 0:tokens].bitcast(F32), ALU.subtract).then_inc(lo_ready[r].sem, 1)
                    yield

            @block.gpsimd
            def _(pool):
                if tokens % P:
                    nc.gpsimd.memset(sq[:, 0, tokens:], 0.0)
                nc.gpsimd.memset(val[:, 0, 0:1], 0.0).then_inc(zeroed.sem, 1)
                if split:
                    for _ in low(pool, 1):
                        pass

            @block.vector
            def _(v):
                for k in range(1, KT):
                    v.wait_ge(squared.sem, squared.at(k + 1))
                    if k > 1:
                        v.wait_ge(added.sem, added.at(k - 1))
                    nc.vector.tensor_tensor(sq[:, 0, 0:tokens], sq[:, 0, 0:tokens], sq[:, k, 0:tokens], ALU.add).then_inc(added.sem, 1)
                v.wait_ge(summed.sem, 1)
                nc.vector.tensor_scalar(rstd[:, :], bank[0][:, 0:tiles], 1.0 / width, EPS, ALU.mult, ALU.add).then_inc(mean_ready.sem, 1)
                v.wait_ge(root_ready.sem, 1)
                nc.vector.reciprocal(rstd[:, :], rstd[:, :]).then_inc(rstd_ready.sem, 1)
                v.wait_ge(spread.sem, 1)
                lows = low(v, 0)
                for k in range(KT):
                    if split and k >= 2:
                        v.wait_ge(lo_ready[k % 2].sem, lo_ready[k % 2].at(k // 2))
                    to = val[:, k % 2, :] if split else dst[:, k, :]
                    for c, (a, n) in enumerate(cols):
                        op = nc.vector.scalar_tensor_tensor(to[:, a:a + n], src[:, k, a:a + n], gain[:, k:k + 1],
                                                            bank[1 + c][:, 0:n], ALU.mult, ALU.mult)
                    op.then_inc(val_ready.sem, 1)
                    if split and k % 2 == 0:
                        next(lows)


def gates(nc, bank, xn, w_small, tri, total, d, tab):
    G = GATED
    with Phase(nc) as ctx:
        def sb(name, shape):
            return ctx.enter_context(nc.sbuf_tensor(f"gates_{name}", shape, F32))
        raw, neg, e, u, z, sp = (sb(x, [P, NC, G]) for x in ("raw", "neg", "e", "u", "z", "sp"))
        bias, rate = sb("bias", [P, G]), sb("rate", [P, G])
        loaded = Signal(nc, ctx, "gates_loaded", 2, 16)
        projected = Signal(nc, ctx, "gates_projected")
        cumulated = Signal(nc, ctx, "gates_cumulated")
        vec = Steps(nc, ctx, "gates_vector_steps")
        sca = Steps(nc, ctx, "gates_scalar_steps")
        vector_at, scalar_at = {"neg": 4, "u": 5, "decays": 14, "sums": 15, "left": 16}, {"sigmoid": 1, "exp": 3, "ln": 4, "decayed": 6}
        with nc.Block() as block:
            @block.sync
            def _(sp_):
                sp_.dma_start(bias[:, :], d["gate_bias"].partition_broadcast(P)).then_inc(loaded.sem, 16)
                sp_.dma_start(rate[:, :], d["gate_rate"].partition_broadcast(P)).then_inc(loaded.sem, 16)

            @block.tensor
            def _(pe):
                for c in range(NC):
                    for k in range(KT):
                        s = slice(CK * c, CK * c + CK)
                        mm = nc.tensor.matmul(bank[0][:, 32 * c:32 * c + 32], xn[:, k, s], w_small[:, k, :],
                                              start=(k == 0), stop=(k == KT - 1))
                mm.then_inc(projected.sem, 1)
                pe.wait_ge(vec.sem, vector_at["decays"])
                for c in range(NC):
                    m = int(c == NC - 1)
                    nc.tensor.matmul(bank[1][:, G * c:G * c + G], tri[:, m, :], tab[:, 0, c, :], start=True, stop=True)
                    mm = nc.tensor.matmul(bank[2][:, G * c:G * c + G], total[:, m, :], tab[:, 0, c, :],
                                          start=True, stop=True)
                mm.then_inc(cumulated.sem, 1)

            @block.scalar
            def _(act):
                projection = bank[0][:, 0:32 * NC].rearrange("p (c h) -> p c h", h=32)
                act.wait_ge(projected.sem, 1)
                nc.scalar.activation(tab[:, 4, :, 0:DN_HEADS], projection[:, :, 0:DN_HEADS],
                                     ACT.Sigmoid).then_inc(sca.step(), 1)
                act.wait_ge(loaded.sem, loaded.at(2))
                nc.scalar.activation(rate[:, :], rate[:, :], ACT.Exp).then_inc(sca.step(), 1)
                act.wait_ge(vec.sem, vector_at["neg"])
                nc.scalar.activation(e[:, :, :], neg[:, :, :], ACT.Exp).then_inc(sca.step(), 1)
                assert sca.n == scalar_at["exp"]
                act.wait_ge(vec.sem, vector_at["u"])
                nc.scalar.activation(z[:, :, :], u[:, :, :], ACT.Ln).then_inc(sca.step(), 1)
                act.wait_ge(vec.sem, vector_at["sums"])
                nc.scalar.activation(tab[:, 2, :, :], tab[:, 1, :, :], ACT.Exp).then_inc(sca.step(), 1)
                act.wait_ge(vec.sem, vector_at["left"])
                nc.scalar.activation(tab[:, 3, :, :], tab[:, 3, :, :], ACT.Exp).then_inc(sca.step(), 1)
                assert sca.n == scalar_at["decayed"]

            @block.vector
            def _(v):
                projection = bank[0][:, 0:32 * NC].rearrange("p (c h) -> p c h", h=32)
                wide = lambda x: x[:, None, :].to_broadcast([P, NC, G])
                v.wait_ge(sca.sem, scalar_at["sigmoid"])
                v.wait_ge(loaded.sem, loaded.at(2))

                def then(op):
                    op.then_inc(vec.step(), 1)
                    v.wait_ge(vec.sem, vec.now())
                then(nc.vector.tensor_tensor(raw[:, :, :], projection[:, :, DN_HEADS:32], wide(bias), ALU.add))
                then(nc.vector.tensor_scalar(sp[:, :, :], raw[:, :, :], 0.0, None, ALU.max))
                then(nc.vector.tensor_scalar(neg[:, :, :], raw[:, :, :], -1.0, None, ALU.mult))
                then(nc.vector.tensor_tensor(neg[:, :, :], neg[:, :, :], raw[:, :, :], ALU.min))
                assert vec.n == vector_at["neg"]
                v.wait_ge(sca.sem, scalar_at["exp"])
                then(nc.vector.tensor_scalar(u[:, :, :], e[:, :, :], 1.0, None, ALU.add))
                then(nc.vector.tensor_scalar(raw[:, :, :], u[:, :, :], 1.0, None, ALU.is_equal))
                then(nc.vector.scalar_tensor_tensor(neg[:, :, :], u[:, :, :], -1.0, raw[:, :, :], ALU.add, ALU.add))
                then(nc.vector.reciprocal(neg[:, :, :], neg[:, :, :]))
                then(nc.vector.tensor_tensor(neg[:, :, :], neg[:, :, :], e[:, :, :], ALU.mult))
                then(nc.vector.tensor_tensor(raw[:, :, :], raw[:, :, :], e[:, :, :], ALU.mult))
                v.wait_ge(sca.sem, scalar_at["ln"])
                then(nc.vector.tensor_tensor(neg[:, :, :], neg[:, :, :], z[:, :, :], ALU.mult))
                then(nc.vector.tensor_tensor(neg[:, :, :], neg[:, :, :], raw[:, :, :], ALU.add))
                then(nc.vector.tensor_tensor(sp[:, :, :], sp[:, :, :], neg[:, :, :], ALU.add))
                then(nc.vector.scalar_tensor_tensor(tab[:, 0, :, :], sp[:, :, :], -1.0, wide(rate), ALU.mult, ALU.mult))
                assert vec.n == vector_at["decays"]
                v.wait_ge(cumulated.sem, 1)
                then(nc.vector.tensor_copy(tab[:, 1, :, :], bank[1][:, 0:NC * G].rearrange("p (c h) -> p c h", h=G)))
                then(nc.vector.tensor_tensor(tab[:, 3, :, :], bank[2][:, 0:NC * G].rearrange("p (c h) -> p c h", h=G),
                                             tab[:, 1, :, :], ALU.subtract))
                assert vec.n == vector_at["left"]
                then(nc.vector.tensor_copy(tab[:, 4, :, DN_HEADS:G], sp[:, :, DN_HEADS:G]))


def delta_net(nc, bank, xn, tab, d, const, mix, out):
    LEVELS = [1, 2, 4, 8, 16, 32, 64]
    A, B, KS_BANK, VN_BANK = bank[0:3], bank[4:7], bank[3], bank[7]
    with Phase(nc) as ctx:
        def sb(name, shape):
            return ctx.enter_context(nc.sbuf_tensor(f"dn_{name}", shape, F32))

        def signal(name, per=1, unit=1, primed=False):
            return Signal(nc, ctx, f"dn_{name}", per, unit, primed)
        w = sb("weights", [P, KT, 4, P])
        hist, cw, nw = sb("history", [P, 3, SEQS, 3]), sb("conv_w", [P, 3, CONV]), sb("norm_w", [P, 1])
        cbuf, acc, qkv = sb("padded", [P, 3, CW]), sb("conv", [P, 3, CW]), sb("qkv", [P, 3, TP])
        zs, cur, negbeg = sb("gate", [P, T]), sb("columns", [P, 5, NC]), sb("neg_beta_decay", [P, NC])
        tail = sb("conv_state", [P, 3, SEQS + 1, 3])
        rqk, ro = sb("rstd_qk", [P, 2, NC]), sb("rstd_o", [P, NC])
        erow = sb("row_decay", [P, TP])
        D, Ds, LT, attn, qdec = (sb(x, [P, TP]) for x in ("decay", "beta_decay", "lower", "attn", "q_decayed"))
        X, Y, BX, Vb, Kd = (sb(x, [P, TP]) for x in ("inv", "inv_t", "bx", "v_beta", "k_decayed"))
        BT = sb("block", [P, 2, TP])
        R, vn, S = sb("residual", [P, P]), sb("v_new", [P, 2, P]), sb("state", [P, 2, P])
        km, S0, vm, S1 = sb("k_masked", [P, SEQS * (P + STEPS)]), sb("sample_in", [P, SEQS, P]), sb("v_masked", [P, SEQS, P]), sb("sample_out", [P, SEQS, P])
        o = sb("o", [P, T])
        ident, ones = const["ident"], const["ones"]
        const = const | {"level": sb("level_masks", [P, 7, P]), "strict": sb("strict_mask", [P, TP])}

        w_loaded = signal("weights_loaded", 3, 16)
        s0_loaded = signal("sample_in_loaded", 1, 16)
        started = signal("inputs_once", 1, 16)
        cur_ready = signal("columns_ready")
        projected = signal("projected", 12)
        evacuated = signal("evacuated", 12)
        hist_in = signal("history_in")
        conv_done = signal("conv_done", 3)
        silu_done = signal("silu_done", 3)
        tail_ready = signal("tail_ready", 2)
        tail_stored = signal("conv_state_stored", 1, 16, primed=True)
        state_stored = signal("state_stored", 1, 16, primed=True)
        sample_stored = signal("sample_state_stored", 1, 16, primed=True)
        o_stored = signal("o_stored", 1, 16, primed=True)
        squared = signal("squared", 2)
        ssq_ready, mean_ready = signal("ssq_ready"), signal("mean_ready")
        root_ready, rqk_ready = signal("root_ready"), signal("rstd_qk_ready")
        qk_spread = signal("rstd_qk_spread", 2)
        qk_ready = signal("qk_ready", 2)
        rows_ready = signal("rows_ready", 2)
        diff_ready = signal("diff_ready")
        erow_ready = signal("row_decay_ready")
        dexp_ready = signal("decay_exp_ready")
        rowb_used = signal("beta_rows_used")
        prod_ready = signal("products_ready", 2)
        lt_ready, attn_ready = signal("lower_ready"), signal("attn_ready")
        qdec_ready = signal("q_decayed_ready")
        turned = signal("tokens_turned", 2)
        v_turned_used = signal("v_turned_used")
        k_turned_used = signal("k_turned_used")
        y1_ready = signal("first_level_ready")
        x_turned = signal("x_turned", 3)
        x1_ready = signal("x_first_ready", 3)
        bt_ready = signal("block_ready", 7)
        bx_mm = signal("bx_product", 18)
        bx_ready = signal("bx_ready", 18)
        yx_mm = signal("yx_product", 18)
        y_ready = signal("inverse_ready", 18)
        ks_ready, r_ready = signal("ks_ready", 9), signal("residual_ready", 9)
        vn_mm, vn_ready = signal("v_new_product", 9), signal("v_new_ready", 9)
        ds_ready, s_ready = signal("state_product", 9), signal("state_ready", 10)
        o_ready, o_out = signal("o_product", 3), signal("o_out", 3)
        km_ready, vm_ready = signal("k_masked_ready"), signal("v_masked_ready")
        osq, o_ssq, o_mean = signal("o_squared"), signal("o_summed"), signal("o_mean")
        o_root, ro_ready, o_spread = signal("o_root"), signal("rstd_o_ready"), signal("rstd_o_spread")
        o_normed, o_done = signal("o_normed", 1, 1, True), signal("o_done", 1, 1, True)
        zeroed = signal("zeroed")
        LAST = DN_HEADS - 1
        VSTEPS = 13
        vec = Steps(nc, ctx, "dn_vector_steps", VSTEPS)

        def c3(t, n):
            return t[:, 384 * n:384 * n + 384]

        with nc.Block() as block:
            @block.sync
            def _(sp):
                sp.dma_start(nw[:, :], d["dn_norm_w"]).then_inc(started.sem, 16)
                sp.dma_start(const["level"][:, :, :], d["level"]).then_inc(started.sem, 16)
                sp.dma_start(const["strict"][:, :], d["strict"]).then_inc(started.sem, 16)

                def load_weights(h):
                    sp.dma_start(w[:, :, :, :], d["w_dn"][bass.ds(h, 1)].rearrange("a p k j n -> (a p) k j n")).then_inc(w_loaded.sem, 16)
                    sp.dma_start(hist[:, :, :, :], d["dn_hist"][bass.ds(h, 1)].rearrange("a p j b n -> (a p) j b n")).then_inc(w_loaded.sem, 16)
                    sp.dma_start(cw[:, :, :], d["dn_conv_w"][bass.ds(h, 1)].rearrange("a p j n -> (a p) j n")).then_inc(w_loaded.sem, 16)

                def load_sample(h):
                    sp.dma_start(S0[:, :, :], d["dn_s0"][bass.ds(h, 1)].rearrange("a p b n -> (a p) b n")).then_inc(s0_loaded.sem, 16)

                def head(h, last):
                    sp.wait_ge(tail_ready.sem, tail_ready.at(2, h))
                    sp.dma_start(out["dn_conv"][bass.ds(h, 1)].rearrange("a p j b n -> (a p) j b n"), tail[:, :, :, :]).then_inc(tail_stored.sem, 16)
                    if not last:
                        sp.wait_ge(projected.sem, projected.at(12, h))
                        sp.wait_ge(conv_done.sem, conv_done.at(3, h))
                        load_weights(h + 1)
                    sp.wait_ge(s_ready.sem, s_ready.at(9, h))
                    sp.dma_start(out["dn_p"][bass.ds(h, 1)].rearrange("a p n -> (a p) n"), S[:, 0, :]).then_inc(state_stored.sem, 16)
                    sp.wait_ge(s_ready.sem, s_ready.at(10, h))
                    sp.dma_start(out["dn_s"][bass.ds(h, 1)].rearrange("a p b n -> (a p) b n"), S1[:, :, :]).then_inc(sample_stored.sem, 16)
                    if not last:
                        sp.wait_ge(o_ready.sem, o_ready.at(3, h))
                        load_sample(h + 1)
                    sp.wait_ge(o_done.sem, o_done.at(1, h))
                    sp.dma_start(mix[bass.ds(h, 1)].rearrange("a p n -> (a p) n"), o[:, :]).then_inc(o_stored.sem, 16)
                load_weights(0)
                load_sample(0)
                with sp.Fori(0, LAST) as h:
                    head(h, False)
                head(LAST, True)
                for sig in (tail_stored, state_stored, sample_stored, o_stored):
                    sp.wait_ge(sig.sem, sig.at(1, LAST))

            @block.tensor
            def _(pe):
                def project(j, c, h):
                    a, n = CHUNKS[c]
                    for k in range(KT):
                        mm = nc.tensor.matmul((A, B)[j % 2][c][:, 0:n], w[:, k, j, :], xn[:, k, a:a + n],
                                              start=(k == 0), stop=(k == KT - 1))
                    mm.then_inc(projected.sem, 1)

                def columns_sums(to, squares):
                    for c in range(NC):
                        n = CK if c < NC - 1 else SAMPLE
                        mm = nc.tensor.matmul(to[0:n, c:c + 1], squares[:, CK * c:CK * c + n], ones[:, 0:1], start=True, stop=True)
                    return mm

                def spread(banks, column):
                    for c in range(NC):
                        n = CK if c < NC - 1 else SAMPLE
                        mm = nc.tensor.matmul(banks[c // 3][:, CK * (c % 3):CK * (c % 3) + n], column[:, c:c + 1].to_broadcast([P, P]),
                                              ident[:, 0:n], start=True, stop=True)
                    return mm

                def head(h, last):
                    pe.wait_ge(w_loaded.sem, w_loaded.at(3, h))
                    pe.wait_ge(o_normed.sem, o_normed.at(1, h - 1))
                    for c in range(3):
                        project(1, c, h)
                    for c in range(3):
                        pe.wait_ge(evacuated.sem, evacuated.at(c + 1, h))
                        project(2, c, h)
                    pe.wait_ge(cur_ready.sem, cur_ready.at(1, h))
                    for q, banks, mask in ((0, B, const["tri"]), (4, A, None)):
                        pe.wait_ge(evacuated.sem, evacuated.at(6 if q == 0 else 9, h))
                        for c in range(NC):
                            rhs = ident[:, :] if mask is None else mask[:, int(c == NC - 1), :]
                            mm = nc.tensor.matmul(banks[c // 3][:, CK * (c % 3):CK * (c % 3) + CK],
                                                  cur[:, q, c:c + 1].to_broadcast([P, P]), rhs, start=True, stop=True)
                        mm.then_inc(rows_ready.sem, 1)
                    pe.wait_ge(diff_ready.sem, diff_ready.at(1, h))
                    pe.wait_ge(erow_ready.sem, erow_ready.at(1, h))
                    project(3, 0, h)
                    project(3, 1, h)
                    pe.wait_ge(squared.sem, squared.at(2, h))
                    for j in range(2):
                        mm = columns_sums(KS_BANK[:, NC * j:NC * j + NC], acc[:, j, :])
                    mm.then_inc(ssq_ready.sem, 1)
                    project(3, 2, h)
                    pe.wait_ge(rqk_ready.sem, rqk_ready.at(1, h))
                    pe.wait_ge(rowb_used.sem, rowb_used.at(1, h))
                    spread(A, rqk[:, 0, :]).then_inc(qk_spread.sem, 1)
                    pe.wait_ge(evacuated.sem, evacuated.at(12, h))
                    spread(B, rqk[:, 1, :]).then_inc(qk_spread.sem, 1)
                    pe.wait_ge(qk_ready.sem, qk_ready.at(2, h))
                    for j, banks in ((1, A), (0, B)):
                        for c in range(NC):
                            s = slice(CK * c, CK * c + CK)
                            mm = nc.tensor.matmul(banks[c // 3][:, CK * (c % 3):CK * (c % 3) + CK], qkv[:, 1, s],
                                                  qkv[:, j, s], start=True, stop=True)
                        mm.then_inc(prod_ready.sem, 1)
                    for j, banks, free in ((2, A, lt_ready), (1, B, attn_ready)):
                        pe.wait_ge(silu_done.sem, silu_done.at(3, h))
                        pe.wait_ge(free.sem, free.at(1, h))
                        for c in range(NC):
                            mm = nc.tensor.transpose(banks[c // 3][:, CK * (c % 3):CK * (c % 3) + CK],
                                                     qkv[:, j, CK * c:CK * c + CK], ident[:, :])
                        mm.then_inc(turned.sem, 1)
                    pe.wait_ge(v_turned_used.sem, v_turned_used.at(1, h))
                    pe.wait_ge(k_turned_used.sem, k_turned_used.at(1, h))
                    pe.wait_ge(y1_ready.sem, y1_ready.at(1, h))
                    for t in range(3):
                        for c in range(3 * t, 3 * t + 3):
                            mm = nc.tensor.transpose(A[t][:, CK * (c % 3):CK * (c % 3) + CK],
                                                     Y[:, CK * c:CK * c + CK], ident[:, :])
                        mm.then_inc(x_turned.sem, 1)
                    for l in range(1, len(LEVELS)):
                        def block_times_x(t):
                            n = 3 * (l - 1) + t
                            if l == 1:
                                pe.wait_ge(x1_ready.sem, x1_ready.at(t + 1, h))
                            else:
                                pe.wait_ge(y_ready.sem, y_ready.at(n - 2, h))
                            pe.wait_ge(bt_ready.sem, bt_ready.at(l + 1, h))
                            for c in range(3 * t, 3 * t + 3):
                                s = slice(CK * c, CK * c + CK)
                                mm = nc.tensor.matmul(A[t][:, CK * (c % 3):CK * (c % 3) + CK], BT[:, l % 2, s], X[:, s],
                                                      start=True, stop=True)
                            mm.then_inc(bx_mm.sem, 1)

                        def corrections(t):
                            n = 3 * (l - 1) + t
                            pe.wait_ge(bx_ready.sem, bx_ready.at(n + 1, h))
                            for c in range(3 * t, 3 * t + 3):
                                s = slice(CK * c, CK * c + CK)
                                mm = nc.tensor.matmul(B[t][:, CK * (c % 3):CK * (c % 3) + CK], BX[:, s], Y[:, s],
                                                      start=True, stop=True)
                                if l < len(LEVELS) - 1:
                                    mm = nc.tensor.matmul(A[t][:, CK * (c % 3):CK * (c % 3) + CK], Y[:, s], BX[:, s],
                                                          start=True, stop=True)
                            mm.then_inc(yx_mm.sem, 1)
                        for t in range(3):
                            block_times_x(t)
                        for t in range(3):
                            corrections(t)
                    pe.wait_ge(y_ready.sem, y_ready.at(18, h))
                    pe.wait_ge(qdec_ready.sem, qdec_ready.at(1, h))
                    for c in range(NC):
                        s = slice(CK * c, CK * c + CK)
                        old = S[:, c % 2, :]
                        pe.wait_ge(s_ready.sem, s_ready.at(c + 1, h))
                        if c < NC - 1:
                            nc.tensor.matmul(KS_BANK[:, 0:P], qkv[:, 1, s], old, start=True, stop=True).then_inc(ks_ready.sem, 1)
                        else:
                            pe.wait_ge(km_ready.sem, km_ready.at(1, h))
                            pe.wait_ge(s0_loaded.sem, s0_loaded.at(1, h))
                            for b in range(SEQS):
                                mm = nc.tensor.matmul(KS_BANK[:, 0:P], km[:, P * b:P * b + P], S0[:, b, :], start=(b == 0), stop=(b == SEQS - 1))
                            mm.then_inc(ks_ready.sem, 1)
                        pe.wait_ge(r_ready.sem, r_ready.at(c + 1, h))
                        nc.tensor.matmul(VN_BANK[:, 0:P], Y[:, s], R[:, :], start=True, stop=True).then_inc(vn_mm.sem, 1)
                        pe.wait_ge(vn_ready.sem, vn_ready.at(c + 1, h))
                        if c < NC - 1:
                            nc.tensor.matmul(A[0][:, 0:P], Kd[:, s], vn[:, c % 2, :], start=True, stop=True).then_inc(ds_ready.sem, 1)
                            to = B[c // 3][:, CK * (c % 3):CK * (c % 3) + CK]
                            nc.tensor.matmul(to, old, qdec[:, s], start=True, stop=False)
                            mm = nc.tensor.matmul(to, vn[:, c % 2, :], attn[:, s], start=False, stop=True)
                        else:
                            pe.wait_ge(vm_ready.sem, vm_ready.at(1, h))
                            for half in range(2):
                                mm = nc.tensor.matmul(A[1 + half][:, 0:512], Kd[:, s],
                                                      vm[:, 4 * half:4 * half + 4, :].rearrange("p b n -> p (b n)"),
                                                      start=True, stop=True)
                            mm.then_inc(ds_ready.sem, 1)
                            a = CK * (c % 3)
                            nc.tensor.matmul(B[2][:, a:a + SAMPLE], vn[:, c % 2, :], attn[:, SEQ:T], start=True, stop=False)
                            for b in range(SEQS):
                                mm = nc.tensor.matmul(B[2][:, a + STEPS * b:a + STEPS * b + STEPS], S0[:, b, :],
                                                      qdec[:, SEQ + STEPS * b:SEQ + STEPS * b + STEPS],
                                                      start=False, stop=(b == SEQS - 1))
                        if c % 3 == 2:
                            mm.then_inc(o_ready.sem, 1)
                    if not last:
                        pe.wait_ge(w_loaded.sem, w_loaded.at(3, h + 1))
                        pe.wait_ge(s_ready.sem, s_ready.at(9, h))
                        project(0, 0, h + 1)
                    pe.wait_ge(osq.sem, osq.at(1, h))
                    pe.wait_ge(r_ready.sem, r_ready.at(9, h))
                    columns_sums(KS_BANK, acc[:, 0, :]).then_inc(o_ssq.sem, 1)
                    if not last:
                        pe.wait_ge(s_ready.sem, s_ready.at(10, h))
                        project(0, 1, h + 1)
                    pe.wait_ge(ro_ready.sem, ro_ready.at(1, h))
                    spread(B, ro).then_inc(o_spread.sem, 1)
                    if not last:
                        project(0, 2, h + 1)
                pe.wait_ge(w_loaded.sem, w_loaded.at(3))
                for c in range(3):
                    project(0, c, 0)
                with pe.Fori(0, LAST) as h:
                    head(h, False)
                head(LAST, True)

            @block.scalar
            def _(act):
                for sig in (o_normed, o_done):
                    act.sem_inc(sig.sem, 1)
                for sig in (tail_stored, state_stored, sample_stored, o_stored):
                    act.sem_inc(sig.sem, 16)

                def evacuate(j, c, h):
                    a, n = CHUNKS[c]
                    act.wait_ge(projected.sem, projected.at(3 * j + c + 1, h))
                    psum = (A, B)[j % 2][c]
                    if j == 3:
                        nc.scalar.activation(zs[:, a:a + n], psum[:, 0:n], ACT.Silu).then_inc(evacuated.sem, 1)
                    elif c < 2:
                        nc.scalar.activation(cbuf[:, j, a + 3:a + 3 + n], psum[:, 0:n], ACT.Copy).then_inc(evacuated.sem, 1)
                    else:
                        nc.scalar.activation(cbuf[:, j, a + 3:SOFF], psum[:, 0:SEQ - a], ACT.Copy)
                        nc.scalar.activation(
                            cbuf[:, j, SOFF:CW].rearrange("p (b n) -> p b n", n=SW)[:, :, 3:SW],
                            psum[:, SEQ - a:n].rearrange("p (b n) -> p b n", n=STEPS), ACT.Copy).then_inc(evacuated.sem, 1)

                def silu(j, h):
                    act.wait_ge(conv_done.sem, conv_done.at(j + 1, h))
                    nc.scalar.activation(qkv[:, j, 0:SEQ], acc[:, j, 0:SEQ], ACT.Silu)
                    nc.scalar.activation(
                        qkv[:, j, SEQ:T].rearrange("p (b n) -> p b n", n=STEPS),
                        acc[:, j, SOFF:CW].rearrange("p (b n) -> p b n", n=SW)[:, :, 0:STEPS], ACT.Silu).then_inc(silu_done.sem, 1)

                def square(j, h):
                    act.wait_ge(silu_done.sem, silu_done.at(j + 1, h))
                    nc.scalar.activation(acc[:, j, 0:T], qkv[:, j, 0:T], ACT.Square).then_inc(squared.sem, 1)

                def head(h, last):
                    evacuate(1, 0, h)
                    silu(0, h)
                    square(0, h)
                    evacuate(1, 1, h)
                    evacuate(1, 2, h)
                    evacuate(2, 0, h)
                    silu(1, h)
                    square(1, h)
                    evacuate(2, 1, h)
                    evacuate(2, 2, h)
                    act.wait_ge(rows_ready.sem, rows_ready.at(1, h))
                    for t in range(3):
                        op = nc.scalar.activation(c3(erow, t), B[t][:, 0:384], ACT.Exp)
                    op.then_inc(erow_ready.sem, 1)
                    act.wait_ge(diff_ready.sem, diff_ready.at(1, h))
                    nc.scalar.activation(D[:, :], D[:, :], ACT.Exp).then_inc(dexp_ready.sem, 1)
                    silu(2, h)
                    act.wait_ge(o_done.sem, o_done.at(1, h - 1))
                    evacuate(3, 0, h)
                    evacuate(3, 1, h)
                    act.wait_ge(mean_ready.sem, mean_ready.at(1, h))
                    nc.scalar.activation(rqk[:, :, :], rqk[:, :, :], ACT.Sqrt).then_inc(root_ready.sem, 1)
                    evacuate(3, 2, h)
                    for l in range(1, len(LEVELS)):
                        for t in range(3):
                            act.wait_ge(bx_mm.sem, bx_mm.at(3 * (l - 1) + t + 1, h))
                            nc.scalar.activation(c3(BX, t), A[t][:, 0:384], ACT.Copy).then_inc(bx_ready.sem, 1)
                    for c in range(NC):
                        act.wait_ge(vn_mm.sem, vn_mm.at(c + 1, h))
                        nc.scalar.activation(vn[:, c % 2, :], VN_BANK[:, 0:P], ACT.Copy).then_inc(vn_ready.sem, 1)
                        if c % 3 == 2:
                            t = c // 3
                            act.wait_ge(o_ready.sem, o_ready.at(t + 1, h))
                            if t == 0:
                                act.wait_ge(o_stored.sem, o_stored.at(1, h - 1))
                            n = CHUNKS[t][1]
                            nc.scalar.activation(o[:, 384 * t:384 * t + n], B[t][:, 0:n], ACT.Copy).then_inc(o_out.sem, 1)
                    act.wait_ge(o_out.sem, o_out.at(3, h))
                    nc.scalar.activation(acc[:, 0, 0:T], o[:, :], ACT.Square).then_inc(osq.sem, 1)
                    if not last:
                        act.wait_ge(tail_ready.sem, tail_ready.at(2, h))
                        evacuate(0, 0, h + 1)
                    act.wait_ge(o_mean.sem, o_mean.at(1, h))
                    nc.scalar.activation(ro[:, :], ro[:, :], ACT.Sqrt).then_inc(o_root.sem, 1)
                    if not last:
                        evacuate(0, 1, h + 1)
                        evacuate(0, 2, h + 1)
                for c in range(3):
                    evacuate(0, c, 0)
                with act.Fori(0, LAST) as h:
                    head(h, False)
                head(LAST, True)

            @block.gpsimd
            def _(pool):
                nc.gpsimd.memset(qkv[:, :, T:TP], 0.0)
                nc.gpsimd.memset(km[:, :], 0.0)
                nc.gpsimd.memset(rqk[:, :, :], 1.0)
                nc.gpsimd.memset(ro[:, :], 1.0)
                nc.gpsimd.memset(cbuf[:, :, 0:3], 0.0).then_inc(zeroed.sem, 1)
                pool.wait_ge(started.sem, started.at(3))
                with pool.Fori(0, DN_HEADS) as h:
                    pool.wait_ge(lt_ready.sem, lt_ready.at(1, h))
                    for l in range(len(LEVELS)):
                        if l >= 2:
                            if l == 2:
                                pool.wait_ge(y1_ready.sem, y1_ready.at(1, h))
                            else:
                                pool.wait_ge(bx_mm.sem, bx_mm.at(3 * (l - 2), h))
                        nc.gpsimd.tensor_tensor(BT[:, l % 2, :].rearrange("p (c n) -> p c n", n=CK),
                                                LT[:, :].rearrange("p (c n) -> p c n", n=CK),
                                                const["level"][:, l:l + 1, :].to_broadcast([P, NC, CK]),
                                                ALU.mult).then_inc(bt_ready.sem, 1)

            @block.vector
            def _(v):
                v.wait_ge(started.sem, started.at(3))
                with v.Fori(0, DN_HEADS) as h:
                    vec.n = 0

                    def then(op):
                        op.then_inc(vec.step(), 1)
                        v.wait_ge(vec.sem, vec.now(h))
                    nc.vector.tensor_copy(cur[:, :, :], tab[:, :, :, bass.ds(h, 1)].rearrange("p q c o -> p q (c o)")).then_inc(cur_ready.sem, 1)
                    v.wait_ge(w_loaded.sem, w_loaded.at(3, h))
                    v.wait_ge(zeroed.sem, 1)
                    nc.vector.tensor_copy(cbuf[:, :, SOFF:CW].rearrange("p j (b n) -> p j b n", n=SW)[:, :, :, 0:3],
                                          hist[:, :, :, :]).then_inc(hist_in.sem, 1)
                    v.wait_ge(hist_in.sem, hist_in.at(1, h))
                    v.wait_ge(cur_ready.sem, cur_ready.at(1, h))
                    then(nc.vector.scalar_tensor_tensor(negbeg[:, :], cur[:, 4, :], -1.0, cur[:, 2, :], ALU.mult, ALU.mult))
                    W = CW - 3
                    for j in range(3):
                        v.wait_ge(evacuated.sem, evacuated.at(3 * j + 3, h))
                        then(nc.vector.tensor_scalar(acc[:, j, 0:W], cbuf[:, j, 0:W], cw[:, j, 0:1], None, ALU.mult))
                        for k in range(1, CONV):
                            op = nc.vector.scalar_tensor_tensor(acc[:, j, 0:W], cbuf[:, j, k:k + W], cw[:, j, k:k + 1],
                                                                acc[:, j, 0:W], ALU.mult, ALU.add)
                            if k < CONV - 1:
                                then(op)
                            else:
                                op.then_inc(conv_done.sem, 1)
                    v.wait_ge(tail_stored.sem, tail_stored.at(1, h - 1))
                    nc.vector.tensor_copy(tail[:, :, 0, :], cbuf[:, :, SEQ:SOFF]).then_inc(tail_ready.sem, 1)
                    nc.vector.tensor_copy(tail[:, :, 1:SEQS + 1, :],
                                          cbuf[:, :, SOFF:CW].rearrange("p j (b n) -> p j b n", n=SW)[:, :, :, STEPS:SW]).then_inc(tail_ready.sem, 1)
                    v.wait_ge(erow_ready.sem, erow_ready.at(1, h))
                    for c in range(NC):
                        op = nc.vector.tensor_scalar(D[:, CK * c:CK * c + CK], B[c // 3][:, CK * (c % 3):CK * (c % 3) + CK],
                                                     cur[:, 1, c:c + 1], 0.0, ALU.subtract, ALU.min)
                    op.then_inc(diff_ready.sem, 1)
                    v.wait_ge(dexp_ready.sem, dexp_ready.at(1, h))
                    then(nc.vector.tensor_tensor(D[:, :], D[:, :], const["incl"][:, :], ALU.mult))
                    then(nc.vector.tensor_tensor(Ds[:, :], D[:, :], const["strict"][:, :], ALU.mult))
                    v.wait_ge(rows_ready.sem, rows_ready.at(2, h))
                    for t in range(3):
                        op = nc.vector.tensor_tensor(c3(Ds, t), c3(Ds, t), A[t][:, 0:384], ALU.mult)
                    op.then_inc(rowb_used.sem, 1)
                    v.wait_ge(ssq_ready.sem, ssq_ready.at(1, h))
                    for j in range(2):
                        nc.vector.tensor_scalar(rqk[:, j, 0:NC - 1], KS_BANK[:, NC * j:NC * j + NC - 1], EPS, None, ALU.add)
                        op = nc.vector.tensor_scalar(rqk[0:SAMPLE, j, NC - 1:NC], KS_BANK[0:SAMPLE, NC * j + NC - 1:NC * j + NC],
                                                     EPS, None, ALU.add)
                    op.then_inc(mean_ready.sem, 1)
                    v.wait_ge(root_ready.sem, root_ready.at(1, h))
                    nc.vector.reciprocal(rqk[:, :, :], rqk[:, :, :]).then_inc(rqk_ready.sem, 1)
                    for j, banks in ((0, A), (1, B)):
                        v.wait_ge(qk_spread.sem, qk_spread.at(j + 1, h))
                        for c, (a, n) in enumerate(CHUNKS):
                            op = nc.vector.scalar_tensor_tensor(qkv[:, j, a:a + n], qkv[:, j, a:a + n], (float(P) ** -0.5, 1.0)[j],
                                                                banks[c][:, 0:n], ALU.mult, ALU.mult)
                        op.then_inc(qk_ready.sem, 1)
                    v.wait_ge(qk_ready.sem, qk_ready.at(2, h))
                    nc.vector.tensor_copy(km[:, :].rearrange("p (b n) -> p b n", n=P + STEPS)[:, :, 0:STEPS],
                                          qkv[:, 1, SEQ:T].rearrange("p (b n) -> p b n", n=STEPS)).then_inc(km_ready.sem, 1)
                    v.wait_ge(erow_ready.sem, erow_ready.at(1, h))
                    nc.vector.tensor_tensor(qdec[:, :], qkv[:, 0, :], erow[:, :], ALU.mult).then_inc(qdec_ready.sem, 1)
                    v.wait_ge(prod_ready.sem, prod_ready.at(1, h))
                    v.wait_ge(rowb_used.sem, rowb_used.at(1, h))
                    for t in range(3):
                        op = nc.vector.tensor_tensor(c3(LT, t), A[t][:, 0:384], c3(Ds, t), ALU.mult)
                    op.then_inc(lt_ready.sem, 1)
                    v.wait_ge(prod_ready.sem, prod_ready.at(2, h))
                    for t in range(3):
                        op = nc.vector.tensor_tensor(c3(attn, t), B[t][:, 0:384], c3(D, t), ALU.mult)
                    op.then_inc(attn_ready.sem, 1)
                    v.wait_ge(bt_ready.sem, bt_ready.at(1, h))
                    nc.vector.tensor_tensor(Y[:, :].rearrange("p (c n) -> p c n", n=CK),
                                            ident[:, None, :].to_broadcast([P, NC, CK]),
                                            BT[:, 0, :].rearrange("p (c n) -> p c n", n=CK), ALU.subtract).then_inc(y1_ready.sem, 1)
                    v.wait_ge(turned.sem, turned.at(1, h))
                    for c in range(NC):
                        op = nc.vector.tensor_scalar(Vb[:, CK * c:CK * c + CK], A[c // 3][:, CK * (c % 3):CK * (c % 3) + CK],
                                                     cur[:, 4, c:c + 1], None, ALU.mult)
                    op.then_inc(v_turned_used.sem, 1)
                    v.wait_ge(turned.sem, turned.at(2, h))
                    for c in range(NC):
                        op = nc.vector.tensor_scalar(Kd[:, CK * c:CK * c + CK], B[c // 3][:, CK * (c % 3):CK * (c % 3) + CK],
                                                     cur[:, 3, c:c + 1], None, ALU.mult)
                    op.then_inc(k_turned_used.sem, 1)
                    for t in range(3):
                        v.wait_ge(x_turned.sem, x_turned.at(t + 1, h))
                        nc.vector.tensor_copy(c3(X, t), A[t][:, 0:384]).then_inc(x1_ready.sem, 1)
                    v.wait_ge(y1_ready.sem, y1_ready.at(1, h))
                    for l in range(1, len(LEVELS)):
                        for t in range(3):
                            n = 3 * (l - 1) + t
                            v.wait_ge(yx_mm.sem, yx_mm.at(n + 1, h))
                            if n < 3:
                                v.wait_ge(x1_ready.sem, x1_ready.at(3, h))
                            else:
                                v.wait_ge(y_ready.sem, y_ready.at(n - 2, h))
                            if l < len(LEVELS) - 1:
                                nc.vector.tensor_tensor(c3(X, t), c3(X, t), A[t][:, 0:384], ALU.subtract)
                            nc.vector.tensor_tensor(c3(Y, t), c3(Y, t), B[t][:, 0:384], ALU.subtract).then_inc(y_ready.sem, 1)
                    v.wait_ge(state_stored.sem, state_stored.at(1, h - 1))
                    nc.vector.memset(S[:, 0, :], 0.0).then_inc(s_ready.sem, 1)
                    for c in range(NC):
                        s = slice(CK * c, CK * c + CK)
                        v.wait_ge(ks_ready.sem, ks_ready.at(c + 1, h))
                        nc.vector.scalar_tensor_tensor(R[:, :], KS_BANK[:, 0:P], negbeg[:, c:c + 1], Vb[:, s],
                                                       ALU.mult, ALU.add).then_inc(r_ready.sem, 1)
                        if c < NC - 1:
                            v.wait_ge(ds_ready.sem, ds_ready.at(c + 1, h))
                            v.wait_ge(s_ready.sem, s_ready.at(c + 1, h))
                            nc.vector.scalar_tensor_tensor(S[:, (c + 1) % 2, :], S[:, c % 2, :],
                                                           erow[:, CK * c + CK - 1:CK * c + CK], A[0][:, 0:P],
                                                           ALU.mult, ALU.add).then_inc(s_ready.sem, 1)
                        else:
                            v.wait_ge(vn_ready.sem, vn_ready.at(9, h))
                            nc.vector.tensor_tensor(vm[:, :, :], vn[:, c % 2:c % 2 + 1, :].to_broadcast([P, SEQS, P]),
                                                    const["seq_of"][:, :, None].to_broadcast([P, SEQS, P]), ALU.mult).then_inc(vm_ready.sem, 1)
                            v.wait_ge(sample_stored.sem, sample_stored.at(1, h - 1))
                            last = erow[:, SEQ:T].rearrange("p (b n) -> p b n", n=STEPS)[:, :, STEPS - 1:STEPS]
                            v.wait_ge(s0_loaded.sem, s0_loaded.at(1, h))
                            then(nc.vector.tensor_tensor(S1[:, :, :], S0[:, :, :], last.to_broadcast([P, SEQS, P]), ALU.mult))
                            v.wait_ge(ds_ready.sem, ds_ready.at(9, h))
                            nc.vector.tensor_tensor(S1[:, 0:4, :], S1[:, 0:4, :], A[1][:, 0:512].rearrange("p (b n) -> p b n", n=P), ALU.add)
                            nc.vector.tensor_tensor(S1[:, 4:8, :], S1[:, 4:8, :], A[2][:, 0:512].rearrange("p (b n) -> p b n", n=P), ALU.add).then_inc(s_ready.sem, 1)
                    v.wait_ge(o_ssq.sem, o_ssq.at(1, h))
                    nc.vector.tensor_scalar(ro[:, 0:NC - 1], KS_BANK[:, 0:NC - 1], 1.0 / P, EPS, ALU.mult, ALU.add)
                    nc.vector.tensor_scalar(ro[0:SAMPLE, NC - 1:NC], KS_BANK[0:SAMPLE, NC - 1:NC], 1.0 / P, EPS,
                                            ALU.mult, ALU.add).then_inc(o_mean.sem, 1)
                    v.wait_ge(o_root.sem, o_root.at(1, h))
                    nc.vector.reciprocal(ro[:, :], ro[:, :]).then_inc(ro_ready.sem, 1)
                    v.wait_ge(o_spread.sem, o_spread.at(1, h))
                    for c, (a, n) in enumerate(CHUNKS):
                        op = nc.vector.scalar_tensor_tensor(o[:, a:a + n], o[:, a:a + n], nw[:, 0:1], B[c][:, 0:n], ALU.mult, ALU.mult)
                    op.then_inc(o_normed.sem, 1)
                    v.wait_ge(o_normed.sem, o_normed.at(1, h))
                    nc.vector.tensor_tensor(o[:, :], o[:, :], zs[:, :], ALU.mult).then_inc(o_done.sem, 1)
                    assert vec.n == VSTEPS, vec.n


def ssd(nc, bank, xn, tab, d, const, mix, out):
    A, B = bank[0:3], bank[4:7]
    Z = (bank[4], bank[3], bank[7])
    SMALL = 3 * SEQS + CONV + 1
    W = CW - 3
    with Phase(nc) as ctx:
        def sb(name, shape):
            return ctx.enter_context(nc.sbuf_tensor(f"ssd_{name}", shape, F32))

        def signal(name, per=1, unit=1, primed=False):
            return Signal(nc, ctx, f"ssd_{name}", per, unit, primed)
        wg, wp = sb("w_bc", [P, KT, 2, P]), sb("w_xz", [P, KT, 2, P])
        sg, sm = sb("small_bc", [P, 2, SMALL]), sb("small_x", [P, SMALL])
        nw, skip = sb("norm_w", [P, PAIRS]), sb("skip_w", [P, PAIRS])
        cb, acc = sb("padded", [P, 2, CW]), sb("conv", [P, 2, CW])
        Bt, Ct, CB, Btok = (sb(x, [P, TP]) for x in ("b", "c", "cb", "b_tokens"))
        xT, zs = sb("x", [P, TP]), sb("gate", [P, T])
        cur = sb("columns", [P, 5, NC, 2])
        erow, D, Cdec = (sb(x, [P, 2, TP]) for x in ("row_decay", "decay", "c_decayed"))
        xd, xde = sb("x_dt", [P, TP]), sb("x_dt_decayed", [P, TP])
        H, S0, S1, xm = sb("states", [P, NC, P]), sb("sample_in", [P, SEQS, P]), sb("sample_out", [P, SEQS, P]), sb("x_masked", [P, SEQS, P])
        tg, tx = sb("tail_bc", [P, 2, SEQS + 1, 3]), sb("tail_x", [P, SEQS + 1, 3])
        y, rstd = sb("y", [P, GP, T]), sb("rstd", [P, T])
        ident, ones = const["ident"], const["ones"]

        once = signal("norm_w_loaded", 2, 16)
        zeroed = signal("zeroed")
        g_loaded = signal("group_loaded", 2, 16)
        g_projected, g_evacuated = signal("bc_projected", 2), signal("bc_evacuated", 2)
        g_conv, g_silu = signal("bc_conv_done", 2), signal("bc_silu_done", 2)
        g_tail = signal("bc_tail_ready")
        g_tail_stored = signal("bc_tail_stored", 1, 16, True)
        g_products = signal("bc_products", 2)
        cb_ready, btok_ready = signal("cb_ready"), signal("b_tokens_ready")
        g_squared, g_summed = signal("group_squared", GP), signal("group_summed", GP)
        g_mean, g_root = signal("group_mean"), signal("group_root")
        g_normed, g_stored = signal("group_normed", 1, 1, True), signal("group_stored", GP, 16, True)
        loaded, s0_loaded = signal("pair_loaded", 2, 16), signal("sample_in_loaded", 1, 16)
        cur_ready = signal("columns_ready")
        projected, evacuated = signal("x_projected"), signal("x_evacuated")
        z_projected, z_evacuated = signal("z_projected", 3), signal("z_evacuated", 3)
        conv_done, silu_done = signal("conv_done"), signal("silu_done")
        tail_ready, tail_stored = signal("tail_ready"), signal("tail_stored", 1, 16, True)
        rows, erow_ready, diff_ready = signal("rows", 2), signal("row_decay_ready", 2), signal("diff_ready", 2)
        dexp = signal("decay_exp_ready", 2)
        turned, xde_ready = signal("x_turned"), signal("x_ready")
        m_ready, cdec_ready = signal("weights_ready"), signal("c_decayed_ready")
        xm_ready = signal("x_masked_ready")
        u_ready, h_ready = signal("state_products"), signal("states_ready", 1, 1, True)
        state_stored = signal("states_stored", 2, 16, True)
        s1_ready = signal("sample_states_ready")
        y_mm, y_ready = signal("y_product"), signal("y_ready", 1, 1, True)
        VSTEPS, GSTEPS = 15, 8
        vec = Steps(nc, ctx, "ssd_vector_steps", VSTEPS)
        gvec = Steps(nc, ctx, "ssd_group_steps", GSTEPS)

        def sample(t):
            return t[:, SOFF:CW].rearrange("p (b n) -> p b n", n=SW)

        def row(a, n):
            names = "pqrs"[:len(a.shape) - 1]
            return a[bass.ds(n, 1)].rearrange(f"a {' '.join(names)} -> (a p) {' '.join(names[1:])}")

        with nc.Block() as block:
            @block.sync
            def _(sp):
                sp.dma_start(nw[:, :], d["ssm_norm_w"]).then_inc(once.sem, 16)
                sp.dma_start(skip[:, :], d["ssm_skip"]).then_inc(once.sem, 16)

                def load_group(g):
                    sp.dma_start(wg[:, :, :, :], row(d["w_bc"], g)).then_inc(g_loaded.sem, 16)
                    sp.dma_start(sg[:, :, :], row(d["ssm_small_bc"], g)).then_inc(g_loaded.sem, 16)

                def load_pair(u):
                    sp.dma_start(wp[:, :, :, :], row(d["w_xz"], u)).then_inc(loaded.sem, 16)
                    sp.dma_start(sm[:, :], row(d["ssm_small_x"], u)).then_inc(loaded.sem, 16)

                def load_sample(u):
                    sp.dma_start(S0[:, :, :], row(d["ssm_s0"], u)).then_inc(s0_loaded.sem, 16)

                def pair(u, last):
                    sp.wait_ge(tail_ready.sem, tail_ready.at(1, u))
                    sp.dma_start(row(out["ssm_conv_x"], u), tx[:, :, :]).then_inc(tail_stored.sem, 16)
                    if not last:
                        sp.wait_ge(z_projected.sem, z_projected.at(3, u))
                        sp.wait_ge(silu_done.sem, silu_done.at(1, u))
                        load_pair(u + 1)
                    sp.wait_ge(h_ready.sem, h_ready.at(1, u))
                    sp.dma_start(row(out["ssm_p"], u), H[:, NC - 1, :]).then_inc(state_stored.sem, 16)
                    sp.wait_ge(s1_ready.sem, s1_ready.at(1, u))
                    sp.dma_start(row(out["ssm_s"], u), S1[:, :, :]).then_inc(state_stored.sem, 16)
                    if not last:
                        sp.wait_ge(y_mm.sem, y_mm.at(1, u))
                        load_sample(u + 1)
                load_group(0)
                load_pair(0)
                load_sample(0)
                for g in range(SSM_GROUPS):
                    if g + 1 < SSM_GROUPS:
                        sp.wait_ge(g_projected.sem, g_projected.at(2, g))
                        sp.wait_ge(g_silu.sem, g_silu.at(2, g))
                        load_group(g + 1)
                    with sp.Fori(0, GP - 1) as p:
                        pair(p + g * GP, False)
                    pair(g * GP + GP - 1, g == SSM_GROUPS - 1)
                    sp.wait_ge(g_tail.sem, g_tail.at(1, g))
                    sp.dma_start(row(out["ssm_conv_bc"], g), tg[:, :, :, :]).then_inc(g_tail_stored.sem, 16)
                    sp.wait_ge(g_normed.sem, g_normed.at(1, g))
                    for k in range(GP):
                        sp.dma_start(row(mix, g * GP + (DN_HEADS + k)), y[:, k, :]).then_inc(g_stored.sem, 16)
                for sig, n, turn in ((tail_stored, 1, PAIRS - 1), (state_stored, 2, PAIRS - 1),
                                     (g_tail_stored, 1, SSM_GROUPS - 1), (g_stored, GP, SSM_GROUPS - 1)):
                    sp.wait_ge(sig.sem, sig.at(n, turn))

            @block.tensor
            def _(pe):
                def project_chunk(w, j, to, c):
                    a, n = CHUNKS[c]
                    for k in range(KT):
                        mm = nc.tensor.matmul(to[:, 0:n], w[:, k, j, :], xn[:, k, a:a + n], start=(k == 0), stop=(k == KT - 1))
                    return mm

                def project(w, j, banks, done):
                    [project_chunk(w, j, banks[c], c) for c in range(3)][-1].then_inc(done.sem, 1)

                with pe.Fori(0, SSM_GROUPS) as g:
                    pe.wait_ge(g_loaded.sem, g_loaded.at(2, g))
                    pe.wait_ge(g_normed.sem, g_normed.at(1, g - 1))
                    project(wg, 0, A, g_projected)
                    project(wg, 1, B, g_projected)
                    pe.wait_ge(g_silu.sem, g_silu.at(2, g))
                    for c in range(NC):
                        s = slice(CK * c, CK * c + CK)
                        mm = nc.tensor.matmul(A[c // 3][:, CK * (c % 3):CK * (c % 3) + CK], Bt[:, s], Ct[:, s], start=True, stop=True)
                    mm.then_inc(g_products.sem, 1)
                    for c in range(NC):
                        s = slice(CK * c, CK * c + CK)
                        mm = nc.tensor.transpose(B[c // 3][:, CK * (c % 3):CK * (c % 3) + CK], Bt[:, s], ident[:, :])
                    mm.then_inc(g_products.sem, 1)
                    with pe.Fori(0, GP) as p:
                        u = g * GP + p
                        pe.wait_ge(loaded.sem, loaded.at(2, u))
                        pe.wait_ge(btok_ready.sem, btok_ready.at(1, g))
                        pe.wait_ge(h_ready.sem, h_ready.at(1, u - 1))
                        project_chunk(wp, 1, Z[0], 0).then_inc(z_projected.sem, 1)
                        pe.wait_ge(cb_ready.sem, cb_ready.at(1, g))
                        pe.wait_ge(y_ready.sem, y_ready.at(1, u - 1))
                        project(wp, 0, A, projected)
                        pe.wait_ge(cur_ready.sem, cur_ready.at(1, u))
                        for e, banks, free in ((0, B, z_evacuated), (1, A, evacuated)):
                            pe.wait_ge(free.sem, free.at(1, u))
                            for c in range(NC):
                                mm = nc.tensor.matmul(banks[c // 3][:, CK * (c % 3):CK * (c % 3) + CK],
                                                      cur[:, 0, c, e:e + 1].to_broadcast([P, P]),
                                                      const["tri"][:, int(c == NC - 1), :], start=True, stop=True)
                            mm.then_inc(rows.sem, 1)
                        project_chunk(wp, 1, Z[1], 1).then_inc(z_projected.sem, 1)
                        pe.wait_ge(silu_done.sem, silu_done.at(1, u))
                        pe.wait_ge(diff_ready.sem, diff_ready.at(2, u))
                        for c in range(NC):
                            mm = nc.tensor.transpose(A[c // 3][:, CK * (c % 3):CK * (c % 3) + CK], xT[:, CK * c:CK * c + CK], ident[:, :])
                        mm.then_inc(turned.sem, 1)
                        project_chunk(wp, 1, Z[2], 2).then_inc(z_projected.sem, 1)
                        pe.wait_ge(z_evacuated.sem, z_evacuated.at(3, u))
                        pe.wait_ge(xde_ready.sem, xde_ready.at(1, u))
                        pe.wait_ge(xm_ready.sem, xm_ready.at(1, u))
                        for c in range(NC - 1):
                            s = slice(CK * c, CK * c + CK)
                            nc.tensor.matmul(B[c // 4][:, P * (c % 4):P * (c % 4) + P], Btok[:, s], xde[:, s], start=True, stop=True)
                        for half, to in enumerate((bank[3], bank[7])):
                            mm = nc.tensor.matmul(to[:, 0:512], Btok[:, SEQ:TP],
                                                  xm[:, 4 * half:4 * half + 4, :].rearrange("p b n -> p (b n)"), start=True, stop=True)
                        mm.then_inc(u_ready.sem, 1)
                        def output(c, e, n):
                            a = CK * (c % 3)
                            return A[c // 3][HALF * e:HALF * e + HALF, a:a + n]
                        pe.wait_ge(m_ready.sem, m_ready.at(1, u))
                        for c in range(NC):
                            n = CK if c < NC - 1 else SAMPLE
                            for e in range(2):
                                nc.tensor.matmul(output(c, e, n), xd[:, CK * c + HALF * e:CK * c + HALF * e + HALF],
                                                 D[:, e, CK * c:CK * c + n], start=(c % 3 == 0), stop=False)
                        pe.wait_ge(cdec_ready.sem, cdec_ready.at(1, u))
                        pe.wait_ge(s0_loaded.sem, s0_loaded.at(1, u))
                        for e in range(2):
                            ch = slice(HALF * e, HALF * e + HALF)
                            whole = output(NC - 1, e, SAMPLE)
                            for b in range(SEQS):
                                t = slice(SEQ + STEPS * b, SEQ + STEPS * b + STEPS)
                                nc.tensor.matmul(whole[:, STEPS * b:STEPS * b + STEPS], S0[:, b, ch],
                                                 Cdec[:, e, t], start=False, stop=False)
                        pe.wait_ge(h_ready.sem, h_ready.at(1, u))
                        for c in range(NC - 1):
                            for e in range(2):
                                ch = slice(HALF * e, HALF * e + HALF)
                                mm = nc.tensor.matmul(output(c, e, CK), H[:, c, ch], Cdec[:, e, CK * c:CK * c + CK],
                                                      start=False, stop=(c % 3 == 2 or c == NC - 2))
                        mm.then_inc(y_mm.sem, 1)
                    for k in range(GP):
                        pe.wait_ge(g_squared.sem, g_squared.at(k + 1, g))
                        for c, (a, n) in enumerate(CHUNKS):
                            mm = nc.tensor.matmul(A[c][:, 0:n], ones[:, :], acc[:, k % 2, a:a + n], start=(k == 0), stop=(k == GP - 1))
                        mm.then_inc(g_summed.sem, 1)

            @block.scalar
            def _(act):
                for sig in (g_tail_stored, tail_stored):
                    act.sem_inc(sig.sem, 16)
                act.sem_inc(g_normed.sem, 1)
                act.sem_inc(g_stored.sem, 16 * GP)
                act.sem_inc(state_stored.sem, 32)
                act.sem_inc(y_ready.sem, 1)
                act.sem_inc(h_ready.sem, 1)

                def evacuate(banks, to, done):
                    for c, (a, n) in enumerate(CHUNKS):
                        if c < 2:
                            nc.scalar.activation(to[:, a + 3:a + 3 + n], banks[c][:, 0:n], ACT.Copy)
                    nc.scalar.activation(to[:, a + 3:SOFF], banks[2][:, 0:SEQ - a], ACT.Copy)
                    nc.scalar.activation(sample(to)[:, :, 3:SW], banks[2][:, SEQ - a:n].rearrange("p (b n) -> p b n", n=STEPS),
                                         ACT.Copy).then_inc(done.sem, 1)

                def silu(to, src, bias, done):
                    nc.scalar.activation(to[:, 0:SEQ], src[:, 0:SEQ], ACT.Silu, bias=bias)
                    nc.scalar.activation(to[:, SEQ:T].rearrange("p (b n) -> p b n", n=STEPS), sample(src)[:, :, 0:STEPS],
                                         ACT.Silu, bias=bias).then_inc(done.sem, 1)

                with act.Fori(0, SSM_GROUPS) as g:
                    for j, banks in ((0, A), (1, B)):
                        act.wait_ge(g_projected.sem, g_projected.at(j + 1, g))
                        evacuate(banks, cb[:, j, :], g_evacuated)
                    for j, to in ((0, Bt), (1, Ct)):
                        act.wait_ge(g_conv.sem, g_conv.at(j + 1, g))
                        silu(to, acc[:, j, :], sg[:, j, SMALL - 1:SMALL], g_silu)
                    act.wait_ge(g_products.sem, g_products.at(2, g))
                    for t in range(3):
                        op = nc.scalar.activation(Btok[:, 384 * t:384 * t + 384], B[t][:, 0:384], ACT.Copy)
                    op.then_inc(btok_ready.sem, 1)
                    act.wait_ge(g_tail.sem, g_tail.at(1, g))
                    with act.Fori(0, GP) as p:
                        u = g * GP + p

                        def gate(c):
                            a, n = CHUNKS[c]
                            act.wait_ge(z_projected.sem, z_projected.at(c + 1, u))
                            nc.scalar.activation(zs[:, a:a + n], Z[c][:, 0:n], ACT.Silu).then_inc(z_evacuated.sem, 1)

                        def decay(e):
                            act.wait_ge(diff_ready.sem, diff_ready.at(e + 1, u))
                            nc.scalar.activation(D[:, e, :], D[:, e, :], ACT.Exp).then_inc(dexp.sem, 1)
                        act.wait_ge(y_ready.sem, y_ready.at(1, u - 1))
                        gate(0)
                        act.wait_ge(projected.sem, projected.at(1, u))
                        evacuate(A, cb[:, 0, :], evacuated)
                        for e, banks in ((0, B), (1, A)):
                            act.wait_ge(rows.sem, rows.at(e + 1, u))
                            for t in range(3):
                                op = nc.scalar.activation(erow[:, e, 384 * t:384 * t + 384], banks[t][:, 0:384], ACT.Exp)
                            op.then_inc(erow_ready.sem, 1)
                        act.wait_ge(conv_done.sem, conv_done.at(1, u))
                        silu(xT, acc[:, 0, :], sm[:, SMALL - 1:SMALL], silu_done)
                        decay(0)
                        gate(1)
                        decay(1)
                        gate(2)
                    act.wait_ge(y_ready.sem, y_ready.at(1, g * GP + (GP - 1)))
                    for k in range(GP):
                        if k >= 2:
                            act.wait_ge(g_summed.sem, g_summed.at(k - 1, g))
                        nc.scalar.activation(acc[:, k % 2, 0:T], y[:, k, :], ACT.Square).then_inc(g_squared.sem, 1)
                    act.wait_ge(g_mean.sem, g_mean.at(1, g))
                    nc.scalar.activation(rstd[:, :], rstd[:, :], ACT.Sqrt).then_inc(g_root.sem, 1)

            @block.gpsimd
            def _(pool):
                nc.gpsimd.memset(xT[:, T:TP], 0.0)
                nc.gpsimd.memset(Bt[:, T:TP], 0.0)
                nc.gpsimd.memset(Ct[:, T:TP], 0.0)
                nc.gpsimd.memset(cb[:, :, 0:3], 0.0).then_inc(zeroed.sem, 1)
                with pool.Fori(0, SSM_GROUPS) as g:
                    with pool.Fori(0, GP) as p:
                        u = g * GP + p
                        pool.wait_ge(g_silu.sem, g_silu.at(2, g))
                        for e in range(2):
                            pool.wait_ge(erow_ready.sem, erow_ready.at(e + 1, u))
                            op = nc.gpsimd.tensor_tensor(Cdec[:, e, :], Ct[:, :], erow[:, e, :], ALU.mult)
                        op.then_inc(cdec_ready.sem, 1)

            @block.vector
            def _(v):
                def conv(j, small, then, done):
                    then(nc.vector.tensor_scalar(acc[:, j, 0:W], cb[:, j, 0:W], small[:, 24:25], None, ALU.mult))
                    for k in range(1, CONV):
                        op = nc.vector.scalar_tensor_tensor(acc[:, j, 0:W], cb[:, j, k:k + W], small[:, 24 + k:25 + k],
                                                            acc[:, j, 0:W], ALU.mult, ALU.add)
                        if k < CONV - 1:
                            then(op)
                        else:
                            op.then_inc(done.sem, 1)

                v.wait_ge(once.sem, once.at(2))
                v.wait_ge(zeroed.sem, 1)
                with v.Fori(0, SSM_GROUPS) as g:
                    gvec.n = 0

                    def gthen(op):
                        op.then_inc(gvec.step(), 1)
                        v.wait_ge(gvec.sem, gvec.now(g))
                    v.wait_ge(g_loaded.sem, g_loaded.at(2, g))
                    for j in range(2):
                        hist = nc.vector.tensor_copy(sample(cb[:, j, :])[:, :, 0:3], sg[:, j, 0:24].rearrange("p (b n) -> p b n", n=3))
                    gthen(hist)
                    for j in range(2):
                        v.wait_ge(g_evacuated.sem, g_evacuated.at(j + 1, g))
                        conv(j, sg[:, j, :], gthen, g_conv)
                    v.wait_ge(g_tail_stored.sem, g_tail_stored.at(1, g - 1))
                    nc.vector.tensor_copy(tg[:, :, 0, :], cb[:, :, SEQ:SOFF])
                    nc.vector.tensor_copy(tg[:, :, 1:SEQS + 1, :],
                                          cb[:, :, SOFF:CW].rearrange("p j (b n) -> p j b n", n=SW)[:, :, :, STEPS:SW]).then_inc(g_tail.sem, 1)
                    v.wait_ge(g_products.sem, g_products.at(1, g))
                    for t in range(3):
                        s = slice(384 * t, 384 * t + 384)
                        op = nc.vector.tensor_tensor(CB[:, s], A[t][:, 0:384], const["incl"][:, s], ALU.mult)
                    op.then_inc(cb_ready.sem, 1)
                    with v.Fori(0, GP) as p:
                        u = g * GP + p
                        vec.n = 0

                        def then(op):
                            op.then_inc(vec.step(), 1)
                            v.wait_ge(vec.sem, vec.now(u))
                        nc.vector.tensor_copy(cur[:, :, :, :].rearrange("p q c e -> p (q c) e"),
                                              tab[:, :, :, bass.ds(u * 2 + DN_HEADS, 2)].rearrange("p q c e -> p (q c) e")).then_inc(cur_ready.sem, 1)
                        v.wait_ge(loaded.sem, loaded.at(2, u))
                        then(nc.vector.tensor_copy(sample(cb[:, 0, :])[:, :, 0:3], sm[:, 0:24].rearrange("p (b n) -> p b n", n=3)))
                        v.wait_ge(evacuated.sem, evacuated.at(1, u))
                        conv(0, sm, then, conv_done)
                        v.wait_ge(tail_stored.sem, tail_stored.at(1, u - 1))
                        nc.vector.tensor_copy(tx[:, 0, :], cb[:, 0, SEQ:SOFF])
                        nc.vector.tensor_copy(tx[:, 1:SEQS + 1, :], sample(cb[:, 0, :])[:, :, STEPS:SW]).then_inc(tail_ready.sem, 1)
                        for e, banks in ((0, B), (1, A)):
                            v.wait_ge(erow_ready.sem, erow_ready.at(e + 1, u))
                            v.wait_ge(cur_ready.sem, cur_ready.at(1, u))
                            for c in range(NC):
                                op = nc.vector.tensor_scalar(D[:, e, CK * c:CK * c + CK], banks[c // 3][:, CK * (c % 3):CK * (c % 3) + CK],
                                                             cur[:, 1, c, e:e + 1], 0.0, ALU.subtract, ALU.min)
                            op.then_inc(diff_ready.sem, 1)
                        v.wait_ge(turned.sem, turned.at(1, u))
                        heads = lambda t: t.rearrange("p (c n) -> p c n", n=HALF)
                        col = lambda q: cur[:, q, :, :].rearrange("p c e -> p (c e)")
                        for t in range(3):
                            op = nc.vector.tensor_tensor(heads(xd[:, 384 * t:384 * t + 384]), heads(A[t][:, 0:384]),
                                                         col(4)[:, 6 * t:6 * t + 6, None].to_broadcast([P, 6, HALF]), ALU.mult)
                        then(op)
                        nc.vector.tensor_tensor(heads(xde[:, :]), heads(xd[:, :]),
                                                col(3)[:, :, None].to_broadcast([P, 2 * NC, HALF]), ALU.mult).then_inc(xde_ready.sem, 1)
                        v.wait_ge(xde_ready.sem, xde_ready.at(1, u))
                        nc.vector.tensor_tensor(xm[:, :, :], xde[:, None, SEQ:TP].to_broadcast([P, SEQS, P]),
                                                const["seq_of"][:, :, None].to_broadcast([P, SEQS, P]), ALU.mult).then_inc(xm_ready.sem, 1)
                        v.wait_ge(cb_ready.sem, cb_ready.at(1, g))
                        v.wait_ge(dexp.sem, dexp.at(2, u))
                        nc.vector.tensor_tensor(D[:, :, :], D[:, :, :], CB[:, None, :].to_broadcast([P, 2, TP]), ALU.mult).then_inc(m_ready.sem, 1)
                        v.wait_ge(state_stored.sem, state_stored.at(2, u - 1))
                        then(nc.vector.memset(H[:, 0, :], 0.0))
                        v.wait_ge(u_ready.sem, u_ready.at(1, u))
                        for c in range(NC - 1):
                            last = CK * c + CK - 1
                            for e in range(2):
                                ch = slice(HALF * e, HALF * e + HALF)
                                op = nc.vector.scalar_tensor_tensor(H[:, c + 1, ch], H[:, c, ch], erow[:, e, last:last + 1],
                                                                    B[c // 4][:, P * (c % 4) + HALF * e:P * (c % 4) + HALF * e + HALF],
                                                                    ALU.mult, ALU.add)
                            if c < NC - 2:
                                then(op)
                            else:
                                op.then_inc(h_ready.sem, 1)
                        v.wait_ge(s0_loaded.sem, s0_loaded.at(1, u))
                        for e in range(2):
                            ch = slice(HALF * e, HALF * e + HALF)
                            lasts = erow[:, e, SEQ:T].rearrange("p (b n) -> p b n", n=STEPS)[:, :, STEPS - 1:STEPS]
                            op = nc.vector.tensor_tensor(S1[:, :, ch], S0[:, :, ch], lasts.to_broadcast([P, SEQS, HALF]), ALU.mult)
                        then(op)
                        nc.vector.tensor_tensor(S1[:, 0:4, :], S1[:, 0:4, :], bank[3][:, 0:512].rearrange("p (b n) -> p b n", n=P), ALU.add)
                        nc.vector.tensor_tensor(S1[:, 4:8, :], S1[:, 4:8, :], bank[7][:, 0:512].rearrange("p (b n) -> p b n", n=P), ALU.add).then_inc(s1_ready.sem, 1)
                        v.wait_ge(y_mm.sem, y_mm.at(1, u))
                        v.wait_ge(g_stored.sem, g_stored.at(GP, g - 1))
                        yp = y[:, bass.ds(p, 1), :].rearrange("p o n -> p (o n)")
                        for c, (a, n) in enumerate(CHUNKS):
                            op = nc.vector.scalar_tensor_tensor(xT[:, a:a + n], xT[:, a:a + n], skip[:, bass.ds(u, 1)], A[c][:, 0:n],
                                                                ALU.mult, ALU.add)
                        then(op)
                        nc.vector.tensor_tensor(yp, xT[:, 0:T], zs[:, :], ALU.mult).then_inc(y_ready.sem, 1)
                        assert vec.n == VSTEPS, vec.n
                    v.wait_ge(g_summed.sem, g_summed.at(GP, g))
                    for c, (a, n) in enumerate(CHUNKS):
                        op = nc.vector.tensor_scalar(rstd[:, a:a + n], A[c][:, 0:n], 1.0 / (GP * P), EPS, ALU.mult, ALU.add)
                    op.then_inc(g_mean.sem, 1)
                    v.wait_ge(g_root.sem, g_root.at(1, g))
                    gthen(nc.vector.reciprocal(rstd[:, :], rstd[:, :]))
                    v.wait_ge(y_ready.sem, y_ready.at(1, g * GP + (GP - 1)))
                    for k in range(GP):
                        op = nc.vector.scalar_tensor_tensor(y[:, k, :], y[:, k, :], nw[:, bass.ds(g * GP + k, 1)], rstd[:, :],
                                                            ALU.mult, ALU.mult)
                    op.then_inc(g_normed.sem, 1)
                    assert gvec.n == GSTEPS, gvec.n


def row_of(a, n):
    names = " ".join("pqrs"[:len(a.shape) - 1])
    return a[bass.ds(n, 1)].rearrange(f"a {names} -> (a {names[0]}) {names[1:]}")


def split_weights(nc, pool, zero, stage, hi, lo, waits, hi_done, done, turn):
    for sig, value in waits:
        pool.wait_ge(sig.sem, value)
    n = stage.shape[-2:]
    nc.gpsimd.tensor_tensor(hi, stage, zero[:, None, :].to_broadcast([P, *n]), ALU.add).then_inc(hi_done.sem, 1)
    pool.wait_ge(hi_done.sem, turn)
    nc.gpsimd.tensor_tensor(lo, stage, hi.bitcast(F32), ALU.subtract).then_inc(done.sem, 1)


def linear(nc, bank, name, rhs, w, K, outs, tokens, how, to):
    cols = CHUNKS if tokens == T else [(0, tokens)]
    wide = to.shape[-1]
    turns = outs // 2
    with Phase(nc) as ctx:
        def pair(what, shape, dt=F32):
            return [ctx.enter_context(nc.sbuf_tensor(f"{name}_{what}{r}", shape, dt)) for r in range(2)]

        def signals(what, unit=1, primed=False):
            return [Signal(nc, ctx, f"{name}_{what}{r}", 1, unit, primed) for r in range(2)]
        wb, wh, wl = pair("w", [P, K, P]), pair("w_hi", [P, K, P], F32R), pair("w_lo", [P, K, P], F32R)
        zero = ctx.enter_context(nc.sbuf_tensor(f"{name}_zero", [P, 1], F32))
        loaded, hi_done, split = signals("loaded", 16), signals("w_hi_done"), signals("w_split", 1, True)
        product, taken = signals("product", 1, True), signals("taken", 1, True)
        zeroed = Signal(nc, ctx, f"{name}_zeroed")
        if how == "store":
            stage = pair("stage", [P, wide])
            stored = signals("stored", 16, True)
        with nc.Block() as block:
            @block.sync
            def _(sp):
                def fetch(i):
                    for r in range(2):
                        sp.wait_ge(split[r].sem, split[r].at(1, i - 1))
                        sp.dma_start(wb[r][:, :, :], row_of(w, i * 2 + r)).then_inc(loaded[r].sem, 16)

                def store(i):
                    for r in range(2):
                        sp.wait_ge(taken[r].sem, taken[r].at(1, i))
                        sp.dma_start(row_of(to, i * 2 + r), stage[r][:, :]).then_inc(stored[r].sem, 16)
                if how == "store":
                    fetch(0)
                    with sp.Fori(1, turns) as i:
                        fetch(i)
                        store(i - 1)
                    store(turns - 1)
                    for r in range(2):
                        sp.wait_ge(stored[r].sem, stored[r].at(1, turns - 1))
                else:
                    with sp.Fori(0, turns) as i:
                        fetch(i)

            @block.gpsimd
            def _(pool):
                for r in range(2):
                    for sig in (product[r], taken[r], split[r]):
                        pool.sem_inc(sig.sem, 1)
                    if how == "store":
                        pool.sem_inc(stored[r].sem, 16)
                        if wide > tokens:
                            nc.gpsimd.memset(stage[r][:, tokens:wide], 0.0)
                nc.gpsimd.memset(zero[:, :], 0.0).then_inc(zeroed.sem, 1)
                pool.wait_ge(zeroed.sem, 1)
                with pool.Fori(0, turns) as i:
                    for r in range(2):
                        split_weights(nc, pool, zero, wb[r][:, :, :], wh[r][:, :, :], wl[r][:, :, :],
                                      ((loaded[r], loaded[r].at(1, i)), (product[r], product[r].at(1, i - 1))),
                                      hi_done[r], split[r], hi_done[r].at(1, i))

            @block.tensor
            def _(pe):
                with pe.Fori(0, turns) as i:
                    for r in range(2):
                        pe.wait_ge(split[r].sem, split[r].at(1, i))
                        pe.wait_ge(taken[r].sem, taken[r].at(1, i - 1))
                        for c, (a, n) in enumerate(cols):
                            for k in range(K):
                                mm = split_product(nc, bank[3 * r + c][:, 0:n], (wh[r][:, k, :], wl[r][:, k, :]),
                                                   [x[:, k, a:a + n] for x in rhs], k == 0, k == K - 1)
                        mm.then_inc(product[r].sem, 1)

            @block.vector
            def _(v):
                v.wait_ge(zeroed.sem, 1)
                with v.Fori(0, turns) as i:
                    for r in range(2):
                        v.wait_ge(product[r].sem, product[r].at(1, i))
                        if how == "store":
                            v.wait_ge(stored[r].sem, stored[r].at(1, i - 1))
                        for c, (a, n) in enumerate(cols):
                            if how == "store":
                                op = nc.vector.tensor_copy(stage[r][:, a:a + n], bank[3 * r + c][:, 0:n])
                                continue
                            dst = to[:, bass.ds(i * 2 + r, 1), a:a + n].rearrange("p o n -> p (o n)")
                            if how == "add":
                                op = nc.vector.tensor_tensor(dst, dst, bank[3 * r + c][:, 0:n], ALU.add)
                            else:
                                op = nc.vector.tensor_copy(dst, bank[3 * r + c][:, 0:n])
                        op.then_inc(taken[r].sem, 1)


def split_pair(nc, ctx, name):
    return tuple(ctx.enter_context(nc.sbuf_tensor(f"{name}_{x}", [P, KT, T], F32R)) for x in ("hi", "lo"))


def split_tiles(nc, name, src, hi, lo, n):
    with Phase(nc) as ctx:
        hi_ready = Signal(nc, ctx, f"{name}_hi_ready", n)
        with nc.Block() as block:
            @block.scalar
            def _(act):
                for k in range(n):
                    nc.scalar.activation(hi[:, k, :], src[:, k, :], ACT.Copy).then_inc(hi_ready.sem, 1)

            @block.vector
            def _(v):
                for k in range(0, n, 2):
                    v.wait_ge(hi_ready.sem, hi_ready.at(k + 1))
                    nc.vector.tensor_tensor(lo[:, k, :], src[:, k, :], hi[:, k, :].bitcast(F32), ALU.subtract)

            @block.gpsimd
            def _(pool):
                for k in range(1, n, 2):
                    pool.wait_ge(hi_ready.sem, hi_ready.at(k + 1))
                    nc.gpsimd.tensor_tensor(lo[:, k, :], src[:, k, :], hi[:, k, :].bitcast(F32), ALU.subtract)


def load(nc, ctx, name, pairs):
    sig = Signal(nc, ctx, f"{name}_loaded", 1, 16)
    with nc.Block() as block:
        @block.sync
        def _(sp):
            for to, src in pairs:
                sp.dma_start(to, src).then_inc(sig.sem, 16)
            sp.wait_ge(sig.sem, sig.at(len(pairs)))


def memory_kv(nc, bank, const, d, out, mkT, mv):
    with Phase(nc) as ctx:
        mn = ctx.enter_context(nc.sbuf_tensor("mem_normed", [P, KT, MEM], F32))
        wv = ctx.enter_context(nc.sbuf_tensor("w_mem_v", [P, KT, D_MODEL], F32))
        load(nc, ctx, "mem", [(mn[:, :, :], d["memT"]), (wv[:, :, :], d["w_mv"])])
        rmsnorm(nc, bank, "mem_norm", mn, mn, const["gains"][:, 2, :], const["ident"][:, :], const["ones"][:, :], MEM, D_MODEL)
        parts = [ctx.enter_context(nc.sbuf_tensor(f"mem_{x}", [P, KT, MEM], F32R)) for x in ("hi", "lo")]
        split_tiles(nc, "mem_split", mn, *parts, KT)
        linear(nc, bank, "mem_k", parts, d["w_mk"], KT, KT, MEM, "copy", mkT)
        product, ready = Signal(nc, ctx, "mem_v_product", 4), Signal(nc, ctx, "mem_v_ready", 4)
        stored = Signal(nc, ctx, "mem_stored", 2, 16)
        with nc.Block() as block:
            @block.tensor
            def _(pe):
                for m in range(2):
                    for half in range(2):
                        for k in range(KT):
                            mm = nc.tensor.matmul(bank[2 * m + half][:, :], mn[:, k, P * m:P * m + P],
                                                  wv[:, k, 512 * half:512 * half + 512], start=(k == 0), stop=(k == KT - 1))
                        mm.then_inc(product.sem, 1)

            @block.vector
            def _(v):
                for m in range(2):
                    for half in range(2):
                        v.wait_ge(product.sem, product.at(2 * m + half + 1))
                        nc.vector.tensor_copy(mv[:, m, 512 * half:512 * half + 512], bank[2 * m + half][:, :]).then_inc(ready.sem, 1)

            @block.sync
            def _(sp):
                sp.dma_start(out["mem_k"], mkT[:, :, :]).then_inc(stored.sem, 16)
                sp.wait_ge(ready.sem, ready.at(4))
                sp.dma_start(out["mem_v"], mv[:, :, :]).then_inc(stored.sem, 16)
                sp.wait_ge(stored.sem, stored.at(2))


def attend_prompt(nc, bank, const, d, qx, mkT, mv, ao):
    H, SC = MEM_HEADS, (D_MODEL // MEM_HEADS) ** -0.5
    with Phase(nc) as ctx:
        def sb(name, shape):
            return ctx.enter_context(nc.sbuf_tensor(f"att_{name}", shape, F32))

        def signal(name, per=1, unit=1, primed=False):
            return Signal(nc, ctx, f"att_{name}", per, unit, primed)
        q, pr, pT = sb("q", [P, KT, P]), sb("probs", [P, H, MEM]), sb("probs_t", [P, 2, H, P])
        top, neg, total, inv = (sb(x, [P, H]) for x in ("top", "neg_top", "total", "inv"))
        loaded, scores = signal("loaded", 1, 16), signal("scores", 1, 1, True)
        top_ready, exped, probs, turned, pT_ready = (signal(x) for x in ("top_ready", "exp_ready", "probs_ready", "turned", "probs_t_ready"))
        product, taken = signal("product"), signal("taken", 1, 1, True)
        vec = Steps(nc, ctx, "att_vector_steps", 2)
        with nc.Block() as block:
            @block.sync
            def _(sp):
                with sp.Fori(0, SEQ // P) as i:
                    sp.wait_ge(scores.sem, scores.at(1, i - 1))
                    sp.dma_start(q[:, :, :], qx[:, :, bass.ds(i * P, P)].rearrange("k p n -> p k n")).then_inc(loaded.sem, 16)

            @block.tensor
            def _(pe):
                with pe.Fori(0, SEQ // P) as i:
                    pe.wait_ge(loaded.sem, loaded.at(1, i))
                    pe.wait_ge(taken.sem, taken.at(1, i - 1))
                    for h in range(H):
                        for k in range(2):
                            mm = nc.tensor.matmul(bank[h // 2][:, MEM * (h % 2):MEM * (h % 2) + MEM], q[:, 2 * h + k, :],
                                                  mkT[:, 2 * h + k, :], start=(k == 0), stop=(k == 1))
                    mm.then_inc(scores.sem, 1)
                    pe.wait_ge(probs.sem, probs.at(1, i))
                    for m in range(2):
                        for h in range(H):
                            mm = nc.tensor.transpose(bank[2 + m][:, P * h:P * h + P], pr[:, h, P * m:P * m + P], const["ident"][:, :])
                    mm.then_inc(turned.sem, 1)
                    pe.wait_ge(pT_ready.sem, pT_ready.at(1, i))
                    for k in range(KT):
                        for m in range(2):
                            mm = nc.tensor.matmul(bank[4 + k // 4][:, P * (k % 4):P * (k % 4) + P], mv[:, m, P * k:P * k + P],
                                                  pT[:, m, k // 2, :], start=(m == 0), stop=(m == 1))
                    mm.then_inc(product.sem, 1)

            @block.scalar
            def _(act):
                act.sem_inc(scores.sem, 1)
                act.sem_inc(taken.sem, 1)
                with act.Fori(0, SEQ // P) as i:
                    act.wait_ge(top_ready.sem, top_ready.at(1, i))
                    for h in range(H):
                        op = nc.scalar.activation(pr[:, h, :], bank[h // 2][:, MEM * (h % 2):MEM * (h % 2) + MEM], ACT.Exp,
                                                  bias=neg[:, h:h + 1], scale=SC, accum_out=total[:, h:h + 1])
                    op.then_inc(exped.sem, 1)
                    act.wait_ge(turned.sem, turned.at(1, i))
                    for m in range(2):
                        op = nc.scalar.activation(pT[:, m, :, :], bank[2 + m][:, :].rearrange("p (h n) -> p h n", n=P), ACT.Copy)
                    op.then_inc(pT_ready.sem, 1)

            @block.vector
            def _(v):
                with v.Fori(0, SEQ // P) as i:
                    vec.n = 0
                    v.wait_ge(scores.sem, scores.at(1, i))
                    for b in range(2):
                        op = nc.vector.tensor_reduce(top[:, 2 * b:2 * b + 2], bank[b][:, :].rearrange("p (h n) -> p h n", n=MEM), AX.X, ALU.max)
                    op.then_inc(vec.step(), 1)
                    v.wait_ge(vec.sem, vec.now(i))
                    nc.vector.tensor_scalar(neg[:, :], top[:, :], -SC, None, ALU.mult).then_inc(top_ready.sem, 1)
                    v.wait_ge(exped.sem, exped.at(1, i))
                    nc.vector.reciprocal(inv[:, :], total[:, :]).then_inc(vec.step(), 1)
                    v.wait_ge(vec.sem, vec.now(i))
                    nc.vector.tensor_tensor(pr[:, :, :], pr[:, :, :], inv[:, :, None].to_broadcast([P, H, MEM]), ALU.mult).then_inc(probs.sem, 1)
                    v.wait_ge(product.sem, product.at(1, i))
                    for b in range(2):
                        op = nc.vector.tensor_copy(ao[:, 4 * b:4 * b + 4, bass.ds(i * P, P)], bank[4 + b][:, :].rearrange("p (k n) -> p k n", n=P))
                    op.then_inc(taken.sem, 1)


def attend_sample(nc, bank, const, d, qx, ao):
    H, SC, R = MEM_HEADS, (D_MODEL // MEM_HEADS) ** -0.5, MEM_HEADS * STEPS
    with Phase(nc) as ctx:
        def sb(name, shape):
            return ctx.enter_context(nc.sbuf_tensor(f"satt_{name}", shape, F32))

        def signal(name, per=1, unit=1, primed=False):
            return Signal(nc, ctx, f"satt_{name}", per, unit, primed)
        q, qm = sb("q", [P, KT, SAMPLE]), sb("q_masked", [P, KT, 4, H, STEPS])
        K, V = sb("k", [P, 4, KT, MEM]), sb("v", [P, 4, 2, D_MODEL])
        pr, pT = sb("probs", [P, MEM]), sb("probs_t", [P, 2, P])
        top, neg, total, inv = (sb(x, [P, 1]) for x in ("top", "neg_top", "total", "inv"))
        q_loaded, zeroed = signal("q_loaded", 1, 16), signal("zeroed")
        k_loaded = [signal(f"k_loaded{b}", 1, 16) for b in range(4)]
        v_loaded = [signal(f"v_loaded{b}", 1, 16) for b in range(4)]
        masked, scores = signal("masked"), signal("scores", 1, 1, True)
        top_ready, exped, probs, turned, pT_ready = (signal(x) for x in ("top_ready", "exp_ready", "probs_ready", "turned", "probs_t_ready"))
        product, taken = signal("product"), signal("taken", 1, 1, True)
        vec = Steps(nc, ctx, "satt_vector_steps", 2)
        with nc.Block() as block:
            @block.sync
            def _(sp):
                sp.dma_start(q[:, :, :], qx[:, :, SEQ:T].rearrange("k p n -> p k n")).then_inc(q_loaded.sem, 16)
                with sp.Fori(0, SEQS // 4) as i:
                    sp.wait_ge(scores.sem, scores.at(1, i - 1))
                    for b in range(4):
                        sp.dma_start(K[:, b, :, :], row_of(d["cache_k"], i * 4 + b)).then_inc(k_loaded[b].sem, 16)
                    sp.wait_ge(taken.sem, taken.at(1, i - 1))
                    for b in range(4):
                        sp.dma_start(V[:, b, :, :], row_of(d["cache_v"], i * 4 + b)).then_inc(v_loaded[b].sem, 16)

            @block.gpsimd
            def _(pool):
                nc.gpsimd.memset(qm[:, :, :, :, :].rearrange("p k b h n -> p (k b h n)"), 0.0).then_inc(zeroed.sem, 1)

            @block.tensor
            def _(pe):
                with pe.Fori(0, SEQS // 4) as i:
                    pe.wait_ge(masked.sem, masked.at(1, i))
                    pe.wait_ge(taken.sem, taken.at(1, i - 1))
                    for b in range(4):
                        pe.wait_ge(k_loaded[b].sem, k_loaded[b].at(1, i))
                        for k in range(KT):
                            mm = nc.tensor.matmul(bank[0][R * b:R * b + R, 0:MEM], qm[:, k, b, :, :].rearrange("p h n -> p (h n)"),
                                                  K[:, b, k, :], start=(k == 0), stop=(k == KT - 1))
                    mm.then_inc(scores.sem, 1)
                    pe.wait_ge(probs.sem, probs.at(1, i))
                    for m in range(2):
                        mm = nc.tensor.transpose(bank[2][:, P * m:P * m + P], pr[:, P * m:P * m + P], const["ident"][:, :])
                    mm.then_inc(turned.sem, 1)
                    pe.wait_ge(pT_ready.sem, pT_ready.at(1, i))
                    for b in range(4):
                        pe.wait_ge(v_loaded[b].sem, v_loaded[b].at(1, i))
                        for k in range(KT):
                            a = STEPS * (4 * k + b)
                            for m in range(2):
                                p0 = R * b + STEPS * (k // 2)
                                mm = nc.tensor.matmul(bank[4][:, a:a + STEPS], V[:, b, m, P * k:P * k + P],
                                                      pT[:, m, p0:p0 + STEPS], start=(m == 0), stop=(m == 1))
                    mm.then_inc(product.sem, 1)

            @block.scalar
            def _(act):
                act.sem_inc(scores.sem, 1)
                act.sem_inc(taken.sem, 1)
                with act.Fori(0, SEQS // 4) as i:
                    act.wait_ge(top_ready.sem, top_ready.at(1, i))
                    nc.scalar.activation(pr[:, :], bank[0][:, 0:MEM], ACT.Exp, bias=neg[:, 0:1], scale=SC,
                                         accum_out=total[:, 0:1]).then_inc(exped.sem, 1)
                    act.wait_ge(turned.sem, turned.at(1, i))
                    nc.scalar.activation(pT[:, :, :], bank[2][:, 0:2 * P].rearrange("p (m n) -> p m n", n=P), ACT.Copy).then_inc(pT_ready.sem, 1)

            @block.vector
            def _(v):
                v.wait_ge(q_loaded.sem, q_loaded.at(1))
                v.wait_ge(zeroed.sem, zeroed.at(1))
                with v.Fori(0, SEQS // 4) as i:
                    vec.n = 0
                    for h in range(H):
                        op = nc.vector.tensor_copy(qm[:, 2 * h:2 * h + 2, :, h, :],
                                                   q[:, 2 * h:2 * h + 2, bass.ds(i * (4 * STEPS), 4 * STEPS)].rearrange("p k (b n) -> p k b n", n=STEPS))
                    op.then_inc(masked.sem, 1)
                    v.wait_ge(scores.sem, scores.at(1, i))
                    nc.vector.tensor_reduce(top[:, :], bank[0][:, 0:MEM], AX.X, ALU.max).then_inc(vec.step(), 1)
                    v.wait_ge(vec.sem, vec.now(i))
                    nc.vector.tensor_scalar(neg[:, :], top[:, :], -SC, None, ALU.mult).then_inc(top_ready.sem, 1)
                    v.wait_ge(exped.sem, exped.at(1, i))
                    nc.vector.reciprocal(inv[:, :], total[:, :]).then_inc(vec.step(), 1)
                    v.wait_ge(vec.sem, vec.now(i))
                    nc.vector.tensor_scalar(pr[:, :], pr[:, :], inv[:, 0:1], None, ALU.mult).then_inc(probs.sem, 1)
                    v.wait_ge(product.sem, product.at(1, i))
                    nc.vector.tensor_copy(ao[:, :, bass.ds(i * (4 * STEPS) + SEQ, 4 * STEPS)],
                                          bank[4][:, 0:KT * 4 * STEPS].rearrange("p (k n) -> p k n", n=4 * STEPS)).then_inc(taken.sem, 1)


def route(nc, bank, const, d, qp, gd):
    PH, TK, NK = PHEADS, TOPK, NKEYS
    LOW = -3.0e38
    PICK, GROUPS = 4, 4
    BANKS = (bank[5], bank[6], bank[7], bank[4])
    LAST = NC - 1
    with Phase(nc) as ctx:
        def sb(name, shape, dt=F32):
            return ctx.enter_context(nc.sbuf_tensor(f"route_{name}", shape, dt))

        def signal(name, per=1, unit=1, primed=False):
            return Signal(nc, ctx, f"route_{name}", per, unit, primed)
        keys, iota = sb("keys", [P, 2, NK]), sb("iota", [P, NK])
        q, s, s2 = sb("q", [P, 2 * PH, P]), sb("scores", [P, 2 * PH, NK]), sb("scores_left", [P, 2 * PH, NK])
        top, ix = sb("top", [P, 2 * PH, TK]), sb("top_index", [P, 2 * PH, TK], U32)
        ixf = sb("top_index_f", [P, 2 * PH, TK])
        cand, cand2 = sb("sums", [P, PH, TK, TK]), sb("sums_left", [P, PH, TK * TK])
        best, pos = sb("best", [P, PH, TK]), sb("position", [P, PH, TK], U32)
        half, halff = sb("rank", [P, 2, PH * TK], U32), sb("rank_f", [P, 2, PH * TK])
        total, blank = sb("total", [P, PH]), sb("blank", [P, 1])
        pick = sb("picks", [P, 3, P])
        pickT = sb("picks_t", [P, 3, P])
        E = [sb(f"onehots{r}", [P, 2, PICK, NK]) for r in range(GROUPS)]
        G = sb("gates", [P, NK, P])
        once, loaded = signal("keys_loaded", 2, 16), signal("loaded", 1, 16)
        scored, s_ready = signal("scored"), signal("scores_ready", 1)
        shifted, exped = signal("shifted"), signal("exp_ready")
        picked, turned, pickT_ready = signal("picked"), signal("turned"), signal("picks_t_ready")
        onehots = [signal(f"onehots_ready{r}") for r in range(GROUPS)]
        weighted = [signal(f"gated_onehots_ready{r}") for r in range(GROUPS)]
        gmm = [signal(f"gates_product{r}", 1, 1, True) for r in range(GROUPS)]
        gout = [signal(f"gates_taken{r}", 1, 1, True) for r in range(GROUPS)]
        stored = signal("stored", 1, 16, True)
        VSTEPS = 17
        vec = Steps(nc, ctx, "route_vector_steps", VSTEPS)
        TURNS = P // (GROUPS * PICK)
        LAST_TURNS = SAMPLE // (GROUPS * PICK)

        with nc.Block() as block:
            @block.sync
            def _(sp):
                sp.dma_start(keys[:, :, :], d["keysT"]).then_inc(once.sem, 16)
                sp.dma_start(iota[:, :], d["iota"].partition_broadcast(P)).then_inc(once.sem, 16)

                def load_q(i):
                    sp.dma_start(q[:, :, :], qp[:, :, bass.ds(i * P, P)].rearrange("k p n -> p k n")).then_inc(loaded.sem, 16)

                def store(i, turns):
                    for r in range(GROUPS):
                        sp.wait_ge(gout[r].sem, gout[r].at(1, i * TURNS + (turns - 1)))
                    n = turns * GROUPS * PICK
                    sp.dma_start(gd[:, :, bass.ds(i * P, n)].rearrange("j i n -> i j n"), G[:, :, 0:n]).then_inc(stored.sem, 16)
                load_q(0)
                with sp.Fori(0, LAST) as i:
                    sp.wait_ge(scored.sem, scored.at(1, i))
                    load_q(i + 1)
                    store(i, TURNS)
                store(LAST, LAST_TURNS)
                sp.wait_ge(stored.sem, stored.at(1, LAST))

            @block.tensor
            def _(pe):
                def scores(i):
                    pe.wait_ge(loaded.sem, loaded.at(1, i))
                    for n in range(2 * PH):
                        mm = nc.tensor.matmul(bank[n // 4][:, P * (n % 4):P * (n % 4) + P], q[:, n, :], keys[:, n % 2, :], start=True, stop=True)
                    mm.then_inc(scored.sem, 1)

                def turn_picks(i):
                    pe.wait_ge(picked.sem, picked.at(1, i))
                    pe.wait_ge(gout[3].sem, gout[3].at(1, i * TURNS - 1))
                    for x in range(3):
                        mm = nc.tensor.transpose(bank[4][:, P * x:P * x + P], pick[:, x, :], const["ident"][:, :])
                    mm.then_inc(turned.sem, 1)

                def products(i, turns):
                    with pe.Fori(0, turns) as j:
                        w = i * TURNS + j
                        for r in range(GROUPS):
                            pe.wait_ge(weighted[r].sem, weighted[r].at(1, w))
                            pe.wait_ge(gout[r].sem, gout[r].at(1, w - 1))
                            for t in range(PICK):
                                mm = nc.tensor.matmul(BANKS[r][:, P * t:P * t + P], E[r][:, 0, t, :], E[r][:, 1, t, :], start=True, stop=True)
                            mm.then_inc(gmm[r].sem, 1)
                pe.wait_ge(once.sem, once.at(2))
                scores(0)
                with pe.Fori(0, LAST) as i:
                    turn_picks(i)
                    pe.wait_ge(s_ready.sem, s_ready.at(1, i))
                    scores(i + 1)
                    products(i, TURNS)
                turn_picks(LAST)
                products(LAST, LAST_TURNS)

            @block.scalar
            def _(act):
                act.sem_inc(stored.sem, 16)
                for r in range(GROUPS):
                    act.sem_inc(gmm[r].sem, 1)
                    act.sem_inc(gout[r].sem, 1)

                def take_scores(i):
                    act.wait_ge(scored.sem, scored.at(1, i))
                    for b in range(4):
                        op = nc.scalar.activation(s[:, 4 * b:4 * b + 4, :], bank[b][:, :].rearrange("p (n k) -> p n k", k=NK), ACT.Copy)
                    op.then_inc(s_ready.sem, 1)

                def exp_and_picks(i):
                    act.wait_ge(shifted.sem, shifted.at(1, i))
                    nc.scalar.activation(best[:, :, :], best[:, :, :], ACT.Exp).then_inc(exped.sem, 1)
                    act.wait_ge(turned.sem, turned.at(1, i))
                    nc.scalar.activation(pickT[:, :, :], bank[4][:, 0:3 * P].rearrange("p (x n) -> p x n", n=P), ACT.Copy).then_inc(pickT_ready.sem, 1)

                def take_gates(i, turns):
                    with act.Fori(0, turns) as j:
                        w = i * TURNS + j
                        for r in range(GROUPS):
                            act.wait_ge(stored.sem, stored.at(1, i - 1))
                            act.wait_ge(gmm[r].sem, gmm[r].at(1, w))
                            nc.scalar.activation(G[:, :, bass.ds(j * (GROUPS * PICK) + PICK * r, PICK)].rearrange("p j n -> p n j"),
                                                 BANKS[r][:, :].rearrange("p (n j) -> p n j", j=NK), ACT.Copy).then_inc(gout[r].sem, 1)
                take_scores(0)
                with act.Fori(0, LAST) as i:
                    exp_and_picks(i)
                    take_scores(i + 1)
                    take_gates(i, TURNS)
                exp_and_picks(LAST)
                take_gates(LAST, LAST_TURNS)

            @block.gpsimd
            def _(pool):
                def weight(i, turns):
                    with pool.Fori(0, turns) as j:
                        w = i * TURNS + j
                        for r in range(GROUPS):
                            pool.wait_ge(onehots[r].sem, onehots[r].at(1, w))
                            at = bass.ds(j * (GROUPS * PICK) + PICK * r, PICK)
                            nc.gpsimd.tensor_tensor(E[r][:, 1, :, :], E[r][:, 1, :, :],
                                                    pickT[:, 0, at][:, :, None].to_broadcast([P, PICK, NK]), ALU.mult).then_inc(weighted[r].sem, 1)
                with pool.Fori(0, LAST) as i:
                    weight(i, TURNS)
                weight(LAST, LAST_TURNS)

            @block.vector
            def _(v):
                def tile(i, turns):
                    vec.n = 0

                    def then(op):
                        op.then_inc(vec.step(), 1)
                        v.wait_ge(vec.sem, vec.now(i))

                    def settled(op):
                        then(op)
                        nc.vector.memset(blank[:, :], 0.0)

                    def top16(rows, values, left, at, index):
                        settled([nc.vector.max(at(n)[:, 0:8], values(n)) for n in range(rows)][-1])
                        for n in range(rows):
                            nc.vector.max_index(index(n)[:, 0:8], at(n)[:, 0:8], values(n))
                            op = nc.vector.match_replace(left(n), at(n)[:, 0:8], values(n), LOW)
                        settled(op)
                        settled([nc.vector.max(at(n)[:, 8:16], left(n)) for n in range(rows)][-1])
                        then([nc.vector.max_index(index(n)[:, 8:16], at(n)[:, 8:16], left(n)) for n in range(rows)][-1])
                    v.wait_ge(s_ready.sem, s_ready.at(1, i))
                    nc.vector.memset(blank[:, :], 0.0)
                    top16(2 * PH, lambda n: s[:, n, :], lambda n: s2[:, n, :], lambda n: top[:, n, :], lambda n: ix[:, n, :])
                    halves = top[:, :, :].rearrange("p (h c) k -> p h c k", c=2)
                    for h in range(PH):
                        op = nc.vector.tensor_tensor(cand[:, h, :, :], halves[:, h, 0, :, None].to_broadcast([P, TK, TK]),
                                                     halves[:, h, 1, None, :].to_broadcast([P, TK, TK]), ALU.add)
                    settled(op)
                    flat = cand[:, :, :, :].rearrange("p h a b -> p h (a b)")
                    top16(PH, lambda n: flat[:, n, :], lambda n: cand2[:, n, :], lambda n: best[:, n, :], lambda n: pos[:, n, :])
                    flatpos = pos[:, :, :].rearrange("p h k -> p (h k)")
                    nc.vector.tensor_scalar(half[:, 0, :], flatpos, 4, None, ALU.logical_shift_right)
                    nc.vector.tensor_scalar(half[:, 1, :], flatpos, 15, None, ALU.bitwise_and)
                    nc.vector.tensor_copy(ixf[:, :, :], ix[:, :, :])
                    then(nc.vector.tensor_copy(total[:, :], best[:, :, 0]))
                    nc.vector.tensor_copy(halff[:, :, :], half[:, :, :])
                    nc.vector.tensor_tensor(best[:, :, :], best[:, :, :], total[:, :, None].to_broadcast([P, PH, TK]),
                                            ALU.subtract).then_inc(shifted.sem, 1)
                    v.wait_ge(shifted.sem, shifted.at(1, i))
                    index = ixf[:, :, :].rearrange("p (h c) k -> p h c k", c=2)
                    for c in range(2):
                        eq = cand[:, :, :, :].rearrange("p h a b -> p (h a) b")
                        then(nc.vector.tensor_tensor(eq, halff[:, c, :, None].to_broadcast([P, PH * TK, TK]),
                                                     iota[:, None, 0:TK].to_broadcast([P, PH * TK, TK]), ALU.is_equal))
                        for h in range(PH):
                            op = nc.vector.tensor_tensor(cand[:, h, :, :], cand[:, h, :, :], index[:, h, c, None, :].to_broadcast([P, TK, TK]), ALU.mult)
                        then(op)
                        if c == 0:
                            then(nc.vector.tensor_reduce(pick[:, 1, :], eq, AX.X, ALU.add))
                        else:
                            nc.vector.tensor_reduce(pick[:, 2, :], eq, AX.X, ALU.add)
                    v.wait_ge(exped.sem, exped.at(1, i))
                    then(nc.vector.tensor_reduce(total[:, :], best[:, :, :], AX.X, ALU.add))
                    then(nc.vector.reciprocal(total[:, :], total[:, :]))
                    nc.vector.tensor_tensor(pick[:, 0, :].rearrange("p (h k) -> p h k", k=TK), best[:, :, :],
                                            total[:, :, None].to_broadcast([P, PH, TK]), ALU.mult).then_inc(picked.sem, 1)
                    assert vec.n == VSTEPS, vec.n
                    with v.Fori(0, turns) as j:
                        w = i * TURNS + j
                        for r in range(GROUPS):
                            v.wait_ge(pickT_ready.sem, pickT_ready.at(1, i))
                            v.wait_ge(gmm[r].sem, gmm[r].at(1, w - 1))
                            at = bass.ds(j * (GROUPS * PICK) + PICK * r, PICK)
                            nc.vector.tensor_tensor(E[r][:, :, :, :], iota[:, None, None, :].to_broadcast([P, 2, PICK, NK]),
                                                    pickT[:, 1:3, at][:, :, :, None].to_broadcast([P, 2, PICK, NK]),
                                                    ALU.is_equal).then_inc(onehots[r].sem, 1)
                v.wait_ge(once.sem, once.at(2))
                with v.Fori(0, LAST) as i:
                    tile(i, TURNS)
                tile(LAST, LAST_TURNS)


def experts(nc, bank, const, d, gd, fn, h):
    GROUP = 4
    M = 3 * GROUP
    O = 3 * KT
    TURNS = NKEYS // GROUP
    ORDER = [("v", 0, 0), ("u", 2, 0), ("v", 1, 0), ("u", 3, 0), ("v", 2, 0), ("v", 3, 0), ("u", 0, 1), ("u", 1, 1)]
    PLACE = {(x, j): n + 3 - 8 * ahead for n, (x, j, ahead) in enumerate(ORDER)}
    with Phase(nc) as ctx:
        def sb(name, shape, dt=F32):
            return ctx.enter_context(nc.sbuf_tensor(f"exp_{name}", shape, dt))

        def signal(name, per=1, unit=1, primed=False):
            return Signal(nc, ctx, f"exp_{name}", per, unit, primed)
        stage = sb("stage", [P, 2, D_MODEL])
        Uh, Ul = sb("u_hi", [P, 2, KT, P], F32R), sb("u_lo", [P, 2, KT, P], F32R)
        Vh, Vl = sb("v_hi", [P, GROUP, D_MODEL], F32R), sb("v_lo", [P, GROUP, D_MODEL], F32R)
        Ah, Al = sb("hidden_hi", [P, GROUP, T], F32R), sb("hidden_lo", [P, GROUP, T], F32R)
        G, act_t, zero = sb("gates", [P, 4, 384]), sb("gelu", [P, 3, 384]), sb("zero", [P, 1])
        zeroed = signal("zeroed")
        loaded = [signal(f"loaded{r}", 4, 16) for r in range(2)]
        hi_done, split = signal("w_hi_done", 8), signal("w_split", 8)
        g_loaded = [signal(f"gates_loaded{r}", M // 4, 16) for r in range(4)]
        hidden = signal("hidden_product", M)
        gelu, gated = signal("gelu_ready", M), signal("gated", M)
        ah_ready, al_ready = signal("hidden_hi_ready", M), signal("hidden_lo_ready", M)
        product, added = signal("product", O, 1, True), signal("added", O, 1, True)

        def earlier(sig, n, back, turn):
            if n > back:
                return sig.at(n - back, turn)
            return None if isinstance(turn, int) and turn == 0 else sig.at(n - back + sig.per, turn - 1)

        def by_turns(engine, first, body):
            first(0)
            with engine.Fori(0, TURNS - 1) as i:
                body(i, False)
            body(TURNS - 1, True)

        with nc.Block() as block:
            @block.sync
            def _(sp):
                def fetch(x, j, turn):
                    r = (PLACE[x, j] + 1) % 2
                    free = earlier(split, PLACE[x, j], 2, turn)
                    if free is not None:
                        sp.wait_ge(split.sem, free)
                    src = row_of(d[f"peer_{x}"], turn * GROUP + j)
                    if x == "u":
                        src = src.rearrange("p k n -> p (k n)")
                    sp.dma_start(stage[:, r, :], src).then_inc(loaded[r].sem, 16)

                def first(turn):
                    fetch("u", 0, 0)
                    fetch("u", 1, 0)

                def body(turn, last):
                    for x, j, ahead in ORDER:
                        if not (last and ahead):
                            fetch(x, j, turn + ahead)
                by_turns(sp, first, body)

            @block.gpsimd
            def _(pool):
                def take(x, j, turn):
                    n = PLACE[x, j]
                    r = (n + 1) % 2
                    waits = [(loaded[r], loaded[r].at((n + 1) // 2, turn))]
                    if x == "v":
                        hi, lo = Vh[:, j:j + 1, :], Vl[:, j:j + 1, :]
                        waits.append((product, product.at(O, turn - 1)))
                        src = stage[:, r:r + 1, :]
                    else:
                        hi, lo = Uh[:, j % 2, :, :], Ul[:, j % 2, :, :]
                        src = stage[:, r, :].rearrange("p (k n) -> p k n", n=P)
                        used = earlier(hidden, 3 * j + 3, 6, turn)
                        if used is not None:
                            waits.append((hidden, used))
                    split_weights(nc, pool, zero, src, hi, lo, waits, hi_done, split, hi_done.at(n, turn))

                def first(turn):
                    nc.gpsimd.memset(zero[:, :], 0.0).then_inc(zeroed.sem, 1)
                    pool.sem_inc(product.sem, O)
                    pool.sem_inc(added.sem, O)
                    pool.wait_ge(zeroed.sem, 1)
                    take("u", 0, 0)
                    take("u", 1, 0)

                def body(turn, last):
                    for x, j, ahead in ORDER:
                        if not (last and ahead):
                            take(x, j, turn + ahead)
                by_turns(pool, first, body)

            @block.tensor
            def _(pe):
                def hidden_tile(j, turn):
                    pe.wait_ge(split.sem, split.at(PLACE["u", j], turn))
                    for c, (a, n) in enumerate(CHUNKS):
                        m = 3 * j + c
                        free = gelu.at(1, turn) if m == 3 else earlier(gelu, m + 1, 4, turn)
                        if free is not None:
                            pe.wait_ge(gelu.sem, free)
                        for k in range(KT):
                            mm = split_product(nc, bank[m % 4][:, 0:n], (Uh[:, j % 2, k, :], Ul[:, j % 2, k, :]),
                                               [x[:, k, a:a + n] for x in fn], k == 0, k == KT - 1)
                        mm.then_inc(hidden.sem, 1)

                def body(turn, last):
                    for j in range(1, GROUP):
                        hidden_tile(j, turn)
                    if not last:
                        hidden_tile(0, turn + 1)
                    pe.wait_ge(split.sem, split.at(PLACE["v", GROUP - 1], turn))
                    pe.wait_ge(al_ready.sem, al_ready.at(M, turn))
                    for k in range(KT):
                        for c, (a, n) in enumerate(CHUNKS):
                            m = 3 * k + c
                            pe.wait_ge(added.sem, added.at(m - 3, turn) if m >= 4 else added.at(O - 3 + m, turn - 1))
                            for j in range(GROUP):
                                s = slice(P * k, P * k + P)
                                mm = split_product(nc, bank[4 + m % 4][:, 0:n], (Vh[:, j, s], Vl[:, j, s]),
                                                   (Ah[:, j, a:a + n], Al[:, j, a:a + n]), j == 0, j == GROUP - 1)
                            mm.then_inc(product.sem, 1)
                by_turns(pe, lambda turn: hidden_tile(0, 0), body)

            @block.scalar
            def _(act):
                def fetch_gates(m, turn):
                    j, c = divmod(m, 3)
                    a, n = CHUNKS[c]
                    act.dma_start(G[:, m % 4, 0:n], row_of(gd, turn * GROUP + j)[:, a:a + n]).then_inc(g_loaded[m % 4].sem, 16)

                def activate(m, turn):
                    n = CHUNKS[m % 3][1]
                    act.wait_ge(hidden.sem, hidden.at(m + 1, turn))
                    free = earlier(al_ready, m + 1, 3, turn)
                    if free is not None:
                        act.wait_ge(al_ready.sem, free)
                    nc.scalar.activation(act_t[:, m % 3, 0:n], bank[m % 4][:, 0:n], ACT.Gelu).then_inc(gelu.sem, 1)

                def high(m, turn, last):
                    a, n = CHUNKS[m % 3]
                    act.wait_ge(product.sem, product.at(O, turn - 1))
                    act.wait_ge(gated.sem, gated.at(m + 1, turn))
                    nc.scalar.activation(Ah[:, m // 3, a:a + n], act_t[:, m % 3, 0:n], ACT.Copy).then_inc(ah_ready.sem, 1)
                    if m + 4 < M:
                        fetch_gates(m + 4, turn)
                    elif not last:
                        fetch_gates(m + 4 - M, turn + 1)

                def first(turn):
                    for m in range(4):
                        fetch_gates(m, 0)
                    act.wait_ge(zeroed.sem, 1)
                    for m in range(3):
                        activate(m, 0)

                def body(turn, last):
                    for m in range(3):
                        high(m, turn, last)
                    for m in range(3, M):
                        activate(m, turn)
                        if m > 3:
                            high(m - 1, turn, last)
                    if not last:
                        activate(0, turn + 1)
                    high(M - 1, turn, last)
                    if not last:
                        activate(1, turn + 1)
                        activate(2, turn + 1)
                by_turns(act, first, body)

            @block.vector
            def _(v):
                def gate(m, turn):
                    n = CHUNKS[m % 3][1]
                    v.wait_ge(gelu.sem, gelu.at(m + 1, turn))
                    v.wait_ge(g_loaded[m % 4].sem, g_loaded[m % 4].at(m // 4 + 1, turn))
                    nc.vector.tensor_tensor(act_t[:, m % 3, 0:n], act_t[:, m % 3, 0:n], G[:, m % 4, 0:n], ALU.mult).then_inc(gated.sem, 1)

                def low(m, turn):
                    a, n = CHUNKS[m % 3]
                    v.wait_ge(ah_ready.sem, ah_ready.at(m + 1, turn))
                    nc.vector.tensor_tensor(Al[:, m // 3, a:a + n], act_t[:, m % 3, 0:n],
                                            Ah[:, m // 3, a:a + n].bitcast(F32), ALU.subtract).then_inc(al_ready.sem, 1)

                def first(turn):
                    for m in range(3):
                        gate(m, 0)

                def body(turn, last):
                    for m in range(3):
                        low(m, turn)
                    for m in range(3, M):
                        gate(m, turn)
                        if m > 3:
                            low(m - 1, turn)
                    low(M - 1, turn)
                    if not last:
                        for m in range(3):
                            gate(m, turn + 1)
                    v.wait_ge(added.sem, added.at(O, turn - 1))
                    for k in range(KT):
                        for c, (a, n) in enumerate(CHUNKS):
                            m = 3 * k + c
                            v.wait_ge(product.sem, product.at(m + 1, turn))
                            nc.vector.tensor_tensor(h[:, k, a:a + n], h[:, k, a:a + n], bank[4 + m % 4][:, 0:n], ALU.add).then_inc(added.sem, 1)
                by_turns(v, first, body)


def trunk(nc, d, out):
    with Phase(nc) as ctx:
        bank = psum_banks(nc, ctx, "psum")
        mix = nc.dram_tensor("mixed_heads", (2 * KT, P, T), F32, kind="Internal").ap()
        const = {n: ctx.enter_context(nc.sbuf_tensor(f"const_{n}", s, F32)) for n, s in (
            ("ident", [P, P]), ("ones", [P, P]), ("gains", [P, 5, KT]))}
        eps = const["eps"] = ctx.enter_context(nc.sbuf_tensor("const_eps", [P, 1], F32))
        names = [n for n in const if n != "eps"]
        loaded = Signal(nc, ctx, "setup_loaded", 1, 16)
        with Phase(nc) as mixer:
            def sb(name, shape):
                return mixer.enter_context(nc.sbuf_tensor(name, shape, F32))
            xn = sb("x_normed", [P, KT, TP])
            tab = sb("gate_table", [P, 5, NC, GATED])
            for n, shape in (("incl", [P, TP]), ("tri", [P, 2, P]), ("total", [P, 2, P]), ("seq_of", [P, SEQS])):
                const[n] = sb(f"const_{n}", shape)
                names.append(n)
            with Phase(nc) as first:
                x = first.enter_context(nc.sbuf_tensor("x_in", [P, KT, T], F32))
                ws = first.enter_context(nc.sbuf_tensor("w_small", [P, KT, 32], F32))
                with nc.Block() as block:
                    @block.sync
                    def _(sp):
                        for n in names:
                            sp.dma_start(const[n].ap() if hasattr(const[n], "ap") else const[n], d[n]).then_inc(loaded.sem, 16)
                        for k in range(KT):
                            sp.dma_start(x[:, k, :], d["xT"][k]).then_inc(loaded.sem, 16)
                        sp.dma_start(ws[:, :, :], d["w_small"]).then_inc(loaded.sem, 16)
                        sp.wait_ge(loaded.sem, loaded.at(len(names) + KT + 1))

                    @block.vector
                    def _(v):
                        nc.vector.memset(eps[:, :], EPS)
                        nc.vector.memset(xn[:, :, T:TP], 0.0)
                rmsnorm(nc, bank, "mix_norm", x, xn, const["gains"][:, 0, :], const["ident"][:, :], const["ones"][:, :], T, D_MODEL)
                gates(nc, bank, xn, ws, const["tri"], const["total"], d, tab)
            delta_net(nc, bank, xn, tab, d, const, mix, out)
            ssd(nc, bank, xn, tab, d, const, mix, out)
        h = ctx.enter_context(nc.sbuf_tensor("residual", [P, KT, T], F32))
        with Phase(nc) as part:
            load(nc, part, "x", [(h[:, k, :], d["xT"][k]) for k in range(KT)])
            for half, name in enumerate(("heads_dn", "heads_ssm")):
                with Phase(nc) as inner:
                    heads = inner.enter_context(nc.sbuf_tensor(f"{name}", [P, KT, T], F32))
                    parts = split_pair(nc, inner, name)
                    load(nc, inner, name, [(heads[:, k, :], mix[half * KT + k]) for k in range(KT)])
                    split_tiles(nc, name, heads, *parts, KT)
                    linear(nc, bank, f"w_{name}", parts, d[f"w_{name}"], KT, KT, T, "add", h)
        with Phase(nc) as part:
            mkT = part.enter_context(nc.sbuf_tensor("mem_keys", [P, KT, MEM], F32))
            mv = part.enter_context(nc.sbuf_tensor("mem_values", [P, 2, D_MODEL], F32))
            qx = nc.dram_tensor("attention_q", (KT, P, T), F32, kind="Internal").ap()
            memory_kv(nc, bank, const, d, out, mkT, mv)
            with Phase(nc) as inner:
                cn = split_pair(nc, inner, "c_normed")
                rmsnorm(nc, bank, "att_norm", h, cn, const["gains"][:, 1, :], const["ident"][:, :], const["ones"][:, :], T, D_MODEL)
                linear(nc, bank, "w_xq", cn, d["w_xq"], KT, KT, T, "store", qx)
            ao = part.enter_context(nc.sbuf_tensor("attended", [P, KT, T], F32))
            attend_prompt(nc, bank, const, d, qx, mkT, mv, ao)
            attend_sample(nc, bank, const, d, qx, ao)
            parts = split_pair(nc, part, "attended")
            split_tiles(nc, "attended", ao, *parts, KT)
            linear(nc, bank, "w_xo", parts, d["w_xo"], KT, KT, T, "add", h)
        with Phase(nc) as part:
            qp = nc.dram_tensor("retrieval_q", (2 * PHEADS, P, TP), F32, kind="Internal").ap()
            gd = nc.dram_tensor("expert_gates", (NKEYS, P, TP), F32, kind="Internal").ap()
            with Phase(nc) as inner:
                fn = split_pair(nc, inner, "f_normed")
                rmsnorm(nc, bank, "ffn_norm", h, fn, const["gains"][:, 3, :], const["ident"][:, :], const["ones"][:, :], T, D_MODEL)
                linear(nc, bank, "w_pq", fn, d["w_pq"], KT, 2 * PHEADS, T, "store", qp)
            route(nc, bank, const, d, qp, gd)
            fn = split_pair(nc, part, "e_normed")
            rmsnorm(nc, bank, "exp_norm", h, fn, const["gains"][:, 3, :], const["ident"][:, :], const["ones"][:, :], T, D_MODEL)
            experts(nc, bank, const, d, gd, fn, h)
        with Phase(nc) as part:
            y = part.enter_context(nc.sbuf_tensor("y_out", [P, KT, T], F32))
            rmsnorm(nc, bank, "final_norm", h, y, const["gains"][:, 4, :], const["ident"][:, :], const["ones"][:, :], T, D_MODEL)
            stored = Signal(nc, part, "y_stored", 1, 16)
            with nc.Block() as block:
                @block.sync
                def _(sp):
                    for k in range(KT):
                        sp.dma_start(out["y"][k], y[:, k, :]).then_inc(stored.sem, 16)
                    sp.wait_ge(stored.sem, stored.at(KT))


def layouts(i):
    f = lambda a: np.ascontiguousarray(a)
    tiles = lambda a, k: a.reshape(k, P, -1).transpose(1, 0, 2)
    w_in = i["w_in"][0]
    qkv, xbc, z_dn, z_ssm, small = np.split(w_in, np.cumsum([3072, 1536, 1024, 1024]), axis=1)
    d = {}
    x = np.concatenate([i["x_prompt"][0], i["x_sample"].reshape(SAMPLE, D_MODEL)])
    d["xT"] = f(x.T.reshape(KT, P, T))
    d["w_small"] = f(tiles(small, KT))
    d["gate_bias"] = f(np.concatenate([i["dn_dt_bias"][0], i["ssm_dt_bias"][0]]))
    d["gate_rate"] = f(np.concatenate([i["dn_A_log"][0], i["ssm_A_log"][0]]))
    col = lambda a: a.reshape(KT, P).T
    d["gains"] = f(np.stack([col(a) for a in (i["g_mix"][0], i["g_xattn"][0], i["g_mem"][0], i["g_ffn"][0], i["g_final"])], 1))
    w = np.concatenate([qkv, z_dn], 1).reshape(KT, P, 4, DN_HEADS, P)
    d["w_dn"] = f(w.transpose(3, 1, 0, 2, 4))
    d["dn_conv_w"] = f(i["dn_conv_w"][0].reshape(CONV, 3, DN_HEADS, P).transpose(2, 3, 1, 0))
    d["dn_hist"] = f(i["state_dn_conv"][0].reshape(SEQS, 3, 3, DN_HEADS, P).transpose(3, 4, 2, 0, 1))
    d["dn_s0"] = f(i["state_dn"][0].transpose(1, 2, 0, 3))
    d["dn_norm_w"] = f(i["dn_norm_w"][0].reshape(P, 1))
    wx, wb, wc = np.split(xbc, [1024, 1280], axis=1)
    d["w_bc"] = f(np.stack([wb, wc], 1).reshape(KT, P, 2, SSM_GROUPS, P).transpose(3, 1, 0, 2, 4))
    d["w_xz"] = f(np.stack([wx, z_ssm], 1).reshape(KT, P, 2, PAIRS, P).transpose(3, 1, 0, 2, 4))
    channels = np.concatenate([i["state_ssm_conv"][0].transpose(2, 0, 1).reshape(-1, 3 * SEQS), i["ssm_conv_w"][0].T,
                               i["ssm_conv_b"][0][:, None]], 1)
    d["ssm_small_x"] = f(channels[:1024].reshape(PAIRS, P, -1))
    d["ssm_small_bc"] = f(channels[1024:].reshape(2, SSM_GROUPS, P, -1).transpose(1, 2, 0, 3))
    d["ssm_skip"] = f(np.repeat(i["ssm_D"][0], HALF).reshape(PAIRS, P).T)
    d["ssm_s0"] = f(i["state_ssm"][0].reshape(SEQS, PAIRS, P, P).transpose(1, 3, 0, 2))
    d["ssm_norm_w"] = f(i["ssm_norm_w"][0].reshape(PAIRS, P).T)
    by_out = lambda a, k: f(a.reshape(k, P, -1, P).transpose(2, 1, 0, 3))
    d["w_heads_dn"], d["w_heads_ssm"] = (by_out(w, KT) for w in np.split(i["w_out"][0], 2))
    d["w_xq"], d["w_xo"], d["w_pq"] = (by_out(i[n][0], KT) for n in ("w_xq", "w_xo", "w_pq"))
    d["w_mk"] = by_out(i["w_mkv"][0][:, :D_MODEL], KT)
    d["w_mv"] = f(tiles(i["w_mkv"][0][:, D_MODEL:], KT))
    d["memT"] = f(tiles(i["mem_prompt"][0].T, KT))
    d["cache_k"] = f(i["cache_mem_k"][0].reshape(SEQS, MEM, KT, P).transpose(0, 3, 2, 1))
    d["cache_v"] = f(i["cache_mem_v"][0].reshape(SEQS, 2, P, D_MODEL).transpose(0, 2, 1, 3))
    d["keysT"] = f(i["peer_sub_keys"][0].transpose(2, 0, 1))
    d["peer_u"] = f(i["peer_u"][0].reshape(NKEYS, NKEYS, KT, P).transpose(1, 3, 2, 0))
    d["peer_v"] = f(i["peer_v"][0].reshape(NKEYS, NKEYS, D_MODEL).transpose(1, 0, 2))
    return d


def shape_constants():
    j, i = np.arange(P)[:, None], np.arange(P)[None, :]
    seq = np.where(np.arange(P) < SAMPLE, np.arange(P) // STEPS, -1 - np.arange(P))
    same = seq[:, None] == seq[None, :]
    d = {"ident": np.eye(P), "ones": np.ones((P, P)), "tri": np.stack([j <= i, (j <= i) & same], 1),
         "total": np.stack([same | True, same], 1)}
    d["seq_of"] = seq[:, None] == np.arange(SEQS)[None, :]
    for name, m in (("incl", j <= i), ("strict", j < i)):
        d[name] = np.concatenate([np.tile(m, (1, NC - 1)), m & same], 1)
    d["iota"] = np.arange(P)
    s = 2 ** np.arange(7)[:, None, None]
    d["level"] = ((i // (2 * s) == j // (2 * s)) & (i // s % 2 == 1) & (j // s % 2 == 0)).transpose(1, 0, 2)
    return {k: np.ascontiguousarray(v, dtype=np.float32) for k, v in d.items()}


OUTS = {"dn_conv": (DN_HEADS, P, 3, SEQS + 1, 3), "dn_p": (DN_HEADS, P, P), "dn_s": (DN_HEADS, P, SEQS, P),
        "ssm_conv_x": (PAIRS, P, SEQS + 1, 3), "ssm_conv_bc": (SSM_GROUPS, P, 2, SEQS + 1, 3),
        "mem_k": (P, KT, MEM), "mem_v": (P, 2, D_MODEL), "y": (KT, P, T),
        "ssm_p": (PAIRS, P, P), "ssm_s": (PAIRS, P, SEQS, P)}


def kernel(**inputs):
    import concourse.bacc as bacc
    from concourse.bass_utils import run_bass_kernel_spmd

    arrays = layouts({k: np.asarray(v) for k, v in inputs.items()}) | shape_constants()
    nc = bacc.Bacc("TRN2", target_bir_lowering=False, num_devices=1)
    d = {k: nc.dram_tensor(f"in_{k}", a.shape, F32, kind="ExternalInput").ap() for k, a in arrays.items()}
    out = {k: nc.dram_tensor(f"out_{k}", s, F32, kind="ExternalOutput").ap() for k, s in OUTS.items()}
    trunk(nc, d, out)
    got = run_bass_kernel_spmd(nc, [{f"in_{k}": a for k, a in arrays.items()}], core_ids=[0]).results[0]
    g = {k: np.asarray(got[f"out_{k}"]) for k in OUTS}
    conv = lambda a: a.transpose(3, 4, 2, 0, 1).reshape(SEQS + 1, 3, -1)
    dn_conv = conv(g["dn_conv"])
    rows = np.concatenate([g["ssm_conv_x"].reshape(1024, SEQS + 1, 3),
                           g["ssm_conv_bc"].transpose(2, 0, 1, 3, 4).reshape(512, SEQS + 1, 3)])
    ssm_conv = rows.transpose(1, 2, 0)
    ssm_p = g["ssm_p"].transpose(0, 2, 1).reshape(1, 1, SSM_HEADS, HALF, P)
    ssm_s = g["ssm_s"].transpose(2, 0, 3, 1).reshape(1, SEQS, SSM_HEADS, HALF, P)
    y = g["y"].reshape(D_MODEL, T).T
    mem_k = g["mem_k"].transpose(2, 1, 0).reshape(1, 1, MEM, MEM_HEADS, -1)
    mem_v = g["mem_v"].transpose(1, 0, 2).reshape(1, 1, MEM, MEM_HEADS, -1)
    return (y[:SEQ].reshape(1, SEQ, D_MODEL), y[SEQ:].reshape(SEQS, STEPS, D_MODEL),
            dn_conv[None, 0:1], g["dn_p"][None, None], ssm_conv[None, 0:1], ssm_p, mem_k, mem_v,
            dn_conv[None, 1:], g["dn_s"].transpose(2, 0, 1, 3)[None], ssm_conv[None, 1:], ssm_s)
```

```python
from contextlib import ExitStack

import concourse.bass as bass
import numpy as np
from concourse import mybir
from concourse.alu_op_type import AluOpType as ALU

F32 = mybir.dt.float32
F32R = mybir.dt.float32r
U32 = mybir.dt.uint32
ACT = mybir.ActivationFunctionType
AX = mybir.AxisListType

D_MODEL, SEQ, SEQS, STEPS = 1024, 1024, 8, 8
SAMPLE = SEQS * STEPS
T = SEQ + SAMPLE
P = 128
CK = 128
NC = SEQ // CK + 1
TP = NC * CK
KT = D_MODEL // P
DN_HEADS, SSM_HEADS, SSM_GROUPS = 8, 16, 2
PAIRS = SSM_HEADS // 2
GP = PAIRS // SSM_GROUPS
HALF = 64
GATED = DN_HEADS + SSM_HEADS
MEM, MEM_HEADS = 256, 4
CONV = 4
CW = SEQ + CONV - 1 + SEQS * (STEPS + CONV - 1)
SOFF = SEQ + CONV - 1
SW = STEPS + CONV - 1
CHUNKS = [(0, 384), (384, 384), (768, 320)]
EPS = 1e-6
PHEADS, NKEYS, TOPK = 8, 128, 16


class Phase(ExitStack):

    def __init__(self, nc):
        super().__init__()
        self.nc, self.sems = nc, []

    def semaphore(self, name):
        self.sems.append(self.nc.alloc_semaphore(name))
        return self.sems[-1]

    def __exit__(self, *failure):
        if self.sems and failure[0] is None:
            self.nc.clear_and_free_semaphores(self.sems)
            self.nc.all_engine_barrier()
        return super().__exit__(*failure)


class Signal:

    def __init__(self, nc, ctx, name, per=1, unit=1, primed=False):
        self.sem = ctx.semaphore(name)
        self.per, self.unit, self.primed = per, unit, primed

    def at(self, n, turn=0):
        if isinstance(turn, int) and turn == 0 and not self.primed:
            return n * self.unit
        return turn * (self.per * self.unit) + (n + (self.per if self.primed else 0)) * self.unit


class Steps:

    def __init__(self, nc, ctx, name, per=0):
        self.sem = ctx.semaphore(name)
        self.per, self.n = per, 0

    def now(self, turn=0):
        return turn * self.per + self.n if self.per else self.n

    def step(self):
        self.n += 1
        return self.sem


def psum_banks(nc, ctx, name):
    return [ctx.enter_context(nc.psum_tensor(f"{name}_bank{i}", [P, 512], F32)) for i in range(8)]


def split_product(nc, out, w, x, start, stop):
    nc.tensor.matmul(out, w[0], x[0], start=start, stop=False)
    nc.tensor.matmul(out, w[0], x[1], start=False, stop=False)
    return nc.tensor.matmul(out, w[1], x[0], start=False, stop=stop)


def rmsnorm(nc, bank, name, src, dst, gain, ident, ones, tokens, width, store=None, kept=None, again=False, behind=None):
    tiles = -(-tokens // P)
    cols = CHUNKS if tokens == T else [(0, tokens)]
    split = isinstance(dst, tuple)
    with Phase(nc) as ctx:
        sq = ctx.enter_context(nc.sbuf_tensor(f"{name}_squares", [P, KT, P * tiles], F32))
        rstd = ctx.enter_context(nc.sbuf_tensor(f"{name}_rstd", [P, tiles], F32)) if kept is None else kept
        val = sq
        zeroed = Signal(nc, ctx, f"{name}_zeroed")
        squared = Signal(nc, ctx, f"{name}_squared", KT)
        added = Signal(nc, ctx, f"{name}_added", KT - 1)
        summed = Signal(nc, ctx, f"{name}_summed")
        mean_ready = Signal(nc, ctx, f"{name}_mean_ready")
        root_ready = Signal(nc, ctx, f"{name}_root_ready")
        rstd_ready = Signal(nc, ctx, f"{name}_rstd_ready")
        spread = Signal(nc, ctx, f"{name}_spread")
        val_ready, hi_ready = Signal(nc, ctx, f"{name}_value_ready", KT), Signal(nc, ctx, f"{name}_hi_ready", KT)
        stored = Signal(nc, ctx, f"{name}_stored", KT, 16)
        blank = ctx.enter_context(nc.sbuf_tensor(f"{name}_blank", [P, 1], F32))
        with nc.Block() as block:
            @block.scalar
            def _(act):
                if not again:
                    for k in range(KT):
                        nc.scalar.activation(sq[:, k, 0:tokens], src[:, k, 0:tokens], ACT.Square).then_inc(squared.sem, 1)
                    act.wait_ge(mean_ready.sem, 1)
                    nc.scalar.activation(rstd[:, :], rstd[:, :], ACT.Sqrt).then_inc(root_ready.sem, 1)
                if split:
                    for k in range(KT):
                        act.wait_ge(val_ready.sem, val_ready.at(k + 1))
                        nc.scalar.activation(dst[0][:, k, 0:tokens], val[:, k, 0:tokens], ACT.Copy).then_inc(hi_ready.sem, 1)

            @block.tensor
            def _(pe):
                if not again:
                    pe.wait_ge(added.sem, added.at(KT - 1))
                    pe.wait_ge(zeroed.sem, 1)
                    for t in range(tiles):
                        mm = nc.tensor.matmul(bank[0][:, t:t + 1], sq[:, 0, P * t:P * t + P], ones[:, 0:1], start=True, stop=True)
                    mm.then_inc(summed.sem, 1)
                    pe.wait_ge(rstd_ready.sem, 1)
                for t in range(tiles):
                    mm = nc.tensor.matmul(bank[1 + t // 3][:, P * (t % 3):P * (t % 3) + P],
                                          rstd[:, t:t + 1].to_broadcast([P, P]), ident, start=True, stop=True)
                mm.then_inc(spread.sem, 1)

            def low(unit, engine, r):
                for k in range(r, KT, 2):
                    engine.wait_ge(hi_ready.sem, hi_ready.at(k + 1))
                    unit.tensor_tensor(dst[1][:, k, 0:tokens], val[:, k, 0:tokens],
                                                            dst[0][:, k, 0:tokens].bitcast(F32), ALU.subtract)

            @block.gpsimd
            def _(pool):
                if tokens % P:
                    nc.gpsimd.memset(sq[:, 0, tokens:], 0.0)
                nc.gpsimd.memset(blank[:, :], 0.0).then_inc(zeroed.sem, 1)
                if split:
                    low(nc.gpsimd, pool, 1)

            @block.vector
            def _(v):
                if not again:
                    for k in range(1, KT):
                        v.wait_ge(squared.sem, squared.at(k + 1))
                        if k > 1:
                            v.wait_ge(added.sem, added.at(k - 1))
                        nc.vector.tensor_tensor(sq[:, 0, 0:tokens], sq[:, 0, 0:tokens], sq[:, k, 0:tokens], ALU.add).then_inc(added.sem, 1)
                    v.wait_ge(summed.sem, 1)
                    nc.vector.tensor_scalar(rstd[:, :], bank[0][:, 0:tiles], 1.0 / width, EPS, ALU.mult, ALU.add).then_inc(mean_ready.sem, 1)
                    v.wait_ge(root_ready.sem, 1)
                    nc.vector.reciprocal(rstd[:, :], rstd[:, :]).then_inc(rstd_ready.sem, 1)
                v.wait_ge(spread.sem, 1)
                for k in range(KT):
                    to = val[:, k, :] if split else dst[:, k, :]
                    for c, (a, n) in enumerate(cols):
                        op = nc.vector.scalar_tensor_tensor(to[:, a:a + n], src[:, k, a:a + n], gain[:, k:k + 1],
                                                            bank[1 + c][:, 0:n], ALU.mult, ALU.mult)
                    op.then_inc(val_ready.sem, 1)
                if split:
                    low(nc.vector, v, 0)

            if behind is not None:
                @block.sync
                def _(sp):
                    sp.wait_ge(*behind)

            if store is not None:
                @block.sync
                def _(sp):
                    for k in range(KT):
                        sp.wait_ge(val_ready.sem, val_ready.at(k + 1))
                        sp.dma_start(store[k], dst[:, k, :]).then_inc(stored.sem, 16)
                    sp.wait_ge(stored.sem, stored.at(KT))


def gates(nc, bank, xn, w_small, ident, tri, total, d, tab):
    G = GATED
    with Phase(nc) as ctx:
        def sb(name, shape):
            return ctx.enter_context(nc.sbuf_tensor(f"gates_{name}", shape, F32))
        raw, neg, e, u, z, sp = (sb(x, [P, NC, G]) for x in ("raw", "neg", "e", "u", "z", "sp"))
        bias, rate = sb("bias", [P, G]), sb("rate", [P, G])
        heads = sb("heads", [32, TP])
        loaded = Signal(nc, ctx, "gates_loaded", 2, 16)
        product, heads_ready = Signal(nc, ctx, "gates_product", 3), Signal(nc, ctx, "gates_heads_ready", 3)
        projected = Signal(nc, ctx, "gates_projected")
        cumulated = Signal(nc, ctx, "gates_cumulated")
        vec = Steps(nc, ctx, "gates_vector_steps")
        sca = Steps(nc, ctx, "gates_scalar_steps")
        vector_at, scalar_at = {"neg": 4, "u": 5, "decays": 14, "sums": 15, "left": 16}, {"sigmoid": 1, "exp": 3, "ln": 4, "decayed": 6}
        with nc.Block() as block:
            @block.sync
            def _(sp_):
                sp_.dma_start(bias[:, :], d["gate_bias"].partition_broadcast(P)).then_inc(loaded.sem, 16)
                sp_.dma_start(rate[:, :], d["gate_rate"].partition_broadcast(P)).then_inc(loaded.sem, 16)

            @block.tensor
            def _(pe):
                for t in range(3):
                    for k in range(KT):
                        mm = nc.tensor.matmul(bank[4 + t][0:32, 0:384], w_small[:, k, :], xn[:, k, 384 * t:384 * t + 384],
                                              start=(k == 0), stop=(k == KT - 1))
                    mm.then_inc(product.sem, 1)
                pe.wait_ge(heads_ready.sem, heads_ready.at(3))
                for c in range(NC):
                    mm = nc.tensor.transpose(bank[0][:, 32 * c:32 * c + 32], heads[:, CK * c:CK * c + CK], ident[0:32, 0:32])
                mm.then_inc(projected.sem, 1)
                pe.wait_ge(vec.sem, vector_at["decays"])
                for c in range(NC):
                    m = int(c == NC - 1)
                    nc.tensor.matmul(bank[1][:, G * c:G * c + G], tri[:, m, :], tab[:, 0, c, :], start=True, stop=True)
                    mm = nc.tensor.matmul(bank[2][:, G * c:G * c + G], total[:, m, :], tab[:, 0, c, :],
                                          start=True, stop=True)
                mm.then_inc(cumulated.sem, 1)

            @block.scalar
            def _(act):
                projection = bank[0][:, 0:32 * NC].rearrange("p (c h) -> p c h", h=32)
                for t in range(3):
                    act.wait_ge(product.sem, product.at(t + 1))
                    nc.scalar.activation(heads[:, 384 * t:384 * t + 384], bank[4 + t][0:32, 0:384], ACT.Copy).then_inc(heads_ready.sem, 1)
                act.wait_ge(projected.sem, 1)
                nc.scalar.activation(tab[:, 4, :, 0:DN_HEADS], projection[:, :, 0:DN_HEADS],
                                     ACT.Sigmoid).then_inc(sca.step(), 1)
                act.wait_ge(loaded.sem, loaded.at(2))
                nc.scalar.activation(rate[:, :], rate[:, :], ACT.Exp).then_inc(sca.step(), 1)
                act.wait_ge(vec.sem, vector_at["neg"])
                nc.scalar.activation(e[:, :, :], neg[:, :, :], ACT.Exp).then_inc(sca.step(), 1)
                assert sca.n == scalar_at["exp"]
                act.wait_ge(vec.sem, vector_at["u"])
                nc.scalar.activation(z[:, :, :], u[:, :, :], ACT.Ln).then_inc(sca.step(), 1)
                act.wait_ge(vec.sem, vector_at["sums"])
                nc.scalar.activation(tab[:, 2, :, :], tab[:, 1, :, :], ACT.Exp).then_inc(sca.step(), 1)
                act.wait_ge(vec.sem, vector_at["left"])
                nc.scalar.activation(tab[:, 3, :, :], tab[:, 3, :, :], ACT.Exp).then_inc(sca.step(), 1)
                assert sca.n == scalar_at["decayed"]

            @block.vector
            def _(v):
                projection = bank[0][:, 0:32 * NC].rearrange("p (c h) -> p c h", h=32)
                wide = lambda x: x[:, None, :].to_broadcast([P, NC, G])
                v.wait_ge(sca.sem, scalar_at["sigmoid"])
                v.wait_ge(loaded.sem, loaded.at(2))

                def then(op):
                    op.then_inc(vec.step(), 1)
                    v.wait_ge(vec.sem, vec.now())
                then(nc.vector.tensor_tensor(raw[:, :, :], projection[:, :, DN_HEADS:32], wide(bias), ALU.add))
                then(nc.vector.tensor_scalar(sp[:, :, :], raw[:, :, :], 0.0, None, ALU.max))
                then(nc.vector.tensor_scalar(neg[:, :, :], raw[:, :, :], -1.0, None, ALU.mult))
                then(nc.vector.tensor_tensor(neg[:, :, :], neg[:, :, :], raw[:, :, :], ALU.min))
                assert vec.n == vector_at["neg"]
                v.wait_ge(sca.sem, scalar_at["exp"])
                then(nc.vector.tensor_scalar(u[:, :, :], e[:, :, :], 1.0, None, ALU.add))
                then(nc.vector.tensor_scalar(raw[:, :, :], u[:, :, :], 1.0, None, ALU.is_equal))
                then(nc.vector.scalar_tensor_tensor(neg[:, :, :], u[:, :, :], -1.0, raw[:, :, :], ALU.add, ALU.add))
                then(nc.vector.reciprocal(neg[:, :, :], neg[:, :, :]))
                then(nc.vector.tensor_tensor(neg[:, :, :], neg[:, :, :], e[:, :, :], ALU.mult))
                then(nc.vector.tensor_tensor(raw[:, :, :], raw[:, :, :], e[:, :, :], ALU.mult))
                v.wait_ge(sca.sem, scalar_at["ln"])
                then(nc.vector.tensor_tensor(neg[:, :, :], neg[:, :, :], z[:, :, :], ALU.mult))
                then(nc.vector.tensor_tensor(neg[:, :, :], neg[:, :, :], raw[:, :, :], ALU.add))
                then(nc.vector.tensor_tensor(sp[:, :, :], sp[:, :, :], neg[:, :, :], ALU.add))
                then(nc.vector.scalar_tensor_tensor(tab[:, 0, :, :], sp[:, :, :], -1.0, wide(rate), ALU.mult, ALU.mult))
                assert vec.n == vector_at["decays"]
                v.wait_ge(cumulated.sem, 1)
                then(nc.vector.tensor_copy(tab[:, 1, :, :], bank[1][:, 0:NC * G].rearrange("p (c h) -> p c h", h=G)))
                then(nc.vector.tensor_tensor(tab[:, 3, :, :], bank[2][:, 0:NC * G].rearrange("p (c h) -> p c h", h=G),
                                             tab[:, 1, :, :], ALU.subtract))
                assert vec.n == vector_at["left"]
                then(nc.vector.tensor_copy(tab[:, 4, :, DN_HEADS:G], sp[:, :, DN_HEADS:G]))


def delta_net(nc, bank, xn, tab, d, const, mix, out):
    LEVELS = [1, 2, 4, 8, 16, 32, 64]
    A, B, SMALL, STATES = bank[0:3], bank[4:7], bank[3], (bank[7], bank[4])
    KS, VN, DS = (SMALL[:, P * n:P * n + P] for n in range(3))
    with Phase(nc) as ctx:
        def sb(name, shape):
            return ctx.enter_context(nc.sbuf_tensor(f"dn_{name}", shape, F32))

        def signal(name, per=1, unit=1, primed=False):
            return Signal(nc, ctx, f"dn_{name}", per, unit, primed)
        w = sb("weights", [P, KT, 4, P])
        hist, cw, nw = sb("history", [P, 3, SEQS, 3]), sb("conv_w", [P, 3, CONV]), sb("norm_w", [P, 1])
        cbuf, acc, qkv = sb("padded", [P, 3, CW]), sb("conv", [P, 3, CW]), sb("qkv", [P, 3, TP])
        zs, cur, negbeg = sb("gate", [P, T]), sb("columns", [P, 5, NC]), sb("neg_beta_decay", [P, NC])
        tail = sb("conv_state", [P, 3, SEQS + 1, 3])
        rqk, ro = sb("rstd_qk", [P, 2, NC]), sb("rstd_o", [P, NC])
        erow = sb("row_decay", [P, TP])
        D, Ds, LT, attn, qdec = (sb(x, [P, TP]) for x in ("decay", "beta_decay", "lower", "attn", "q_decayed"))
        X, Y, BX, Vb, Kd = (sb(x, [P, TP]) for x in ("inv", "inv_t", "bx", "v_beta", "k_decayed"))
        BT = sb("block", [P, 2, TP])
        R, vn, S = sb("residual", [P, P]), sb("v_new", [P, 2, P]), sb("state", [P, 2, P])
        km, S0, vm, S1 = sb("k_masked", [P, SEQS * (P + STEPS)]), sb("sample_in", [P, SEQS, P]), sb("v_masked", [P, SEQS, P]), sb("sample_out", [P, SEQS, P])
        o = sb("o", [P, T])
        ident, ones = const["ident"], const["ones"]
        const = const | {"level": sb("level_masks", [P, 7, P]), "strict": sb("strict_mask", [P, TP])}

        w_loaded = signal("weights_loaded", 3, 16)
        s0_loaded = signal("sample_in_loaded", 1, 16)
        started = signal("inputs_once", 1, 16)
        cur_ready = signal("columns_ready")
        projected = signal("projected", 12)
        evacuated = signal("evacuated", 12)
        hist_in = signal("history_in")
        conv_done = signal("conv_done", 3)
        silu_done = signal("silu_done", 3)
        tail_ready = signal("tail_ready", 2)
        tail_stored = signal("conv_state_stored", 1, 16, primed=True)
        state_stored = signal("state_stored", 1, 16, primed=True)
        sample_stored = signal("sample_state_stored", 1, 16, primed=True)
        o_stored = signal("o_stored", 1, 16, primed=True)
        squared = signal("squared", 2)
        ssq_ready, mean_ready = signal("ssq_ready"), signal("mean_ready")
        root_ready, rqk_ready = signal("root_ready"), signal("rstd_qk_ready")
        qk_spread = signal("rstd_qk_spread", 2)
        qk_ready = signal("qk_ready", 2)
        rows_ready = signal("rows_ready", 2)
        diff_ready = signal("diff_ready")
        erow_ready = signal("row_decay_ready")
        dexp_ready = signal("decay_exp_ready")
        rowb_used = signal("beta_rows_used")
        prod_ready = signal("products_ready", 2)
        lt_ready, attn_ready = signal("lower_ready"), signal("attn_ready")
        qdec_ready = signal("q_decayed_ready")
        turned = signal("tokens_turned", 2)
        v_turned_used = signal("v_turned_used")
        k_turned_used = signal("k_turned_used")
        y1_ready = signal("first_level_ready")
        x_turned = signal("x_turned", 3)
        x1_ready = signal("x_first_ready", 3)
        bt_ready = signal("block_ready", 7)
        bx_mm = signal("bx_product", 18)
        bx_ready = signal("bx_ready", 18)
        yx_mm = signal("yx_product", 18)
        y_ready = signal("inverse_ready", 18)
        ks_ready, r_ready = signal("ks_ready", 9), signal("residual_ready", 9)
        vn_mm, vn_ready = signal("v_new_product", 9), signal("v_new_ready", 9)
        ds_ready, s_ready = signal("state_product", 9), signal("state_ready", 10)
        o_ready, o_out = signal("o_product", 3), signal("o_out", 3)
        km_ready, vm_ready = signal("k_masked_ready"), signal("v_masked_ready")
        osq, o_ssq, o_mean = signal("o_squared"), signal("o_summed"), signal("o_mean")
        o_root, ro_ready, o_spread = signal("o_root"), signal("rstd_o_ready"), signal("rstd_o_spread")
        o_normed, o_done = signal("o_normed", 1, 1, True), signal("o_done", 1, 1, True)
        zeroed = signal("zeroed")
        LAST = DN_HEADS - 1
        PROJECTED = (A, A, B, A)
        VSTEPS = 13
        vec = Steps(nc, ctx, "dn_vector_steps", VSTEPS)

        def c3(t, n):
            return t[:, 384 * n:384 * n + 384]

        with nc.Block() as block:
            @block.sync
            def _(sp):
                sp.dma_start(nw[:, :], d["dn_norm_w"]).then_inc(started.sem, 16)
                sp.dma_start(const["level"][:, :, :], d["level"]).then_inc(started.sem, 16)
                sp.dma_start(const["strict"][:, :], d["strict"]).then_inc(started.sem, 16)

                def load_weights(h):
                    sp.dma_start(w[:, :, :, :], d["w_dn"][bass.ds(h, 1)].rearrange("a p k j n -> (a p) k j n")).then_inc(w_loaded.sem, 16)
                    sp.dma_start(hist[:, :, :, :], d["dn_hist"][bass.ds(h, 1)].rearrange("a p j b n -> (a p) j b n")).then_inc(w_loaded.sem, 16)
                    sp.dma_start(cw[:, :, :], d["dn_conv_w"][bass.ds(h, 1)].rearrange("a p j n -> (a p) j n")).then_inc(w_loaded.sem, 16)

                def load_sample(h):
                    sp.dma_start(S0[:, :, :], d["dn_s0"][bass.ds(h, 1)].rearrange("a p b n -> (a p) b n")).then_inc(s0_loaded.sem, 16)

                def head(h, last):
                    sp.wait_ge(tail_ready.sem, tail_ready.at(2, h))
                    sp.dma_start(out["dn_conv"][bass.ds(h, 1)].rearrange("a p j b n -> (a p) j b n"), tail[:, :, :, :]).then_inc(tail_stored.sem, 16)
                    if not last:
                        sp.wait_ge(projected.sem, projected.at(12, h))
                        sp.wait_ge(conv_done.sem, conv_done.at(3, h))
                        load_weights(h + 1)
                    sp.wait_ge(s_ready.sem, s_ready.at(9, h))
                    sp.dma_start(out["dn_p"][bass.ds(h, 1)].rearrange("a p n -> (a p) n"), S[:, 0, :]).then_inc(state_stored.sem, 16)
                    sp.wait_ge(s_ready.sem, s_ready.at(10, h))
                    sp.dma_start(out["dn_s"][bass.ds(h, 1)].rearrange("a p b n -> (a p) b n"), S1[:, :, :]).then_inc(sample_stored.sem, 16)
                    if not last:
                        sp.wait_ge(o_ready.sem, o_ready.at(3, h))
                        load_sample(h + 1)
                    sp.wait_ge(o_done.sem, o_done.at(1, h))
                    sp.dma_start(mix[bass.ds(h, 1)].rearrange("a p n -> (a p) n"), o[:, :]).then_inc(o_stored.sem, 16)
                load_weights(0)
                load_sample(0)
                with sp.Fori(0, LAST) as h:
                    head(h, False)
                head(LAST, True)
                for sig in (tail_stored, state_stored, sample_stored, o_stored):
                    sp.wait_ge(sig.sem, sig.at(1, LAST))

            @block.tensor
            def _(pe):
                def project_step(j, c, k):
                    a, n = CHUNKS[c]
                    mm = nc.tensor.matmul(PROJECTED[j][c][:, 0:n], w[:, k, j, :], xn[:, k, a:a + n], start=(k == 0), stop=(k == KT - 1))
                    if k == KT - 1:
                        mm.then_inc(projected.sem, 1)

                def project(j, c):
                    for k in range(KT):
                        project_step(j, c, k)

                def columns_sums(to, squares):
                    for c in range(NC):
                        n = CK if c < NC - 1 else SAMPLE
                        mm = nc.tensor.matmul(to[0:n, c:c + 1], squares[:, CK * c:CK * c + n], ones[:, 0:1], start=True, stop=True)
                    return mm

                def spread(banks, column):
                    for c in range(NC):
                        n = CK if c < NC - 1 else SAMPLE
                        mm = nc.tensor.matmul(banks[c // 3][:, CK * (c % 3):CK * (c % 3) + n], column[:, c:c + 1].to_broadcast([P, P]),
                                              ident[:, 0:n], start=True, stop=True)
                    return mm

                def head(h, last):
                    def rows(q, banks, mask):
                        for c in range(NC):
                            rhs = ident[:, :] if mask is None else mask[:, int(c == NC - 1), :]
                            mm = nc.tensor.matmul(banks[c // 3][:, CK * (c % 3):CK * (c % 3) + CK],
                                                  cur[:, q, c:c + 1].to_broadcast([P, P]), rhs, start=True, stop=True)
                        mm.then_inc(rows_ready.sem, 1)
                    pe.wait_ge(o_normed.sem, o_normed.at(1, h - 1))
                    project(2, 0)
                    pe.wait_ge(cur_ready.sem, cur_ready.at(1, h))
                    pe.wait_ge(evacuated.sem, evacuated.at(6, h))
                    rows(0, A, const["tri"])
                    project(2, 1)
                    project(2, 2)
                    pe.wait_ge(diff_ready.sem, diff_ready.at(1, h))
                    pe.wait_ge(erow_ready.sem, erow_ready.at(1, h))
                    project(3, 0)
                    pe.wait_ge(evacuated.sem, evacuated.at(9, h))
                    rows(4, B, None)
                    pe.wait_ge(squared.sem, squared.at(2, h))
                    for j in range(2):
                        mm = columns_sums(SMALL[:, NC * j:NC * j + NC], acc[:, j, :])
                    mm.then_inc(ssq_ready.sem, 1)
                    project(3, 1)
                    project(3, 2)
                    pe.wait_ge(rqk_ready.sem, rqk_ready.at(1, h))
                    pe.wait_ge(rowb_used.sem, rowb_used.at(1, h))
                    spread(B, rqk[:, 0, :]).then_inc(qk_spread.sem, 1)
                    pe.wait_ge(evacuated.sem, evacuated.at(12, h))
                    spread(A, rqk[:, 1, :]).then_inc(qk_spread.sem, 1)
                    pe.wait_ge(qk_ready.sem, qk_ready.at(2, h))
                    for j, banks in ((1, A), (0, B)):
                        for c in range(NC):
                            s = slice(CK * c, CK * c + CK)
                            mm = nc.tensor.matmul(banks[c // 3][:, CK * (c % 3):CK * (c % 3) + CK], qkv[:, 1, s],
                                                  qkv[:, j, s], start=True, stop=True)
                        mm.then_inc(prod_ready.sem, 1)
                    for j, banks, free in ((2, A, lt_ready), (1, B, attn_ready)):
                        pe.wait_ge(silu_done.sem, silu_done.at(3, h))
                        pe.wait_ge(free.sem, free.at(1, h))
                        for c in range(NC):
                            mm = nc.tensor.transpose(banks[c // 3][:, CK * (c % 3):CK * (c % 3) + CK],
                                                     qkv[:, j, CK * c:CK * c + CK], ident[:, :])
                        mm.then_inc(turned.sem, 1)
                    pe.wait_ge(v_turned_used.sem, v_turned_used.at(1, h))
                    pe.wait_ge(y1_ready.sem, y1_ready.at(1, h))
                    for t in range(3):
                        for c in range(3 * t, 3 * t + 3):
                            mm = nc.tensor.transpose(A[t][:, CK * (c % 3):CK * (c % 3) + CK],
                                                     Y[:, CK * c:CK * c + CK], ident[:, :])
                        mm.then_inc(x_turned.sem, 1)
                    for l in range(1, len(LEVELS)):
                        def block_times_x(t):
                            n = 3 * (l - 1) + t
                            if l == 1:
                                pe.wait_ge(x1_ready.sem, x1_ready.at(t + 1, h))
                            else:
                                pe.wait_ge(y_ready.sem, y_ready.at(n - 2, h))
                            pe.wait_ge(bt_ready.sem, bt_ready.at(l + 1, h))
                            for c in range(3 * t, 3 * t + 3):
                                s = slice(CK * c, CK * c + CK)
                                mm = nc.tensor.matmul(A[t][:, CK * (c % 3):CK * (c % 3) + CK], BT[:, l % 2, s], X[:, s],
                                                      start=True, stop=True)
                            mm.then_inc(bx_mm.sem, 1)

                        def corrections(t):
                            n = 3 * (l - 1) + t
                            pe.wait_ge(bx_ready.sem, bx_ready.at(n + 1, h))
                            if n == 0:
                                pe.wait_ge(k_turned_used.sem, k_turned_used.at(1, h))
                            for c in range(3 * t, 3 * t + 3):
                                s = slice(CK * c, CK * c + CK)
                                mm = nc.tensor.matmul(B[t][:, CK * (c % 3):CK * (c % 3) + CK], BX[:, s], Y[:, s],
                                                      start=True, stop=True)
                                if l < len(LEVELS) - 1:
                                    mm = nc.tensor.matmul(A[t][:, CK * (c % 3):CK * (c % 3) + CK], Y[:, s], BX[:, s],
                                                          start=True, stop=True)
                            mm.then_inc(yx_mm.sem, 1)
                        for t in range(3):
                            block_times_x(t)
                        for t in range(3):
                            corrections(t)
                    steps = iter([(c, k) for c in range(3) for k in range(KT)])

                    def q_step():
                        if not last:
                            project_step(0, *next(steps))
                    pe.wait_ge(y_ready.sem, y_ready.at(18, h))
                    pe.wait_ge(qdec_ready.sem, qdec_ready.at(1, h))
                    if not last:
                        pe.wait_ge(w_loaded.sem, w_loaded.at(3, h + 1))
                    for c in range(NC):
                        s = slice(CK * c, CK * c + CK)
                        old = S[:, c % 2, :]
                        pe.wait_ge(s_ready.sem, s_ready.at(c + 1, h))
                        if c < NC - 1:
                            nc.tensor.matmul(KS, qkv[:, 1, s], old, start=True, stop=True).then_inc(ks_ready.sem, 1)
                            q_step()
                        else:
                            pe.wait_ge(km_ready.sem, km_ready.at(1, h))
                            pe.wait_ge(s0_loaded.sem, s0_loaded.at(1, h))
                            for b in range(SEQS):
                                mm = nc.tensor.matmul(KS, km[:, P * b:P * b + P], S0[:, b, :], start=(b == 0), stop=(b == SEQS - 1))
                            mm.then_inc(ks_ready.sem, 1)
                        pe.wait_ge(r_ready.sem, r_ready.at(c + 1, h))
                        nc.tensor.matmul(VN, Y[:, s], R[:, :], start=True, stop=True).then_inc(vn_mm.sem, 1)
                        if c < NC - 1:
                            q_step()
                        pe.wait_ge(vn_ready.sem, vn_ready.at(c + 1, h))
                        if c < NC - 1:
                            nc.tensor.matmul(DS, Kd[:, s], vn[:, c % 2, :], start=True, stop=True).then_inc(ds_ready.sem, 1)
                            to = B[c // 3][:, CK * (c % 3):CK * (c % 3) + CK]
                            nc.tensor.matmul(to, old, qdec[:, s], start=True, stop=False)
                            mm = nc.tensor.matmul(to, vn[:, c % 2, :], attn[:, s], start=False, stop=True)
                            if c % 3 == 2:
                                mm.then_inc(o_ready.sem, 1)
                            q_step()
                        else:
                            pe.wait_ge(vm_ready.sem, vm_ready.at(1, h))
                            pe.wait_ge(o_out.sem, o_out.at(1, h))
                            for half in range(2):
                                mm = nc.tensor.matmul(STATES[half][:, 0:512], Kd[:, s],
                                                      vm[:, 4 * half:4 * half + 4, :].rearrange("p b n -> p (b n)"),
                                                      start=True, stop=True)
                            mm.then_inc(ds_ready.sem, 1)
                            a = CK * (c % 3)
                            nc.tensor.matmul(B[2][:, a:a + SAMPLE], vn[:, c % 2, :], attn[:, SEQ:T], start=True, stop=False)
                            for b in range(SEQS):
                                mm = nc.tensor.matmul(B[2][:, a + STEPS * b:a + STEPS * b + STEPS], S0[:, b, :],
                                                      qdec[:, SEQ + STEPS * b:SEQ + STEPS * b + STEPS],
                                                      start=False, stop=(b == SEQS - 1))
                            mm.then_inc(o_ready.sem, 1)
                    if not last:
                        pe.wait_ge(evacuated.sem, evacuated.at(3, h + 1))
                        project(1, 0)
                    pe.wait_ge(osq.sem, osq.at(1, h))
                    columns_sums(SMALL, acc[:, 0, :]).then_inc(o_ssq.sem, 1)
                    if not last:
                        project(1, 1)
                    pe.wait_ge(ro_ready.sem, ro_ready.at(1, h))
                    pe.wait_ge(s_ready.sem, s_ready.at(10, h))
                    spread(B, ro).then_inc(o_spread.sem, 1)
                    if not last:
                        project(1, 2)
                pe.wait_ge(w_loaded.sem, w_loaded.at(3))
                for c in range(3):
                    project(0, c)
                for c in range(3):
                    pe.wait_ge(evacuated.sem, evacuated.at(c + 1))
                    project(1, c)
                with pe.Fori(0, LAST) as h:
                    head(h, False)
                head(LAST, True)

            @block.scalar
            def _(act):
                for sig in (o_normed, o_done):
                    act.sem_inc(sig.sem, 1)
                for sig in (tail_stored, state_stored, sample_stored, o_stored):
                    act.sem_inc(sig.sem, 16)

                def evacuate(j, c, h):
                    a, n = CHUNKS[c]
                    act.wait_ge(projected.sem, projected.at(3 * j + c + 1, h))
                    psum = PROJECTED[j][c]
                    if j == 3:
                        nc.scalar.activation(zs[:, a:a + n], psum[:, 0:n], ACT.Silu).then_inc(evacuated.sem, 1)
                    elif c < 2:
                        nc.scalar.activation(cbuf[:, j, a + 3:a + 3 + n], psum[:, 0:n], ACT.Copy).then_inc(evacuated.sem, 1)
                    else:
                        nc.scalar.activation(cbuf[:, j, a + 3:SOFF], psum[:, 0:SEQ - a], ACT.Copy)
                        nc.scalar.activation(
                            cbuf[:, j, SOFF:CW].rearrange("p (b n) -> p b n", n=SW)[:, :, 3:SW],
                            psum[:, SEQ - a:n].rearrange("p (b n) -> p b n", n=STEPS), ACT.Copy).then_inc(evacuated.sem, 1)

                def silu(j, h):
                    act.wait_ge(conv_done.sem, conv_done.at(j + 1, h))
                    nc.scalar.activation(qkv[:, j, 0:SEQ], acc[:, j, 0:SEQ], ACT.Silu)
                    nc.scalar.activation(
                        qkv[:, j, SEQ:T].rearrange("p (b n) -> p b n", n=STEPS),
                        acc[:, j, SOFF:CW].rearrange("p (b n) -> p b n", n=SW)[:, :, 0:STEPS], ACT.Silu).then_inc(silu_done.sem, 1)

                def square(j, h):
                    act.wait_ge(silu_done.sem, silu_done.at(j + 1, h))
                    nc.scalar.activation(acc[:, j, 0:T], qkv[:, j, 0:T], ACT.Square).then_inc(squared.sem, 1)

                def by_token(to, banks, q):
                    for c in range(NC):
                        op = nc.scalar.activation(to[:, CK * c:CK * c + CK], banks[c // 3][:, CK * (c % 3):CK * (c % 3) + CK],
                                                  ACT.Copy, scale=cur[:, q, c:c + 1])
                    return op

                def head(h, last):
                    silu(0, h)
                    square(0, h)
                    act.wait_ge(rows_ready.sem, rows_ready.at(1, h))
                    for t in range(3):
                        op = nc.scalar.activation(c3(erow, t), A[t][:, 0:384], ACT.Exp)
                    op.then_inc(erow_ready.sem, 1)
                    silu(1, h)
                    square(1, h)
                    evacuate(2, 0, h)
                    act.wait_ge(diff_ready.sem, diff_ready.at(1, h))
                    nc.scalar.activation(D[:, :], D[:, :], ACT.Exp).then_inc(dexp_ready.sem, 1)
                    evacuate(2, 1, h)
                    evacuate(2, 2, h)
                    silu(2, h)
                    act.wait_ge(o_done.sem, o_done.at(1, h - 1))
                    evacuate(3, 0, h)
                    act.wait_ge(mean_ready.sem, mean_ready.at(1, h))
                    nc.scalar.activation(rqk[:, :, :], rqk[:, :, :], ACT.Sqrt).then_inc(root_ready.sem, 1)
                    evacuate(3, 1, h)
                    evacuate(3, 2, h)
                    act.wait_ge(turned.sem, turned.at(1, h))
                    by_token(Vb, A, 4).then_inc(v_turned_used.sem, 1)
                    act.wait_ge(turned.sem, turned.at(2, h))
                    by_token(Kd, B, 3).then_inc(k_turned_used.sem, 1)
                    for l in range(1, len(LEVELS)):
                        for t in range(3):
                            act.wait_ge(bx_mm.sem, bx_mm.at(3 * (l - 1) + t + 1, h))
                            nc.scalar.activation(c3(BX, t), A[t][:, 0:384], ACT.Copy).then_inc(bx_ready.sem, 1)
                    if not last:
                        act.wait_ge(tail_ready.sem, tail_ready.at(2, h))
                    for c in range(NC):
                        act.wait_ge(vn_mm.sem, vn_mm.at(c + 1, h))
                        nc.scalar.activation(vn[:, c % 2, :], VN, ACT.Copy).then_inc(vn_ready.sem, 1)
                        if c % 3 == 2:
                            t = c // 3
                            act.wait_ge(o_ready.sem, o_ready.at(t + 1, h))
                            if t == 0:
                                act.wait_ge(o_stored.sem, o_stored.at(1, h - 1))
                            n = CHUNKS[t][1]
                            nc.scalar.activation(o[:, 384 * t:384 * t + n], B[t][:, 0:n], ACT.Copy).then_inc(o_out.sem, 1)
                        if c in (3, 6) and not last:
                            evacuate(0, c // 3 - 1, h + 1)
                        if c == NC - 2 and not last:
                            evacuate(0, 2, h + 1)
                    act.wait_ge(o_out.sem, o_out.at(3, h))
                    nc.scalar.activation(acc[:, 0, 0:T], o[:, :], ACT.Square).then_inc(osq.sem, 1)
                    if not last:
                        evacuate(1, 0, h + 1)
                    act.wait_ge(o_mean.sem, o_mean.at(1, h))
                    nc.scalar.activation(ro[:, :], ro[:, :], ACT.Sqrt).then_inc(o_root.sem, 1)
                    if not last:
                        evacuate(1, 1, h + 1)
                        evacuate(1, 2, h + 1)
                for c in range(3):
                    evacuate(0, c, 0)
                for c in range(3):
                    evacuate(1, c, 0)
                with act.Fori(0, LAST) as h:
                    head(h, False)
                head(LAST, True)

            @block.gpsimd
            def _(pool):
                nc.gpsimd.memset(qkv[:, :, T:TP], 0.0)
                nc.gpsimd.memset(km[:, :], 0.0)
                nc.gpsimd.memset(rqk[:, :, :], 1.0)
                nc.gpsimd.memset(ro[:, :], 1.0)
                nc.gpsimd.memset(cbuf[:, :, 0:3], 0.0).then_inc(zeroed.sem, 1)
                pool.wait_ge(started.sem, started.at(3))
                with pool.Fori(0, DN_HEADS) as h:
                    pool.wait_ge(lt_ready.sem, lt_ready.at(1, h))
                    for l in range(len(LEVELS)):
                        if l >= 2:
                            if l == 2:
                                pool.wait_ge(y1_ready.sem, y1_ready.at(1, h))
                            else:
                                pool.wait_ge(bx_mm.sem, bx_mm.at(3 * (l - 2), h))
                        nc.gpsimd.tensor_tensor(BT[:, l % 2, :].rearrange("p (c n) -> p c n", n=CK),
                                                LT[:, :].rearrange("p (c n) -> p c n", n=CK),
                                                const["level"][:, l:l + 1, :].to_broadcast([P, NC, CK]),
                                                ALU.mult).then_inc(bt_ready.sem, 1)

            @block.vector
            def _(v):
                v.wait_ge(started.sem, started.at(3))
                with v.Fori(0, DN_HEADS) as h:
                    vec.n = 0

                    def then(op):
                        op.then_inc(vec.step(), 1)
                        v.wait_ge(vec.sem, vec.now(h))
                    nc.vector.tensor_copy(cur[:, :, :], tab[:, :, :, bass.ds(h, 1)].rearrange("p q c o -> p q (c o)")).then_inc(cur_ready.sem, 1)
                    v.wait_ge(w_loaded.sem, w_loaded.at(3, h))
                    v.wait_ge(zeroed.sem, 1)
                    nc.vector.tensor_copy(cbuf[:, :, SOFF:CW].rearrange("p j (b n) -> p j b n", n=SW)[:, :, :, 0:3],
                                          hist[:, :, :, :]).then_inc(hist_in.sem, 1)
                    v.wait_ge(hist_in.sem, hist_in.at(1, h))
                    v.wait_ge(cur_ready.sem, cur_ready.at(1, h))
                    then(nc.vector.scalar_tensor_tensor(negbeg[:, :], cur[:, 4, :], -1.0, cur[:, 2, :], ALU.mult, ALU.mult))
                    W = CW - 3

                    def conv(j):
                        v.wait_ge(evacuated.sem, evacuated.at(3 * j + 3, h))
                        then(nc.vector.tensor_scalar(acc[:, j, 0:W], cbuf[:, j, 0:W], cw[:, j, 0:1], None, ALU.mult))
                        for k in range(1, CONV):
                            op = nc.vector.scalar_tensor_tensor(acc[:, j, 0:W], cbuf[:, j, k:k + W], cw[:, j, k:k + 1],
                                                                acc[:, j, 0:W], ALU.mult, ALU.add)
                            if k < CONV - 1:
                                then(op)
                            else:
                                op.then_inc(conv_done.sem, 1)
                    conv(0)
                    conv(1)
                    v.wait_ge(erow_ready.sem, erow_ready.at(1, h))
                    for c in range(NC):
                        op = nc.vector.tensor_scalar(D[:, CK * c:CK * c + CK], A[c // 3][:, CK * (c % 3):CK * (c % 3) + CK],
                                                     cur[:, 1, c:c + 1], 0.0, ALU.subtract, ALU.min)
                    op.then_inc(diff_ready.sem, 1)
                    v.wait_ge(dexp_ready.sem, dexp_ready.at(1, h))
                    then(nc.vector.tensor_tensor(D[:, :], D[:, :], const["incl"][:, :], ALU.mult))
                    then(nc.vector.tensor_tensor(Ds[:, :], D[:, :], const["strict"][:, :], ALU.mult))
                    conv(2)
                    v.wait_ge(tail_stored.sem, tail_stored.at(1, h - 1))
                    nc.vector.tensor_copy(tail[:, :, 0, :], cbuf[:, :, SEQ:SOFF]).then_inc(tail_ready.sem, 1)
                    nc.vector.tensor_copy(tail[:, :, 1:SEQS + 1, :],
                                          cbuf[:, :, SOFF:CW].rearrange("p j (b n) -> p j b n", n=SW)[:, :, :, STEPS:SW]).then_inc(tail_ready.sem, 1)
                    v.wait_ge(rows_ready.sem, rows_ready.at(2, h))
                    for t in range(3):
                        op = nc.vector.tensor_tensor(c3(Ds, t), c3(Ds, t), B[t][:, 0:384], ALU.mult)
                    op.then_inc(rowb_used.sem, 1)
                    v.wait_ge(ssq_ready.sem, ssq_ready.at(1, h))
                    for j in range(2):
                        nc.vector.tensor_scalar(rqk[:, j, 0:NC - 1], SMALL[:, NC * j:NC * j + NC - 1], EPS, None, ALU.add)
                        op = nc.vector.tensor_scalar(rqk[0:SAMPLE, j, NC - 1:NC], SMALL[0:SAMPLE, NC * j + NC - 1:NC * j + NC],
                                                     EPS, None, ALU.add)
                    op.then_inc(mean_ready.sem, 1)
                    v.wait_ge(root_ready.sem, root_ready.at(1, h))
                    nc.vector.reciprocal(rqk[:, :, :], rqk[:, :, :]).then_inc(rqk_ready.sem, 1)
                    for j, banks in ((0, B), (1, A)):
                        v.wait_ge(qk_spread.sem, qk_spread.at(j + 1, h))
                        for c, (a, n) in enumerate(CHUNKS):
                            op = nc.vector.scalar_tensor_tensor(qkv[:, j, a:a + n], qkv[:, j, a:a + n], (float(P) ** -0.5, 1.0)[j],
                                                                banks[c][:, 0:n], ALU.mult, ALU.mult)
                        op.then_inc(qk_ready.sem, 1)
                    v.wait_ge(qk_ready.sem, qk_ready.at(2, h))
                    nc.vector.tensor_copy(km[:, :].rearrange("p (b n) -> p b n", n=P + STEPS)[:, :, 0:STEPS],
                                          qkv[:, 1, SEQ:T].rearrange("p (b n) -> p b n", n=STEPS)).then_inc(km_ready.sem, 1)
                    v.wait_ge(erow_ready.sem, erow_ready.at(1, h))
                    nc.vector.tensor_tensor(qdec[:, :], qkv[:, 0, :], erow[:, :], ALU.mult).then_inc(qdec_ready.sem, 1)
                    v.wait_ge(prod_ready.sem, prod_ready.at(1, h))
                    v.wait_ge(rowb_used.sem, rowb_used.at(1, h))
                    for t in range(3):
                        op = nc.vector.tensor_tensor(c3(LT, t), A[t][:, 0:384], c3(Ds, t), ALU.mult)
                    op.then_inc(lt_ready.sem, 1)
                    v.wait_ge(prod_ready.sem, prod_ready.at(2, h))
                    for t in range(3):
                        op = nc.vector.tensor_tensor(c3(attn, t), B[t][:, 0:384], c3(D, t), ALU.mult)
                    op.then_inc(attn_ready.sem, 1)
                    v.wait_ge(bt_ready.sem, bt_ready.at(1, h))
                    nc.vector.tensor_tensor(Y[:, :].rearrange("p (c n) -> p c n", n=CK),
                                            ident[:, None, :].to_broadcast([P, NC, CK]),
                                            BT[:, 0, :].rearrange("p (c n) -> p c n", n=CK), ALU.subtract).then_inc(y1_ready.sem, 1)
                    for t in range(3):
                        v.wait_ge(x_turned.sem, x_turned.at(t + 1, h))
                        nc.vector.tensor_copy(c3(X, t), A[t][:, 0:384]).then_inc(x1_ready.sem, 1)
                    v.wait_ge(y1_ready.sem, y1_ready.at(1, h))
                    for l in range(1, len(LEVELS)):
                        for t in range(3):
                            n = 3 * (l - 1) + t
                            v.wait_ge(yx_mm.sem, yx_mm.at(n + 1, h))
                            if n < 3:
                                v.wait_ge(x1_ready.sem, x1_ready.at(3, h))
                            else:
                                v.wait_ge(y_ready.sem, y_ready.at(n - 2, h))
                            if l < len(LEVELS) - 1:
                                nc.vector.tensor_tensor(c3(X, t), c3(X, t), A[t][:, 0:384], ALU.subtract)
                            nc.vector.tensor_tensor(c3(Y, t), c3(Y, t), B[t][:, 0:384], ALU.subtract).then_inc(y_ready.sem, 1)
                    v.wait_ge(state_stored.sem, state_stored.at(1, h - 1))
                    nc.vector.memset(S[:, 0, :], 0.0).then_inc(s_ready.sem, 1)
                    for c in range(NC):
                        s = slice(CK * c, CK * c + CK)
                        v.wait_ge(ks_ready.sem, ks_ready.at(c + 1, h))
                        if c == 0:
                            v.wait_ge(v_turned_used.sem, v_turned_used.at(1, h))
                        nc.vector.scalar_tensor_tensor(R[:, :], KS, negbeg[:, c:c + 1], Vb[:, s],
                                                       ALU.mult, ALU.add).then_inc(r_ready.sem, 1)
                        if c < NC - 1:
                            v.wait_ge(ds_ready.sem, ds_ready.at(c + 1, h))
                            v.wait_ge(s_ready.sem, s_ready.at(c + 1, h))
                            nc.vector.scalar_tensor_tensor(S[:, (c + 1) % 2, :], S[:, c % 2, :],
                                                           erow[:, CK * c + CK - 1:CK * c + CK], DS,
                                                           ALU.mult, ALU.add).then_inc(s_ready.sem, 1)
                        else:
                            v.wait_ge(vn_ready.sem, vn_ready.at(9, h))
                            nc.vector.tensor_tensor(vm[:, :, :], vn[:, c % 2:c % 2 + 1, :].to_broadcast([P, SEQS, P]),
                                                    const["seq_of"][:, :, None].to_broadcast([P, SEQS, P]), ALU.mult).then_inc(vm_ready.sem, 1)
                            v.wait_ge(sample_stored.sem, sample_stored.at(1, h - 1))
                            last = erow[:, SEQ:T].rearrange("p (b n) -> p b n", n=STEPS)[:, :, STEPS - 1:STEPS]
                            v.wait_ge(s0_loaded.sem, s0_loaded.at(1, h))
                            then(nc.vector.tensor_tensor(S1[:, :, :], S0[:, :, :], last.to_broadcast([P, SEQS, P]), ALU.mult))
                            v.wait_ge(ds_ready.sem, ds_ready.at(9, h))
                            nc.vector.tensor_tensor(S1[:, 0:4, :], S1[:, 0:4, :], STATES[0][:, 0:512].rearrange("p (b n) -> p b n", n=P), ALU.add)
                            nc.vector.tensor_tensor(S1[:, 4:8, :], S1[:, 4:8, :], STATES[1][:, 0:512].rearrange("p (b n) -> p b n", n=P), ALU.add).then_inc(s_ready.sem, 1)
                    v.wait_ge(o_ssq.sem, o_ssq.at(1, h))
                    nc.vector.tensor_scalar(ro[:, 0:NC - 1], SMALL[:, 0:NC - 1], 1.0 / P, EPS, ALU.mult, ALU.add)
                    nc.vector.tensor_scalar(ro[0:SAMPLE, NC - 1:NC], SMALL[0:SAMPLE, NC - 1:NC], 1.0 / P, EPS,
                                            ALU.mult, ALU.add).then_inc(o_mean.sem, 1)
                    v.wait_ge(o_root.sem, o_root.at(1, h))
                    nc.vector.reciprocal(ro[:, :], ro[:, :]).then_inc(ro_ready.sem, 1)
                    v.wait_ge(o_spread.sem, o_spread.at(1, h))
                    for c, (a, n) in enumerate(CHUNKS):
                        op = nc.vector.scalar_tensor_tensor(o[:, a:a + n], o[:, a:a + n], nw[:, 0:1], B[c][:, 0:n], ALU.mult, ALU.mult)
                    op.then_inc(o_normed.sem, 1)
                    v.wait_ge(o_normed.sem, o_normed.at(1, h))
                    nc.vector.tensor_tensor(o[:, :], o[:, :], zs[:, :], ALU.mult).then_inc(o_done.sem, 1)
                    assert vec.n == VSTEPS, vec.n


def ssd(nc, bank, xn, tab, d, const, mix, out):
    A, B = bank[0:3], bank[4:7]
    Z = (bank[4], bank[3], bank[7])
    SMALL = 3 * SEQS + CONV + 1
    W = CW - 3
    with Phase(nc) as ctx:
        def sb(name, shape):
            return ctx.enter_context(nc.sbuf_tensor(f"ssd_{name}", shape, F32))

        def signal(name, per=1, unit=1, primed=False):
            return Signal(nc, ctx, f"ssd_{name}", per, unit, primed)
        wg, wp = sb("w_bc", [P, KT, 2, P]), sb("w_xz", [P, KT, 2, P])
        sg, sm = sb("small_bc", [P, 2, SMALL]), sb("small_x", [P, SMALL])
        nw, skip = sb("norm_w", [P, PAIRS]), sb("skip_w", [P, PAIRS])
        cb, acc = sb("padded", [P, 2, CW]), sb("conv", [P, 2, CW])
        Bt, Ct, CB, Btok = (sb(x, [P, TP]) for x in ("b", "c", "cb", "b_tokens"))
        xT, zs = sb("x", [P, TP]), sb("gate", [P, T])
        cur = sb("columns", [P, 5, NC, 2])
        erow, D, Cdec = (sb(x, [P, 2, TP]) for x in ("row_decay", "decay", "c_decayed"))
        xd, xde = sb("x_dt", [P, TP]), sb("x_dt_decayed", [P, TP])
        H, S0, S1, xm = sb("states", [P, NC, P]), sb("sample_in", [P, SEQS, P]), sb("sample_out", [P, SEQS, P]), sb("x_masked", [P, SEQS, P])
        tg, tx = sb("tail_bc", [P, 2, SEQS + 1, 3]), sb("tail_x", [P, SEQS + 1, 3])
        y, rstd = sb("y", [P, GP, T]), sb("rstd", [P, T])
        ident, ones = const["ident"], const["ones"]

        once = signal("norm_w_loaded", 2, 16)
        zeroed = signal("zeroed")
        g_loaded = signal("group_loaded", 2, 16)
        g_projected, g_evacuated = signal("bc_projected", 2), signal("bc_evacuated", 2)
        g_conv, g_silu = signal("bc_conv_done", 2), signal("bc_silu_done", 2)
        g_tail = signal("bc_tail_ready")
        g_tail_stored = signal("bc_tail_stored", 1, 16, True)
        g_products = signal("bc_products", 2)
        cb_ready, btok_ready = signal("cb_ready"), signal("b_tokens_ready")
        g_squared, g_summed = signal("group_squared", GP), signal("group_summed", GP)
        g_mean, g_root = signal("group_mean", 1, 1, True), signal("group_root")
        g_normed, g_stored = signal("group_normed", 1, 1, True), signal("group_stored", GP, 16, True)
        loaded, s0_loaded = signal("pair_loaded", 2, 16), signal("sample_in_loaded", 1, 16)
        cur_ready = signal("columns_ready")
        projected, evacuated = signal("x_projected"), signal("x_evacuated")
        z_projected, z_evacuated = signal("z_projected", 3), signal("z_evacuated", 3)
        conv_done, silu_done = signal("conv_done"), signal("silu_done")
        tail_ready, tail_stored = signal("tail_ready"), signal("tail_stored", 1, 16, True)
        rows, erow_ready, diff_ready = signal("rows", 2), signal("row_decay_ready", 2), signal("diff_ready", 2)
        dexp = signal("decay_exp_ready", 2)
        turned, xde_ready = signal("x_turned"), signal("x_ready")
        m_ready, cdec_ready = signal("weights_ready"), signal("c_decayed_ready")
        xm_ready = signal("x_masked_ready")
        u_ready, h_ready = signal("state_products"), signal("states_ready", 1, 1, True)
        state_stored = signal("states_stored", 2, 16, True)
        s1_ready = signal("sample_states_ready")
        y_mm, y_ready = signal("y_product"), signal("y_ready", 1, 1, True)
        VSTEPS, GSTEPS = 15, 8
        vec = Steps(nc, ctx, "ssd_vector_steps", VSTEPS)
        gvec = Steps(nc, ctx, "ssd_group_steps", GSTEPS)

        def sample(t):
            return t[:, SOFF:CW].rearrange("p (b n) -> p b n", n=SW)

        def row(a, n):
            names = "pqrs"[:len(a.shape) - 1]
            return a[bass.ds(n, 1)].rearrange(f"a {' '.join(names)} -> (a p) {' '.join(names[1:])}")

        with nc.Block() as block:
            @block.sync
            def _(sp):
                sp.dma_start(nw[:, :], d["ssm_norm_w"]).then_inc(once.sem, 16)
                sp.dma_start(skip[:, :], d["ssm_skip"]).then_inc(once.sem, 16)

                def load_group(g):
                    sp.dma_start(wg[:, :, :, :], row(d["w_bc"], g)).then_inc(g_loaded.sem, 16)
                    sp.dma_start(sg[:, :, :], row(d["ssm_small_bc"], g)).then_inc(g_loaded.sem, 16)

                def load_pair(u):
                    sp.dma_start(wp[:, :, :, :], row(d["w_xz"], u)).then_inc(loaded.sem, 16)
                    sp.dma_start(sm[:, :], row(d["ssm_small_x"], u)).then_inc(loaded.sem, 16)

                def load_sample(u):
                    sp.dma_start(S0[:, :, :], row(d["ssm_s0"], u)).then_inc(s0_loaded.sem, 16)

                def pair(u, last):
                    sp.wait_ge(tail_ready.sem, tail_ready.at(1, u))
                    sp.dma_start(row(out["ssm_conv_x"], u), tx[:, :, :]).then_inc(tail_stored.sem, 16)
                    if not last:
                        sp.wait_ge(z_projected.sem, z_projected.at(3, u))
                        sp.wait_ge(silu_done.sem, silu_done.at(1, u))
                        load_pair(u + 1)
                    sp.wait_ge(h_ready.sem, h_ready.at(1, u))
                    sp.dma_start(row(out["ssm_p"], u), H[:, NC - 1, :]).then_inc(state_stored.sem, 16)
                    sp.wait_ge(s1_ready.sem, s1_ready.at(1, u))
                    sp.dma_start(row(out["ssm_s"], u), S1[:, :, :]).then_inc(state_stored.sem, 16)
                    if not last:
                        sp.wait_ge(y_mm.sem, y_mm.at(1, u))
                        load_sample(u + 1)
                load_group(0)
                load_pair(0)
                load_sample(0)
                for g in range(SSM_GROUPS):
                    if g + 1 < SSM_GROUPS:
                        sp.wait_ge(g_projected.sem, g_projected.at(2, g))
                        sp.wait_ge(g_silu.sem, g_silu.at(2, g))
                        load_group(g + 1)
                    with sp.Fori(0, GP - 1) as p:
                        pair(p + g * GP, False)
                    pair(g * GP + GP - 1, g == SSM_GROUPS - 1)
                    sp.wait_ge(g_tail.sem, g_tail.at(1, g))
                    sp.dma_start(row(out["ssm_conv_bc"], g), tg[:, :, :, :]).then_inc(g_tail_stored.sem, 16)
                    sp.wait_ge(g_normed.sem, g_normed.at(1, g))
                    for k in range(GP):
                        sp.dma_start(row(mix, g * GP + (DN_HEADS + k)), y[:, k, :]).then_inc(g_stored.sem, 16)
                for sig, n, turn in ((tail_stored, 1, PAIRS - 1), (state_stored, 2, PAIRS - 1),
                                     (g_tail_stored, 1, SSM_GROUPS - 1), (g_stored, GP, SSM_GROUPS - 1)):
                    sp.wait_ge(sig.sem, sig.at(n, turn))

            @block.tensor
            def _(pe):
                def project_chunk(w, j, to, c):
                    a, n = CHUNKS[c]
                    for k in range(KT):
                        mm = nc.tensor.matmul(to[:, 0:n], w[:, k, j, :], xn[:, k, a:a + n], start=(k == 0), stop=(k == KT - 1))
                    return mm

                def project(w, j, banks, done):
                    [project_chunk(w, j, banks[c], c) for c in range(3)][-1].then_inc(done.sem, 1)

                with pe.Fori(0, SSM_GROUPS) as g:
                    pe.wait_ge(g_loaded.sem, g_loaded.at(2, g))
                    project(wg, 0, B, g_projected)
                    pe.wait_ge(g_mean.sem, g_mean.at(1, g - 1))
                    project(wg, 1, A, g_projected)
                    pe.wait_ge(g_silu.sem, g_silu.at(2, g))
                    for c in range(NC):
                        s = slice(CK * c, CK * c + CK)
                        mm = nc.tensor.matmul(A[c // 3][:, CK * (c % 3):CK * (c % 3) + CK], Bt[:, s], Ct[:, s], start=True, stop=True)
                    mm.then_inc(g_products.sem, 1)
                    for c in range(NC):
                        s = slice(CK * c, CK * c + CK)
                        mm = nc.tensor.transpose(B[c // 3][:, CK * (c % 3):CK * (c % 3) + CK], Bt[:, s], ident[:, :])
                    mm.then_inc(g_products.sem, 1)
                    with pe.Fori(0, GP) as p:
                        u = g * GP + p
                        pe.wait_ge(loaded.sem, loaded.at(2, u))
                        pe.wait_ge(btok_ready.sem, btok_ready.at(1, g))
                        pe.wait_ge(h_ready.sem, h_ready.at(1, u - 1))
                        project_chunk(wp, 1, Z[0], 0).then_inc(z_projected.sem, 1)
                        pe.wait_ge(cb_ready.sem, cb_ready.at(1, g))
                        pe.wait_ge(y_ready.sem, y_ready.at(1, u - 1))
                        project(wp, 0, A, projected)
                        pe.wait_ge(cur_ready.sem, cur_ready.at(1, u))
                        for e, banks, free in ((0, B, z_evacuated), (1, A, evacuated)):
                            pe.wait_ge(free.sem, free.at(1, u))
                            for c in range(NC):
                                mm = nc.tensor.matmul(banks[c // 3][:, CK * (c % 3):CK * (c % 3) + CK],
                                                      cur[:, 0, c, e:e + 1].to_broadcast([P, P]),
                                                      const["tri"][:, int(c == NC - 1), :], start=True, stop=True)
                            mm.then_inc(rows.sem, 1)
                        project_chunk(wp, 1, Z[1], 1).then_inc(z_projected.sem, 1)
                        pe.wait_ge(silu_done.sem, silu_done.at(1, u))
                        pe.wait_ge(diff_ready.sem, diff_ready.at(2, u))
                        for c in range(NC):
                            mm = nc.tensor.transpose(A[c // 3][:, CK * (c % 3):CK * (c % 3) + CK], xT[:, CK * c:CK * c + CK], ident[:, :])
                        mm.then_inc(turned.sem, 1)
                        project_chunk(wp, 1, Z[2], 2).then_inc(z_projected.sem, 1)
                        pe.wait_ge(z_evacuated.sem, z_evacuated.at(3, u))
                        pe.wait_ge(xde_ready.sem, xde_ready.at(1, u))
                        pe.wait_ge(xm_ready.sem, xm_ready.at(1, u))
                        for c in range(NC - 1):
                            s = slice(CK * c, CK * c + CK)
                            nc.tensor.matmul(B[c // 4][:, P * (c % 4):P * (c % 4) + P], Btok[:, s], xde[:, s], start=True, stop=True)
                        for half, to in enumerate((bank[3], bank[7])):
                            mm = nc.tensor.matmul(to[:, 0:512], Btok[:, SEQ:TP],
                                                  xm[:, 4 * half:4 * half + 4, :].rearrange("p b n -> p (b n)"), start=True, stop=True)
                        mm.then_inc(u_ready.sem, 1)
                        def output(c, e, n):
                            a = CK * (c % 3)
                            return A[c // 3][HALF * e:HALF * e + HALF, a:a + n]
                        pe.wait_ge(m_ready.sem, m_ready.at(1, u))
                        for c in range(NC):
                            n = CK if c < NC - 1 else SAMPLE
                            for e in range(2):
                                nc.tensor.matmul(output(c, e, n), xd[:, CK * c + HALF * e:CK * c + HALF * e + HALF],
                                                 D[:, e, CK * c:CK * c + n], start=(c % 3 == 0), stop=False)
                        pe.wait_ge(cdec_ready.sem, cdec_ready.at(1, u))
                        pe.wait_ge(s0_loaded.sem, s0_loaded.at(1, u))
                        for e in range(2):
                            ch = slice(HALF * e, HALF * e + HALF)
                            whole = output(NC - 1, e, SAMPLE)
                            for b in range(SEQS):
                                t = slice(SEQ + STEPS * b, SEQ + STEPS * b + STEPS)
                                nc.tensor.matmul(whole[:, STEPS * b:STEPS * b + STEPS], S0[:, b, ch],
                                                 Cdec[:, e, t], start=False, stop=False)
                        pe.wait_ge(h_ready.sem, h_ready.at(1, u))
                        for c in range(NC - 1):
                            for e in range(2):
                                ch = slice(HALF * e, HALF * e + HALF)
                                mm = nc.tensor.matmul(output(c, e, CK), H[:, c, ch], Cdec[:, e, CK * c:CK * c + CK],
                                                      start=False, stop=(c % 3 == 2 or c == NC - 2))
                        mm.then_inc(y_mm.sem, 1)
                    for k in range(GP):
                        pe.wait_ge(g_squared.sem, g_squared.at(k + 1, g))
                        for c, (a, n) in enumerate(CHUNKS):
                            mm = nc.tensor.matmul(A[c][:, 0:n], ones[:, :], acc[:, k % 2, a:a + n], start=(k == 0), stop=(k == GP - 1))
                        mm.then_inc(g_summed.sem, 1)

            @block.scalar
            def _(act):
                for sig in (g_tail_stored, tail_stored):
                    act.sem_inc(sig.sem, 16)
                act.sem_inc(g_normed.sem, 1)
                act.sem_inc(g_mean.sem, 1)
                act.sem_inc(g_stored.sem, 16 * GP)
                act.sem_inc(state_stored.sem, 32)
                act.sem_inc(y_ready.sem, 1)
                act.sem_inc(h_ready.sem, 1)

                def evacuate(banks, to, done):
                    for c, (a, n) in enumerate(CHUNKS):
                        if c < 2:
                            nc.scalar.activation(to[:, a + 3:a + 3 + n], banks[c][:, 0:n], ACT.Copy)
                    nc.scalar.activation(to[:, a + 3:SOFF], banks[2][:, 0:SEQ - a], ACT.Copy)
                    nc.scalar.activation(sample(to)[:, :, 3:SW], banks[2][:, SEQ - a:n].rearrange("p (b n) -> p b n", n=STEPS),
                                         ACT.Copy).then_inc(done.sem, 1)

                def silu(to, src, bias, done):
                    nc.scalar.activation(to[:, 0:SEQ], src[:, 0:SEQ], ACT.Silu, bias=bias)
                    nc.scalar.activation(to[:, SEQ:T].rearrange("p (b n) -> p b n", n=STEPS), sample(src)[:, :, 0:STEPS],
                                         ACT.Silu, bias=bias).then_inc(done.sem, 1)

                with act.Fori(0, SSM_GROUPS) as g:
                    for j, banks in ((0, B), (1, A)):
                        act.wait_ge(g_projected.sem, g_projected.at(j + 1, g))
                        evacuate(banks, cb[:, j, :], g_evacuated)
                    for j, to in ((0, Bt), (1, Ct)):
                        act.wait_ge(g_conv.sem, g_conv.at(j + 1, g))
                        silu(to, acc[:, j, :], sg[:, j, SMALL - 1:SMALL], g_silu)
                    act.wait_ge(g_products.sem, g_products.at(2, g))
                    for t in range(3):
                        op = nc.scalar.activation(Btok[:, 384 * t:384 * t + 384], B[t][:, 0:384], ACT.Copy)
                    op.then_inc(btok_ready.sem, 1)
                    act.wait_ge(g_tail.sem, g_tail.at(1, g))
                    with act.Fori(0, GP) as p:
                        u = g * GP + p

                        def gate(c):
                            a, n = CHUNKS[c]
                            act.wait_ge(z_projected.sem, z_projected.at(c + 1, u))
                            nc.scalar.activation(zs[:, a:a + n], Z[c][:, 0:n], ACT.Silu).then_inc(z_evacuated.sem, 1)

                        def decay(e):
                            act.wait_ge(diff_ready.sem, diff_ready.at(e + 1, u))
                            nc.scalar.activation(D[:, e, :], D[:, e, :], ACT.Exp).then_inc(dexp.sem, 1)
                        act.wait_ge(y_ready.sem, y_ready.at(1, u - 1))
                        gate(0)
                        act.wait_ge(projected.sem, projected.at(1, u))
                        evacuate(A, cb[:, 0, :], evacuated)
                        for e, banks in ((0, B), (1, A)):
                            act.wait_ge(rows.sem, rows.at(e + 1, u))
                            for t in range(3):
                                op = nc.scalar.activation(erow[:, e, 384 * t:384 * t + 384], banks[t][:, 0:384], ACT.Exp)
                            op.then_inc(erow_ready.sem, 1)
                        act.wait_ge(conv_done.sem, conv_done.at(1, u))
                        silu(xT, acc[:, 0, :], sm[:, SMALL - 1:SMALL], silu_done)
                        decay(0)
                        gate(1)
                        decay(1)
                        gate(2)
                    act.wait_ge(y_ready.sem, y_ready.at(1, g * GP + (GP - 1)))
                    for k in range(GP):
                        if k >= 2:
                            act.wait_ge(g_summed.sem, g_summed.at(k - 1, g))
                        nc.scalar.activation(acc[:, k % 2, 0:T], y[:, k, :], ACT.Square).then_inc(g_squared.sem, 1)
                    act.wait_ge(g_mean.sem, g_mean.at(1, g))
                    nc.scalar.activation(rstd[:, :], rstd[:, :], ACT.Sqrt).then_inc(g_root.sem, 1)

            @block.gpsimd
            def _(pool):
                nc.gpsimd.memset(xT[:, T:TP], 0.0)
                nc.gpsimd.memset(Bt[:, T:TP], 0.0)
                nc.gpsimd.memset(Ct[:, T:TP], 0.0)
                nc.gpsimd.memset(cb[:, :, 0:3], 0.0).then_inc(zeroed.sem, 1)
                with pool.Fori(0, SSM_GROUPS) as g:
                    with pool.Fori(0, GP) as p:
                        u = g * GP + p
                        pool.wait_ge(g_silu.sem, g_silu.at(2, g))
                        for e in range(2):
                            pool.wait_ge(erow_ready.sem, erow_ready.at(e + 1, u))
                            op = nc.gpsimd.tensor_tensor(Cdec[:, e, :], Ct[:, :], erow[:, e, :], ALU.mult)
                        op.then_inc(cdec_ready.sem, 1)

            @block.vector
            def _(v):
                def conv(j, small, then, done):
                    then(nc.vector.tensor_scalar(acc[:, j, 0:W], cb[:, j, 0:W], small[:, 24:25], None, ALU.mult))
                    for k in range(1, CONV):
                        op = nc.vector.scalar_tensor_tensor(acc[:, j, 0:W], cb[:, j, k:k + W], small[:, 24 + k:25 + k],
                                                            acc[:, j, 0:W], ALU.mult, ALU.add)
                        if k < CONV - 1:
                            then(op)
                        else:
                            op.then_inc(done.sem, 1)

                v.wait_ge(once.sem, once.at(2))
                v.wait_ge(zeroed.sem, 1)
                with v.Fori(0, SSM_GROUPS) as g:
                    gvec.n = 0

                    def gthen(op):
                        op.then_inc(gvec.step(), 1)
                        v.wait_ge(gvec.sem, gvec.now(g))
                    v.wait_ge(g_loaded.sem, g_loaded.at(2, g))
                    for j in range(2):
                        hist = nc.vector.tensor_copy(sample(cb[:, j, :])[:, :, 0:3], sg[:, j, 0:24].rearrange("p (b n) -> p b n", n=3))
                    gthen(hist)
                    for j in range(2):
                        v.wait_ge(g_evacuated.sem, g_evacuated.at(j + 1, g))
                        conv(j, sg[:, j, :], gthen, g_conv)
                    v.wait_ge(g_tail_stored.sem, g_tail_stored.at(1, g - 1))
                    nc.vector.tensor_copy(tg[:, :, 0, :], cb[:, :, SEQ:SOFF])
                    nc.vector.tensor_copy(tg[:, :, 1:SEQS + 1, :],
                                          cb[:, :, SOFF:CW].rearrange("p j (b n) -> p j b n", n=SW)[:, :, :, STEPS:SW]).then_inc(g_tail.sem, 1)
                    v.wait_ge(g_products.sem, g_products.at(1, g))
                    for t in range(3):
                        s = slice(384 * t, 384 * t + 384)
                        op = nc.vector.tensor_tensor(CB[:, s], A[t][:, 0:384], const["incl"][:, s], ALU.mult)
                    op.then_inc(cb_ready.sem, 1)
                    with v.Fori(0, GP) as p:
                        u = g * GP + p
                        vec.n = 0

                        def then(op):
                            op.then_inc(vec.step(), 1)
                            v.wait_ge(vec.sem, vec.now(u))
                        nc.vector.tensor_copy(cur[:, :, :, :].rearrange("p q c e -> p (q c) e"),
                                              tab[:, :, :, bass.ds(u * 2 + DN_HEADS, 2)].rearrange("p q c e -> p (q c) e")).then_inc(cur_ready.sem, 1)
                        v.wait_ge(loaded.sem, loaded.at(2, u))
                        then(nc.vector.tensor_copy(sample(cb[:, 0, :])[:, :, 0:3], sm[:, 0:24].rearrange("p (b n) -> p b n", n=3)))
                        v.wait_ge(evacuated.sem, evacuated.at(1, u))
                        conv(0, sm, then, conv_done)
                        v.wait_ge(tail_stored.sem, tail_stored.at(1, u - 1))
                        nc.vector.tensor_copy(tx[:, 0, :], cb[:, 0, SEQ:SOFF])
                        nc.vector.tensor_copy(tx[:, 1:SEQS + 1, :], sample(cb[:, 0, :])[:, :, STEPS:SW]).then_inc(tail_ready.sem, 1)
                        for e, banks in ((0, B), (1, A)):
                            v.wait_ge(erow_ready.sem, erow_ready.at(e + 1, u))
                            v.wait_ge(cur_ready.sem, cur_ready.at(1, u))
                            for c in range(NC):
                                op = nc.vector.tensor_scalar(D[:, e, CK * c:CK * c + CK], banks[c // 3][:, CK * (c % 3):CK * (c % 3) + CK],
                                                             cur[:, 1, c, e:e + 1], 0.0, ALU.subtract, ALU.min)
                            op.then_inc(diff_ready.sem, 1)
                        v.wait_ge(turned.sem, turned.at(1, u))
                        heads = lambda t: t.rearrange("p (c n) -> p c n", n=HALF)
                        col = lambda q: cur[:, q, :, :].rearrange("p c e -> p (c e)")
                        for t in range(3):
                            op = nc.vector.tensor_tensor(heads(xd[:, 384 * t:384 * t + 384]), heads(A[t][:, 0:384]),
                                                         col(4)[:, 6 * t:6 * t + 6, None].to_broadcast([P, 6, HALF]), ALU.mult)
                        then(op)
                        nc.vector.tensor_tensor(heads(xde[:, :]), heads(xd[:, :]),
                                                col(3)[:, :, None].to_broadcast([P, 2 * NC, HALF]), ALU.mult).then_inc(xde_ready.sem, 1)
                        v.wait_ge(xde_ready.sem, xde_ready.at(1, u))
                        nc.vector.tensor_tensor(xm[:, :, :], xde[:, None, SEQ:TP].to_broadcast([P, SEQS, P]),
                                                const["seq_of"][:, :, None].to_broadcast([P, SEQS, P]), ALU.mult).then_inc(xm_ready.sem, 1)
                        v.wait_ge(cb_ready.sem, cb_ready.at(1, g))
                        v.wait_ge(dexp.sem, dexp.at(2, u))
                        nc.vector.tensor_tensor(D[:, :, :], D[:, :, :], CB[:, None, :].to_broadcast([P, 2, TP]), ALU.mult).then_inc(m_ready.sem, 1)
                        v.wait_ge(state_stored.sem, state_stored.at(2, u - 1))
                        then(nc.vector.memset(H[:, 0, :], 0.0))
                        v.wait_ge(u_ready.sem, u_ready.at(1, u))
                        for c in range(NC - 1):
                            last = CK * c + CK - 1
                            for e in range(2):
                                ch = slice(HALF * e, HALF * e + HALF)
                                op = nc.vector.scalar_tensor_tensor(H[:, c + 1, ch], H[:, c, ch], erow[:, e, last:last + 1],
                                                                    B[c // 4][:, P * (c % 4) + HALF * e:P * (c % 4) + HALF * e + HALF],
                                                                    ALU.mult, ALU.add)
                            if c < NC - 2:
                                then(op)
                            else:
                                op.then_inc(h_ready.sem, 1)
                        v.wait_ge(s0_loaded.sem, s0_loaded.at(1, u))
                        for e in range(2):
                            ch = slice(HALF * e, HALF * e + HALF)
                            lasts = erow[:, e, SEQ:T].rearrange("p (b n) -> p b n", n=STEPS)[:, :, STEPS - 1:STEPS]
                            op = nc.vector.tensor_tensor(S1[:, :, ch], S0[:, :, ch], lasts.to_broadcast([P, SEQS, HALF]), ALU.mult)
                        then(op)
                        nc.vector.tensor_tensor(S1[:, 0:4, :], S1[:, 0:4, :], bank[3][:, 0:512].rearrange("p (b n) -> p b n", n=P), ALU.add)
                        nc.vector.tensor_tensor(S1[:, 4:8, :], S1[:, 4:8, :], bank[7][:, 0:512].rearrange("p (b n) -> p b n", n=P), ALU.add).then_inc(s1_ready.sem, 1)
                        v.wait_ge(y_mm.sem, y_mm.at(1, u))
                        v.wait_ge(g_stored.sem, g_stored.at(GP, g - 1))
                        yp = y[:, bass.ds(p, 1), :].rearrange("p o n -> p (o n)")
                        for c, (a, n) in enumerate(CHUNKS):
                            op = nc.vector.scalar_tensor_tensor(xT[:, a:a + n], xT[:, a:a + n], skip[:, bass.ds(u, 1)], A[c][:, 0:n],
                                                                ALU.mult, ALU.add)
                        then(op)
                        nc.vector.tensor_tensor(yp, xT[:, 0:T], zs[:, :], ALU.mult).then_inc(y_ready.sem, 1)
                        assert vec.n == VSTEPS, vec.n
                    v.wait_ge(g_summed.sem, g_summed.at(GP, g))
                    for c, (a, n) in enumerate(CHUNKS):
                        op = nc.vector.tensor_scalar(rstd[:, a:a + n], A[c][:, 0:n], 1.0 / (GP * P), EPS, ALU.mult, ALU.add)
                    op.then_inc(g_mean.sem, 1)
                    v.wait_ge(g_root.sem, g_root.at(1, g))
                    gthen(nc.vector.reciprocal(rstd[:, :], rstd[:, :]))
                    v.wait_ge(y_ready.sem, y_ready.at(1, g * GP + (GP - 1)))
                    for k in range(GP):
                        op = nc.vector.scalar_tensor_tensor(y[:, k, :], y[:, k, :], nw[:, bass.ds(g * GP + k, 1)], rstd[:, :],
                                                            ALU.mult, ALU.mult)
                    op.then_inc(g_normed.sem, 1)
                    assert gvec.n == GSTEPS, gvec.n


def row_of(a, n):
    names = " ".join("pqrs"[:len(a.shape) - 1])
    return a[bass.ds(n, 1)].rearrange(f"a {names} -> (a {names[0]}) {names[1:]}")


def split_weights(nc, pool, zero, stage, hi, lo, waits, hi_done, done, turn):
    for sig, value in waits:
        pool.wait_ge(sig.sem, value)
    n = stage.shape[-2:]
    nc.gpsimd.tensor_tensor(hi, stage, zero[:, None, :].to_broadcast([P, *n]), ALU.add).then_inc(hi_done.sem, 1)
    pool.wait_ge(hi_done.sem, turn)
    nc.gpsimd.tensor_tensor(lo, stage, hi.bitcast(F32), ALU.subtract).then_inc(done.sem, 1)


def linear(nc, bank, name, rhs, w, K, outs, tokens, how, to, prefetch=(), behind=None):
    cols = CHUNKS if tokens == T else [(0, tokens)]
    wide = to.shape[-1]
    turns = outs // 2
    with Phase(nc) as ctx:
        def pair(what, shape, dt=F32):
            return [ctx.enter_context(nc.sbuf_tensor(f"{name}_{what}{r}", shape, dt)) for r in range(2)]

        def signals(what, unit=1, primed=False):
            return [Signal(nc, ctx, f"{name}_{what}{r}", 1, unit, primed) for r in range(2)]
        wb, wh, wl = pair("w", [P, K, P]), pair("w_hi", [P, K, P], F32R), pair("w_lo", [P, K, P], F32R)
        loaded, hi_done, split = signals("loaded", 16), signals("w_hi_done"), signals("w_split", 1, True)
        product, taken = signals("product", 1, True), signals("taken", 1, True)
        zeroed = Signal(nc, ctx, f"{name}_zeroed", 2)
        if how == "store":
            stage = pair("stage", [P, wide])
            stored = signals("stored", 16, True)
        with nc.Block() as block:
            @block.sync
            def _(sp):
                def fetch(i):
                    for r in range(2):
                        sp.wait_ge(split[r].sem, split[r].at(1, i - 1))
                        sp.dma_start(wb[r][:, :, :], row_of(w, i * 2 + r)).then_inc(loaded[r].sem, 16)

                def store(i):
                    for r in range(2):
                        sp.wait_ge(taken[r].sem, taken[r].at(1, i))
                        sp.dma_start(row_of(to, i * 2 + r), stage[r][:, :]).then_inc(stored[r].sem, 16)
                fetch(0)
                for dst, src, sig in prefetch:
                    sp.dma_start(dst, src).then_inc(sig.sem, 16)
                if how == "store":
                    with sp.Fori(1, turns) as i:
                        fetch(i)
                        store(i - 1)
                    store(turns - 1)
                    for r in range(2):
                        sp.wait_ge(stored[r].sem, stored[r].at(1, turns - 1))
                else:
                    with sp.Fori(1, turns) as i:
                        fetch(i)

            @block.scalar
            def _(act):
                with act.Fori(0, turns) as i:
                    for r in range(2):
                        act.wait_ge(loaded[r].sem, loaded[r].at(1, i))
                        act.wait_ge(product[r].sem, product[r].at(1, i - 1))
                        nc.scalar.activation(wh[r][:, :, :], wb[r][:, :, :], ACT.Copy).then_inc(hi_done[r].sem, 1)

            @block.gpsimd
            def _(pool):
                for r in range(2):
                    for sig in (product[r], taken[r], split[r]):
                        pool.sem_inc(sig.sem, 1)
                    if how == "store":
                        pool.sem_inc(stored[r].sem, 16)
                        nc.gpsimd.memset(stage[r][:, :], 0.0).then_inc(zeroed.sem, 1)
                with pool.Fori(0, turns) as i:
                    for r in range(2):
                        pool.wait_ge(hi_done[r].sem, hi_done[r].at(1, i))
                        nc.gpsimd.tensor_tensor(wl[r][:, :, :], wb[r][:, :, :], wh[r][:, :, :].bitcast(F32), ALU.subtract).then_inc(split[r].sem, 1)

            @block.tensor
            def _(pe):
                with pe.Fori(0, turns) as i:
                    for r in range(2):
                        pe.wait_ge(split[r].sem, split[r].at(1, i))
                        pe.wait_ge(taken[r].sem, taken[r].at(1, i - 1))
                        for c, (a, n) in enumerate(cols):
                            for k in range(K):
                                mm = split_product(nc, bank[3 * r + c][:, 0:n], (wh[r][:, k, :], wl[r][:, k, :]),
                                                   [x[:, k, a:a + n] for x in rhs], k == 0, k == K - 1)
                        mm.then_inc(product[r].sem, 1)

            @block.vector
            def _(v):
                if how == "store":
                    v.wait_ge(zeroed.sem, zeroed.at(2))
                with v.Fori(0, turns) as i:
                    for r in range(2):
                        if behind is not None:
                            v.wait_ge(*behind)
                        v.wait_ge(product[r].sem, product[r].at(1, i))
                        if how == "store":
                            v.wait_ge(stored[r].sem, stored[r].at(1, i - 1))
                        for c, (a, n) in enumerate(cols):
                            if how == "store":
                                op = nc.vector.tensor_copy(stage[r][:, a:a + n], bank[3 * r + c][:, 0:n])
                                continue
                            dst = to[:, bass.ds(i * 2 + r, 1), a:a + n].rearrange("p o n -> p (o n)")
                            if how == "add":
                                op = nc.vector.tensor_tensor(dst, dst, bank[3 * r + c][:, 0:n], ALU.add)
                            else:
                                op = nc.vector.tensor_copy(dst, bank[3 * r + c][:, 0:n])
                        op.then_inc(taken[r].sem, 1)


def split_pair(nc, ctx, name):
    return tuple(ctx.enter_context(nc.sbuf_tensor(f"{name}_{x}", [P, KT, T], F32R)) for x in ("hi", "lo"))


def split_tiles(nc, name, src, hi, lo, n, loaded=None, loads=()):
    with Phase(nc) as ctx:
        hi_ready = Signal(nc, ctx, f"{name}_hi_ready", n)
        with nc.Block() as block:
            @block.sync
            def _(sp):
                for to, at, sig in loads:
                    sp.dma_start(to, at).then_inc(sig.sem, 16)

            @block.scalar
            def _(act):
                for k in range(n):
                    if loaded:
                        act.wait_ge(loaded[k].sem, loaded[k].at(1))
                    nc.scalar.activation(hi[:, k, :], src[:, k, :], ACT.Copy).then_inc(hi_ready.sem, 1)

            @block.vector
            def _(v):
                for k in range(0, n, 2):
                    v.wait_ge(hi_ready.sem, hi_ready.at(k + 1))
                    nc.vector.tensor_tensor(lo[:, k, :], src[:, k, :], hi[:, k, :].bitcast(F32), ALU.subtract)

            @block.gpsimd
            def _(pool):
                for k in range(1, n, 2):
                    pool.wait_ge(hi_ready.sem, hi_ready.at(k + 1))
                    nc.gpsimd.tensor_tensor(lo[:, k, :], src[:, k, :], hi[:, k, :].bitcast(F32), ALU.subtract)


def load(nc, ctx, name, pairs):
    sig = Signal(nc, ctx, f"{name}_loaded", 1, 16)
    with nc.Block() as block:
        @block.sync
        def _(sp):
            for to, src in pairs:
                sp.dma_start(to, src).then_inc(sig.sem, 16)
            sp.wait_ge(sig.sem, sig.at(len(pairs)))


def memory_kv(nc, bank, const, d, out, mkT, mv):
    with Phase(nc) as ctx:
        mn = ctx.enter_context(nc.sbuf_tensor("mem_normed", [P, KT, MEM], F32))
        wv = ctx.enter_context(nc.sbuf_tensor("w_mem_v", [P, KT, D_MODEL], F32))
        load(nc, ctx, "mem", [(mn[:, :, :], d["memT"]), (wv[:, :, :], d["w_mv"])])
        rmsnorm(nc, bank, "mem_norm", mn, mn, const["gains"][:, 2, :], const["ident"][:, :], const["ones"][:, :], MEM, D_MODEL)
        parts = [ctx.enter_context(nc.sbuf_tensor(f"mem_{x}", [P, KT, MEM], F32R)) for x in ("hi", "lo")]
        split_tiles(nc, "mem_split", mn, *parts, KT)
        linear(nc, bank, "mem_k", parts, d["w_mk"], KT, KT, MEM, "copy", mkT)
        product, ready = Signal(nc, ctx, "mem_v_product", 4), Signal(nc, ctx, "mem_v_ready", 4)
        stored = Signal(nc, ctx, "mem_stored", 2, 16)
        with nc.Block() as block:
            @block.tensor
            def _(pe):
                for m in range(2):
                    for half in range(2):
                        for k in range(KT):
                            mm = nc.tensor.matmul(bank[2 * m + half][:, :], mn[:, k, P * m:P * m + P],
                                                  wv[:, k, 512 * half:512 * half + 512], start=(k == 0), stop=(k == KT - 1))
                        mm.then_inc(product.sem, 1)

            @block.vector
            def _(v):
                for m in range(2):
                    for half in range(2):
                        v.wait_ge(product.sem, product.at(2 * m + half + 1))
                        nc.vector.tensor_copy(mv[:, m, 512 * half:512 * half + 512], bank[2 * m + half][:, :]).then_inc(ready.sem, 1)

            @block.sync
            def _(sp):
                sp.dma_start(out["mem_k"], mkT[:, :, :]).then_inc(stored.sem, 16)
                sp.wait_ge(ready.sem, ready.at(4))
                sp.dma_start(out["mem_v"], mv[:, :, :]).then_inc(stored.sem, 16)
                sp.wait_ge(stored.sem, stored.at(2))


class Cache:

    def __init__(self, nc, ctx, d):
        self.d = d
        self.k = ctx.enter_context(nc.sbuf_tensor("cache_k", [P, 4, KT, MEM], F32))
        self.v = ctx.enter_context(nc.sbuf_tensor("cache_v", [P, 4, 2, D_MODEL], F32))
        self.k_loaded = [Signal(nc, ctx, f"cache_k_loaded{b}", 1, 16) for b in range(4)]
        self.v_loaded = [Signal(nc, ctx, f"cache_v_loaded{b}", 1, 16) for b in range(4)]

    def load_k(self, sp, i, b):
        sp.dma_start(self.k[:, b, :, :], row_of(self.d["cache_k"], i * 4 + b)).then_inc(self.k_loaded[b].sem, 16)

    def load_v(self, sp, i, b):
        sp.dma_start(self.v[:, b, :, :], row_of(self.d["cache_v"], i * 4 + b)).then_inc(self.v_loaded[b].sem, 16)


def attend_prompt(nc, bank, const, d, qx, mkT, mv, ao, cache):
    H, SC, TILES = MEM_HEADS, (D_MODEL // MEM_HEADS) ** -0.5, SEQ // P
    with Phase(nc) as ctx:
        def sb(name, shape):
            return ctx.enter_context(nc.sbuf_tensor(f"att_{name}", shape, F32))

        def signal(name, per=1, unit=1, primed=False):
            return Signal(nc, ctx, f"att_{name}", per, unit, primed)
        q, pr, pT = sb("q", [P, KT, P]), sb("probs", [P, H, MEM]), sb("probs_t", [P, 2, H, P])
        top, neg, total, inv = (sb(x, [P, H]) for x in ("top", "neg_top", "total", "inv"))
        loaded, scores = signal("loaded", 1, 16), signal("scores")
        top_found, top_ready, exped, inv_ready = (signal(x) for x in ("top_found", "top_ready", "exp_ready", "inv_ready"))
        probs, turned, pT_ready = (signal(x) for x in ("probs_ready", "turned", "probs_t_ready"))
        product, taken = signal("product"), signal("taken", 1, 1, True)
        with nc.Block() as block:
            @block.sync
            def _(sp):
                def load_q(i):
                    sp.dma_start(q[:, :, :], qx[:, :, bass.ds(i * P, P)].rearrange("k p n -> p k n")).then_inc(loaded.sem, 16)
                load_q(0)

                def next_q(i):
                    sp.wait_ge(scores.sem, scores.at(1, i))
                    load_q(i + 1)
                for b in range(4):
                    next_q(b)
                    cache.load_k(sp, 0, b)
                    cache.load_v(sp, 0, b)
                with sp.Fori(4, TILES - 1) as i:
                    next_q(i)

            @block.tensor
            def _(pe):
                def make_scores(i):
                    pe.wait_ge(loaded.sem, loaded.at(1, i))
                    for h in range(H):
                        for k in range(2):
                            mm = nc.tensor.matmul(bank[h // 2][:, MEM * (h % 2):MEM * (h % 2) + MEM], q[:, 2 * h + k, :],
                                                  mkT[:, 2 * h + k, :], start=(k == 0), stop=(k == 1))
                    mm.then_inc(scores.sem, 1)

                def attend(i):
                    pe.wait_ge(probs.sem, probs.at(1, i))
                    for m in range(2):
                        for h in range(H):
                            mm = nc.tensor.transpose(bank[2 + m][:, P * h:P * h + P], pr[:, h, P * m:P * m + P], const["ident"][:, :])
                    mm.then_inc(turned.sem, 1)
                    pe.wait_ge(pT_ready.sem, pT_ready.at(1, i))
                    pe.wait_ge(taken.sem, taken.at(1, i - 1))
                    for k in range(KT):
                        for m in range(2):
                            mm = nc.tensor.matmul(bank[4 + k // 4][:, P * (k % 4):P * (k % 4) + P], mv[:, m, P * k:P * k + P],
                                                  pT[:, m, k // 2, :], start=(m == 0), stop=(m == 1))
                    mm.then_inc(product.sem, 1)
                make_scores(0)
                with pe.Fori(0, TILES - 1) as i:
                    pe.wait_ge(exped.sem, exped.at(1, i))
                    make_scores(i + 1)
                    attend(i)
                attend(TILES - 1)

            @block.scalar
            def _(act):
                act.sem_inc(taken.sem, 1)

                def exp(i):
                    act.wait_ge(top_ready.sem, top_ready.at(1, i))
                    for h in range(H):
                        op = nc.scalar.activation(pr[:, h, :], bank[h // 2][:, MEM * (h % 2):MEM * (h % 2) + MEM], ACT.Exp,
                                                  bias=neg[:, h:h + 1], scale=SC, accum_out=total[:, h:h + 1])
                    op.then_inc(exped.sem, 1)

                def take_turned(i):
                    act.wait_ge(turned.sem, turned.at(1, i))
                    for m in range(2):
                        op = nc.scalar.activation(pT[:, m, :, :], bank[2 + m][:, :].rearrange("p (h n) -> p h n", n=P), ACT.Copy)
                    op.then_inc(pT_ready.sem, 1)
                exp(0)
                with act.Fori(0, TILES - 1) as i:
                    take_turned(i)
                    exp(i + 1)
                take_turned(TILES - 1)

            @block.vector
            def _(v):
                def find_top(i):
                    v.wait_ge(scores.sem, scores.at(1, i))
                    for b in range(2):
                        op = nc.vector.tensor_reduce(top[:, 2 * b:2 * b + 2], bank[b][:, :].rearrange("p (h n) -> p h n", n=MEM), AX.X, ALU.max)
                    op.then_inc(top_found.sem, 1)
                    v.wait_ge(top_found.sem, top_found.at(1, i))
                    nc.vector.tensor_scalar(neg[:, :], top[:, :], -SC, None, ALU.mult).then_inc(top_ready.sem, 1)

                def normalize(i):
                    v.wait_ge(exped.sem, exped.at(1, i))
                    nc.vector.reciprocal(inv[:, :], total[:, :]).then_inc(inv_ready.sem, 1)
                    v.wait_ge(inv_ready.sem, inv_ready.at(1, i))
                    nc.vector.tensor_tensor(pr[:, :, :], pr[:, :, :], inv[:, :, None].to_broadcast([P, H, MEM]), ALU.mult).then_inc(probs.sem, 1)

                def take(i):
                    v.wait_ge(product.sem, product.at(1, i))
                    for b in range(2):
                        op = nc.vector.tensor_copy(ao[:, 4 * b:4 * b + 4, bass.ds(i * P, P)], bank[4 + b][:, :].rearrange("p (k n) -> p k n", n=P))
                    op.then_inc(taken.sem, 1)
                find_top(0)
                with v.Fori(0, TILES - 1) as i:
                    normalize(i)
                    find_top(i + 1)
                    take(i)
                normalize(TILES - 1)
                take(TILES - 1)


def attend_sample(nc, bank, const, d, qx, ao, cache):
    H, SC, R = MEM_HEADS, (D_MODEL // MEM_HEADS) ** -0.5, MEM_HEADS * STEPS
    with Phase(nc) as ctx:
        def sb(name, shape):
            return ctx.enter_context(nc.sbuf_tensor(f"satt_{name}", shape, F32))

        def signal(name, per=1, unit=1, primed=False):
            return Signal(nc, ctx, f"satt_{name}", per, unit, primed)
        q, qm = sb("q", [P, KT, SAMPLE]), sb("q_masked", [P, KT, 4, H, STEPS])
        K, V, k_loaded, v_loaded = cache.k, cache.v, cache.k_loaded, cache.v_loaded
        pr, pT = sb("probs", [P, MEM]), sb("probs_t", [P, 2, P])
        top, neg, total, inv = (sb(x, [P, 1]) for x in ("top", "neg_top", "total", "inv"))
        q_loaded, zeroed = signal("q_loaded", 1, 16), signal("zeroed")
        masked, scores = signal("masked"), signal("scores", 1, 1, True)
        top_ready, exped, probs, turned, pT_ready = (signal(x) for x in ("top_ready", "exp_ready", "probs_ready", "turned", "probs_t_ready"))
        rows = sb("rows", [P, D_MODEL])
        product, rows_ready, rows_turned = signal("product"), signal("rows_ready"), signal("rows_turned")
        taken = signal("taken", 1, 1, True)
        vec = Steps(nc, ctx, "satt_vector_steps", 2)
        with nc.Block() as block:
            @block.sync
            def _(sp):
                sp.dma_start(q[:, :, :], qx[:, :, SEQ:T].rearrange("k p n -> p k n")).then_inc(q_loaded.sem, 16)
                with sp.Fori(1, SEQS // 4) as i:
                    sp.wait_ge(scores.sem, scores.at(1, i - 1))
                    for b in range(4):
                        cache.load_k(sp, i, b)
                    sp.wait_ge(taken.sem, taken.at(1, i - 1))
                    for b in range(4):
                        cache.load_v(sp, i, b)

            @block.gpsimd
            def _(pool):
                nc.gpsimd.memset(qm[:, :, :, :, :].rearrange("p k b h n -> p (k b h n)"), 0.0).then_inc(zeroed.sem, 1)

            @block.tensor
            def _(pe):
                with pe.Fori(0, SEQS // 4) as i:
                    pe.wait_ge(masked.sem, masked.at(1, i))
                    pe.wait_ge(taken.sem, taken.at(1, i - 1))
                    for b in range(4):
                        pe.wait_ge(k_loaded[b].sem, k_loaded[b].at(1, i))
                        for k in range(KT):
                            mm = nc.tensor.matmul(bank[0][R * b:R * b + R, 0:MEM], qm[:, k, b, :, :].rearrange("p h n -> p (h n)"),
                                                  K[:, b, k, :], start=(k == 0), stop=(k == KT - 1))
                    mm.then_inc(scores.sem, 1)
                    pe.wait_ge(probs.sem, probs.at(1, i))
                    for m in range(2):
                        mm = nc.tensor.transpose(bank[2][:, P * m:P * m + P], pr[:, P * m:P * m + P], const["ident"][:, :])
                    mm.then_inc(turned.sem, 1)
                    pe.wait_ge(pT_ready.sem, pT_ready.at(1, i))
                    for b in range(4):
                        pe.wait_ge(v_loaded[b].sem, v_loaded[b].at(1, i))
                        for half in range(2):
                            for m in range(2):
                                mm = nc.tensor.matmul(bank[4 + half][R * b:R * b + R, :], pT[:, m, R * b:R * b + R],
                                                      V[:, b, m, 512 * half:512 * half + 512], start=(m == 0), stop=(m == 1))
                    mm.then_inc(product.sem, 1)
                    pe.wait_ge(rows_ready.sem, rows_ready.at(1, i))
                    for k in range(KT):
                        mm = nc.tensor.transpose(bank[6 + k // 4][:, P * (k % 4):P * (k % 4) + P], rows[:, P * k:P * k + P], const["ident"][:, :])
                    mm.then_inc(rows_turned.sem, 1)

            @block.scalar
            def _(act):
                act.sem_inc(scores.sem, 1)
                act.sem_inc(taken.sem, 1)
                with act.Fori(0, SEQS // 4) as i:
                    act.wait_ge(top_ready.sem, top_ready.at(1, i))
                    nc.scalar.activation(pr[:, :], bank[0][:, 0:MEM], ACT.Exp, bias=neg[:, 0:1], scale=SC,
                                         accum_out=total[:, 0:1]).then_inc(exped.sem, 1)
                    act.wait_ge(turned.sem, turned.at(1, i))
                    nc.scalar.activation(pT[:, :, :], bank[2][:, 0:2 * P].rearrange("p (m n) -> p m n", n=P), ACT.Copy).then_inc(pT_ready.sem, 1)

            @block.vector
            def _(v):
                v.wait_ge(q_loaded.sem, q_loaded.at(1))
                v.wait_ge(zeroed.sem, zeroed.at(1))
                with v.Fori(0, SEQS // 4) as i:
                    vec.n = 0
                    for h in range(H):
                        op = nc.vector.tensor_copy(qm[:, 2 * h:2 * h + 2, :, h, :],
                                                   q[:, 2 * h:2 * h + 2, bass.ds(i * (4 * STEPS), 4 * STEPS)].rearrange("p k (b n) -> p k b n", n=STEPS))
                    op.then_inc(masked.sem, 1)
                    v.wait_ge(scores.sem, scores.at(1, i))
                    nc.vector.tensor_reduce(top[:, :], bank[0][:, 0:MEM], AX.X, ALU.max).then_inc(vec.step(), 1)
                    v.wait_ge(vec.sem, vec.now(i))
                    nc.vector.tensor_scalar(neg[:, :], top[:, :], -SC, None, ALU.mult).then_inc(top_ready.sem, 1)
                    v.wait_ge(exped.sem, exped.at(1, i))
                    nc.vector.reciprocal(inv[:, :], total[:, :]).then_inc(vec.step(), 1)
                    v.wait_ge(vec.sem, vec.now(i))
                    nc.vector.tensor_scalar(pr[:, :], pr[:, :], inv[:, 0:1], None, ALU.mult).then_inc(probs.sem, 1)
                    v.wait_ge(product.sem, product.at(1, i))
                    for half in range(2):
                        op = nc.vector.tensor_copy(rows[:, 512 * half:512 * half + 512], bank[4 + half][:, :])
                    op.then_inc(rows_ready.sem, 1)
                    v.wait_ge(rows_turned.sem, rows_turned.at(1, i))
                    for h in range(H):
                        own = bank[6 + h // 2][:, 2 * P * (h % 2):2 * P * (h % 2) + 2 * P].rearrange("p (k b r) -> p k b r", k=2, r=R)
                        op = nc.vector.tensor_copy(
                            ao[:, 2 * h:2 * h + 2, bass.ds(i * (4 * STEPS) + SEQ, 4 * STEPS)].rearrange("p k (b n) -> p k b n", n=STEPS),
                            own[:, :, :, STEPS * h:STEPS * h + STEPS])
                    op.then_inc(taken.sem, 1)


def route(nc, bank, const, d, qp, gd, stored, room):
    PH, TK, NK = PHEADS, TOPK, NKEYS
    LOW = -3.0e38
    buffers = []
    PICK, GROUPS = 4, 4
    BANKS = (bank[5], bank[6], bank[7], bank[4])
    LAST = NC - 1
    with Phase(nc) as ctx:
        def sb(name, shape, dt=F32):
            buffers.append(ctx.enter_context(nc.sbuf_tensor(f"route_{name}", shape, dt)))
            return buffers[-1]

        def signal(name, per=1, unit=1, primed=False):
            return Signal(nc, ctx, f"route_{name}", per, unit, primed)
        keys, iota = sb("keys", [P, 2, NK]), sb("iota", [P, NK])
        q, s, s2 = sb("q", [P, 2 * PH, P]), sb("scores", [P, 2 * PH, NK]), sb("scores_left", [P, 2 * PH, NK])
        top, ix = sb("top", [P, 2 * PH, TK]), sb("top_index", [P, 2 * PH, TK], U32)
        ixf = sb("top_index_f", [P, 2 * PH, TK])
        cand, cand2 = sb("sums", [P, PH, TK, TK]), sb("sums_left", [P, PH, TK * TK])
        best, pos = sb("best", [P, PH, TK]), sb("position", [P, PH, TK], U32)
        half, halff = sb("rank", [P, 2, PH * TK], U32), sb("rank_f", [P, 2, PH * TK])
        total, blank = sb("total", [P, PH]), sb("blank", [P, 1])
        gate = sb("picked_gates", [P, P])
        pickT = sb("picks_t", [P, 3, P])
        terms = (cand[:, :, :, :].rearrange("p h a b -> p (h a b)"), cand2[:, :, :].rearrange("p h n -> p (h n)"))
        E = [sb(f"onehots{r}", [P, 2, PICK, NK]) for r in range(GROUPS)]
        used = 4 * sum(int(np.prod(x.shape[1:])) for x in buffers)
        sb("room", [P, -(-max(room - used, 0) // 4)])
        G = sb("gates", [P, NK, P])
        once, loaded = signal("keys_loaded", 2, 16), signal("loaded", 1, 16)
        scored, s_ready = signal("scored"), signal("scores_ready", 1)
        shifted, exped = signal("shifted"), signal("exp_ready")
        terms_ready, picked = signal("key_terms_ready", 2), signal("gates_picked")
        turned, pickT_ready = signal("turned"), signal("picks_t_ready")
        onehots = [signal(f"onehots_ready{r}") for r in range(GROUPS)]
        weighted = [signal(f"gated_onehots_ready{r}") for r in range(GROUPS)]
        gmm = [signal(f"gates_product{r}", 1, 1, True) for r in range(GROUPS)]
        gout = [signal(f"gates_taken{r}", 1, 1, True) for r in range(GROUPS)]
        halves_found, sums_found = signal("halves_found"), signal("sums_found")
        VSTEPS, HSTEPS = 7, 3
        vec, hvec = Steps(nc, ctx, "route_vector_steps", VSTEPS), Steps(nc, ctx, "route_halves_steps", HSTEPS)
        TURNS = P // (GROUPS * PICK)
        LAST_TURNS = SAMPLE // (GROUPS * PICK)

        with nc.Block() as block:
            @block.sync
            def _(sp):
                sp.dma_start(keys[:, :, :], d["keysT"]).then_inc(once.sem, 16)
                sp.dma_start(iota[:, :], d["iota"].partition_broadcast(P)).then_inc(once.sem, 16)

                def load_q(i):
                    sp.dma_start(q[:, :, :], qp[:, :, bass.ds(i * P, P)].rearrange("k p n -> p k n")).then_inc(loaded.sem, 16)

                def store(i, turns):
                    for r in range(GROUPS):
                        sp.wait_ge(gout[r].sem, gout[r].at(1, i * TURNS + (turns - 1)))
                    n = turns * GROUPS * PICK
                    sp.dma_start(gd[:, :, bass.ds(i * P, n)].rearrange("j i n -> i j n"), G[:, :, 0:n]).then_inc(stored.sem, 16)
                load_q(0)
                sp.wait_ge(scored.sem, scored.at(1))
                load_q(1)
                with sp.Fori(0, LAST - 1) as i:
                    sp.wait_ge(scored.sem, scored.at(1, i + 1))
                    load_q(i + 2)
                    store(i, TURNS)
                store(LAST - 1, TURNS)
                store(LAST, LAST_TURNS)

            @block.tensor
            def _(pe):
                def scores(i):
                    pe.wait_ge(loaded.sem, loaded.at(1, i))
                    for n in range(2 * PH):
                        mm = nc.tensor.matmul(bank[n // 4][:, P * (n % 4):P * (n % 4) + P], q[:, n, :], keys[:, n % 2, :], start=True, stop=True)
                    mm.then_inc(scored.sem, 1)

                def turn_picks(i):
                    pe.wait_ge(gout[3].sem, gout[3].at(1, i * TURNS - 1))
                    for x in range(2):
                        pe.wait_ge(terms_ready.sem, terms_ready.at(x + 1, i))
                        for n in range(TK):
                            nc.tensor.matmul(bank[4][:, P * x + P:P * x + 2 * P], terms[x][:, P * n:P * n + P], const["ident"][:, :],
                                             start=(n == 0), stop=(n == TK - 1))
                    pe.wait_ge(picked.sem, picked.at(1, i))
                    nc.tensor.transpose(bank[4][:, 0:P], gate[:, :], const["ident"][:, :]).then_inc(turned.sem, 1)

                def products(i, turns):
                    with pe.Fori(0, turns) as j:
                        w = i * TURNS + j
                        for r in range(GROUPS):
                            pe.wait_ge(weighted[r].sem, weighted[r].at(1, w))
                            pe.wait_ge(gout[r].sem, gout[r].at(1, w - 1))
                            for t in range(PICK):
                                mm = nc.tensor.matmul(BANKS[r][:, P * t:P * t + P], E[r][:, 0, t, :], E[r][:, 1, t, :], start=True, stop=True)
                            mm.then_inc(gmm[r].sem, 1)
                pe.wait_ge(once.sem, once.at(2))
                scores(0)
                with pe.Fori(0, LAST) as i:
                    pe.wait_ge(s_ready.sem, s_ready.at(1, i))
                    scores(i + 1)
                    turn_picks(i)
                    products(i, TURNS)
                turn_picks(LAST)
                products(LAST, LAST_TURNS)

            @block.scalar
            def _(act):
                act.sem_inc(stored.sem, 16)
                for r in range(GROUPS):
                    act.sem_inc(gmm[r].sem, 1)
                    act.sem_inc(gout[r].sem, 1)

                def take_scores(i):
                    act.wait_ge(scored.sem, scored.at(1, i))
                    for b in range(4):
                        op = nc.scalar.activation(s[:, 4 * b:4 * b + 4, :], bank[b][:, :].rearrange("p (n k) -> p n k", k=NK), ACT.Copy)
                    op.then_inc(s_ready.sem, 1)

                def exp_and_picks(i):
                    act.wait_ge(shifted.sem, shifted.at(1, i))
                    nc.scalar.activation(best[:, :, :], best[:, :, :], ACT.Exp).then_inc(exped.sem, 1)
                    act.wait_ge(turned.sem, turned.at(1, i))
                    nc.scalar.activation(pickT[:, :, :], bank[4][:, 0:3 * P].rearrange("p (x n) -> p x n", n=P), ACT.Copy).then_inc(pickT_ready.sem, 1)

                def take_gates(i, turns):
                    with act.Fori(0, turns) as j:
                        w = i * TURNS + j
                        for r in range(GROUPS):
                            act.wait_ge(stored.sem, stored.at(1, i - 1))
                            act.wait_ge(gmm[r].sem, gmm[r].at(1, w))
                            nc.scalar.activation(G[:, :, bass.ds(j * (GROUPS * PICK) + PICK * r, PICK)].rearrange("p j n -> p n j"),
                                                 BANKS[r][:, :].rearrange("p (n j) -> p n j", j=NK), ACT.Copy).then_inc(gout[r].sem, 1)
                take_scores(0)
                with act.Fori(0, LAST) as i:
                    act.wait_ge(halves_found.sem, halves_found.at(1, i))
                    take_scores(i + 1)
                    exp_and_picks(i)
                    take_gates(i, TURNS)
                exp_and_picks(LAST)
                take_gates(LAST, LAST_TURNS)

            @block.gpsimd
            def _(pool):
                def weight(i, turns):
                    with pool.Fori(0, turns) as j:
                        w = i * TURNS + j
                        for r in range(GROUPS):
                            pool.wait_ge(onehots[r].sem, onehots[r].at(1, w))
                            at = bass.ds(j * (GROUPS * PICK) + PICK * r, PICK)
                            nc.gpsimd.tensor_tensor(E[r][:, 1, :, :], E[r][:, 1, :, :],
                                                    pickT[:, 0, at][:, :, None].to_broadcast([P, PICK, NK]), ALU.mult).then_inc(weighted[r].sem, 1)
                with pool.Fori(0, LAST) as i:
                    weight(i, TURNS)
                weight(LAST, LAST_TURNS)

            @block.vector
            def _(v):
                def then(op, steps, i):
                    op.then_inc(steps.step(), 1)
                    v.wait_ge(steps.sem, steps.now(i))

                def settled(op, steps, i):
                    then(op, steps, i)
                    nc.vector.memset(blank[:, :], 0.0)

                def top16(rows, values, left, at, index, steps, i, found):
                    settled([nc.vector.max(at(n)[:, 0:8], values(n)) for n in range(rows)][-1], steps, i)
                    for n in range(rows):
                        nc.vector.max_index(index(n)[:, 0:8], at(n)[:, 0:8], values(n))
                        op = nc.vector.match_replace(left(n), at(n)[:, 0:8], values(n), LOW)
                    settled(op, steps, i)
                    settled([nc.vector.max(at(n)[:, 8:16], left(n)) for n in range(rows)][-1], steps, i)
                    [nc.vector.max_index(index(n)[:, 8:16], at(n)[:, 8:16], left(n)) for n in range(rows)][-1].then_inc(found.sem, 1)

                def search_halves(i):
                    hvec.n = 0
                    v.wait_ge(s_ready.sem, s_ready.at(1, i))
                    nc.vector.memset(blank[:, :], 0.0)
                    top16(2 * PH, lambda n: s[:, n, :], lambda n: s2[:, n, :], lambda n: top[:, n, :], lambda n: ix[:, n, :],
                          hvec, i, halves_found)
                    assert hvec.n == HSTEPS, hvec.n

                def search_sums(i):
                    vec.n = 0
                    v.wait_ge(halves_found.sem, halves_found.at(1, i))
                    halves = top[:, :, :].rearrange("p (h c) k -> p h c k", c=2)
                    for h in range(PH):
                        op = nc.vector.tensor_tensor(cand[:, h, :, :], halves[:, h, 0, :, None].to_broadcast([P, TK, TK]),
                                                     halves[:, h, 1, None, :].to_broadcast([P, TK, TK]), ALU.add)
                    settled(op, vec, i)
                    flat = cand[:, :, :, :].rearrange("p h a b -> p h (a b)")
                    top16(PH, lambda n: flat[:, n, :], lambda n: cand2[:, n, :], lambda n: best[:, n, :], lambda n: pos[:, n, :],
                          vec, i, sums_found)
                    v.wait_ge(sums_found.sem, sums_found.at(1, i))
                    flatpos = pos[:, :, :].rearrange("p h k -> p (h k)")
                    nc.vector.tensor_scalar(half[:, 0, :], flatpos, 4, None, ALU.logical_shift_right)
                    nc.vector.tensor_scalar(half[:, 1, :], flatpos, 15, None, ALU.bitwise_and)
                    nc.vector.tensor_copy(ixf[:, :, :], ix[:, :, :])
                    then(nc.vector.tensor_copy(total[:, :], best[:, :, 0]), vec, i)
                    nc.vector.tensor_copy(halff[:, :, :], half[:, :, :])
                    nc.vector.tensor_tensor(best[:, :, :], best[:, :, :], total[:, :, None].to_broadcast([P, PH, TK]),
                                            ALU.subtract).then_inc(shifted.sem, 1)
                    v.wait_ge(shifted.sem, shifted.at(1, i))
                    index = ixf[:, :, :].rearrange("p (h c) k -> p h c k", c=2)
                    for c in range(2):
                        for n in range(TK):
                            op = nc.vector.scalar_tensor_tensor(terms[c][:, P * n:P * n + P].rearrange("p (h k) -> p h k", k=TK),
                                                                halff[:, c, :].rearrange("p (h k) -> p h k", k=TK), float(n),
                                                                index[:, :, c, n:n + 1].to_broadcast([P, PH, TK]), ALU.is_equal, ALU.mult)
                        op.then_inc(terms_ready.sem, 1)
                    v.wait_ge(exped.sem, exped.at(1, i))
                    then(nc.vector.tensor_reduce(total[:, :], best[:, :, :], AX.X, ALU.add), vec, i)
                    then(nc.vector.reciprocal(total[:, :], total[:, :]), vec, i)
                    nc.vector.tensor_tensor(gate[:, :].rearrange("p (h k) -> p h k", k=TK), best[:, :, :],
                                            total[:, :, None].to_broadcast([P, PH, TK]), ALU.mult).then_inc(picked.sem, 1)
                    assert vec.n == VSTEPS, vec.n

                def make_onehots(i, turns):
                    with v.Fori(0, turns) as j:
                        w = i * TURNS + j
                        for r in range(GROUPS):
                            v.wait_ge(pickT_ready.sem, pickT_ready.at(1, i))
                            v.wait_ge(gmm[r].sem, gmm[r].at(1, w - 1))
                            at = bass.ds(j * (GROUPS * PICK) + PICK * r, PICK)
                            nc.vector.tensor_tensor(E[r][:, :, :, :], iota[:, None, None, :].to_broadcast([P, 2, PICK, NK]),
                                                    pickT[:, 1:3, at][:, :, :, None].to_broadcast([P, 2, PICK, NK]),
                                                    ALU.is_equal).then_inc(onehots[r].sem, 1)
                v.wait_ge(once.sem, once.at(2))
                search_halves(0)
                with v.Fori(0, LAST) as i:
                    search_sums(i)
                    search_halves(i + 1)
                    make_onehots(i, TURNS)
                search_sums(LAST)
                make_onehots(LAST, LAST_TURNS)


def experts(nc, bank, const, d, gd, fn, h):
    GROUP = 4
    M = 3 * GROUP
    O = 3 * KT
    TURNS = NKEYS // GROUP
    ORDER = [("v", 0, 0), ("u", 2, 0), ("v", 1, 0), ("u", 3, 0), ("v", 2, 0), ("v", 3, 0), ("u", 0, 1), ("u", 1, 1)]
    PLACE = {(x, j): n + 3 - 8 * ahead for n, (x, j, ahead) in enumerate(ORDER)}
    with Phase(nc) as ctx:
        def sb(name, shape, dt=F32):
            return ctx.enter_context(nc.sbuf_tensor(f"exp_{name}", shape, dt))

        def signal(name, per=1, unit=1, primed=False):
            return Signal(nc, ctx, f"exp_{name}", per, unit, primed)
        stage = sb("stage", [P, 2, D_MODEL])
        Uh, Ul = sb("u_hi", [P, 2, KT, P], F32R), sb("u_lo", [P, 2, KT, P], F32R)
        Vh, Vl = sb("v_hi", [P, GROUP, D_MODEL], F32R), sb("v_lo", [P, GROUP, D_MODEL], F32R)
        Ah, Al = sb("hidden_hi", [P, GROUP, T], F32R), sb("hidden_lo", [P, GROUP, T], F32R)
        G, act_t, zero = sb("gates", [P, 4, 384]), sb("gelu", [P, 3, 384]), sb("zero", [P, 1])
        zeroed = signal("zeroed")
        loaded = [signal(f"loaded{r}", 4, 16) for r in range(2)]
        hi_done, split = signal("w_hi_done", 8), signal("w_split", 8)
        g_loaded = [signal(f"gates_loaded{r}", M // 4, 16) for r in range(4)]
        hidden = signal("hidden_product", M)
        gelu, gated = signal("gelu_ready", M), signal("gated", M)
        ah_ready, al_ready = signal("hidden_hi_ready", M), signal("hidden_lo_ready", M)
        product, added = signal("product", O, 1, True), signal("added", O, 1, True)

        def earlier(sig, n, back, turn):
            if n > back:
                return sig.at(n - back, turn)
            return None if isinstance(turn, int) and turn == 0 else sig.at(n - back + sig.per, turn - 1)

        def by_turns(engine, first, body):
            first(0)
            with engine.Fori(0, TURNS - 1) as i:
                body(i, False)
            body(TURNS - 1, True)

        with nc.Block() as block:
            @block.sync
            def _(sp):
                def fetch(x, j, turn):
                    r = (PLACE[x, j] + 1) % 2
                    free = earlier(split, PLACE[x, j], 2, turn)
                    if free is not None:
                        sp.wait_ge(split.sem, free)
                    src = row_of(d[f"peer_{x}"], turn * GROUP + j)
                    if x == "u":
                        src = src.rearrange("p k n -> p (k n)")
                    sp.dma_start(stage[:, r, :], src).then_inc(loaded[r].sem, 16)

                def first(turn):
                    fetch("u", 0, 0)
                    fetch("u", 1, 0)

                def body(turn, last):
                    for x, j, ahead in ORDER:
                        if not (last and ahead):
                            fetch(x, j, turn + ahead)
                by_turns(sp, first, body)

            @block.gpsimd
            def _(pool):
                def take(x, j, turn):
                    n = PLACE[x, j]
                    r = (n + 1) % 2
                    waits = [(loaded[r], loaded[r].at((n + 1) // 2, turn))]
                    if x == "v":
                        hi, lo = Vh[:, j:j + 1, :], Vl[:, j:j + 1, :]
                        waits.append((product, product.at(O, turn - 1)))
                        src = stage[:, r:r + 1, :]
                    else:
                        hi, lo = Uh[:, j % 2, :, :], Ul[:, j % 2, :, :]
                        src = stage[:, r, :].rearrange("p (k n) -> p k n", n=P)
                        used = earlier(hidden, 3 * j + 3, 6, turn)
                        if used is not None:
                            waits.append((hidden, used))
                    split_weights(nc, pool, zero, src, hi, lo, waits, hi_done, split, hi_done.at(n, turn))

                def first(turn):
                    nc.gpsimd.memset(zero[:, :], 0.0).then_inc(zeroed.sem, 1)
                    pool.sem_inc(product.sem, O)
                    pool.sem_inc(added.sem, O)
                    pool.wait_ge(zeroed.sem, 1)
                    take("u", 0, 0)
                    take("u", 1, 0)

                def body(turn, last):
                    for x, j, ahead in ORDER:
                        if not (last and ahead):
                            take(x, j, turn + ahead)
                by_turns(pool, first, body)

            @block.tensor
            def _(pe):
                def hidden_tile(j, turn):
                    pe.wait_ge(split.sem, split.at(PLACE["u", j], turn))
                    for c, (a, n) in enumerate(CHUNKS):
                        m = 3 * j + c
                        free = gelu.at(1, turn) if m == 3 else earlier(gelu, m + 1, 4, turn)
                        if free is not None:
                            pe.wait_ge(gelu.sem, free)
                        for k in range(KT):
                            mm = split_product(nc, bank[m % 4][:, 0:n], (Uh[:, j % 2, k, :], Ul[:, j % 2, k, :]),
                                               [x[:, k, a:a + n] for x in fn], k == 0, k == KT - 1)
                        mm.then_inc(hidden.sem, 1)

                def body(turn, last):
                    for j in range(1, GROUP):
                        hidden_tile(j, turn)
                    if not last:
                        hidden_tile(0, turn + 1)
                    pe.wait_ge(split.sem, split.at(PLACE["v", GROUP - 1], turn))
                    pe.wait_ge(al_ready.sem, al_ready.at(M, turn))
                    for k in range(KT):
                        for c, (a, n) in enumerate(CHUNKS):
                            m = 3 * k + c
                            pe.wait_ge(added.sem, added.at(m - 3, turn) if m >= 4 else added.at(O - 3 + m, turn - 1))
                            for j in range(GROUP):
                                s = slice(P * k, P * k + P)
                                mm = split_product(nc, bank[4 + m % 4][:, 0:n], (Vh[:, j, s], Vl[:, j, s]),
                                                   (Ah[:, j, a:a + n], Al[:, j, a:a + n]), j == 0, j == GROUP - 1)
                            mm.then_inc(product.sem, 1)
                by_turns(pe, lambda turn: hidden_tile(0, 0), body)

            @block.scalar
            def _(act):
                def fetch_gates(m, turn):
                    j, c = divmod(m, 3)
                    a, n = CHUNKS[c]
                    act.dma_start(G[:, m % 4, 0:n], row_of(gd, turn * GROUP + j)[:, a:a + n]).then_inc(g_loaded[m % 4].sem, 16)

                def activate(m, turn):
                    n = CHUNKS[m % 3][1]
                    act.wait_ge(hidden.sem, hidden.at(m + 1, turn))
                    free = earlier(al_ready, m + 1, 3, turn)
                    if free is not None:
                        act.wait_ge(al_ready.sem, free)
                    nc.scalar.activation(act_t[:, m % 3, 0:n], bank[m % 4][:, 0:n], ACT.Gelu).then_inc(gelu.sem, 1)

                def high(m, turn, last):
                    a, n = CHUNKS[m % 3]
                    act.wait_ge(product.sem, product.at(O, turn - 1))
                    act.wait_ge(gated.sem, gated.at(m + 1, turn))
                    nc.scalar.activation(Ah[:, m // 3, a:a + n], act_t[:, m % 3, 0:n], ACT.Copy).then_inc(ah_ready.sem, 1)
                    if m + 4 < M:
                        fetch_gates(m + 4, turn)
                    elif not last:
                        fetch_gates(m + 4 - M, turn + 1)

                def first(turn):
                    for m in range(4):
                        fetch_gates(m, 0)
                    act.wait_ge(zeroed.sem, 1)
                    for m in range(3):
                        activate(m, 0)

                def body(turn, last):
                    for m in range(3):
                        high(m, turn, last)
                    for m in range(3, M):
                        activate(m, turn)
                        if m > 3:
                            high(m - 1, turn, last)
                    if not last:
                        activate(0, turn + 1)
                    high(M - 1, turn, last)
                    if not last:
                        activate(1, turn + 1)
                        activate(2, turn + 1)
                by_turns(act, first, body)

            @block.vector
            def _(v):
                def gate(m, turn):
                    n = CHUNKS[m % 3][1]
                    v.wait_ge(gelu.sem, gelu.at(m + 1, turn))
                    v.wait_ge(g_loaded[m % 4].sem, g_loaded[m % 4].at(m // 4 + 1, turn))
                    nc.vector.tensor_tensor(act_t[:, m % 3, 0:n], act_t[:, m % 3, 0:n], G[:, m % 4, 0:n], ALU.mult).then_inc(gated.sem, 1)

                def low(m, turn):
                    a, n = CHUNKS[m % 3]
                    v.wait_ge(ah_ready.sem, ah_ready.at(m + 1, turn))
                    nc.vector.tensor_tensor(Al[:, m // 3, a:a + n], act_t[:, m % 3, 0:n],
                                            Ah[:, m // 3, a:a + n].bitcast(F32), ALU.subtract).then_inc(al_ready.sem, 1)

                def first(turn):
                    for m in range(3):
                        gate(m, 0)

                def body(turn, last):
                    for m in range(3):
                        low(m, turn)
                    for m in range(3, M):
                        gate(m, turn)
                        if m > 3:
                            low(m - 1, turn)
                    low(M - 1, turn)
                    if not last:
                        for m in range(3):
                            gate(m, turn + 1)
                    v.wait_ge(added.sem, added.at(O, turn - 1))
                    for k in range(KT):
                        for c, (a, n) in enumerate(CHUNKS):
                            m = 3 * k + c
                            v.wait_ge(product.sem, product.at(m + 1, turn))
                            nc.vector.tensor_tensor(h[:, k, a:a + n], h[:, k, a:a + n], bank[4 + m % 4][:, 0:n], ALU.add).then_inc(added.sem, 1)
                by_turns(v, first, body)


def trunk(nc, d, out):
    with Phase(nc) as ctx:
        bank = psum_banks(nc, ctx, "psum")
        mix = nc.dram_tensor("mixed_heads", (2 * KT, P, T), F32, kind="Internal").ap()
        const = {n: ctx.enter_context(nc.sbuf_tensor(f"const_{n}", s, F32)) for n, s in (
            ("ident", [P, P]), ("ones", [P, P]), ("gains", [P, 5, KT]))}
        eps = const["eps"] = ctx.enter_context(nc.sbuf_tensor("const_eps", [P, 1], F32))
        names = [n for n in const if n != "eps"]
        loaded = Signal(nc, ctx, "setup_loaded", 1, 16)
        with Phase(nc) as mixer:
            def sb(name, shape):
                return mixer.enter_context(nc.sbuf_tensor(name, shape, F32))
            xn = sb("x_normed", [P, KT, TP])
            tab = sb("gate_table", [P, 5, NC, GATED])
            for n, shape in (("incl", [P, TP]), ("tri", [P, 2, P]), ("total", [P, 2, P]), ("seq_of", [P, SEQS])):
                const[n] = sb(f"const_{n}", shape)
                names.append(n)
            with Phase(nc) as first:
                x = first.enter_context(nc.sbuf_tensor("x_in", [P, KT, T], F32))
                ws = first.enter_context(nc.sbuf_tensor("w_small", [P, KT, 32], F32))
                with nc.Block() as block:
                    @block.sync
                    def _(sp):
                        for n in names:
                            sp.dma_start(const[n].ap() if hasattr(const[n], "ap") else const[n], d[n]).then_inc(loaded.sem, 16)
                        for k in range(KT):
                            sp.dma_start(x[:, k, :], d["xT"][k]).then_inc(loaded.sem, 16)
                        sp.dma_start(ws[:, :, :], d["w_small"]).then_inc(loaded.sem, 16)
                        sp.wait_ge(loaded.sem, loaded.at(len(names) + KT + 1))

                    @block.vector
                    def _(v):
                        nc.vector.memset(eps[:, :], EPS)
                        nc.vector.memset(xn[:, :, T:TP], 0.0)
                rmsnorm(nc, bank, "mix_norm", x, xn, const["gains"][:, 0, :], const["ident"][:, :], const["ones"][:, :], T, D_MODEL)
                gates(nc, bank, xn, ws, const["ident"], const["tri"], const["total"], d, tab)
            delta_net(nc, bank, xn, tab, d, const, mix, out)
            ssd(nc, bank, xn, tab, d, const, mix, out)
        h = ctx.enter_context(nc.sbuf_tensor("residual", [P, KT, T], F32))
        with Phase(nc) as part:
            heads = part.enter_context(nc.sbuf_tensor("heads", [P, KT, T], F32))
            parts = split_pair(nc, part, "heads")
            loaded = [[Signal(nc, part, f"heads_{x}_loaded{k}", 1, 16) for k in range(KT)] for x in ("dn", "ssm")]
            h_loaded = Signal(nc, part, "residual_loaded", KT, 16)
            dn_loads, ssm_loads = ([(heads[:, k, :], mix[KT * x + k], loaded[x][k]) for k in range(KT)] for x in range(2))
            h_loads = [(h[:, k, :], d["xT"][k], h_loaded) for k in range(KT)]
            split_tiles(nc, "heads_dn", heads, *parts, KT, loaded=loaded[0], loads=dn_loads + h_loads)
            linear(nc, bank, "w_heads_dn", parts, d["w_heads_dn"], KT, KT, T, "add", h, prefetch=ssm_loads,
                   behind=(h_loaded.sem, h_loaded.at(KT)))
            split_tiles(nc, "heads_ssm", heads, *parts, KT, loaded=loaded[1])
            linear(nc, bank, "w_heads_ssm", parts, d["w_heads_ssm"], KT, KT, T, "add", h)
        with Phase(nc) as part:
            mkT = part.enter_context(nc.sbuf_tensor("mem_keys", [P, KT, MEM], F32))
            mv = part.enter_context(nc.sbuf_tensor("mem_values", [P, 2, D_MODEL], F32))
            qx = nc.dram_tensor("attention_q", (KT, P, T), F32, kind="Internal").ap()
            memory_kv(nc, bank, const, d, out, mkT, mv)
            with Phase(nc) as inner:
                cn = split_pair(nc, inner, "c_normed")
                rmsnorm(nc, bank, "att_norm", h, cn, const["gains"][:, 1, :], const["ident"][:, :], const["ones"][:, :], T, D_MODEL)
                linear(nc, bank, "w_xq", cn, d["w_xq"], KT, KT, T, "store", qx)
            ao = part.enter_context(nc.sbuf_tensor("attended", [P, KT, T], F32))
            with Phase(nc) as inner:
                cache = Cache(nc, inner, d)
                attend_prompt(nc, bank, const, d, qx, mkT, mv, ao, cache)
                attend_sample(nc, bank, const, d, qx, ao, cache)
            parts = split_pair(nc, part, "attended")
            split_tiles(nc, "attended", ao, *parts, KT)
            linear(nc, bank, "w_xo", parts, d["w_xo"], KT, KT, T, "add", h)
        with Phase(nc) as part:
            qp = nc.dram_tensor("retrieval_q", (2 * PHEADS, P, TP), F32, kind="Internal").ap()
            gd = nc.dram_tensor("expert_gates", (NKEYS, P, TP), F32, kind="Internal").ap()
            rstd = part.enter_context(nc.sbuf_tensor("ffn_rstd", [P, NC], F32))
            with Phase(nc) as inner:
                fn = split_pair(nc, inner, "f_normed")
                rmsnorm(nc, bank, "ffn_norm", h, fn, const["gains"][:, 3, :], const["ident"][:, :], const["ones"][:, :], T, D_MODEL,
                        kept=rstd)
                linear(nc, bank, "w_pq", fn, d["w_pq"], KT, 2 * PHEADS, T, "store", qp)
            gates_stored = Signal(nc, part, "gates_stored", 1, 16, True)
            norm_room = (2 * KT * T + KT * TP + 8) * 4
            route(nc, bank, const, d, qp, gd, gates_stored, norm_room)
            fn = split_pair(nc, part, "e_normed")
            rmsnorm(nc, bank, "exp_norm", h, fn, const["gains"][:, 3, :], const["ident"][:, :], const["ones"][:, :], T, D_MODEL,
                    kept=rstd, again=True, behind=(gates_stored.sem, gates_stored.at(1, NC - 1)))
            experts(nc, bank, const, d, gd, fn, h)
        with Phase(nc) as part:
            y = part.enter_context(nc.sbuf_tensor("y_out", [P, KT, T], F32))
            rmsnorm(nc, bank, "final_norm", h, y, const["gains"][:, 4, :], const["ident"][:, :], const["ones"][:, :], T, D_MODEL,
                    store=out["y"])


def layouts(i):
    f = lambda a: np.ascontiguousarray(a)
    tiles = lambda a, k: a.reshape(k, P, -1).transpose(1, 0, 2)
    w_in = i["w_in"][0]
    qkv, xbc, z_dn, z_ssm, small = np.split(w_in, np.cumsum([3072, 1536, 1024, 1024]), axis=1)
    d = {}
    x = np.concatenate([i["x_prompt"][0], i["x_sample"].reshape(SAMPLE, D_MODEL)])
    d["xT"] = f(x.T.reshape(KT, P, T))
    d["w_small"] = f(tiles(small, KT))
    d["gate_bias"] = f(np.concatenate([i["dn_dt_bias"][0], i["ssm_dt_bias"][0]]))
    d["gate_rate"] = f(np.concatenate([i["dn_A_log"][0], i["ssm_A_log"][0]]))
    col = lambda a: a.reshape(KT, P).T
    d["gains"] = f(np.stack([col(a) for a in (i["g_mix"][0], i["g_xattn"][0], i["g_mem"][0], i["g_ffn"][0], i["g_final"])], 1))
    w = np.concatenate([qkv, z_dn], 1).reshape(KT, P, 4, DN_HEADS, P)
    d["w_dn"] = f(w.transpose(3, 1, 0, 2, 4))
    d["dn_conv_w"] = f(i["dn_conv_w"][0].reshape(CONV, 3, DN_HEADS, P).transpose(2, 3, 1, 0))
    d["dn_hist"] = f(i["state_dn_conv"][0].reshape(SEQS, 3, 3, DN_HEADS, P).transpose(3, 4, 2, 0, 1))
    d["dn_s0"] = f(i["state_dn"][0].transpose(1, 2, 0, 3))
    d["dn_norm_w"] = f(i["dn_norm_w"][0].reshape(P, 1))
    wx, wb, wc = np.split(xbc, [1024, 1280], axis=1)
    d["w_bc"] = f(np.stack([wb, wc], 1).reshape(KT, P, 2, SSM_GROUPS, P).transpose(3, 1, 0, 2, 4))
    d["w_xz"] = f(np.stack([wx, z_ssm], 1).reshape(KT, P, 2, PAIRS, P).transpose(3, 1, 0, 2, 4))
    channels = np.concatenate([i["state_ssm_conv"][0].transpose(2, 0, 1).reshape(-1, 3 * SEQS), i["ssm_conv_w"][0].T,
                               i["ssm_conv_b"][0][:, None]], 1)
    d["ssm_small_x"] = f(channels[:1024].reshape(PAIRS, P, -1))
    d["ssm_small_bc"] = f(channels[1024:].reshape(2, SSM_GROUPS, P, -1).transpose(1, 2, 0, 3))
    d["ssm_skip"] = f(np.repeat(i["ssm_D"][0], HALF).reshape(PAIRS, P).T)
    d["ssm_s0"] = f(i["state_ssm"][0].reshape(SEQS, PAIRS, P, P).transpose(1, 3, 0, 2))
    d["ssm_norm_w"] = f(i["ssm_norm_w"][0].reshape(PAIRS, P).T)
    by_out = lambda a, k: f(a.reshape(k, P, -1, P).transpose(2, 1, 0, 3))
    d["w_heads_dn"], d["w_heads_ssm"] = (by_out(w, KT) for w in np.split(i["w_out"][0], 2))
    d["w_xq"], d["w_xo"], d["w_pq"] = (by_out(i[n][0], KT) for n in ("w_xq", "w_xo", "w_pq"))
    d["w_mk"] = by_out(i["w_mkv"][0][:, :D_MODEL], KT)
    d["w_mv"] = f(tiles(i["w_mkv"][0][:, D_MODEL:], KT))
    d["memT"] = f(tiles(i["mem_prompt"][0].T, KT))
    d["cache_k"] = f(i["cache_mem_k"][0].reshape(SEQS, MEM, KT, P).transpose(0, 3, 2, 1))
    d["cache_v"] = f(i["cache_mem_v"][0].reshape(SEQS, 2, P, D_MODEL).transpose(0, 2, 1, 3))
    d["keysT"] = f(i["peer_sub_keys"][0].transpose(2, 0, 1))
    d["peer_u"] = f(i["peer_u"][0].reshape(NKEYS, NKEYS, KT, P).transpose(1, 3, 2, 0))
    d["peer_v"] = f(i["peer_v"][0].reshape(NKEYS, NKEYS, D_MODEL).transpose(1, 0, 2))
    return d


def shape_constants():
    j, i = np.arange(P)[:, None], np.arange(P)[None, :]
    seq = np.where(np.arange(P) < SAMPLE, np.arange(P) // STEPS, -1 - np.arange(P))
    same = seq[:, None] == seq[None, :]
    d = {"ident": np.eye(P), "ones": np.ones((P, P)), "tri": np.stack([j <= i, (j <= i) & same], 1),
         "total": np.stack([same | True, same], 1)}
    d["seq_of"] = seq[:, None] == np.arange(SEQS)[None, :]
    for name, m in (("incl", j <= i), ("strict", j < i)):
        d[name] = np.concatenate([np.tile(m, (1, NC - 1)), m & same], 1)
    d["iota"] = np.arange(P)
    s = 2 ** np.arange(7)[:, None, None]
    d["level"] = ((i // (2 * s) == j // (2 * s)) & (i // s % 2 == 1) & (j // s % 2 == 0)).transpose(1, 0, 2)
    return {k: np.ascontiguousarray(v, dtype=np.float32) for k, v in d.items()}


OUTS = {"dn_conv": (DN_HEADS, P, 3, SEQS + 1, 3), "dn_p": (DN_HEADS, P, P), "dn_s": (DN_HEADS, P, SEQS, P),
        "ssm_conv_x": (PAIRS, P, SEQS + 1, 3), "ssm_conv_bc": (SSM_GROUPS, P, 2, SEQS + 1, 3),
        "mem_k": (P, KT, MEM), "mem_v": (P, 2, D_MODEL), "y": (KT, P, T),
        "ssm_p": (PAIRS, P, P), "ssm_s": (PAIRS, P, SEQS, P)}


def kernel(**inputs):
    import concourse.bacc as bacc
    from concourse.bass_utils import run_bass_kernel_spmd

    arrays = layouts({k: np.asarray(v) for k, v in inputs.items()}) | shape_constants()
    nc = bacc.Bacc("TRN2", target_bir_lowering=False, num_devices=1)
    d = {k: nc.dram_tensor(f"in_{k}", a.shape, F32, kind="ExternalInput").ap() for k, a in arrays.items()}
    out = {k: nc.dram_tensor(f"out_{k}", s, F32, kind="ExternalOutput").ap() for k, s in OUTS.items()}
    trunk(nc, d, out)
    got = run_bass_kernel_spmd(nc, [{f"in_{k}": a for k, a in arrays.items()}], core_ids=[0]).results[0]
    g = {k: np.asarray(got[f"out_{k}"]) for k in OUTS}
    conv = lambda a: a.transpose(3, 4, 2, 0, 1).reshape(SEQS + 1, 3, -1)
    dn_conv = conv(g["dn_conv"])
    rows = np.concatenate([g["ssm_conv_x"].reshape(1024, SEQS + 1, 3),
                           g["ssm_conv_bc"].transpose(2, 0, 1, 3, 4).reshape(512, SEQS + 1, 3)])
    ssm_conv = rows.transpose(1, 2, 0)
    ssm_p = g["ssm_p"].transpose(0, 2, 1).reshape(1, 1, SSM_HEADS, HALF, P)
    ssm_s = g["ssm_s"].transpose(2, 0, 3, 1).reshape(1, SEQS, SSM_HEADS, HALF, P)
    y = g["y"].reshape(D_MODEL, T).T
    mem_k = g["mem_k"].transpose(2, 1, 0).reshape(1, 1, MEM, MEM_HEADS, -1)
    mem_v = g["mem_v"].transpose(1, 0, 2).reshape(1, 1, MEM, MEM_HEADS, -1)
    return (y[:SEQ].reshape(1, SEQ, D_MODEL), y[SEQ:].reshape(SEQS, STEPS, D_MODEL),
            dn_conv[None, 0:1], g["dn_p"][None, None], ssm_conv[None, 0:1], ssm_p, mem_k, mem_v,
            dn_conv[None, 1:], g["dn_s"].transpose(2, 0, 1, 3)[None], ssm_conv[None, 1:], ssm_s)
```
